# Optimizing a Trainium2 kernel written in Bass

```python
import math
import jax, jax.numpy as jnp
from jax import lax
import numpy as np

D_MODEL = 1024
BATCH = 1
SEQ = 512
DEPTH = 1
DEC_BATCH = 8
DEC_SEQ = 8
PAST_LEN = 2048
PAGE_SIZE = 128

SSM_WIDTH = D_MODEL // 2
SSM_CH = 16
SSM_GROUPS = SSM_WIDTH // SSM_CH
SSM_STATE = 64
ATTN_WIDTH = D_MODEL - SSM_WIDTH
HEAD_DIM = 64
N_HEADS = ATTN_WIDTH // HEAD_DIM
N_KV = 2
GQA_REP = N_HEADS // N_KV
KV_WIDTH = N_KV * HEAD_DIM
ROPE_DIM = HEAD_DIM // 4
ROPE_THETA = 500000.0
CMP_STRIDE = 16
CMP_BLOCK = 2 * CMP_STRIDE
CMP_HIDDEN = 2 * HEAD_DIM
SEL_BLOCK = 64
SEL_TOPN = 16
CMP_PER_SEL = SEL_BLOCK // CMP_STRIDE
FORCE_BONUS = 1000.0
WINDOW = 512
Q_BLOCK = 128
PLE_DIM = 256
PEER_HEADS = 8
PEER_KEYS = 128
PEER_EXPERTS = PEER_KEYS * PEER_KEYS
PEER_QDIM = 256
PEER_TOPK = 16
PEER_CHUNK = 256
RMS_EPS = 1e-6
NEG = -1e30
IN_COLS = SSM_WIDTH + ATTN_WIDTH + 6 * KV_WIDTH + 3 * N_HEADS

kernel_name = 'hymba_s5_nsa_peer_decode_step'

def rms_norm(x, g):
    xf = x.astype(jnp.float32)
    y = xf * lax.rsqrt(jnp.mean(xf * xf, axis=-1, keepdims=True) + RMS_EPS)
    return (y * g.astype(jnp.float32)).astype(x.dtype)

def rope_partial(x, pos):
    half = ROPE_DIM // 2
    inv = jnp.power(ROPE_THETA, -jnp.arange(half, dtype=jnp.float32) / half)
    ang = pos.astype(jnp.float32)[:, None] * inv[None, :]
    cos = jnp.cos(ang)[:, None, :]
    sin = jnp.sin(ang)[:, None, :]
    xf = x.astype(jnp.float32)
    x1 = xf[..., :half]
    x2 = xf[..., half:ROPE_DIM]
    out = jnp.concatenate([x1 * cos - x2 * sin, x2 * cos + x1 * sin, xf[..., ROPE_DIM:]], axis=-1)
    return out.astype(x.dtype)

def masked_softmax(s, mask):
    s = jnp.where(mask, s.astype(jnp.float32), NEG)
    p = jax.nn.softmax(s, axis=-1)
    return jnp.where(mask, p, 0.0)

def project(x, pos, lw):
    bsz, t, _ = x.shape
    z = rms_norm(x, lw['g_mix']) @ lw['w_in']
    cuts = np.cumsum([SSM_WIDTH, ATTN_WIDTH] + [KV_WIDTH] * 6).tolist()
    u, q, kc, vc, ks, vs, kw, vw, gl = jnp.split(z, cuts, axis=-1)
    heads = lambda a: a.reshape(bsz, t, N_KV, HEAD_DIM)
    q = rope_partial(rms_norm(q.reshape(bsz, t, N_HEADS, HEAD_DIM), lw['g_q']), pos)
    ks = rope_partial(rms_norm(heads(ks), lw['g_k_sel']), pos)
    kw = rope_partial(rms_norm(heads(kw), lw['g_k_win']), pos)
    gates = jax.nn.sigmoid(gl.astype(jnp.float32)).reshape(bsz, t, 3, N_HEADS)
    return u, q, heads(kc), heads(vc), ks, heads(vs), kw, heads(vw), gates

def _complex_affine_combine(e1, e2):
    a1r, a1i, b1r, b1i = e1
    a2r, a2i, b2r, b2i = e2
    return (a1r * a2r - a1i * a2i, a1r * a2i + a1i * a2r,
            a2r * b1r - a2i * b1i + b2r, a2r * b1i + a2i * b1r + b2i)

def ssm_mixer(u, s0_re, s0_im, lw):
    f32 = jnp.float32
    bsz, t, _ = u.shape
    a_re = lw['ssm_a_re'].astype(f32)
    a_im = lw['ssm_a_im'].astype(f32)
    dt = jnp.exp(lw['ssm_log_dt'].astype(f32))[:, None]
    mag = jnp.exp(a_re * dt)
    ab_re = mag * jnp.cos(a_im * dt)
    ab_im = mag * jnp.sin(a_im * dt)
    den = a_re * a_re + a_im * a_im
    f_re = ((ab_re - 1.0) * a_re + ab_im * a_im) / den
    f_im = (ab_im * a_re - (ab_re - 1.0) * a_im) / den
    b_re = lw['ssm_b_re'].astype(f32)
    b_im = lw['ssm_b_im'].astype(f32)
    bb_re = f_re[..., None] * b_re - f_im[..., None] * b_im
    bb_im = f_re[..., None] * b_im + f_im[..., None] * b_re
    uf = u.astype(f32).reshape(bsz, t, SSM_GROUPS, SSM_CH)
    bu_re = jnp.einsum('btgc,gpc->btgp', uf, bb_re)
    bu_im = jnp.einsum('btgc,gpc->btgp', uf, bb_im)
    a_t_re = jnp.broadcast_to(ab_re, bu_re.shape)
    a_t_im = jnp.broadcast_to(ab_im, bu_im.shape)
    pr, pim, xr, xi = lax.associative_scan(_complex_affine_combine, (a_t_re, a_t_im, bu_re, bu_im), axis=1)
    s0r = s0_re.astype(f32)[:, None]
    s0i = s0_im.astype(f32)[:, None]
    xr = xr + pr * s0r - pim * s0i
    xi = xi + pr * s0i + pim * s0r
    c_re = lw['ssm_c_re'].astype(f32)
    c_im = lw['ssm_c_im'].astype(f32)
    y = jnp.einsum('btgp,gcp->btgc', xr, c_re) - jnp.einsum('btgp,gcp->btgc', xi, c_im)
    y = y.reshape(bsz, t, SSM_WIDTH) + lw['ssm_d'].astype(f32) * u.astype(f32)
    zg = jax.nn.gelu(y)
    out = zg * jax.nn.sigmoid(zg @ lw['ssm_w_glu'].astype(f32) + lw['ssm_b_glu'].astype(f32))
    return out.astype(u.dtype), xr[:, -1], xi[:, -1]

def pad_rows(rows, mult):
    extra = (-rows.shape[1]) % mult
    return jnp.pad(rows, ((0, 0), (0, extra), (0, 0), (0, 0)))

def compress_rows(rows, pe, w1, w2):
    bsz, t, g, hd = rows.shape
    nblk = t // CMP_STRIDE
    half = CMP_STRIDE * hd
    blk = rows.reshape(bsz, nblk, CMP_STRIDE, g, hd).transpose(0, 1, 3, 2, 4).reshape(bsz, nblk, g, half)
    h = jnp.einsum('bngk,skh->bngsh', blk, w1.reshape(2, half, CMP_HIDDEN))
    pre = h[:, :-1, :, 0] + h[:, 1:, :, 1] + pe.reshape(-1) @ w1
    return jax.nn.gelu(pre) @ w2

def compressed_kv(k_rows, v_rows, lw):
    kc = compress_rows(k_rows, lw['cmp_pe_k'], lw['cmp_w1_k'], lw['cmp_w2_k'])
    vc = compress_rows(v_rows, lw['cmp_pe_v'], lw['cmp_w1_v'], lw['cmp_w2_v'])
    kc_end = jnp.arange(kc.shape[1], dtype=jnp.int32) * CMP_STRIDE + (CMP_BLOCK - 1)
    kc = rope_partial(rms_norm(kc, lw['g_k_cmp']), kc_end)
    return kc, vc, kc_end

def sel_blocks(rows):
    bsz, t, g, hd = rows.shape
    return rows.reshape(bsz, t // SEL_BLOCK, SEL_BLOCK, g, hd).transpose(0, 3, 1, 2, 4)

def nsa_block(q, qpos, gates, kc, vc, kc_end, ks_bt, vs_bt, kw, vw, kwpos, n_sel):
    f32 = jnp.float32
    bsz, nq = q.shape[0], q.shape[1]
    qg = q.astype(f32).reshape(bsz, nq, N_KV, GQA_REP, HEAD_DIM) * (HEAD_DIM ** -0.5)
    s = jnp.einsum('bqgrd,bcgd->bqgrc', qg, kc.astype(f32))
    cmask = (kc_end[None, :] <= qpos[:, None])[None, :, None, None, :]
    p_cmp = masked_softmax(s, cmask)
    o_cmp = jnp.einsum('bqgrc,bcgd->bqgrd', p_cmp, vc.astype(f32))
    ns = ks_bt.shape[2]
    nc = kc.shape[1]
    imp = jnp.pad(p_cmp.sum(axis=3), ((0, 0), (0, 0), (0, 0), (0, ns * CMP_PER_SEL - nc)))
    imp = imp.reshape(bsz, nq, N_KV, ns, CMP_PER_SEL).sum(axis=-1)
    blk = jnp.arange(ns, dtype=jnp.int32)[None, :]
    cur = (qpos // SEL_BLOCK)[:, None]
    forced = ((blk == 0) | (blk == cur) | (blk == cur - 1))[None, :, None, :]
    future = (blk > cur)[None, :, None, :]
    score = jnp.where(future, NEG, jnp.where(forced, imp + FORCE_BONUS, imp))
    _, sel = lax.top_k(score, n_sel)
    b_ix = jnp.arange(bsz)[:, None, None, None]
    g_ix = jnp.arange(N_KV)[None, None, :, None]
    k_sel = ks_bt[b_ix, g_ix, sel].reshape(bsz, nq, N_KV, n_sel * SEL_BLOCK, HEAD_DIM).astype(f32)
    v_sel = vs_bt[b_ix, g_ix, sel].reshape(bsz, nq, N_KV, n_sel * SEL_BLOCK, HEAD_DIM).astype(f32)
    kpos = (sel[..., None] * SEL_BLOCK + jnp.arange(SEL_BLOCK, dtype=jnp.int32)).reshape(bsz, nq, N_KV, n_sel * SEL_BLOCK)
    smask = (kpos <= qpos[None, :, None, None])[:, :, :, None, :]
    s = jnp.einsum('bqgrd,bqgkd->bqgrk', qg, k_sel)
    o_sel = jnp.einsum('bqgrk,bqgkd->bqgrd', masked_softmax(s, smask), v_sel)
    s = jnp.einsum('bqgrd,bkgd->bqgrk', qg, kw.astype(f32))
    diff = qpos[:, None] - kwpos[None, :]
    wmask = ((diff >= 0) & (diff < WINDOW) & (kwpos[None, :] >= 0))[None, :, None, None, :]
    o_win = jnp.einsum('bqgrk,bkgd->bqgrd', masked_softmax(s, wmask), vw.astype(f32))
    g = gates.reshape(bsz, nq, 3, N_KV, GQA_REP)[..., None]
    o = g[:, :, 0] * o_cmp + g[:, :, 1] * o_sel + g[:, :, 2] * o_win
    return o.reshape(bsz, nq, ATTN_WIDTH)

def attention_prompt(q, kc_rows, vc_rows, ks, vs, kw, vw, gates, lw):
    bsz, t = q.shape[0], q.shape[1]
    kc, vc, kc_end = compressed_kv(pad_rows(kc_rows, SEL_BLOCK), pad_rows(vc_rows, SEL_BLOCK), lw)
    ks_bt = sel_blocks(pad_rows(ks, SEL_BLOCK))
    vs_bt = sel_blocks(pad_rows(vs, SEL_BLOCK))
    n_sel = min(SEL_TOPN, ks_bt.shape[2])
    nb = t // Q_BLOCK
    wb = WINDOW // Q_BLOCK

    def band(rows):
        p = jnp.pad(rows, ((0, 0), (WINDOW, 0), (0, 0), (0, 0))).reshape(bsz, nb + wb, Q_BLOCK, N_KV, HEAD_DIM)
        return jnp.concatenate([p[:, m:m + nb] for m in range(wb + 1)], axis=2).swapaxes(0, 1)

    kwpos = (jnp.arange(nb, dtype=jnp.int32) * Q_BLOCK - WINDOW)[:, None] + jnp.arange((wb + 1) * Q_BLOCK, dtype=jnp.int32)[None, :]
    blocks = lambda a: a.reshape(bsz, nb, Q_BLOCK, *a.shape[2:]).swapaxes(0, 1)
    qpos = jnp.arange(t, dtype=jnp.int32).reshape(nb, Q_BLOCK)

    def step(args):
        qb, qp, gb, kwb, vwb, kp = args
        return nsa_block(qb, qp, gb, kc, vc, kc_end, ks_bt, vs_bt, kwb, vwb, kp, n_sel)

    o = lax.map(step, (blocks(q), qpos, blocks(gates), band(kw), band(vw), kwpos))
    return o.swapaxes(0, 1).reshape(bsz, t, ATTN_WIDTH)

def gather_pages(pool, page_table):
    g = pool[page_table]
    return g.reshape(g.shape[0], g.shape[1] * g.shape[2], *pool.shape[2:])

def attention_sample(q, pos, kc_new, vc_new, ks_new, vs_new, kw_new, vw_new, gates,
                     past_kc, past_vc, past_ks, past_vs, buf_kw, buf_vw, past_len, lw):
    cat = lambda a, b: jnp.concatenate([a, b.astype(a.dtype)], axis=1)
    kc, vc, kc_end = compressed_kv(pad_rows(cat(past_kc, kc_new), SEL_BLOCK), pad_rows(cat(past_vc, vc_new), SEL_BLOCK), lw)
    ks_bt = sel_blocks(pad_rows(cat(past_ks, ks_new), SEL_BLOCK))
    vs_bt = sel_blocks(pad_rows(cat(past_vs, vs_new), SEL_BLOCK))
    n_sel = min(SEL_TOPN, ks_bt.shape[2])
    kw_all = cat(buf_kw, kw_new)
    vw_all = cat(buf_vw, vw_new)
    nbuf = buf_kw.shape[1]
    kwpos = past_len - nbuf + jnp.arange(kw_all.shape[1], dtype=jnp.int32)
    o = nsa_block(q, pos, gates, kc, vc, kc_end, ks_bt, vs_bt, kw_all, vw_all, kwpos, n_sel)
    keep = min(WINDOW, kw_all.shape[1])
    return o, kw_all[:, -keep:], vw_all[:, -keep:]

def peer_ffn(x, w_q, subkeys, u_tab, v_tab):
    shp = x.shape
    xt = x.reshape(-1, D_MODEL)
    n = xt.shape[0]
    q = (xt @ w_q).astype(jnp.float32).reshape(n, PEER_HEADS, 2, PEER_QDIM // 2)
    s = jnp.einsum('nhsd,hskd->nhsk', q, subkeys.astype(jnp.float32))
    v_top, i_top = lax.top_k(s, PEER_TOPK)
    cand = (v_top[:, :, 0, :, None] + v_top[:, :, 1, None, :]).reshape(n, PEER_HEADS, PEER_TOPK * PEER_TOPK)
    cand_idx = (i_top[:, :, 0, :, None] * PEER_KEYS + i_top[:, :, 1, None, :]).reshape(n, PEER_HEADS, PEER_TOPK * PEER_TOPK)
    vals, cpos = lax.top_k(cand, PEER_TOPK)
    eidx = jnp.take_along_axis(cand_idx, cpos, axis=-1)
    gate = jax.nn.softmax(vals, axis=-1)
    c = min(PEER_CHUNK, n)
    npad = (-n) % c
    xp = jnp.pad(xt, ((0, npad), (0, 0))).reshape(-1, c, D_MODEL)
    ep = jnp.pad(eidx, ((0, npad), (0, 0), (0, 0))).reshape(-1, c, PEER_HEADS, PEER_TOPK)
    gp = jnp.pad(gate, ((0, npad), (0, 0), (0, 0))).reshape(-1, c, PEER_HEADS, PEER_TOPK)

    def chunk(args):
        xc, ec, gc = args
        act = jax.nn.gelu(jnp.einsum('chkd,cd->chk', u_tab[ec].astype(jnp.float32), xc.astype(jnp.float32)))
        return jnp.einsum('chk,chkd->cd', gc * act, v_tab[ec].astype(jnp.float32))

    out = lax.map(chunk, (xp, ep, gp)).reshape(-1, D_MODEL)[:n]
    return out.reshape(shp).astype(x.dtype)

def finish_layer(x, ssm_y, attn_o, ple, lw):
    mixed = jnp.concatenate([rms_norm(ssm_y.astype(x.dtype), lw['g_out_ssm']),
                             rms_norm(attn_o.astype(x.dtype), lw['g_out_attn'])], axis=-1) @ lw['w_out']
    h = x + mixed
    h = h + peer_ffn(rms_norm(h, lw['g_ffn']), lw['peer_w_q'], lw['peer_subkeys'], lw['peer_u'], lw['peer_v'])
    gate = jax.nn.sigmoid(rms_norm(h, lw['g_ple']) @ lw['ple_w_gate'])
    return h + gate * (ple @ lw['ple_w_proj'])

def setup_inputs(seed: int = 0) -> dict:
    key = jax.random.key(seed)
    ks = jax.random.split(key, 64)
    ctr = [0]

    def nk():
        k = ks[ctr[0]]
        ctr[0] += 1
        return k

    def nrm(shape, scale):
        return scale * jax.random.normal(nk(), shape, jnp.float32)

    def gain(shape):
        return 1.0 + 0.05 * jax.random.normal(nk(), shape, jnp.float32)

    n_pages = PAST_LEN // PAGE_SIZE
    n_used = DEC_BATCH * n_pages
    n_pool = n_used + n_used // 4
    win_buf = min(WINDOW, PAST_LEN)
    pool_shape = (DEPTH, n_pool, PAGE_SIZE, N_KV, HEAD_DIM)
    win_shape = (DEPTH, DEC_BATCH, win_buf, N_KV, HEAD_DIM)
    st_shape = (DEPTH, DEC_BATCH, SSM_GROUPS, SSM_STATE)
    inp = {}
    inp['x_prompt'] = nrm((BATCH, SEQ, D_MODEL), 1.0)
    inp['x_sample'] = nrm((DEC_BATCH, DEC_SEQ, D_MODEL), 1.0)
    inp['cache_k_cmp'] = nrm(pool_shape, 1.0)
    inp['cache_v_cmp'] = nrm(pool_shape, 1.0)
    inp['cache_k_sel'] = nrm(pool_shape, 1.0)
    inp['cache_v_sel'] = nrm(pool_shape, 1.0)
    inp['cache_k_win'] = nrm(win_shape, 1.0)
    inp['cache_v_win'] = nrm(win_shape, 1.0)
    inp['state_ssm_re'] = nrm(st_shape, 0.1)
    inp['state_ssm_im'] = nrm(st_shape, 0.1)
    inp['page_table'] = jax.random.permutation(nk(), n_pool)[:n_used].reshape(DEC_BATCH, n_pages).astype(jnp.int32)
    inp['p_prompt'] = nrm((DEPTH, BATCH, SEQ, PLE_DIM), 1.0)
    inp['p_sample'] = nrm((DEPTH, DEC_BATCH, DEC_SEQ, PLE_DIM), 1.0)
    L = DEPTH
    inp['g_mix'] = gain((L, D_MODEL))
    inp['w_in'] = nrm((L, D_MODEL, IN_COLS), D_MODEL ** -0.5)
    inp['ssm_a_re'] = -0.5 + nrm((L, SSM_GROUPS, SSM_STATE), 0.01)
    inp['ssm_a_im'] = jnp.pi * jnp.arange(SSM_STATE, dtype=jnp.float32) + nrm((L, SSM_GROUPS, SSM_STATE), 0.01)
    inp['ssm_log_dt'] = jax.random.uniform(nk(), (L, SSM_GROUPS), jnp.float32, math.log(0.001), math.log(0.1))
    inp['ssm_b_re'] = nrm((L, SSM_GROUPS, SSM_STATE, SSM_CH), (0.5 / SSM_CH) ** 0.5)
    inp['ssm_b_im'] = nrm((L, SSM_GROUPS, SSM_STATE, SSM_CH), (0.5 / SSM_CH) ** 0.5)
    inp['ssm_c_re'] = nrm((L, SSM_GROUPS, SSM_CH, SSM_STATE), (0.5 / SSM_STATE) ** 0.5)
    inp['ssm_c_im'] = nrm((L, SSM_GROUPS, SSM_CH, SSM_STATE), (0.5 / SSM_STATE) ** 0.5)
    inp['ssm_d'] = nrm((L, SSM_WIDTH), 1.0)
    inp['ssm_w_glu'] = nrm((L, SSM_WIDTH, SSM_WIDTH), SSM_WIDTH ** -0.5)
    inp['ssm_b_glu'] = nrm((L, SSM_WIDTH), 0.01)
    inp['g_q'] = gain((L, HEAD_DIM))
    inp['g_k_cmp'] = gain((L, HEAD_DIM))
    inp['g_k_sel'] = gain((L, HEAD_DIM))
    inp['g_k_win'] = gain((L, HEAD_DIM))
    inp['cmp_pe_k'] = nrm((L, CMP_BLOCK, HEAD_DIM), 0.1)
    inp['cmp_w1_k'] = nrm((L, CMP_BLOCK * HEAD_DIM, CMP_HIDDEN), (CMP_BLOCK * HEAD_DIM) ** -0.5)
    inp['cmp_w2_k'] = nrm((L, CMP_HIDDEN, HEAD_DIM), CMP_HIDDEN ** -0.5)
    inp['cmp_pe_v'] = nrm((L, CMP_BLOCK, HEAD_DIM), 0.1)
    inp['cmp_w1_v'] = nrm((L, CMP_BLOCK * HEAD_DIM, CMP_HIDDEN), (CMP_BLOCK * HEAD_DIM) ** -0.5)
    inp['cmp_w2_v'] = nrm((L, CMP_HIDDEN, HEAD_DIM), CMP_HIDDEN ** -0.5)
    inp['g_out_ssm'] = gain((L, SSM_WIDTH))
    inp['g_out_attn'] = gain((L, ATTN_WIDTH))
    inp['w_out'] = nrm((L, D_MODEL, D_MODEL), D_MODEL ** -0.5)
    inp['g_ffn'] = gain((L, D_MODEL))
    inp['peer_w_q'] = nrm((L, D_MODEL, PEER_HEADS * PEER_QDIM), D_MODEL ** -0.5)
    inp['peer_subkeys'] = nrm((L, PEER_HEADS, 2, PEER_KEYS, PEER_QDIM // 2), (PEER_QDIM // 2) ** -0.5)
    inp['peer_u'] = nrm((L, PEER_EXPERTS, D_MODEL), D_MODEL ** -0.5)
    inp['peer_v'] = nrm((L, PEER_EXPERTS, D_MODEL), PEER_HEADS ** -0.5)
    inp['g_ple'] = gain((L, D_MODEL))
    inp['ple_w_gate'] = nrm((L, D_MODEL, D_MODEL), D_MODEL ** -0.5)
    inp['ple_w_proj'] = nrm((L, PLE_DIM, D_MODEL), PLE_DIM ** -0.5)
    return inp

def reference(x_prompt, x_sample, cache_k_cmp, cache_v_cmp, cache_k_sel, cache_v_sel, cache_k_win, cache_v_win,
              state_ssm_re, state_ssm_im, page_table, p_prompt, p_sample,
              g_mix, w_in, ssm_a_re, ssm_a_im, ssm_log_dt, ssm_b_re, ssm_b_im, ssm_c_re, ssm_c_im, ssm_d,
              ssm_w_glu, ssm_b_glu, g_q, g_k_cmp, g_k_sel, g_k_win, cmp_pe_k, cmp_w1_k, cmp_w2_k,
              cmp_pe_v, cmp_w1_v, cmp_w2_v, g_out_ssm, g_out_attn, w_out, g_ffn, peer_w_q, peer_subkeys,
              peer_u, peer_v, g_ple, ple_w_gate, ple_w_proj):
    bp, tp, _ = x_prompt.shape
    bs, ts, _ = x_sample.shape
    past_len = page_table.shape[1] * cache_k_cmp.shape[2]
    pos_p = jnp.arange(tp, dtype=jnp.int32)
    pos_s = past_len + jnp.arange(ts, dtype=jnp.int32)
    hp, hs = x_prompt, x_sample
    prompt_states, sample_states = [], []
    for i in range(DEPTH):
        lw = dict(g_mix=g_mix[i], w_in=w_in[i], ssm_a_re=ssm_a_re[i], ssm_a_im=ssm_a_im[i],
                  ssm_log_dt=ssm_log_dt[i], ssm_b_re=ssm_b_re[i], ssm_b_im=ssm_b_im[i],
                  ssm_c_re=ssm_c_re[i], ssm_c_im=ssm_c_im[i], ssm_d=ssm_d[i], ssm_w_glu=ssm_w_glu[i],
                  ssm_b_glu=ssm_b_glu[i], g_q=g_q[i], g_k_cmp=g_k_cmp[i], g_k_sel=g_k_sel[i],
                  g_k_win=g_k_win[i], cmp_pe_k=cmp_pe_k[i], cmp_w1_k=cmp_w1_k[i], cmp_w2_k=cmp_w2_k[i],
                  cmp_pe_v=cmp_pe_v[i], cmp_w1_v=cmp_w1_v[i], cmp_w2_v=cmp_w2_v[i],
                  g_out_ssm=g_out_ssm[i], g_out_attn=g_out_attn[i], w_out=w_out[i], g_ffn=g_ffn[i],
                  peer_w_q=peer_w_q[i], peer_subkeys=peer_subkeys[i], peer_u=peer_u[i], peer_v=peer_v[i],
                  g_ple=g_ple[i], ple_w_gate=ple_w_gate[i], ple_w_proj=ple_w_proj[i])
        u, q, kc, vc, ks, vs, kw, vw, gates = project(hp, pos_p, lw)
        zeros = jnp.zeros((bp, SSM_GROUPS, SSM_STATE), jnp.float32)
        ssm_y, sre, sim = ssm_mixer(u, zeros, zeros, lw)
        attn = attention_prompt(q, kc, vc, ks, vs, kw, vw, gates, lw)
        keep = min(WINDOW, tp)
        prompt_states.append((kc, vc, ks, vs, kw[:, -keep:], vw[:, -keep:], sre, sim))
        hp = finish_layer(hp, ssm_y, attn, p_prompt[i], lw)
        u, q, kc, vc, ks, vs, kw, vw, gates = project(hs, pos_s, lw)
        ssm_y, sre, sim = ssm_mixer(u, state_ssm_re[i], state_ssm_im[i], lw)
        attn, kw_buf, vw_buf = attention_sample(
            q, pos_s, kc, vc, ks, vs, kw, vw, gates,
            gather_pages(cache_k_cmp[i], page_table), gather_pages(cache_v_cmp[i], page_table),
            gather_pages(cache_k_sel[i], page_table), gather_pages(cache_v_sel[i], page_table),
            cache_k_win[i], cache_v_win[i], past_len, lw)
        sample_states.append((kc, vc, ks, vs, kw_buf, vw_buf, sre, sim))
        hs = finish_layer(hs, ssm_y, attn, p_sample[i], lw)
    (p_kc, p_vc, p_ks, p_vs, p_kw, p_vw, p_sre, p_sim) = [jnp.stack(a) for a in zip(*prompt_states)]
    (s_kc, s_vc, s_ks, s_vs, s_kw, s_vw, s_sre, s_sim) = [jnp.stack(a) for a in zip(*sample_states)]
    return (hp, hs, p_kc, p_vc, p_ks, p_vs, p_kw, p_vw, p_sre, p_sim,
            s_kc, s_vc, s_ks, s_vs, s_kw, s_vw, s_sre, s_sim)


_drawn_inputs = setup_inputs


def setup_inputs(seed=0):
    import zlib

    import numpy as np

    out = dict(_drawn_inputs(seed))
    spreads = {}
    factors = {'ssm_a_re': 3.927, 'ssm_b_glu': 7.44, 'g_q': 2.883, 'g_k_cmp': 3.39, 'g_ple': 8.0}
    for name, (base, spread) in spreads.items():
        noise = np.random.default_rng([zlib.crc32(name.encode()), seed]).standard_normal(out[name].shape)
        drawn = base * np.exp(spread * noise) if base else spread * noise
        out[name] = __import__('jax').numpy.asarray(drawn.astype(out[name].dtype))
    for name, factor in factors.items():
        out[name] = (out[name] * factor).astype(out[name].dtype)
    return out
```

```python
from contextlib import ExitStack
import math

import numpy as np
import concourse.bass as bass
from concourse import mybir
from concourse.alu_op_type import AluOpType as ALU

F32 = mybir.dt.float32
I32 = mybir.dt.int32
U32 = mybir.dt.uint32
ACT = mybir.ActivationFunctionType
AX = mybir.AxisListType

P = 128
D = 1024
KD = D // P
T_PROMPT = 512
SEQS = 8
STEPS = 8
T_SAMPLE = SEQS * STEPS
T = T_PROMPT + T_SAMPLE
HALF = T // 2
TILES = 5
TILE_ROWS = [128, 128, 128, 128, 64]
CHUNKS = T // 8
PROMPT_CHUNKS = T_PROMPT // 8
GROUPS = 32
CH = 16
HD = 64
REP = 4
PAST = 2048
PAGES = 16
POOL = 160
NBLK = 128
EPS = 1e-6
NEG = -1e30
GONE = -3e38
SCALE = HD ** -0.5
KEYS = 128
PH = 8
TOPK = 16
WCOLS = 1816
ZQ, ZB, ZC = 512, 1024, 1536


class Shared:
    pass


class Chain:

    def __init__(self, eng, sem):
        self.eng, self.sem, self.n = eng, sem, 0

    def go(self, ins):
        self.n += 1
        ins.then_inc(self.sem, 1)

    def wait(self):
        self.eng.wait_ge(self.sem, self.n)

    def __call__(self, ins):
        self.go(ins)
        self.wait()


def project_stage(nc, k):
    with ExitStack() as ctx:
        sb = lambda n, s, d=F32: ctx.enter_context(nc.sbuf_tensor(n, s, d))
        sem = k.sem
        w = sb("w_in_sb", [P, KD, WCOLS])
        sq = sb("x_squared", [P, KD, T])
        norm = sb("a_T", [P, KD, T])
        rinv = sb("x_rinv", [P, T])
        gmix = sb("g_mix_sb", [P, KD])
        g12 = sb("head_gains", [P, 768])
        rope = sb("rope_sb", [P, TILES, 3, 8])
        hsq = sb("head_squares", [P, 2, 768])
        ms = sb("head_ms", [P, 2, 3, 12])
        ra = sb("rope_a", [P, 12, 16])
        rb = sb("rope_b", [P, 12, 16])
        um = k.mixT[:, 0:4].rearrange("p i (j c) -> p i j c", j=8)
        pz = ctx.enter_context(nc.psum_tensor("pz", [P, 2, 3, 512], F32))
        pu = ctx.enter_context(nc.psum_tensor("pu", [P, 2, 512], F32))
        ld_x, ld_w, ld_c = sem("ld_x"), sem("ld_w"), sem("ld_c")
        squared, ssq_done, ms_ready, rinv_ready = sem("x_sq"), sem("ssq"), sem("x_ms"), sem("x_ri")
        a_ready, u_done, u_free, z_done, z_free = sem("a_rdy"), sem("u_done"), sem("u_free"), sem("z_done"), sem("z_free")
        hsq_ready, hms_ready, hri_ready, rows_ready = sem("hsq"), sem("hms"), sem("hri"), sem("rows")
        tr_done, tr_free, tr_dve = sem("tr_done"), sem("tr_free"), sem("tr_dve")
        kv_copied, ustore, ust, v_ch, const_ready = sem("kv_cp"), sem("u_st"), sem("u_sto"), sem("p_vch"), sem("const")
        gate_ready = sem("gate_rdy")
        block = ctx.enter_context(nc.Block())

        @block.sync
        def _(sp):
            for h in range(2):
                sp.dma_start(k.hT[:, 4 * h:4 * h + 4, :], k.d["xT"][:, 4 * h:4 * h + 4, :]).then_inc(ld_x, 16)
            sp.dma_start(gmix[:], k.d["g_mix"]).then_inc(ld_c, 16)
            sp.dma_start(g12[:], k.d["g_heads"].to_broadcast([P, 768])).then_inc(ld_c, 16)
            sp.dma_start(rope[:], k.d["rope"]).then_inc(ld_c, 16)
            for i in range(KD):
                sp.dma_start(w[:, i, :], k.d["w_in"][:, i, :]).then_inc(ld_w, 16)
            for i in range(4):
                sp.wait_ge(u_free, 2 * i + 2)
                sp.dma_start(k.d["u_scr"][P * i:P * i + P], um[:, i]).then_inc(ust, 16)
            sp.wait_ge(ust, 64)
            for j in range(8):
                sp.dma_start(k.U[16 * j:16 * j + 16],
                             k.d["u_scr"][:, j, :].rearrange("(g c) n -> c g n", c=CH)).then_inc(k.u_loaded, 16)
            sp.wait_ge(rows_ready, TILES)
            sp.wait_ge(kv_copied, TILES)
            for n, src in enumerate((k.kv[:, :, 0:128], k.kv[:, :, 128:256], k.qk[:, :, 512:640],
                                     k.kv[:, :, 256:384], k.qk[:, :, 640:768], k.kv[:, :, 384:512])):
                sp.dma_start(k.o["rows_p"][n].rearrange("(a p) f -> p a f", p=P), src[:, 0:4]).then_inc(k.stored, 16)
                if n < 4:
                    sp.dma_start(k.o["rows_s"][n], src[0:64, 4]).then_inc(k.stored, 16)
                else:
                    for s in range(SEQS):
                        sp.dma_start(k.o["rows_s"][n][s, 504:512, :], src[8 * s:8 * s + 8, 4]).then_inc(k.stored, 16)
            k.n_stored += 16 * (6 + 4 + 16)
            for n in range(2):
                sp.dma_start(k.o["rows_s"][4 + n][:, 0:504, :], k.d["win_rows"][n][:, 8:512, :]).then_inc(k.stored, 16)
            k.n_stored += 32

        @block.gpsimd
        def _(pool):
            pool.memset(k.ident[:], 0.0).then_inc(const_ready, 1)
            pool.memset(k.ones[:], 1.0).then_inc(const_ready, 1)
            pool.wait_ge(const_ready, 2)
            pool.affine_select(out=k.ident[:], in_=k.ident[:], compare_op=ALU.not_equal, fill=1.0, base=0,
                               pattern=[[-1, P]], channel_multiplier=1).then_inc(const_ready, 1)

        @block.scalar
        def _(act):
            for i in range(KD):
                if i % 4 == 0:
                    act.wait_ge(ld_x, 32)
                nc.scalar.activation(sq[:, i, :], k.hT[:, i, :], ACT.Square).then_inc(squared, 1)
            act.wait_ge(ms_ready, 1)
            nc.scalar.activation(rinv[:], rinv[:], ACT.Sqrt).then_inc(rinv_ready, 1)
            for i in range(4):
                for h in range(2):
                    act.wait_ge(u_done, 2 * i + h + 1)
                    nc.scalar.activation(um[:, i, :, 36 * h:36 * h + 36],
                                         pu[:, h, 0:HALF].rearrange("p (c j) -> p j c", j=8),
                                         ACT.Copy).then_inc(u_free, 1)
            for t in range(TILES):
                m, b = TILE_ROWS[t], t % 2
                act.wait_ge(z_done, t + 1)
                if t >= 2:
                    act.wait_ge(rows_ready, t - 1)
                nc.scalar.activation(hsq[0:m, b, 0:512], pz[0:m, b, 0, :], ACT.Square).then_inc(hsq_ready, 1)
                nc.scalar.activation(hsq[0:m, b, 512:640], pz[0:m, b, 1, 256:384], ACT.Square).then_inc(hsq_ready, 1)
                nc.scalar.activation(hsq[0:m, b, 640:768], pz[0:m, b, 2, 0:128], ACT.Square).then_inc(hsq_ready, 1)
                nc.scalar.activation(k.kv[0:m, t, 0:256], pz[0:m, b, 1, 0:256], ACT.Copy)
                nc.scalar.activation(k.kv[0:m, t, 256:384], pz[0:m, b, 1, 384:512], ACT.Copy)
                nc.scalar.activation(k.kv[0:m, t, 384:512], pz[0:m, b, 2, 128:256], ACT.Copy)
                nc.scalar.activation(k.gates[0:m, t, :], pz[0:m, b, 2, 256:280], ACT.Copy).then_inc(kv_copied, 1)
                act.wait_ge(hms_ready, t + 1)
                nc.scalar.activation(ms[0:m, b, 2, :], ms[0:m, b, 1, :], ACT.Sqrt).then_inc(hri_ready, 1)
            for t in range(TILES):
                m, b = TILE_ROWS[t], t % 2
                act.wait_ge(tr_done, t + 1)
                for i in range(4):
                    nc.scalar.activation(k.qT[:, i, P * t:P * t + m], pz[:, b, 0, P * i:P * i + m], ACT.Copy)
                nc.scalar.activation(k.ksT[:, P * t:P * t + m], pz[:, b, 1, 0:m], ACT.Copy)
                nc.scalar.activation(k.kwT[:, P * t:P * t + m], pz[:, b, 1, 128:128 + m], ACT.Copy).then_inc(tr_free, 1)
            act.wait_ge(kv_copied, TILES)
            for t in (0, 4):
                m, e = (128, 4) if t == 0 else (64, 5)
                nc.scalar.activation(k.gates[0:m, t:e, :], k.gates[0:m, t:e, :], ACT.Exp, scale=-1.0).then_inc(gate_ready, 1)

        @block.vector
        def _(dve):
            v = Chain(dve, v_ch)
            dve.wait_ge(ssq_done, 1)
            for h in range(2):
                v.go(nc.vector.tensor_scalar(rinv[:, HALF * h:HALF * h + HALF], pu[:, h, 0:HALF], 1.0 / D, EPS,
                                             ALU.mult, ALU.add))
            v.wait()
            nc.vector.reciprocal(rinv[:], rinv[:]).then_inc(ms_ready, 1)
            dve.wait_ge(rinv_ready, 1)
            dve.wait_ge(ld_c, 48)
            dve.wait_ge(ld_x, 32)
            for i in range(KD):
                nc.vector.scalar_tensor_tensor(out=norm[:, i, :], in0=k.hT[:, i, :], scalar=gmix[:, i:i + 1],
                                               in1=rinv[:], op0=ALU.mult, op1=ALU.mult).then_inc(a_ready, 1)
            for t in range(TILES):
                m, b = TILE_ROWS[t], t % 2
                dve.wait_ge(hsq_ready, 3 * t + 3)
                v(nc.vector.tensor_reduce(ms[0:m, b, 0, :], hsq[0:m, b, :].rearrange("p (h d) -> p h d", d=HD),
                                          AX.X, ALU.add))
                v(nc.vector.tensor_scalar(ms[0:m, b, 0, :], ms[0:m, b, 0, :], 1.0 / HD, EPS, ALU.mult, ALU.add))
                nc.vector.reciprocal(ms[0:m, b, 1, :], ms[0:m, b, 0, :]).then_inc(hms_ready, 1)
                dve.wait_ge(hri_ready, t + 1)
                qk3 = k.qk[0:m, t, :].rearrange("p (h d) -> p h d", d=HD)
                for lo, hi, src in ((0, 8, pz[0:m, b, 0, :]), (8, 10, pz[0:m, b, 1, 256:384]),
                                    (10, 12, pz[0:m, b, 2, 0:128])):
                    v.go(nc.vector.tensor_tensor(qk3[:, lo:hi], src.rearrange("p (h d) -> p h d", d=HD),
                                                 ms[0:m, b, 2, lo:hi].unsqueeze(2).to_broadcast([m, hi - lo, HD]),
                                                 ALU.mult))
                dve.wait_ge(kv_copied, t + 1)
                v.wait()
                v(nc.vector.tensor_tensor(k.qk[0:m, t, :], k.qk[0:m, t, :], g12[0:m, :], ALU.mult))
                cos, sin, nsin = (rope[0:m, t, i, :].unsqueeze(1).to_broadcast([m, 12, 8]) for i in range(3))
                x1, x2 = qk3[:, :, 0:8], qk3[:, :, 8:16]
                v.go(nc.vector.tensor_tensor(ra[0:m, :, 0:8], x1, cos, ALU.mult))
                v.go(nc.vector.tensor_tensor(ra[0:m, :, 8:16], x2, cos, ALU.mult))
                v.go(nc.vector.tensor_tensor(rb[0:m, :, 0:8], x2, nsin, ALU.mult))
                v(nc.vector.tensor_tensor(rb[0:m, :, 8:16], x1, sin, ALU.mult))
                nc.vector.tensor_tensor(qk3[:, :, 0:16], ra[0:m], rb[0:m], ALU.add).then_inc(rows_ready, 1)
            for t in range(4):
                dve.wait_ge(tr_done, t + 1)
                for kv in range(2):
                    for g in range(2):
                        for r2 in range(2):
                            src = pz[g * 64:g * 64 + 64, t % 2, 2, P * kv:P * kv + P]
                            last = nc.vector.tensor_copy(k.cmp_prompt[r2 * 64:r2 * 64 + 64, t, kv, g],
                                                         src.rearrange("p (b i r) -> p r i b", r=2, i=8)[:, r2])
                last.then_inc(tr_dve, 1)
            for n, (t, e, m) in enumerate(((0, 4, 128), (4, 5, 64))):
                dve.wait_ge(gate_ready, n + 1)
                v(nc.vector.tensor_scalar(k.gates[0:m, t:e, :], k.gates[0:m, t:e, :], 1.0, None, ALU.add))
                v(nc.vector.reciprocal(k.gates[0:m, t:e, :], k.gates[0:m, t:e, :]))

        @block.tensor
        def _(pe):
            pe.wait_ge(const_ready, 3)
            for i in range(KD):
                pe.wait_ge(squared, i + 1)
                for h in range(2):
                    mm = nc.tensor.matmul(pu[:, h, 0:HALF], k.ones[:], sq[:, i, HALF * h:HALF * h + HALF],
                                          start=(i == 0), stop=(i == KD - 1))
            mm.then_inc(ssq_done, 1)
            pe.wait_ge(a_ready, KD)
            pe.wait_ge(ld_w, 16 * KD)
            for c in range(4):
                for h in range(2):
                    if c:
                        pe.wait_ge(u_free, 2 * (c - 1) + h + 1)
                    for i in range(KD):
                        mm = nc.tensor.matmul(pu[:, h, 0:HALF], w[:, i, P * c:P * c + P],
                                              norm[:, i, HALF * h:HALF * h + HALF], start=(i == 0), stop=(i == KD - 1))
                    mm.then_inc(u_done, 1)
            for t in range(TILES):
                m, b = TILE_ROWS[t], t % 2
                if t >= 2:
                    pe.wait_ge(rows_ready, t - 1)
                    pe.wait_ge(kv_copied, t - 1)
                for bank, (lo, n) in enumerate(((ZQ, 512), (ZB, 512), (ZC, 280))):
                    for i in range(KD):
                        mm = nc.tensor.matmul(pz[0:m, b, bank, 0:n], norm[:, i, P * t:P * t + m], w[:, i, lo:lo + n],
                                              start=(i == 0), stop=(i == KD - 1))
                mm.then_inc(z_done, 1)
            for t in range(TILES):
                m, b = TILE_ROWS[t], t % 2
                pe.wait_ge(rows_ready, TILES)
                pe.wait_ge(kv_copied, TILES)
                if t >= 2:
                    pe.wait_ge(tr_free, t - 1)
                    pe.wait_ge(tr_dve, t - 1)
                for i in range(6):
                    dst = pz[:, b, 0, P * i:P * i + m] if i < 4 else pz[:, b, 1, P * (i - 4):P * (i - 4) + m]
                    mm = nc.tensor.transpose(dst, k.qk[0:m, t, P * i:P * i + P], k.ident[0:m, 0:m])
                if t < 4:
                    for kv in range(2):
                        mm = nc.tensor.transpose(pz[:, b, 2, P * kv:P * kv + P],
                                                 k.kv[:, t, P * kv:P * kv + P], k.ident[:])
                mm.then_inc(tr_done, 1)


VCH = [(0, 7), (7, 14), (14, 21), (21, 28), (28, 32)]
MAGIC = 12582912.0
TWO_PI_PARTS = (6.28125, 0.0019350051879882812, 3.019915981956753e-07)


def ssm_stage(nc, k):
    with ExitStack() as ctx:
        sb = lambda n, s, d=F32: ctx.enter_context(nc.sbuf_tensor(n, s, d))
        sem = k.sem
        are, aim, ldt = sb("a_re", [P, GROUPS]), sb("a_im", [P, GROUPS]), sb("log_dt", [P, GROUPS])
        bc4 = sb("b_and_c", [P, 4, GROUPS, CH])
        b1, b2, c1, c2 = (bc4[:, n] for n in range(4))
        s0, s0x = sb("s0", [P, GROUPS, SEQS]), sb("s0_swapped", [P, GROUPS, SEQS])
        dT, sg, perm = sb("dT", [CH, GROUPS]), sb("sigma", [P, 1]), sb("swap_matrix", [P, P])
        tmp = sb("s_tmp", [P, 8, GROUPS])
        x1, x2 = sb("x1", [P, GROUPS, CH]), sb("x2", [P, GROUPS, CH])
        pr, pi = sb("pow_re", [P, 9, GROUPS]), sb("pow_im", [P, 9, GROUPS])
        rr, ri = sb("rot8_re", [P, 7, GROUPS]), sb("rot8_im", [P, 7, GROUPS])
        m8 = sb("mag8", [P, GROUPS])
        A = sb("state_in", [P, GROUPS, 8, CH])
        cp = sb("state_out_w", [P, GROUPS, 9, CH])
        big1 = sb("s_big1", [P, 32 * GROUPS])
        ms_ = sb("state_in_T", [P, GROUPS, P])
        zw = sb("z_and_w", [P, 4, GROUPS, 64])
        hz = zw[0:CH].rearrange("p a g n -> p (a g n)").rearrange("p (g z n) -> p g z n", g=GROUPS, z=2)
        tz = A[:].rearrange("p g j c -> p g (j c)")
        vs = k.cmp[:].rearrange("p a s n -> p (a s n)").rearrange("p (g c) -> p g c", c=CHUNKS)
        z, w = zw[:, 0], zw[:, 1]
        rc, rs = (zw[:, n].rearrange("p g c -> p (g c)").rearrange("p (c g) -> p c g", c=64) for n in (2, 3))
        ss = ms_[:].rearrange("p g n -> p (g n)")[:, 0:GROUPS * CHUNKS].rearrange("p (g c) -> p g c", c=CHUNKS)
        st = sb("s_final", [P, GROUPS, 9])
        ps = ctx.enter_context(nc.psum_tensor("ps_ssm", [P, 8, 512], F32))
        ld, ld0, vch, dt_r, mag_in, mag_r, ang_r, trig_r = (sem(n) for n in (
            "s_ld", "s_ld0", "s_vch", "s_dt", "s_magin", "s_mag", "s_ang", "s_trig"))
        a_ready, tr_done, tr_free, h_done, h_free = (sem(n) for n in ("s_A", "s_tr", "s_trf", "s_h", "s_hf"))
        hz_zero, hz_ready, tz_ld, v_done, v_free, sw_done, sw_free = (sem(n) for n in (
            "s_hz0", "s_hz", "s_tz", "s_v", "s_vf", "s_sw", "s_swf"))
        scan_ready, sb_done, sb_free, ss_ready, st_ready, y_done, y_free, y_st = (sem(n) for n in (
            "s_scan", "s_sb", "s_sbf", "s_ss", "s_stf", "s_y", "s_yf", "s_yst"))
        y = vs
        block = ctx.enter_context(nc.Block())

        @block.sync
        def _(sp):
            for dst, src in ((are[:], k.d["a_re"]), (aim[:], k.d["a_im"]), (sg[:], k.d["sigma"]), (b1, k.d["b1"]), (b2, k.d["b2"]),
                             (c1, k.d["c1"]), (c2, k.d["c2"]), (dT[:], k.d["dT"]), (perm[:], k.d["swap"])):
                sp.dma_start(dst, src).then_inc(ld, 16)
            sp.dma_start(ldt[:], k.d["log_dt"].to_broadcast([P, GROUPS])).then_inc(ld0, 16)
            sp.dma_start(s0[:], k.d["s0"]).then_inc(ld, 16)
            sp.dma_start(s0x[:], k.d["s0x"]).then_inc(ld, 16)
            sp.wait_ge(hz_ready, 1)
            for j in range(8):
                zeros = (8 - j) * CH
                sp.dma_start(tz[CH * j:CH * j + CH],
                             hz.rearrange("c g z n -> c g (z n)")[:, :, zeros:zeros + P]).then_inc(tz_ld, 16)
            sp.wait_ge(st_ready, 2)
            sp.dma_start(k.o["ssm_state"], st[:]).then_inc(k.stored, 16)
            k.n_stored += 16
            sp.wait_ge(y_free, 5)
            for j in range(8):
                sp.dma_start(k.d["y_scr"][:, j, :].rearrange("(g c) n -> c g n", c=CH), y[CH * j:CH * j + CH]).then_inc(y_st, 16)
            sp.wait_ge(y_st, 128)
            sp.dma_start(k.yT[:], k.d["y_scr"].rearrange("(i p) j n -> p i (j n)", p=P)).then_inc(k.y_loaded, 16)

        @block.gpsimd
        def _(pool):
            pool.memset(hz, 0.0).then_inc(hz_zero, 1)

        @block.scalar
        def _(act):
            act.wait_ge(ld0, 16)
            nc.scalar.activation(ldt[:], ldt[:], ACT.Exp).then_inc(dt_r, 1)
            act.wait_ge(mag_in, 1)
            nc.scalar.activation(tmp[:, 0], tmp[:, 0], ACT.Exp).then_inc(mag_r, 1)
            act.wait_ge(ang_r, 1)
            nc.scalar.activation(tmp[:, 2], tmp[:, 2], ACT.Sin).then_inc(trig_r, 1)
            nc.scalar.activation(tmp[:, 3], tmp[:, 3], ACT.Sin).then_inc(trig_r, 1)
            for i in range(8):
                act.wait_ge(tr_done, i + 1)
                nc.scalar.activation(ms_[:, 4 * i:4 * i + 4, :], ps[:, i % 3, :].rearrange("p (g n) -> p g n", g=4),
                                     ACT.Copy).then_inc(tr_free, 1)
            act.wait_ge(hz_zero, 1)
            for i in range(8):
                act.wait_ge(h_done, i + 1)
                nc.scalar.activation(hz[:, 4 * i:4 * i + 4, 1, :], ps[0:CH, 3 + i % 3, :].rearrange("p (g n) -> p g n", g=4),
                                     ACT.Copy).then_inc(h_free, 1)
            for q, (g0, g1) in enumerate(VCH):
                act.wait_ge(v_done, q + 1)
                nc.scalar.activation(vs[:, g0:g1, :], ps[:, q, 0:(g1 - g0) * CHUNKS].rearrange("p (g c) -> p g c", c=CHUNKS),
                                     ACT.Copy).then_inc(v_free, 1)
            act.wait_ge(st_ready, 2)
            for q, (g0, g1) in enumerate(VCH):
                act.wait_ge(y_done, q + 1)
                nc.scalar.activation(y[:, g0:g1, :], ps[:, q, 0:(g1 - g0) * CHUNKS].rearrange("p (g c) -> p g c", c=CHUNKS),
                                     ACT.Copy).then_inc(y_free, 1)

        @block.vector
        def _(dve):
            v = Chain(dve, vch)
            tt = lambda o, a, b, op: nc.vector.tensor_tensor(o, a, b, op)
            scratch = big1[:]

            def cmul(outr, outi, ar, ai, br, bi, shape):
                t1 = scratch[:, 0:shape[0] * shape[1]].rearrange("p (a b) -> p a b", a=shape[0])
                v.go(tt(outr, ar, br, ALU.mult))
                v.go(tt(outi, ar, bi, ALU.mult))
                v(tt(t1, ai, bi, ALU.mult))
                v(tt(outr, outr, t1, ALU.subtract))
                v(tt(t1, ai, br, ALU.mult))
                v(tt(outi, outi, t1, ALU.add))

            dve.wait_ge(ld, 16 * 11)
            dve.wait_ge(dt_r, 1)
            v(nc.vector.tensor_scalar(aim[:], aim[:], sg[:, 0:1], None, ALU.mult))
            tt(tmp[:, 0], are[:], ldt[:], ALU.mult).then_inc(mag_in, 1)
            v(tt(tmp[:, 1], aim[:], ldt[:], ALU.mult))
            v(nc.vector.tensor_scalar(tmp[:, 4], tmp[:, 1], 1.0 / (2 * math.pi), MAGIC, ALU.mult, ALU.add))
            v(nc.vector.tensor_scalar(tmp[:, 4], tmp[:, 4], -MAGIC, None, ALU.add))
            for part in TWO_PI_PARTS:
                v(nc.vector.scalar_tensor_tensor(out=tmp[:, 1], in0=tmp[:, 4], scalar=-part, in1=tmp[:, 1],
                                                 op0=ALU.mult, op1=ALU.add))
            v(nc.vector.tensor_scalar(tmp[:, 2], tmp[:, 1], 3.1415925, -3.1415925, ALU.min, ALU.max))
            v(nc.vector.tensor_scalar(tmp[:, 3], tmp[:, 2], -1.0, None, ALU.mult))
            v(tt(tmp[:, 3], tmp[:, 3], tmp[:, 2], ALU.max))
            nc.vector.tensor_scalar(tmp[:, 3], tmp[:, 3], -1.0, math.pi / 2, ALU.mult, ALU.add).then_inc(ang_r, 1)
            dve.wait_ge(mag_r, 1)
            dve.wait_ge(trig_r, 2)
            mag, sn, cs = tmp[:, 0], tmp[:, 2], tmp[:, 3]
            v.go(nc.vector.memset(pr[:, 0], 1.0))
            v.go(nc.vector.memset(pi[:, 0], 0.0))
            v.go(tt(pr[:, 1], mag, cs, ALU.mult))
            v(tt(pi[:, 1], mag, sn, ALU.mult))
            v.go(nc.vector.tensor_scalar(tmp[:, 4], pr[:, 1], -1.0, None, ALU.add))
            v.go(tt(tmp[:, 5], are[:], are[:], ALU.mult))
            v(tt(tmp[:, 6], aim[:], aim[:], ALU.mult))
            v(tt(tmp[:, 5], tmp[:, 5], tmp[:, 6], ALU.add))
            v(nc.vector.reciprocal(tmp[:, 5], tmp[:, 5]))
            v.go(tt(tmp[:, 6], tmp[:, 4], are[:], ALU.mult))
            v(tt(tmp[:, 7], pi[:, 1], aim[:], ALU.mult))
            v(tt(tmp[:, 6], tmp[:, 6], tmp[:, 7], ALU.add))
            v.go(tt(tmp[:, 7], pi[:, 1], are[:], ALU.mult))
            v(tt(tmp[:, 4], tmp[:, 4], aim[:], ALU.mult))
            v(tt(tmp[:, 7], tmp[:, 7], tmp[:, 4], ALU.subtract))
            v.go(tt(tmp[:, 6], tmp[:, 6], tmp[:, 5], ALU.mult))
            v(tt(tmp[:, 7], tmp[:, 7], tmp[:, 5], ALU.mult))
            bc = lambda a: a.unsqueeze(2).to_broadcast([P, GROUPS, CH])
            sc3 = scratch[:, 0:GROUPS * CH].rearrange("p (g c) -> p g c", c=CH)
            v.go(tt(x1[:], b1, bc(tmp[:, 6]), ALU.mult))
            v.go(tt(x2[:], b2, bc(tmp[:, 6]), ALU.mult))
            v(tt(sc3, b2, bc(tmp[:, 7]), ALU.mult))
            v(tt(x1[:], x1[:], sc3, ALU.subtract))
            v(tt(sc3, b1, bc(tmp[:, 7]), ALU.mult))
            v(tt(x2[:], x2[:], sc3, ALU.add))
            for n in (1, 2, 4):
                one = lambda t: t[:, n:n + 1, :].to_broadcast([P, n, GROUPS])
                cmul(pr[:, n + 1:2 * n + 1], pi[:, n + 1:2 * n + 1], pr[:, 1:n + 1], pi[:, 1:n + 1], one(pr), one(pi), (n, GROUPS))
            for j in range(8):
                v.go(tt(A[:, :, j, :], x1[:], bc(pr[:, 7 - j]), ALU.mult))
                v(tt(sc3, x2[:], bc(pi[:, 7 - j]), ALU.mult))
                last = tt(A[:, :, j, :], A[:, :, j, :], sc3, ALU.subtract)
                if j < 7:
                    v(last)
                else:
                    last.then_inc(a_ready, 1)
            dve.wait_ge(a_ready, 1)
            for l in range(9):
                v.go(tt(cp[:, :, l, :], c1, bc(pr[:, l]), ALU.mult))
                v(tt(sc3, c2, bc(pi[:, l]), ALU.mult))
                v(tt(cp[:, :, l, :], cp[:, :, l, :], sc3, ALU.subtract))
            nc.vector.tensor_scalar(cp[:].rearrange("p g l c -> p (g l c)"), cp[:].rearrange("p g l c -> p (g l c)"),
                                    sg[:, 0:1], None, ALU.mult).then_inc(a_ready, 1)
            v.go(nc.vector.tensor_copy(rr[:, 3:4, :], tmp[:, 3:4, :]))
            v(nc.vector.tensor_copy(ri[:, 3:4, :], tmp[:, 2:3, :]))
            src = 3
            for dst in (4, 5, 0):
                cmul(rr[:, dst:dst + 1], ri[:, dst:dst + 1], rr[:, src:src + 1], ri[:, src:src + 1],
                     rr[:, src:src + 1], ri[:, src:src + 1], (1, GROUPS))
                src = dst
            v(tt(m8[:], mag, mag, ALU.mult))
            v(tt(m8[:], m8[:], m8[:], ALU.mult))
            v(tt(m8[:], m8[:], m8[:], ALU.mult))
            dve.wait_ge(h_free, 8)
            dI = scratch[0:CH, 0:GROUPS * CH].rearrange("p (g c) -> p g c", c=CH)
            v(tt(dI, k.ident[0:CH, 0:CH].unsqueeze(1).to_broadcast([CH, GROUPS, CH]),
                 dT[:].unsqueeze(2).to_broadcast([CH, GROUPS, CH]), ALU.mult))
            tt(hz[:, :, 1, 0:CH], hz[:, :, 1, 0:CH], dI, ALU.add).then_inc(hz_ready, 1)
            gc = lambda t, g0, g1: t[:, :, g0:g1].rearrange("p c g -> p g c")
            dve.wait_ge(tz_ld, 128)
            v.go(nc.vector.memset(rc[:, 0], 1.0))
            v(nc.vector.memset(rs[:, 0], 0.0))
            for i in range(6):
                n = 1 << i
                step = lambda t: t[:, i:i + 1, :].to_broadcast([P, n, GROUPS])
                cmul(rc[:, n:2 * n], rs[:, n:2 * n], rc[:, 0:n], rs[:, 0:n], step(rr), step(ri), (n, GROUPS))
                if i < 5:
                    cmul(rr[:, i + 1:i + 2], ri[:, i + 1:i + 2], rr[:, i:i + 1], ri[:, i:i + 1],
                         rr[:, i:i + 1], ri[:, i:i + 1], (1, GROUPS))
            for q, (g0, g1) in enumerate(VCH):
                n = g1 - g0
                t3 = scratch[:, 0:n * 64].rearrange("p (g c) -> p g c", c=64)
                dve.wait_ge(v_free, q + 1)
                v.go(tt(z[:, g0:g1, :], vs[:, g0:g1, 0:64], gc(rc, g0, g1), ALU.mult))
                dve.wait_ge(sw_done, q + 1)
                last = tt(t3, ps[:, (5 + q) % 8, 0:n * CHUNKS].rearrange("p (g c) -> p g c", c=CHUNKS)[:, :, 0:64],
                          gc(rs, g0, g1), ALU.mult)
                last.then_inc(sw_free, 1)
                dve.wait_ge(sw_free, q + 1)
                v.wait()
                v(tt(z[:, g0:g1, :], z[:, g0:g1, :], t3, ALU.add))
            mg = bc4[:].rearrange("p a g c -> p (a g c)").rearrange("p (g c) -> p g c", c=64)
            v(nc.vector.tensor_copy(mg, m8[:].unsqueeze(2).to_broadcast([P, GROUPS, 64])))
            v(nc.vector.memset(mg[:, :, 0:1], 0.0))
            nc.vector.tensor_tensor_scan(w.rearrange("p g c -> p (g c)"), mg.rearrange("p g c -> p (g c)"),
                                         z.rearrange("p g c -> p (g c)"), 0.0, ALU.mult, ALU.add).then_inc(scan_ready, 1)
            dve.wait_ge(scan_ready, 1)
            v.go(nc.vector.memset(ss[:, :, 0:1], 0.0))
            v.go(nc.vector.tensor_copy(ss[:, :, 64:72], s0[:]))
            for q, (g0, g1) in enumerate(VCH):
                n = g1 - g0
                t3 = scratch[:, 0:n * 64].rearrange("p (g c) -> p g c", c=64)
                dve.wait_ge(sb_done, q + 1)
                v.go(tt(z[:, g0:g1, :], w[:, g0:g1, :], gc(rc, g0, g1), ALU.mult))
                tt(t3, ps[:, (5 + q) % 8, 0:n * 64].rearrange("p (g c) -> p g c", c=64), gc(rs, g0, g1),
                   ALU.mult).then_inc(sb_free, 1)
                dve.wait_ge(sb_free, q + 1)
                v.wait()
                v.go(tt(ss[:, g0:g1, 1:64], z[:, g0:g1, 0:63], t3[:, :, 0:63], ALU.subtract))
                v(tt(st[:, g0:g1, 0:1], z[:, g0:g1, 63:64], t3[:, :, 63:64], ALU.subtract))
            nc.vector.memset(tmp[:, 1], 0.0).then_inc(ss_ready, 1)
            b8 = lambda t: t[:, 8, :].unsqueeze(2).to_broadcast([P, GROUPS, SEQS])
            se = st[:, :, 1:9]
            v.go(tt(se, s0[:], b8(pr), ALU.mult))
            v(tt(s0x[:], s0x[:], b8(pi), ALU.mult))
            v(tt(se, se, s0x[:], ALU.subtract))
            tt(se, se, vs[:, :, 64:72], ALU.add).then_inc(st_ready, 2)

        @block.tensor
        def _(pe):
            pe.wait_ge(a_ready, 1)
            for i in range(8):
                if i >= 3:
                    pe.wait_ge(tr_free, i - 2)
                for g in range(4 * i, 4 * i + 4):
                    mm = nc.tensor.transpose(ps[:, i % 3, P * (g % 4):P * (g % 4) + P],
                                             A[:, g].rearrange("p j c -> p (j c)"), k.ident[:])
                mm.then_inc(tr_done, 1)
            pe.wait_ge(a_ready, 2)
            for i in range(8):
                if i >= 3:
                    pe.wait_ge(h_free, i - 2)
                for g in range(4 * i, 4 * i + 4):
                    mm = nc.tensor.matmul(ps[0:CH, 3 + i % 3, P * (g % 4):P * (g % 4) + P], x1[:, g, :],
                                          cp[:, g, 0:8, :].rearrange("p l c -> p (l c)"), start=True, stop=True)
                mm.then_inc(h_done, 1)
            pe.wait_ge(k.u_loaded, 128)
            pe.wait_ge(tr_free, 8)
            pe.wait_ge(h_free, 8)
            for q, (g0, g1) in enumerate(VCH):
                for g in range(g0, g1):
                    mm = nc.tensor.matmul(ps[:, q, CHUNKS * (g - g0):CHUNKS * (g - g0 + 1)], ms_[:, g, :], k.U[:, g, :],
                                          start=True, stop=True)
                mm.then_inc(v_done, 1)
            for q, (g0, g1) in enumerate(VCH):
                pe.wait_ge(v_free, q + 1)
                mm = nc.tensor.matmul(ps[:, (5 + q) % 8, 0:(g1 - g0) * CHUNKS], perm[:],
                                      vs[:, g0:g1, :].rearrange("p g c -> p (g c)"), start=True, stop=True)
                mm.then_inc(sw_done, 1)
            pe.wait_ge(scan_ready, 1)
            for q, (g0, g1) in enumerate(VCH):
                pe.wait_ge(sw_free, q + 1)
                nc.tensor.matmul(ps[:, (5 + q) % 8, 0:(g1 - g0) * 64], perm[:],
                                 w[:, g0:g1, :].rearrange("p g c -> p (g c)"), start=True, stop=True).then_inc(sb_done, 1)
            pe.wait_ge(tz_ld, 128)
            pe.wait_ge(ss_ready, 1)
            pe.wait_ge(sb_free, 5)
            for q, (g0, g1) in enumerate(VCH):
                for g in range(g0, g1):
                    dst = ps[:, q, CHUNKS * (g - g0):CHUNKS * (g - g0 + 1)]
                    nc.tensor.matmul(dst, tz[:, g, :], k.U[:, g, :], start=True, stop=False)
                    mm = nc.tensor.matmul(dst, cp[:, g, 1:9, :].rearrange("p l c -> p (l c)"), ss[:, g, :],
                                          start=False, stop=True)
                mm.then_inc(y_done, 1)


def glu_stage(nc, k):
    with ExitStack() as ctx:
        sb = lambda n, s, d=F32: ctx.enter_context(nc.sbuf_tensor(n, s, d))
        sem = k.sem
        w = sb("w_glu_sb", [P, 4, 512])
        bg, gs = sb("b_glu_sb", [P, 4]), sb("g_out_ssm_sb", [P, 4])
        sig, sq = sb("glu_sig", [P, 4, T]), sb("glu_sq", [P, 4, T])
        rinv = sb("glu_rinv", [P, T])
        ps = ctx.enter_context(nc.psum_tensor("ps_glu", [P, 4, 2, 512], F32))
        ld, ld_sm, zg, mmd, sigd, outd, sqd, ssqd, msd, rid, vch = (sem(n) for n in (
            "g_ld", "g_ls", "g_zg", "g_mm", "g_sig", "g_out", "g_sq", "g_ssq", "g_ms", "g_ri", "g_vch"))
        block = ctx.enter_context(nc.Block())

        @block.sync
        def _(sp):
            sp.dma_start(w[:], k.d["w_glu"]).then_inc(ld, 16)
            sp.dma_start(bg[:], k.d["b_glu"]).then_inc(ld_sm, 16)
            sp.dma_start(gs[:], k.d["g_out_ssm"]).then_inc(ld_sm, 16)

        @block.scalar
        def _(act):
            act.wait_ge(k.y_loaded, 16)
            for i in range(4):
                nc.scalar.activation(k.yT[:, i], k.yT[:, i], ACT.Gelu_apprx_tanh).then_inc(zg, 1)
            act.wait_ge(ld_sm, 32)
            for c in range(4):
                act.wait_ge(mmd, c + 1)
                for h in range(2):
                    nc.scalar.activation(sig[:, c, HALF * h:HALF * h + HALF], ps[:, c, h, 0:HALF], ACT.Sigmoid,
                                         bias=bg[:, c:c + 1]).then_inc(sigd, 1)
            for c in range(4):
                act.wait_ge(outd, c + 1)
                nc.scalar.activation(sq[:, c], sig[:, c], ACT.Square).then_inc(sqd, 1)
            act.wait_ge(msd, 1)
            nc.scalar.activation(rinv[:], rinv[:], ACT.Sqrt).then_inc(rid, 1)

        @block.vector
        def _(dve):
            v = Chain(dve, vch)
            for c in range(4):
                dve.wait_ge(sigd, 2 * c + 2)
                nc.vector.tensor_tensor(sig[:, c], sig[:, c], k.yT[:, c], ALU.mult).then_inc(outd, 1)
            dve.wait_ge(ssqd, 1)
            for h in range(2):
                v.go(nc.vector.tensor_scalar(rinv[:, HALF * h:HALF * h + HALF], ps[:, h, 0, 0:HALF], 1.0 / 512, EPS,
                                             ALU.mult, ALU.add))
            v.wait()
            nc.vector.reciprocal(rinv[:], rinv[:]).then_inc(msd, 1)
            dve.wait_ge(rid, 1)
            for c in range(4):
                tok = lambda a: a.rearrange("p (j c) -> p j c", j=8)
                v.go(nc.vector.scalar_tensor_tensor(out=k.mixT[:, c].rearrange("p (c j) -> p j c", j=8),
                                                    in0=tok(sig[:, c]), scalar=gs[:, c:c + 1], in1=tok(rinv[:]),
                                                    op0=ALU.mult, op1=ALU.mult))

        @block.tensor
        def _(pe):
            pe.wait_ge(ld, 16)
            pe.wait_ge(zg, 4)
            for c in range(4):
                for h in range(2):
                    for i in range(4):
                        mm = nc.tensor.matmul(ps[:, c, h, 0:HALF], w[:, i, P * c:P * c + P],
                                              k.yT[:, i, HALF * h:HALF * h + HALF], start=(i == 0), stop=(i == 3))
                mm.then_inc(mmd, 1)
            pe.wait_ge(sigd, 8)
            for c in range(4):
                pe.wait_ge(sqd, c + 1)
                for h in range(2):
                    mm = nc.tensor.matmul(ps[:, h, 0, 0:HALF], k.ones[:], sq[:, c, HALF * h:HALF * h + HALF],
                                          start=(c == 0), stop=(c == 3))
            mm.then_inc(ssqd, 1)


PAIRS = SEQS // 2


def gather_pages(sp, nc, dst, pool, pages, first, loaded):
    with sp.Fori(0, 8) as i:
        at = [sp.value_load(pages[0:1, bass.ds(4 * i + (first + n), 1)], min_val=0, max_val=POOL - 1) for n in range(4)]
        for n in range(4):
            sp.dma_start(dst[:, bass.ds(4 * i + n, 1), :].rearrange("p o f -> p (o f)"),
                         pool[bass.ds(at[n], 1)].rearrange("o p f -> (o p) f")).then_inc(loaded, 16)


def compress_stage(nc, k):
    with ExitStack() as ctx:
        sb = lambda n, s, d=F32: ctx.enter_context(nc.sbuf_tensor(n, s, d))
        sem = k.sem
        pages = [sb(f"cmp_pages{n}", [P, 32, 256]) for n in range(2)]
        w1, w2, pe_ = sb("cmp_w1", [P, 2, 16, P]), sb("cmp_w2", [P, 2, HD]), sb("cmp_pe", [P, 2, 16])
        bias = sb("cmp_bias", [P, 2])
        shifted, pre = sb("cmp_h1", [P, 2, 256]), sb("cmp_pre", [P, 2, 256])
        rope, gain = sb("cmp_rope", [P, 3, 8]), sb("cmp_gain", [P, HD])
        kr, sq = sb("cmp_k_rows", [P, 9, P]), sb("cmp_sq", [P, 9, P])
        ms = sb("cmp_ms", [P, 2, 18])
        ra, rb = sb("cmp_ra", [P, 18, 16]), sb("cmp_rb", [P, 18, 16])
        ph = ctx.enter_context(nc.psum_tensor("ph", [P, 2, 512], F32))
        po = ctx.enter_context(nc.psum_tensor("po_cmp", [P, 2, 512], F32))
        pb = ctx.enter_context(nc.psum_tensor("pb_cmp", [P, 512], F32))
        pt = ctx.enter_context(nc.psum_tensor("pt_cmp", [P, 3, 512], F32))
        ld, got, bias_done, bias_ready = (sem(n) for n in ("c_ld", "c_got0", "c_bias", "c_biasr"))
        got = [got, sem("c_got1")]
        h_done, h1_copied, pre_ready, act_ready, out_done, out_free = (sem(n) for n in (
            "c_h", "c_h1", "c_pre", "c_act", "c_out", "c_outf"))
        zeroed, vch, sqd, msd, rid, kready, trd = (sem(n) for n in (
            "c_zero", "c_vch", "c_sq", "c_ms", "c_ri", "c_k", "c_tr"))
        units = [(p, kv, g) for p in range(PAIRS + 1) for kv in range(2) for g in range(2)]
        block = ctx.enter_context(nc.Block())

        @block.sync
        def _(sp):
            sp.dma_start(w1[:], k.d["cmp_w1"]).then_inc(ld, 16)
            for dst, src in ((w2, k.d["cmp_w2"]), (pe_, k.d["cmp_pe"]), (rope, k.d["cmp_rope"])):
                sp.dma_start(dst[:], src).then_inc(ld, 16)
            sp.dma_start(gain[:], k.d["g_k_cmp"].to_broadcast([P, HD])).then_inc(ld, 16)
            sp.dma_start(k.pages[:], k.d["page_table"]).then_inc(k.pages_ld, 16)
            sp.wait_ge(k.pages_ld, 16)
            for p in range(PAIRS):
                if p >= 2:
                    sp.wait_ge(h_done, 4 * (p - 1))
                gather_pages(sp, nc, pages[p % 2], k.d["cmp_pool"], k.pages, 32 * p, got[p % 2])

        @block.gpsimd
        def _(pool):
            pool.memset(kr[:], 0.0).then_inc(zeroed, 1)
            pool.memset(k.vcmp, 0.0).then_inc(zeroed, 1)

        @block.scalar
        def _(act):
            act.wait_ge(bias_done, 1)
            nc.scalar.activation(bias[:], pb[:, 0:2], ACT.Copy).then_inc(bias_ready, 1)
            act.wait_ge(bias_ready, 1)
            act.wait_ge(zeroed, 2)
            for u, (p, kv, g) in enumerate(units):
                n, seqs = (256, 2) if p < PAIRS else (32, 1)
                act.wait_ge(h_done, u + 1)
                nc.scalar.activation(shifted[:, u % 2, 0:n], ph[:, u % 2, 256:256 + n], ACT.Copy).then_inc(h1_copied, 1)
                act.wait_ge(pre_ready, u + 1)
                nc.scalar.activation(pre[:, u % 2, 0:n], pre[:, u % 2, 0:n], ACT.Gelu_apprx_tanh,
                                     bias=bias[:, kv:kv + 1]).then_inc(act_ready, 1)
                if u % 4 == 3:
                    act.wait_ge(out_done, u + 1)
                    rows, s0 = (127, 2 * p) if p < PAIRS else (31, 8)
                    src = po[0:rows, p % 2, 0:256 * seqs].rearrange("p (s kv f) -> p s kv f", s=seqs, kv=2)
                    nc.scalar.activation(kr[0:rows, s0:s0 + seqs, :], src[:, :, 0], ACT.Copy)
                    nc.scalar.activation(k.vcmp[0:rows, s0:s0 + seqs, :], src[:, :, 1], ACT.Copy).then_inc(out_free, 1)
            act.wait_ge(out_free, PAIRS + 1)
            nc.scalar.activation(sq[:], kr[:], ACT.Square).then_inc(sqd, 1)
            act.wait_ge(msd, 1)
            nc.scalar.activation(ms[:, 1], ms[:, 0], ACT.Sqrt).then_inc(rid, 1)
            for q in range(3):
                act.wait_ge(trd, q + 1)
                nc.scalar.activation(k.kcT[:, 3 * q:3 * q + 3, :], pt[:, q, 0:384].rearrange("p (s n) -> p s n", s=3), ACT.Copy)

        @block.vector
        def _(dve):
            v = Chain(dve, vch)
            dve.wait_ge(ld, 80)
            for u, (p, kv, g) in enumerate(units):
                n, seqs = (128, 2) if p < PAIRS else (32, 1)
                dve.wait_ge(h1_copied, u + 1)
                if u >= 2:
                    dve.wait_ge(out_done, u - 1)
                if u < 2:
                    v(nc.vector.memset(pre[:, u % 2, :], 0.0))
                sq3 = lambda a: a.rearrange("p (s n) -> p s n", s=seqs)
                nc.vector.tensor_tensor(sq3(pre[:, u % 2, 0:n * seqs])[:, :, 0:n - 1],
                                        sq3(ph[:, u % 2, 0:n * seqs])[:, :, 0:n - 1],
                                        sq3(shifted[:, u % 2, 0:n * seqs])[:, :, 1:n], ALU.add).then_inc(pre_ready, 1)
            dve.wait_ge(sqd, 1)
            v(nc.vector.tensor_reduce(ms[:, 0], sq[:].rearrange("p s (g d) -> p (s g) d", g=2), AX.X, ALU.add))
            v(nc.vector.tensor_scalar(ms[:, 0], ms[:, 0], 1.0 / HD, EPS, ALU.mult, ALU.add))
            nc.vector.reciprocal(ms[:, 0], ms[:, 0]).then_inc(msd, 1)
            dve.wait_ge(rid, 1)
            k3 = kr[:].rearrange("p s (g d) -> p (s g) d", g=2)
            v(nc.vector.tensor_tensor(k3, k3, ms[:, 1].unsqueeze(2).to_broadcast([P, 18, HD]), ALU.mult))
            v(nc.vector.tensor_tensor(k3, k3, gain[:].unsqueeze(1).to_broadcast([P, 18, HD]), ALU.mult))
            cos, sin, nsin = (rope[:, i, :].unsqueeze(1).to_broadcast([P, 18, 8]) for i in range(3))
            v.go(nc.vector.tensor_tensor(ra[:, :, 0:8], k3[:, :, 0:8], cos, ALU.mult))
            v.go(nc.vector.tensor_tensor(ra[:, :, 8:16], k3[:, :, 8:16], cos, ALU.mult))
            v.go(nc.vector.tensor_tensor(rb[:, :, 0:8], k3[:, :, 8:16], nsin, ALU.mult))
            v(nc.vector.tensor_tensor(rb[:, :, 8:16], k3[:, :, 0:8], sin, ALU.mult))
            nc.vector.tensor_tensor(k3[:, :, 0:16], ra[:], rb[:], ALU.add).then_inc(kready, 1)

        @block.tensor
        def _(pe):
            pe.wait_ge(ld, 80)
            for kv in range(2):
                for i in range(16):
                    mm = nc.tensor.matmul(pb[:, kv:kv + 1], w1[:, kv, i, :], pe_[:, kv, i:i + 1],
                                          start=(i == 0), stop=(i == 15))
            mm.then_inc(bias_done, 1)

            def second(u):
                p, kv, g = units[u]
                n, seqs = (127, 2) if p < PAIRS else (31, 1)
                pe.wait_ge(act_ready, u + 1)
                if u % 4 == 0 and p >= 2:
                    pe.wait_ge(out_free, p - 1)
                for s in range(seqs):
                    off = s * 256 + kv * 128 + g * 64
                    mm = nc.tensor.matmul(po[0:n, p % 2, off:off + 64], pre[:, u % 2, 128 * s:128 * s + n], w2[:, kv, :],
                                          start=True, stop=True)
                mm.then_inc(out_done, 1)

            for u, (p, kv, g) in enumerate(units):
                if u >= 2:
                    pe.wait_ge(pre_ready, u - 1)
                if p < PAIRS:
                    if u % 4 == 0:
                        pe.wait_ge(got[p % 2], 512 * (p // 2 + 1))
                    src = pages[p % 2][:].rearrange("p t (kv g i b) -> p t kv g i b", kv=2, g=2, i=8)
                    n = 256
                else:
                    src, n = k.cmp_prompt[:], 32
                for s in range(2):
                    for i in range(8):
                        mm = nc.tensor.matmul(ph[:, u % 2, 256 * s:256 * s + n], w1[:, kv, 8 * s + i, :],
                                              src[:, :, kv, g, i, :], start=(i == 0), stop=(i == 7))
                mm.then_inc(h_done, 1)
                if u >= 1:
                    second(u - 1)
            second(len(units) - 1)
            pe.wait_ge(kready, 1)
            for q in range(3):
                for s in range(3):
                    mm = nc.tensor.transpose(pt[:, q, P * s:P * s + P], kr[:, 3 * q + s, :], k.ident[:])
                mm.then_inc(trd, 1)


CMP, SEL, WIN = range(3)
S_AT = [(2, 256), (2, 0), (1, 0), (0, 0)]
P_AT = [0, 128, 384, 768]
PT_AT = [0, 512, 896, 1152]
PT_BANK = [(0, 0), (1, 0), (2, 0), (2, 256)]
NCP = 31


def prompt_attention_stage(nc, k):
    with ExitStack() as ctx:
        sb = lambda n, s, d=F32: ctx.enter_context(nc.sbuf_tensor(n, s, d))
        sem = k.sem
        causal, cmask, valid = sb("causal", [P, P]), sb("cmp_mask", [P, 4, NCP]), sb("cmp_valid", [P, 4])
        prob, pt = sb("prob", [P, 2, 1280]), sb("prob_T", [P, 2, 1280])
        pc = sb("prob_cmp", [P, 2, 4, NCP])
        mx, rs = sb("pa_max", [P, 2, 4]), sb("pa_sum", [P, 2, 4])
        s_ps = ctx.enter_context(nc.psum_tensor("pa_s", [P, 4, 512], F32))
        t_ps = ctx.enter_context(nc.psum_tensor("pa_t", [P, 3, 512], F32))
        o_ps = ctx.enter_context(nc.psum_tensor("pa_o", [P, 512], F32))
        ld, s_done, s_used, mx_ready, e_done, scaled, t_done, t_copied, t_cdve, pv_done, o_free, vch = (sem(n) for n in (
            "pa_ld", "pa_sd", "pa_su", "pa_mx", "pa_e", "pa_sc", "pa_td", "pa_tc", "pa_tcd", "pa_pv", "pa_of", "pa_v"))
        units = [(r, g, br) for r in range(REP) for g in range(2) for br in (CMP, SEL, WIN)]
        N = len(units)
        big = lambda n: sum(1 for x in units[:n] if x[2] != CMP)
        block = ctx.enter_context(nc.Block())

        @block.sync
        def _(sp):
            for dst, src in ((causal, k.d["causal"]), (cmask, k.d["cmp_mask"]), (valid, k.d["cmp_valid"])):
                sp.dma_start(dst[:], src).then_inc(ld, 16)

        @block.scalar
        def _(act):
            def evac(n):
                br = units[n][2]
                act.wait_ge(t_done, n + 1)
                if n >= 2:
                    act.wait_ge(pv_done, n - 1)
                if br == CMP:
                    nc.scalar.activation(pt[0:NCP, n % 2, 0:512], t_ps[0:NCP, 0, :], ACT.Copy).then_inc(t_copied, 1)
                else:
                    nc.scalar.activation(pt[:, n % 2, 0:512], t_ps[:, 0, :], ACT.Copy)
                    nc.scalar.activation(pt[:, n % 2, 896:1280], t_ps[:, 2, 0:384], ACT.Copy).then_inc(t_copied, 1)

            for n, (r, g, br) in enumerate(units):
                act.wait_ge(mx_ready, n + 1)
                if br == CMP:
                    nc.scalar.activation(pc[:, n % 2], pc[:, n % 2], ACT.Exp, scale=SCALE).then_inc(e_done, 1)
                else:
                    if n >= 2:
                        act.wait_ge(t_done, n - 1)
                    for i in range(4):
                        bank, at = S_AT[i]
                        e = nc.scalar.activation(prob[:, n % 2, P_AT[i]:P_AT[i] + P * (i + 1)],
                                                 s_ps[:, bank, at:at + P * (i + 1)], ACT.Exp, bias=mx[:, n % 2, i:i + 1],
                                                 scale=SCALE, accum_out=rs[:, n % 2, i:i + 1])
                    e.then_inc(e_done, 1)
                if n >= 1:
                    evac(n - 1)
                    if n % 6 == 0:
                        act.wait_ge(pv_done, n)
                        nc.scalar.activation(k.mixT[:, 4 + n // 6 - 1, 0:T_PROMPT], o_ps[:], ACT.Copy).then_inc(o_free, 1)
            evac(N - 1)
            act.wait_ge(pv_done, N)
            nc.scalar.activation(k.mixT[:, 7, 0:T_PROMPT], o_ps[:], ACT.Copy).then_inc(o_free, 1)

        @block.vector
        def _(dve):
            v = Chain(dve, vch)
            dve.wait_ge(ld, 48)

            def gate(n):
                r, g, br = units[n]
                return k.gates[:, 0:4, 8 * br + 4 * g + r]

            def scores(n):
                dve.wait_ge(s_done, n + 1)
                b = n % 2
                if units[n][2] == CMP:
                    if n >= 2:
                        dve.wait_ge(t_done, n - 1)
                    v(nc.vector.tensor_tensor(pc[:, b], s_ps[:, 3, 0:4 * NCP].rearrange("p (i c) -> p i c", i=4),
                                              cmask[:], ALU.add))
                    v(nc.vector.tensor_reduce(mx[:, b], pc[:, b], AX.X, ALU.max))
                    nc.vector.tensor_tensor(pc[:, b], pc[:, b], mx[:, b].unsqueeze(2).to_broadcast([P, 4, NCP]),
                                            ALU.subtract).then_inc(mx_ready, 1)
                else:
                    for i in range(4):
                        bank, at = S_AT[i]
                        d = s_ps[:, bank, at + P * i:at + P * i + P]
                        v.go(nc.vector.tensor_tensor(d, d, causal[:], ALU.add))
                    v.wait()
                    for i in range(4):
                        bank, at = S_AT[i]
                        v.go(nc.vector.tensor_reduce(mx[:, b, i:i + 1], s_ps[:, bank, at:at + P * (i + 1)], AX.X, ALU.max))
                    v.wait()
                    nc.vector.tensor_scalar(mx[:, b], mx[:, b], -SCALE, None, ALU.mult).then_inc(mx_ready, 1)

            def scale(n):
                dve.wait_ge(e_done, n + 1)
                b = n % 2
                if units[n][2] == CMP:
                    v(nc.vector.tensor_reduce(rs[:, b], pc[:, b], AX.X, ALU.add))
                    v(nc.vector.reciprocal(rs[:, b], rs[:, b]))
                    v(nc.vector.tensor_tensor(rs[:, b], rs[:, b], gate(n), ALU.mult))
                    v(nc.vector.tensor_tensor(rs[:, b], rs[:, b], valid[:], ALU.mult))
                    nc.vector.tensor_tensor(pc[:, b], pc[:, b], rs[:, b].unsqueeze(2).to_broadcast([P, 4, NCP]),
                                            ALU.mult).then_inc(scaled, 1)
                else:
                    v(nc.vector.reciprocal(rs[:, b], rs[:, b]))
                    v(nc.vector.tensor_tensor(rs[:, b], rs[:, b], gate(n), ALU.mult))
                    for i in range(4):
                        pr = prob[:, b, P_AT[i]:P_AT[i] + P * (i + 1)]
                        m = nc.vector.tensor_scalar(pr, pr, rs[:, b, i:i + 1], None, ALU.mult)
                    m.then_inc(scaled, 1)

            def evac(n):
                if units[n][2] != CMP:
                    dve.wait_ge(t_done, n + 1)
                    if n >= 2:
                        dve.wait_ge(pv_done, n - 1)
                    nc.vector.tensor_copy(pt[:, n % 2, 512:896], t_ps[:, 1, 0:384]).then_inc(t_cdve, 1)

            for n in range(N + 1):
                if n < N:
                    scores(n)
                    scale(n)
                if n >= 1:
                    evac(n - 1)

        @block.tensor
        def _(pe):
            def scores(n):
                r, g, br = units[n]
                h = slice(64 * g, 64 * g + 64)
                if br == CMP:
                    if n >= 3:
                        pe.wait_ge(mx_ready, n - 2)
                    for i in range(4):
                        mm = nc.tensor.matmul(s_ps[:, 3, NCP * i:NCP * i + NCP], k.qT[h, r, P * i:P * i + P],
                                              k.kcT[h, 8, 0:NCP], start=True, stop=True)
                else:
                    if big(n):
                        pe.wait_ge(e_done, n if units[n - 1][2] != CMP else n - 1)
                    kT = k.ksT if br == SEL else k.kwT
                    for i in range(4):
                        bank, at = S_AT[i]
                        mm = nc.tensor.matmul(s_ps[:, bank, at:at + P * (i + 1)], k.qT[h, r, P * i:P * i + P],
                                              kT[h, 0:P * (i + 1)], start=True, stop=True)
                mm.then_inc(s_done, 1)

            def values(n):
                r, g, br = units[n]
                h = slice(64 * g, 64 * g + 64)
                pe.wait_ge(scaled, n + 1)
                if n >= 1:
                    pe.wait_ge(t_copied, n)
                    if big(n):
                        pe.wait_ge(t_cdve, big(n))
                if br == CMP:
                    for i in range(4):
                        mm = nc.tensor.transpose(t_ps[0:NCP, 0, P * i:P * i + P], pc[:, n % 2, i, :], k.ident[:])
                else:
                    for j in range(4):
                        bank, at = PT_BANK[j]
                        for i in range(j, 4):
                            mm = nc.tensor.transpose(t_ps[:, bank, at + P * (i - j):at + P * (i - j) + P],
                                                     prob[:, n % 2, P_AT[i] + P * j:P_AT[i] + P * j + P], k.ident[:])
                mm.then_inc(t_done, 1)
                pe.wait_ge(t_copied, n + 1)
                if br == CMP:
                    if n % 6 == 0 and n:
                        pe.wait_ge(o_free, n // 6)
                    mm = nc.tensor.matmul(o_ps[h, :], k.vcmp[0:NCP, 8, h], pt[0:NCP, n % 2, 0:512], start=True, stop=False)
                else:
                    pe.wait_ge(t_cdve, big(n + 1))
                    lo = 256 if br == SEL else 384
                    for j in (3, 2, 1, 0):
                        mm = nc.tensor.matmul(o_ps[h, P * j:512], k.kv[:, j, lo + 64 * g:lo + 64 * g + 64],
                                              pt[:, n % 2, PT_AT[j]:PT_AT[j] + P * (4 - j)], start=False,
                                              stop=(br == WIN and j == 0))
                mm.then_inc(pv_done, 1)

            for n in range(N + 1):
                if n < N:
                    scores(n)
                if n >= 1:
                    values(n - 1)


NKEYS = PAST + 64
NSEL = 33


def sample_attention_stage(nc, k):
    with ExitStack() as ctx:
        sb = lambda n, s, d=F32: ctx.enter_context(nc.sbuf_tensor(n, s, d))
        sem = k.sem
        pages = [sb(f"sel_pages{n}", [P, 32, 256]) for n in range(2)]
        kw, vw = sb("win_k", [P, 2, 2, 512]), sb("win_v", [P, 2, 2, 4, P])
        q = sb("q_heads", [P, SEQS, 64])
        same, pick, mine = sb("same_query", [P, P]), sb("pick_rows", [64, PAIRS, P]), sb("my_head", [P, 8])
        newm, winm, force = sb("new_mask", [P, PAIRS, 64]), sb("win_mask", [P, 8]), sb("force_row", [P, NSEL])
        gt = sb("sample_gates", [P, PAIRS, 3])
        gtmp = sb("gates_tmp", [P, PAIRS, 3, 8])
        pc, ss, sw = sb("sa_pc", [P, P]), sb("sa_sel", [P, NKEYS]), sb("sa_win", [P, 576])
        pt = sb("sa_pt", [P, 23, P])
        st = sb("sa_stats", [P, 16])
        sc = sb("sa_score", [P, 3, NSEL])
        top = sb("sa_top", [P, 2, 8])
        ps = ctx.enter_context(nc.psum_tensor("sa_ps", [P, 8, 512], F32))
        ld, got, gotw = sem("sa_ld"), [sem("sa_got0"), sem("sa_got1")], [sem("sa_gw0"), sem("sa_gw1")]
        q_ready, g_mm, vch, s_small, s_sel = (sem(n) for n in ("sa_q", "sa_gm", "sa_v", "sa_ss", "sa_sl"))
        cmx, ce, pn, imp, wcp, wmx, we, smx, se = (sem(n) for n in (
            "sa_cmx", "sa_ce", "sa_pn", "sa_imp", "sa_wcp", "sa_wmx", "sa_we", "sa_smx", "sa_se"))
        c_sc, w_sc, s_sc, td, ta, tv, pv, of = (sem(n) for n in (
            "sa_csc", "sa_wsc", "sa_ssc", "sa_td", "sa_ta", "sa_tv", "sa_pv", "sa_of"))
        banks = [[0, 1, 2, 3], [4, 5], [6, 7, 8, 9], [10, 11, 12, 13], [14, 15, 16, 17], [18, 19, 20, 21], [22]]
        NB = len(banks)
        rows_of = lambda b: 127 if b == 0 else 64 if b in (5, 22) else P
        block = ctx.enter_context(nc.Block())

        @block.sync
        def _(sp):
            for dst, src in ((same, k.d["same"]), (pick, k.d["pick"]), (mine, k.d["mine"]), (newm, k.d["new_mask"]),
                             (winm, k.d["win_mask"]), (force, k.d["force"])):
                sp.dma_start(dst[:], src).then_inc(ld, 16)
            for p in range(PAIRS):
                if p >= 2:
                    sp.wait_ge(pv, p - 1)
                for s in range(2):
                    sp.dma_start(kw[:, p % 2, s], k.d["win_kT"][2 * p + s]).then_inc(gotw[p % 2], 16)
                    sp.dma_start(vw[:, p % 2, s], k.d["win_rows"][1][2 * p + s].rearrange("(a p) f -> p a f", p=P)).then_inc(gotw[p % 2], 16)
                gather_pages(sp, nc, pages[p % 2], k.d["sel_pool"], k.pages, 32 * p, got[p % 2])

        @block.scalar
        def _(act):
            for p in range(PAIRS):
                act.wait_ge(s_small, p + 1)
                if p:
                    act.wait_ge(td, NB * p)
                nc.scalar.activation(sw[:, 0:512], ps[:, 5, :], ACT.Copy).then_inc(wcp, 1)
                act.wait_ge(cmx, p + 1)
                nc.scalar.activation(pc[:, 0:127], ps[:, 4, 128:255], ACT.Exp, bias=st[:, 0:1], scale=SCALE,
                                     accum_out=st[:, 1:2]).then_inc(ce, 1)
                act.wait_ge(wmx, p + 1)
                nc.scalar.activation(sw[:], sw[:], ACT.Exp, bias=st[:, 4:5], scale=SCALE,
                                     accum_out=st[:, 5:6]).then_inc(we, 1)
                act.wait_ge(smx, p + 1)
                nc.scalar.activation(ss[:], ss[:], ACT.Exp, bias=st[:, 8:9], scale=SCALE,
                                     accum_out=st[:, 9:10]).then_inc(se, 1)
                for b in range(0, NB, 2):
                    act.wait_ge(td, NB * p + b + 1)
                    if p and b == 0:
                        act.wait_ge(pv, p)
                    lo, n = banks[b][0], len(banks[b])
                    if b == NB - 1:
                        nc.scalar.activation(pt[0:64, lo, :], ps[0:64, b % 4, 0:P], ACT.Copy).then_inc(ta, 1)
                    elif b == 0:
                        nc.scalar.activation(pt[0:127, 0, :], ps[0:127, 0, 0:P], ACT.Copy)
                        nc.scalar.activation(pt[:, 1:4, :], ps[:, 0, P:512].rearrange("p (n f) -> p n f", n=3), ACT.Copy).then_inc(ta, 1)
                    else:
                        nc.scalar.activation(pt[:, lo:lo + n, :], ps[:, b % 4, 0:P * n].rearrange("p (n f) -> p n f", n=n),
                                             ACT.Copy).then_inc(ta, 1)

        @block.vector
        def _(dve):
            v = Chain(dve, vch)
            V = nc.vector
            v(V.memset(q[:], 0.0))
            for g in range(2):
                h = slice(64 * g, 64 * g + 64)
                V.tensor_copy(q[h, :, 32 * g:32 * g + 32].rearrange("p s (r t) -> p s r t", r=REP),
                              k.qT[h, :, T_PROMPT:T].rearrange("p r (s t) -> p s r t", t=STEPS)).then_inc(q_ready, 1)
            dve.wait_ge(ld, 96)
            dve.wait_ge(g_mm, 1)
            v(V.tensor_tensor(gtmp[:].rearrange("p a b h -> p (a b) h"), ps[:, 7, 0:96].rearrange("p (a h) -> p a h", h=8),
                              mine[:].unsqueeze(1).to_broadcast([P, 12, 8]), ALU.mult))
            v(V.tensor_reduce(gt[:].rearrange("p a b -> p (a b)"), gtmp[:].rearrange("p a b h -> p (a b) h"), AX.X, ALU.add))
            v(V.memset(pc[:], 0.0))
            for p in range(PAIRS):
                dve.wait_ge(s_small, p + 1)
                if p:
                    dve.wait_ge(td, NB * p)
                v(V.tensor_reduce(st[:, 0:1], ps[:, 4, 128:255], AX.X, ALU.max))
                V.tensor_scalar(st[:, 0:1], st[:, 0:1], -SCALE, None, ALU.mult).then_inc(cmx, 1)
                dve.wait_ge(wcp, p + 1)
                v.go(V.tensor_tensor(sw[:, 0:8], sw[:, 0:8], winm[:], ALU.add))
                dve.wait_ge(ce, p + 1)
                v(V.tensor_tensor(sw[:, 512:576], ps[:, 4, 64:128], newm[:, p], ALU.add))
                v(V.tensor_reduce(st[:, 4:5], sw[:], AX.X, ALU.max))
                V.tensor_scalar(st[:, 4:5], st[:, 4:5], -SCALE, None, ALU.mult).then_inc(wmx, 1)
                v(V.reciprocal(st[:, 1:2], st[:, 1:2]))
                V.tensor_scalar(pc[:, 0:127], pc[:, 0:127], st[:, 1:2], None, ALU.mult).then_inc(pn, 1)
                dve.wait_ge(imp, p + 1)
                v(V.memset(sc[:, 0, 32:33], 0.0))
                v(V.tensor_reduce(sc[:, 0, 0:32], ps[:, 4, 256:384].rearrange("p (b c) -> p b c", c=4), AX.X, ALU.add))
                v(V.tensor_tensor(sc[:, 0], sc[:, 0], force[:], ALU.add))
                v(V.max(top[:, 0], sc[:, 0]))
                v(V.match_replace(sc[:, 1], top[:, 0], sc[:, 0], GONE))
                v(V.max(top[:, 1], sc[:, 1]))
                v(V.match_replace(sc[:, 2], top[:, 1], sc[:, 1], GONE))
                v(V.tensor_scalar(sc[:, 0], sc[:, 2], GONE / 2, NEG, ALU.is_gt, ALU.mult))
                V.tensor_scalar(pc[:, 0:127], pc[:, 0:127], gt[:, p, 0:1], None, ALU.mult).then_inc(c_sc, 1)
                dve.wait_ge(s_sel, p + 1)
                for c in range(4):
                    b3 = lambda a: a.rearrange("p (b n) -> p b n", n=64)
                    v.go(V.tensor_tensor(b3(ss[:, 512 * c:512 * c + 512]), b3(ps[:, c, :]),
                                         sc[:, 0, 8 * c:8 * c + 8].unsqueeze(2).to_broadcast([P, 8, 64]), ALU.add))
                v(V.scalar_tensor_tensor(out=ss[:, PAST:NKEYS], in0=ps[:, 4, 0:64], scalar=sc[:, 0, 32:33],
                                         in1=newm[:, p], op0=ALU.add, op1=ALU.add))
                v(V.tensor_reduce(st[:, 8:9], ss[:], AX.X, ALU.max))
                V.tensor_scalar(st[:, 8:9], st[:, 8:9], -SCALE, None, ALU.mult).then_inc(smx, 1)
                dve.wait_ge(we, p + 1)
                v(V.reciprocal(st[:, 5:6], st[:, 5:6]))
                v(V.tensor_tensor(st[:, 5:6], st[:, 5:6], gt[:, p, 2:3], ALU.mult))
                V.tensor_scalar(sw[:], sw[:], st[:, 5:6], None, ALU.mult).then_inc(w_sc, 1)
                dve.wait_ge(se, p + 1)
                v(V.reciprocal(st[:, 9:10], st[:, 9:10]))
                v(V.tensor_tensor(st[:, 9:10], st[:, 9:10], gt[:, p, 1:2], ALU.mult))
                V.tensor_scalar(ss[:], ss[:], st[:, 9:10], None, ALU.mult).then_inc(s_sc, 1)
                for b in range(1, NB, 2):
                    dve.wait_ge(td, NB * p + b + 1)
                    if p and b == 1:
                        dve.wait_ge(pv, p)
                    lo, n = banks[b][0], len(banks[b])
                    if b == 1:
                        V.tensor_copy(pt[:, 4, :], ps[:, 1, 0:P])
                        V.tensor_copy(pt[0:64, 5, :], ps[0:64, 1, P:2 * P]).then_inc(tv, 1)
                    else:
                        V.tensor_copy(pt[:, lo:lo + n, :], ps[:, b % 4, 0:P * n].rearrange("p (n f) -> p n f", n=n)).then_inc(tv, 1)
                dve.wait_ge(pv, p + 1)
                for g in range(2):
                    h = slice(64 * g, 64 * g + 64)
                    V.tensor_copy(k.mixT[h, 4:8, T_PROMPT + 16 * p:T_PROMPT + 16 * p + 16].rearrange("p r (s t) -> p r s t", t=STEPS),
                                  ps[h, 6, 0:P].rearrange("p (s g r t) -> p g r s t", s=2, g=2, r=REP)[:, g]).then_inc(of, 1)

        @block.tensor
        def _(pe):
            pe.wait_ge(ld, 96)
            for p in range(PAIRS):
                mm = nc.tensor.matmul(ps[:, 7, 24 * p:24 * p + 24], pick[:, p, :], k.gates[0:64, 4, :], start=True, stop=True)
            mm.then_inc(g_mm, 1)
            pe.wait_ge(q_ready, 2)
            for p in range(PAIRS):
                kp = pages[p % 2]
                if p:
                    pe.wait_ge(smx, p)
                pe.wait_ge(gotw[p % 2], 64 * (p // 2 + 1))
                for s in range(2):
                    rows = slice(64 * s, 64 * s + 64)
                    qs = q[:, 2 * p + s, :]
                    nc.tensor.matmul(ps[rows, 4, 128:255], qs, k.kcT[:, 2 * p + s, 0:127], start=True, stop=True)
                    nc.tensor.matmul(ps[rows, 4, 0:64], qs, k.ksT[:, T_PROMPT:T], start=True, stop=True)
                    nc.tensor.matmul(ps[rows, 4, 64:128], qs, k.kwT[:, T_PROMPT:T], start=True, stop=True)
                    mm = nc.tensor.matmul(ps[rows, 5, :], qs, kw[:, p % 2, s], start=True, stop=True)
                mm.then_inc(s_small, 1)
                if p:
                    pe.wait_ge(ta, 4 * p)
                    pe.wait_ge(tv, 3 * p)
                pe.wait_ge(got[p % 2], 512 * (p // 2 + 1))
                for s in range(2):
                    for c in range(4):
                        mm = nc.tensor.matmul(ps[64 * s:64 * s + 64, c, :], q[:, 2 * p + s, :],
                                              kp[:, 16 * s + 4 * c:16 * s + 4 * c + 4, 0:P], start=True, stop=True)
                mm.then_inc(s_sel, 1)
                pe.wait_ge(pn, p + 1)
                pe.wait_ge(wmx, p + 1)
                nc.tensor.matmul(ps[:, 4, 256:384], same[:], pc[:], start=True, stop=True).then_inc(imp, 1)
                pe.wait_ge(c_sc, p + 1)
                pe.wait_ge(w_sc, p + 1)
                pe.wait_ge(smx, p + 1)
                for b, blocks in enumerate(banks):
                    if b == 2:
                        pe.wait_ge(s_sc, p + 1)
                    if b >= 4:
                        pe.wait_ge(tv if b % 2 else ta, (3 if b % 2 else 4) * p + (b - 4) // 2 + 1)
                    for n, blk in enumerate(blocks):
                        src = (pc[:, 0:127] if blk == 0 else sw[:, P * (blk - 1):P * (blk - 1) + rows_of(blk)] if blk < 6
                               else ss[:, P * (blk - 6):P * (blk - 6) + rows_of(blk)])
                        mm = nc.tensor.transpose(ps[0:rows_of(blk), b % 4, P * n:P * n + P], src, k.ident[:])
                    mm.then_inc(td, 1)
                pe.wait_ge(ta, 4 * p + 4)
                pe.wait_ge(tv, 3 * p + 3)
                if p:
                    pe.wait_ge(of, 2 * p)
                for s in range(2):
                    for blk in range(23):
                        m = rows_of(blk)
                        val = (k.vcmp[0:127, 2 * p + s, :] if blk == 0 else vw[:, p % 2, s, blk - 1, :] if blk < 5
                               else k.kv[0:64, 4, 384:512] if blk == 5
                               else kp[:, 16 * s + blk - 6, P:2 * P] if blk < 22 else k.kv[0:64, 4, 256:384])
                        mm = nc.tensor.matmul(ps[:, 6, 64 * s:64 * s + 64], val, pt[0:m, blk, 64 * s:64 * s + 64],
                                              start=(blk == 0), stop=(blk == 22))
                mm.then_inc(pv, 1)


def mix_and_retrieve_stage(nc, k):
    with ExitStack() as ctx:
        sb = lambda n, s, d=F32: ctx.enter_context(nc.sbuf_tensor(n, s, d))
        sem = k.sem
        wo, wq, sk = sb("w_out_sb", [P, KD, 512]), sb("w_q_sb", [P, 2, KD, 512]), sb("subkeys_sb", [P, 16, KEYS])
        ga, gf = sb("g_attn_sb", [P, 4]), sb("g_ffn_sb", [P, KD])
        rinv = sb("m_rinv", [P, T])
        sq = sb("m_sq", [P, KD, T])
        qp = sb("peer_q", [P, 16, T])
        iota = sb("iota16", [P, 16])
        scr = sb("k_scr", [P, 16, KEYS])
        v16, i16, i16f = sb("v16", [P, 16, 16]), sb("i16", [P, 16, 16], U32), sb("i16f", [P, 16, 16])
        cand, eq = scr[:].rearrange("p a b -> p (a b)").rearrange("p (h c) -> p h c", h=PH), sb("eq", [P, PH, 16, 16])
        scr2 = sb("c_scr", [P, PH, 256])
        vals, cpos, ab = sb("vals", [P, PH, 16]), sb("cpos", [P, PH, 16], U32), sb("ab", [P, 2, PH, 16], U32)
        abf, idx, gsum = sb("abf", [P, 2, PH, 16]), sb("idx", [P, 3, P]), sb("gsum", [P, 2, PH])
        ps = ctx.enter_context(nc.psum_tensor("m_ps", [P, 8, 512], F32))
        ld, wo_ld, wo_free = sem("m_ld"), [sem("m_wo0"), sem("m_wo1")], sem("m_wof")
        wq_ld = [sem("m_wq0"), sem("m_wq1")]
        asq, ssq, msr, rir, an, mixd, hsq, hn_r, qd, qc, vch = (sem(n) for n in (
            "m_asq", "m_ssq", "m_msr", "m_rir", "m_an", "m_mix", "m_hsq", "m_hn", "m_qd", "m_qc", "m_v"))
        sd, s_used, eready, ed, tk, trd, trc = (sem(n) for n in ("m_sd", "m_su", "m_er", "m_ed", "m_tk", "m_trd", "m_trc"))
        block = ctx.enter_context(nc.Block())

        @block.sync
        def _(sp):
            sp.dma_start(wo[:], k.d["w_out"][:, :, 0:512]).then_inc(wo_ld[0], 16)
            for dst, src in ((ga, k.d["g_out_attn"]), (gf, k.d["g_ffn"]), (sk, k.d["subkeys"]), (iota, k.d["iota16"])):
                sp.dma_start(dst[:], src).then_inc(ld, 16)
            for c in range(2):
                sp.dma_start(wq[:, c], k.d["w_q"][:, :, 512 * c:512 * c + 512]).then_inc(wq_ld[c], 16)
            sp.wait_ge(mixd, 8)
            sp.dma_start(wo[:], k.d["w_out"][:, :, 512:1024]).then_inc(wo_ld[1], 16)
            for c in range(2, 4):
                sp.wait_ge(qd, 8 * (c - 1))
                sp.dma_start(wq[:, c % 2], k.d["w_q"][:, :, 512 * c:512 * c + 512]).then_inc(wq_ld[c % 2], 16)

        @block.scalar
        def _(act):
            for c in range(4):
                nc.scalar.activation(sq[:, c], k.mixT[:, 4 + c], ACT.Square).then_inc(asq, 1)
            act.wait_ge(msr, 1)
            nc.scalar.activation(rinv[:], rinv[:], ACT.Sqrt).then_inc(rir, 1)
            for c in range(KD):
                act.wait_ge(hsq, c + 1)
                nc.scalar.activation(sq[:, c], k.hT[:, c], ACT.Square).then_inc(asq, 1)
            act.wait_ge(msr, 2)
            nc.scalar.activation(rinv[:], rinv[:], ACT.Sqrt).then_inc(rir, 1)
            for u in range(32):
                act.wait_ge(qd, u + 1)
                c, h = u // 2, u % 2
                nc.scalar.activation(qp[:, c, HALF * h:HALF * h + HALF], ps[:, u % 4, 0:HALF], ACT.Copy).then_inc(qc, 1)
            for t in range(TILES):
                m = TILE_ROWS[t]
                act.wait_ge(eready, t + 1)
                nc.scalar.activation(vals[0:m], vals[0:m], ACT.Exp).then_inc(ed, 1)
                act.wait_ge(trd, t + 1)
                for n in range(3):
                    e = nc.scalar.activation(k.idxT[:, n, P * t:P * t + m], ps[:, 4 * (t % 2), P * n:P * n + m], ACT.Copy)
                e.then_inc(trc, 1)

        @block.vector
        def _(dve):
            v = Chain(dve, vch)
            V = nc.vector

            def mean_square(dim, n):
                dve.wait_ge(ssq, n)
                for h in range(2):
                    v.go(V.tensor_scalar(rinv[:, HALF * h:HALF * h + HALF], ps[:, 6 + h, 0:HALF], 1.0 / dim, EPS, ALU.mult, ALU.add))
                v.wait()
                V.reciprocal(rinv[:], rinv[:]).then_inc(msr, 1)
                dve.wait_ge(rir, n)

            dve.wait_ge(ld, 64)
            mean_square(512, 1)
            for c in range(4):
                V.scalar_tensor_tensor(out=k.mixT[:, 4 + c], in0=k.mixT[:, 4 + c], scalar=ga[:, c:c + 1], in1=rinv[:],
                                       op0=ALU.mult, op1=ALU.mult).then_inc(an, 1)
            for c in range(KD):
                for h in range(2):
                    dve.wait_ge(mixd, 2 * c + h + 1)
                    hs = k.hT[:, c, HALF * h:HALF * h + HALF]
                    add = V.tensor_tensor(hs, hs, ps[:, 2 * (c % 2) + h, 0:HALF], ALU.add)
                    v.go(add)
                v.wait()
                V.memset(gsum[:, 0, 0:1], 0.0).then_inc(hsq, 1)
            mean_square(D, 2)
            for c in range(KD):
                V.scalar_tensor_tensor(out=k.hn[:, c], in0=k.hT[:, c], scalar=gf[:, c:c + 1], in1=rinv[:],
                                       op0=ALU.mult, op1=ALU.mult).then_inc(hn_r, 1)
            for t in range(TILES):
                m = TILE_ROWS[t]
                dve.wait_ge(sd, t + 1)
                ops = ps[0:m, 4 * (t % 2):4 * (t % 2) + 4].rearrange("p b (n c) -> p (b n) c", n=4)
                for u in range(16):
                    v.go(V.max(v16[0:m, u, 0:8], ops[:, u]))
                v.wait()
                for u in range(16):
                    v.go(V.max_index(i16[0:m, u, 0:8], v16[0:m, u, 0:8], ops[:, u]))
                    v.go(V.match_replace(scr[0:m, u], v16[0:m, u, 0:8], ops[:, u], GONE))
                v.wait()
                V.memset(gsum[0:1, 0, 0:1], 0.0).then_inc(s_used, 1)
                for u in range(16):
                    v.go(V.max(v16[0:m, u, 8:16], scr[0:m, u]))
                v.wait()
                for u in range(16):
                    v.go(V.max_index(i16[0:m, u, 8:16], v16[0:m, u, 8:16], scr[0:m, u]))
                v.wait()
                vh = v16[0:m].rearrange("p (h s) a -> p h s a", s=2)
                v.go(V.tensor_copy(i16f[0:m].rearrange("p a b -> p (a b)"), i16[0:m].rearrange("p a b -> p (a b)")))
                for h in range(PH):
                    v.go(V.tensor_tensor(cand[0:m, h].rearrange("p (a b) -> p a b", a=16),
                                         v16[0:m, 2 * h].unsqueeze(2).to_broadcast([m, 16, 16]),
                                         v16[0:m, 2 * h + 1].unsqueeze(1).to_broadcast([m, 16, 16]), ALU.add))
                v.wait()
                for h in range(PH):
                    v.go(V.max(vals[0:m, h, 0:8], cand[0:m, h]))
                v.wait()
                for h in range(PH):
                    v.go(V.max_index(cpos[0:m, h, 0:8], vals[0:m, h, 0:8], cand[0:m, h]))
                    v.go(V.match_replace(scr2[0:m, h], vals[0:m, h, 0:8], cand[0:m, h], GONE))
                v.wait()
                for h in range(PH):
                    v.go(V.max(vals[0:m, h, 8:16], scr2[0:m, h]))
                v.wait()
                for h in range(PH):
                    v.go(V.max_index(cpos[0:m, h, 8:16], vals[0:m, h, 8:16], scr2[0:m, h]))
                v(V.tensor_copy(gsum[0:m, 0], vals[0:m, :, 0]))
                V.tensor_tensor(vals[0:m], vals[0:m], gsum[0:m, 0].unsqueeze(2).to_broadcast([m, PH, 16]),
                                ALU.subtract).then_inc(eready, 1)
                v.go(V.tensor_scalar(ab[0:m, 0], cpos[0:m], 4, None, ALU.logical_shift_right))
                v(V.tensor_scalar(ab[0:m, 1], cpos[0:m], 15, None, ALU.bitwise_and))
                v(V.tensor_copy(abf[0:m].rearrange("p a h c -> p (a h c)"), ab[0:m].rearrange("p a h c -> p (a h c)")))
                if t:
                    dve.wait_ge(trd, t)
                e3 = eq[0:m].rearrange("p h c a -> p (h c) a")
                for s in range(2):
                    v(V.tensor_tensor(e3, abf[0:m, s].rearrange("p h c -> p (h c)").unsqueeze(2).to_broadcast([m, P, 16]),
                                      iota[0:m].unsqueeze(1).to_broadcast([m, P, 16]), ALU.is_equal))
                    fs = i16f[0:m].rearrange("p (h s) a -> p h s a", s=2)[:, :, s]
                    v(V.tensor_tensor(eq[0:m], eq[0:m], fs.unsqueeze(2).to_broadcast([m, PH, 16, 16]), ALU.mult))
                    v(V.tensor_reduce(idx[0:m, s], e3, AX.X, ALU.add))
                dve.wait_ge(ed, t + 1)
                v(V.tensor_reduce(gsum[0:m, 0], vals[0:m], AX.X, ALU.add))
                v(V.reciprocal(gsum[0:m, 1], gsum[0:m, 0]))
                V.tensor_tensor(idx[0:m, 2].rearrange("p (h c) -> p h c", h=PH), vals[0:m],
                                gsum[0:m, 1].unsqueeze(2).to_broadcast([m, PH, 16]), ALU.mult).then_inc(tk, 1)

        @block.tensor
        def _(pe):
            def column_sums(n, first):
                for c in range(n):
                    pe.wait_ge(asq, first + c + 1)
                    for h in range(2):
                        mm = nc.tensor.matmul(ps[:, 6 + h, 0:HALF], k.ones[:], sq[:, c, HALF * h:HALF * h + HALF],
                                              start=(c == 0), stop=(c == n - 1))
                mm.then_inc(ssq, 1)

            column_sums(4, 0)
            pe.wait_ge(an, 4)
            for c in range(KD):
                if c % 4 == 0:
                    pe.wait_ge(wo_ld[c // 4], 16)
                for h in range(2):
                    if c >= 2:
                        pe.wait_ge(hsq, c - 1)
                    for i in range(KD):
                        mm = nc.tensor.matmul(ps[:, 2 * (c % 2) + h, 0:HALF], wo[:, i, P * (c % 4):P * (c % 4) + P],
                                              k.mixT[:, i, HALF * h:HALF * h + HALF], start=(i == 0), stop=(i == KD - 1))
                    mm.then_inc(mixd, 1)
            column_sums(KD, 4)
            pe.wait_ge(hn_r, KD)
            for u in range(32):
                c, h = u // 2, u % 2
                if u % 8 == 0:
                    pe.wait_ge(wq_ld[(u // 8) % 2], 16 * (u // 16 + 1))
                if u >= 4:
                    pe.wait_ge(qc, u - 3)
                for i in range(KD):
                    mm = nc.tensor.matmul(ps[:, u % 4, 0:HALF], wq[:, (u // 8) % 2, i, P * (c % 4):P * (c % 4) + P],
                                          k.hn[:, i, HALF * h:HALF * h + HALF], start=(i == 0), stop=(i == KD - 1))
                mm.then_inc(qd, 1)
            pe.wait_ge(qc, 32)
            pe.wait_ge(ld, 64)

            def transposes(t):
                m = TILE_ROWS[t]
                pe.wait_ge(tk, t + 1)
                pe.wait_ge(s_used, t + 1)
                for n in range(3):
                    mm = nc.tensor.transpose(ps[:, 4 * (t % 2), P * n:P * n + m], idx[0:m, n], k.ident[0:m, 0:m])
                mm.then_inc(trd, 1)

            for t in range(TILES):
                m = TILE_ROWS[t]
                if t >= 2:
                    pe.wait_ge(trc, t - 1)
                for u in range(16):
                    mm = nc.tensor.matmul(ps[0:m, 4 * (t % 2) + u // 4, P * (u % 4):P * (u % 4) + P],
                                          qp[:, u, P * t:P * t + m], sk[:, u, :], start=True, stop=True)
                mm.then_inc(sd, 1)
                if t >= 1:
                    transposes(t - 1)
            transposes(TILES - 1)


TB = 32
NTB = T // TB
EG = 4
NG = KEYS // EG


def gate_matrix_stage(nc, k):
    with ExitStack() as ctx:
        sb = lambda n, s, d=F32: ctx.enter_context(nc.sbuf_tensor(n, s, d))
        sem = k.sem
        iota = sb("iota128", [P, KEYS])
        oh1, oh2 = sb("one_hot1", [P, 8, KEYS]), sb("one_hot2", [P, 8, KEYS])
        stage = sb("gate_stage", [P, 2, NG, TB, EG])
        ps = ctx.enter_context(nc.psum_tensor("g_ps", [P, 8, 512], F32))
        ld, hot, multiplied, copied = (sem(n) for n in ("gm_ld", "gm_hot", "gm_multiplied", "gm_copied"))
        block = ctx.enter_context(nc.Block())

        @block.sync
        def _(sp):
            sp.dma_start(iota[:], k.d["iota128"]).then_inc(ld, 16)
            with sp.Fori(0, NTB // 2) as i:
                for b in range(2):
                    sp.wait_ge(copied, 16 * i + 8 * b + 16)
                    sp.dma_start(k.d["gate_scr"][:, :, bass.ds(2 * i + b, 1), :].rearrange("g p o f -> p g (o f)"),
                                 stage[:, b].rearrange("p g t e -> p g (t e)")).then_inc(k.gm_stored[b], 16)

        @block.vector
        def _(dve):
            dve.wait_ge(ld, 16)
            with dve.Fori(0, NTB) as i:
                for n in range(TB):
                    if n % 4 == 0:
                        dve.wait_ge(multiplied, 8 * i + n // 4 + 1)
                    nc.vector.tensor_scalar(oh1[:, n % 8], iota[:], k.idxT[:, 0, bass.ds(TB * i + n, 1)], None, ALU.is_equal)
                    nc.vector.tensor_scalar(oh2[:, n % 8], iota[:], k.idxT[:, 1, bass.ds(TB * i + n, 1)],
                                            k.idxT[:, 2, bass.ds(TB * i + n, 1)], ALU.is_equal, ALU.mult).then_inc(hot, 1)

        @block.tensor
        def _(pe):
            pe.sem_inc(multiplied, 2)
            with pe.Fori(0, NTB) as i:
                for n in range(TB):
                    q = n // 4
                    if n % 4 == 0:
                        pe.wait_ge(copied, 8 * i + q + 1)
                    pe.wait_ge(hot, TB * i + n + 1)
                    mm = nc.tensor.matmul(ps[:, q, KEYS * (n % 4):KEYS * (n % 4) + KEYS], oh1[:, n % 8], oh2[:, n % 8],
                                          start=True, stop=True)
                    if n % 4 == 3:
                        mm.then_inc(multiplied, 1)

        @block.scalar
        def _(act):
            act.sem_inc(copied, 8)
            for b in range(2):
                act.sem_inc(k.gm_stored[b], 16)
            with act.Fori(0, NTB // 2) as i:
                for b in range(2):
                    act.wait_ge(k.gm_stored[b], 16 * i + 16)
                    for q in range(8):
                        act.wait_ge(multiplied, 16 * i + 8 * b + q + 3)
                        nc.scalar.activation(stage[:, b, :, 4 * q:4 * q + 4, :].rearrange("p g t e -> p t g e"),
                                             ps[:, q, :].rearrange("p (t g e) -> p t g e", t=4, g=NG),
                                             ACT.Copy).then_inc(copied, 1)


def experts_stage(nc, k):
    with ExitStack() as ctx:
        sb = lambda n, s, d=F32: ctx.enter_context(nc.sbuf_tensor(n, s, d))
        sem = k.sem
        ut = sb("u_tab", [P, 2, EG, KD, P])
        vt = sb("v_tab", [P, 2, EG, D])
        gt = sb("g_tab", [P, 2, T, EG])
        act_, wt = sb("e_act", [P, 2, T]), sb("e_wt", [P, 2, EG, T])
        ps = ctx.enter_context(nc.psum_tensor("e_ps", [P, 8, 512], F32))
        u_ld, v_ld, g_ld = ([sem(f"e_{x}{b}") for b in range(2)] for x in "uvg")
        up_done, gelu_done, weighted, down_done, added = (sem(n) for n in ("e_up", "e_gelu", "e_weighted", "e_down", "e_added"))
        block = ctx.enter_context(nc.Block())

        UD0 = WD0 = EG + 1
        OD0 = KD + 1
        GELU0 = ADD0 = 2

        @block.sync
        def _(sp):
            for b in range(2):
                sp.wait_ge(k.gm_stored[b], 16 + 16 * (NTB // 2))
            with sp.Fori(0, NG // 2) as i:
                for b in range(2):
                    G = 2 * i + b
                    sp.wait_ge(up_done, EG * G + 1)
                    sp.dma_start(ut[:, b].rearrange("p e k n -> p (e k n)"),
                                 k.d["u_tab"][bass.ds(G, 1)].rearrange("o p f -> (o p) f")).then_inc(u_ld[b], 16)
                    sp.wait_ge(weighted, EG * G + 1)
                    sp.dma_start(gt[:, b].rearrange("p t e -> p (t e)"),
                                 k.d["gate_scr"][bass.ds(G, 1)].rearrange("o p a f -> (o p) (a f)")).then_inc(g_ld[b], 16)
                    sp.wait_ge(down_done, KD * G + 1)
                    sp.dma_start(vt[:, b].rearrange("p e d -> p (e d)"),
                                 k.d["v_tab"][:, bass.ds(G, 1), :].rearrange("p o f -> p (o f)")).then_inc(v_ld[b], 16)

        @block.scalar
        def _(act):
            act.sem_inc(gelu_done, GELU0)
            with act.Fori(0, NG) as G:
                for e in range(EG):
                    n = EG * G + e
                    act.wait_ge(up_done, n + (UD0 + 1))
                    act.wait_ge(weighted, n + (WD0 - 1))
                    nc.scalar.activation(act_[:, e % 2].rearrange("p (h n) -> p h n", h=2), ps[:, 2 * (e % 2):2 * (e % 2) + 2, 0:HALF],
                                         ACT.Gelu_apprx_tanh).then_inc(gelu_done, 1)

        @block.vector
        def _(dve):
            def weights(G, b, turn):
                dve.wait_ge(g_ld[b], 16 * turn + 16)
                dve.wait_ge(down_done, KD * G + 1)
                for e in range(EG):
                    dve.wait_ge(gelu_done, EG * G + (e + GELU0 + 1))
                    nc.vector.tensor_tensor(wt[:, b, e], act_[:, e % 2], gt[:, b, :, e], ALU.mult).then_inc(weighted, 1)

            def sums(G):
                for c in range(KD):
                    dve.wait_ge(down_done, KD * G + (c + OD0 + 1))
                    h = k.hT[:, c].rearrange("p (h n) -> p h n", h=2)
                    nc.vector.tensor_tensor(h, h, ps[:, 4 + 2 * (c % 2):6 + 2 * (c % 2), 0:HALF], ALU.add).then_inc(added, 1)

            dve.sem_inc(weighted, WD0)
            dve.sem_inc(added, ADD0)
            weights(0, 0, 0)
            with dve.Fori(0, NG // 2 - 1) as i:
                weights(2 * i + 1, 1, i)
                sums(2 * i)
                weights(2 * i + 2, 0, i + 1)
                sums(2 * i + 1)
            weights(NG - 1, 1, NG // 2 - 1)
            sums(NG - 2)
            sums(NG - 1)

        @block.tensor
        def _(pe):
            def up(G, b, turn):
                pe.wait_ge(u_ld[b], 16 * turn + 16)
                for e in range(EG):
                    pe.wait_ge(gelu_done, EG * G + (e + 1))
                    for h in range(2):
                        for i in range(KD):
                            mm = nc.tensor.matmul(ps[:, 2 * (e % 2) + h, 0:HALF], ut[:, b, e, i], k.hn[:, i, HALF * h:HALF * h + HALF],
                                                  start=(i == 0), stop=(i == KD - 1))
                    mm.then_inc(up_done, 1)

            def down(G, b, turn):
                pe.wait_ge(v_ld[b], 16 * turn + 16)
                pe.wait_ge(weighted, EG * G + (EG + WD0))
                for c in range(KD):
                    pe.wait_ge(added, KD * G + (c + 1))
                    for h in range(2):
                        for e in range(EG):
                            mm = nc.tensor.matmul(ps[:, 4 + 2 * (c % 2) + h, 0:HALF], vt[:, b, e, P * c:P * c + P],
                                                  wt[:, b, e, HALF * h:HALF * h + HALF], start=(e == 0), stop=(e == EG - 1))
                    mm.then_inc(down_done, 1)

            pe.sem_inc(up_done, UD0)
            pe.sem_inc(down_done, OD0)
            up(0, 0, 0)
            with pe.Fori(0, NG // 2 - 1) as i:
                up(2 * i + 1, 1, i)
                down(2 * i, 0, i)
                up(2 * i + 2, 0, i + 1)
                down(2 * i + 1, 1, i)
            up(NG - 1, 1, NG // 2 - 1)
            down(NG - 2, 0, NG // 2 - 1)
            down(NG - 1, 1, NG // 2 - 1)


def ple_stage(nc, k):
    with ExitStack() as ctx:
        sb = lambda n, s, d=F32: ctx.enter_context(nc.sbuf_tensor(n, s, d))
        sem = k.sem
        wg, wp, pT, gp = sb("w_gate_sb", [P, KD, D]), sb("w_proj_sb", [P, 2, D]), sb("ple_T", [P, 2, T]), sb("g_ple_sb", [P, KD])
        sq, rinv, gate = sb("l_sq", [P, KD, T]), sb("l_rinv", [P, T]), sb("l_gate", [P, 4, HALF])
        ps = ctx.enter_context(nc.psum_tensor("l_ps", [P, 8, 512], F32))
        ld, sqd, ssq, msr, rir, hr, gd, pd, sg, out, vch = (sem(n) for n in (
            "l_ld", "l_sqd", "l_ssq", "l_msr", "l_rir", "l_hr", "l_gd", "l_pd", "l_sg", "l_out", "l_v"))
        block = ctx.enter_context(nc.Block())

        @block.sync
        def _(sp):
            for dst, src in ((wg, k.d["w_gate"]), (wp, k.d["w_proj"]), (pT, k.d["ple_in"]), (gp, k.d["g_ple"])):
                sp.dma_start(dst[:], src).then_inc(ld, 16)
            for c in range(KD):
                sp.wait_ge(out, 2 * c + 2)
                sp.dma_start(k.o["yT"][:, c], k.hT[:, c]).then_inc(k.stored, 16)
            k.n_stored += 16 * KD

        @block.scalar
        def _(act):
            for c in range(KD):
                nc.scalar.activation(sq[:, c], k.hT[:, c], ACT.Square).then_inc(sqd, 1)
            act.wait_ge(msr, 1)
            nc.scalar.activation(rinv[:], rinv[:], ACT.Sqrt).then_inc(rir, 1)
            for u in range(16):
                act.wait_ge(gd, u + 1)
                if u >= 4:
                    act.wait_ge(out, u - 3)
                nc.scalar.activation(gate[:, u % 4], ps[:, u % 4, 0:HALF], ACT.Sigmoid).then_inc(sg, 1)

        @block.vector
        def _(dve):
            v = Chain(dve, vch)
            V = nc.vector
            dve.wait_ge(ssq, 1)
            for h in range(2):
                v.go(V.tensor_scalar(rinv[:, HALF * h:HALF * h + HALF], ps[:, 6 + h, 0:HALF], 1.0 / D, EPS, ALU.mult, ALU.add))
            v.wait()
            V.reciprocal(rinv[:], rinv[:]).then_inc(msr, 1)
            dve.wait_ge(rir, 1)
            dve.wait_ge(ld, 64)
            for c in range(KD):
                V.scalar_tensor_tensor(out=k.hn[:, c], in0=k.hT[:, c], scalar=gp[:, c:c + 1], in1=rinv[:],
                                       op0=ALU.mult, op1=ALU.mult).then_inc(hr, 1)
            for u in range(16):
                c, h = u // 2, u % 2
                dve.wait_ge(sg, u + 1)
                dve.wait_ge(pd, u + 1)
                v(V.tensor_tensor(gate[:, u % 4], gate[:, u % 4], ps[:, 4 + u % 4, 0:HALF], ALU.mult))
                hs = k.hT[:, c, HALF * h:HALF * h + HALF]
                V.tensor_tensor(hs, hs, gate[:, u % 4], ALU.add).then_inc(out, 1)

        @block.tensor
        def _(pe):
            for c in range(KD):
                pe.wait_ge(sqd, c + 1)
                for h in range(2):
                    mm = nc.tensor.matmul(ps[:, 6 + h, 0:HALF], k.ones[:], sq[:, c, HALF * h:HALF * h + HALF],
                                          start=(c == 0), stop=(c == KD - 1))
            mm.then_inc(ssq, 1)
            pe.wait_ge(ld, 64)
            pe.wait_ge(hr, KD)
            for u in range(16):
                c, h = u // 2, u % 2
                if u >= 4:
                    pe.wait_ge(sg, u - 3)
                    pe.wait_ge(out, u - 3)
                for i in range(KD):
                    mm = nc.tensor.matmul(ps[:, u % 4, 0:HALF], wg[:, i, P * c:P * c + P], k.hn[:, i, HALF * h:HALF * h + HALF],
                                          start=(i == 0), stop=(i == KD - 1))
                mm.then_inc(gd, 1)
                for i in range(2):
                    mm = nc.tensor.matmul(ps[:, 4 + u % 4, 0:HALF], wp[:, i, P * c:P * c + P], pT[:, i, HALF * h:HALF * h + HALF],
                                          start=(i == 0), stop=(i == 1))
                mm.then_inc(pd, 1)


EARLY = [project_stage, ssm_stage, glu_stage, compress_stage, prompt_attention_stage, sample_attention_stage]
LATE = [mix_and_retrieve_stage, gate_matrix_stage, experts_stage, ple_stage]


def build(nc, d, o, upto=99):
    k = Shared()
    k.d, k.o, k.n_stored = d, o, 0
    with ExitStack() as ctx:
        held = []

        def stage_sem(name):
            held.append(nc.alloc_semaphore(name))
            return held[-1]

        k.sem = lambda n: ctx.enter_context(nc.semaphore(n))
        sb = lambda n, s, dt=F32: ctx.enter_context(nc.sbuf_tensor(n, s, dt))
        k.stored = k.sem("stored")
        k.u_loaded = k.sem("u_loaded")
        k.y_loaded = k.sem("y_loaded")
        k.ident = sb("ident", [P, P])
        k.ones = sb("ones", [P, P])
        k.hT = sb("hT", [P, KD, T])
        k.mixT = sb("mixT", [P, 8, T])
        with ExitStack() as early:
            sbe = lambda n, s, dt=F32: early.enter_context(nc.sbuf_tensor(n, s, dt))
            k.yT = k.mixT[:, 4:8]
            k.U = sbe("U", [P, GROUPS, CHUNKS])
            k.qT = sbe("qT", [P, 4, T])
            k.ksT = sbe("ksT", [P, T])
            k.kwT = sbe("kwT", [P, T])
            k.qk = sbe("qk_rows", [P, TILES, 768])
            k.kv = sbe("kv_rows", [P, TILES, 512])
            k.gates = sbe("gates", [P, TILES, 24])
            k.cmp = sbe("v_and_k_cmp", [P, 2, 9, P])
            k.vcmp, k.kcT = k.cmp[:, 0], k.cmp[:, 1]
            k.pages = sbe("page_table_sb", [1, P], I32)
            k.pages_ld = k.sem("pages_ld")
            k.cmp_prompt = sbe("cmp_prompt", [P, 4, 2, 2, 8, 8])
            keep, k.sem = k.sem, stage_sem
            for n, stage in enumerate(EARLY):
                if upto > n:
                    stage(nc, k)
        nc.clear_and_free_semaphores(held)
        nc.all_engine_barrier()
        k.sem = keep
        k.hn = sb("hn", [P, KD, T])
        k.idxT = sb("idx_T", [P, 3, T])
        k.gm_stored = [k.sem("gm_stored0"), k.sem("gm_stored1")]
        for n, stage in enumerate(LATE):
            if upto > n + len(EARLY):
                stage(nc, k)
        with nc.Block() as block:
            @block.sync
            def _(sp):
                sp.wait_ge(k.stored, k.n_stored)


def host_layout(i):
    f = lambda a: np.ascontiguousarray(np.asarray(a))
    a = {}
    kmaj = lambda m: f(m.reshape(-1, P, m.shape[1]).transpose(1, 0, 2))
    x = np.concatenate([np.asarray(i["x_prompt"])[0], np.asarray(i["x_sample"]).reshape(T_SAMPLE, D)], 0)
    a["xT"] = kmaj(x.T)
    a["g_mix"] = f(np.asarray(i["g_mix"])[0].reshape(KD, P).T)
    w = np.asarray(i["w_in"])[0]
    q = w[:, 512:1024].reshape(D, 2, REP, HD).transpose(0, 2, 1, 3).reshape(D, 512)
    cols = [w[:, 0:512], q, w[:, 1024:1152], w[:, 1152:1280], w[:, 1280:1408], w[:, 1408:1536], w[:, 1536:1664],
            w[:, 1664:1792], w[:, 1792:1816]]
    a["w_in"] = kmaj(np.concatenate(cols, 1))
    gq, gs, gw = (np.asarray(i[n])[0] for n in ("g_q", "g_k_sel", "g_k_win"))
    a["g_heads"] = f(np.concatenate([np.tile(gq, 8), np.tile(gs, 2), np.tile(gw, 2)])[None, :])

    def rope_table(pos):
        inv = np.power(np.float32(500000.0), -np.arange(8, dtype=np.float32) / 8)
        ang = pos.astype(np.float32)[:, None] * inv[None, :].astype(np.float32)
        return np.stack([np.cos(ang), np.sin(ang), -np.sin(ang)], 1).astype(np.float32)

    pos = np.concatenate([np.arange(T_PROMPT), np.tile(PAST + np.arange(STEPS), SEQS), np.zeros(64)])
    a["rope"] = f(rope_table(pos).reshape(TILES, P, 3, 8).transpose(1, 0, 2, 3))
    for n, name in enumerate(("cache_k_win", "cache_v_win")):
        a[f"win_rows{n}"] = f(np.asarray(i[name])[0].reshape(SEQS, 512, P))
    g = lambda n: np.asarray(i[n])[0]
    dup = lambda a, b: f(np.concatenate([a, b], 0))
    ar, ai = g("ssm_a_re").T, g("ssm_a_im").T
    a["a_re"], a["a_im"] = dup(ar, ar), dup(ai, ai)
    a["log_dt"] = f(g("ssm_log_dt")[None, :])
    br, bi = (g(n).transpose(1, 0, 2) for n in ("ssm_b_re", "ssm_b_im"))
    cr, ci = (g(n).transpose(2, 0, 1) for n in ("ssm_c_re", "ssm_c_im"))
    sr, si = (g(n).transpose(2, 1, 0) for n in ("state_ssm_re", "state_ssm_im"))
    a["b1"], a["b2"], a["c1"], a["c2"] = dup(br, bi), dup(bi, br), dup(cr, ci), dup(ci, cr)
    a["s0"], a["s0x"] = dup(sr, si), dup(si, sr)
    a["dT"] = f(g("ssm_d").reshape(GROUPS, CH).T)
    a["sigma"] = np.concatenate([np.ones((64, 1)), -np.ones((64, 1))]).astype(np.float32)
    a["swap"] = f(np.roll(np.eye(P, dtype=np.float32), 64, 1))
    a["w_glu"] = kmaj(g("ssm_w_glu"))
    a["b_glu"] = f(g("ssm_b_glu").reshape(4, P).T)
    a["g_out_ssm"] = f(g("g_out_ssm").reshape(4, P).T)
    ck, cv = g("cache_k_cmp"), g("cache_v_cmp")
    lay = lambda c: c.reshape(POOL, 8, 8, 2, 2, HD).transpose(0, 3, 5, 4, 2, 1).reshape(POOL, P, 1, 2, 8, 8)
    a["cmp_pool"] = f(np.concatenate([lay(ck), lay(cv)], 2).reshape(POOL, P, 256))
    w1 = np.stack([g("cmp_w1_k"), g("cmp_w1_v")])
    a["cmp_w1"] = f(w1.reshape(2, 16, P, P).transpose(2, 0, 1, 3))
    a["cmp_w2"] = f(np.stack([g("cmp_w2_k"), g("cmp_w2_v")]).transpose(1, 0, 2))
    a["cmp_pe"] = f(np.stack([g("cmp_pe_k"), g("cmp_pe_v")]).reshape(2, 16, P).transpose(2, 0, 1))
    a["cmp_rope"] = rope_table(16 * np.arange(P) + 31)
    a["g_k_cmp"] = f(g("g_k_cmp")[None, :])
    a["page_table"] = f(np.asarray(i["page_table"]).reshape(1, P))
    q = np.arange(P)
    a["causal"] = np.where(q[None, :] <= q[:, None], 0.0, NEG).astype(np.float32)
    end = 16 * np.arange(NCP) + 31
    ok = end[None, None, :] <= (P * np.arange(4)[None, :, None] + q[:, None, None])
    a["cmp_mask"] = np.where(ok, 0.0, NEG).astype(np.float32)
    a["cmp_valid"] = ok.any(2).astype(np.float32)
    rs, rg, rr, rt = (x.ravel() for x in np.meshgrid(np.arange(2), np.arange(2), np.arange(4), np.arange(8), indexing="ij"))
    a["same"] = ((rs[:, None] == rs) & (rg[:, None] == rg) & (rt[:, None] == rt)).astype(np.float32)
    tok = np.arange(64)
    a["pick"] = np.stack([(tok[:, None] == (2 * p + rs) * 8 + rt) for p in range(PAIRS)], 1).astype(np.float32)
    a["mine"] = (np.arange(8)[None, :] == (rg * REP + rr)[:, None]).astype(np.float32)
    new = [(tok[None, :] // 8 == (2 * p + rs)[:, None]) & (tok[None, :] % 8 <= rt[:, None]) for p in range(PAIRS)]
    a["new_mask"] = np.where(np.stack(new, 1), 0.0, NEG).astype(np.float32)
    a["win_mask"] = np.where(np.arange(8)[None, :] <= rt[:, None], NEG, 0.0).astype(np.float32)
    a["force"] = np.tile(np.where(np.isin(np.arange(NSEL), (0, 31, 32)), 1000.0, 0.0).astype(np.float32), (P, 1))
    sk = g("cache_k_sel").transpose(0, 2, 3, 1).reshape(POOL, P, P)
    a["sel_pool"] = f(np.concatenate([sk, g("cache_v_sel").reshape(POOL, P, P)], 2))
    a["win_kT"] = f(g("cache_k_win").transpose(0, 2, 3, 1).reshape(SEQS, P, 512))
    wo = g("w_out")
    a["w_out"] = kmaj(np.concatenate([wo[:512], wo[512:].reshape(2, REP, HD, D).transpose(1, 0, 2, 3).reshape(512, D)]))
    a["g_out_attn"] = f(g("g_out_attn").reshape(2, REP, HD).transpose(0, 2, 1).reshape(P, REP))
    a["g_ffn"], a["g_ple"] = (f(g(n).reshape(KD, P).T) for n in ("g_ffn", "g_ple"))
    a["w_q"], a["w_gate"], a["w_proj"] = (kmaj(g(n)) for n in ("peer_w_q", "ple_w_gate", "ple_w_proj"))
    a["subkeys"] = f(g("peer_subkeys").reshape(16, KEYS, P).transpose(2, 0, 1))
    a["iota16"] = np.tile(np.arange(16, dtype=np.float32), (P, 1))
    a["iota128"] = np.tile(np.arange(P, dtype=np.float32), (P, 1))
    a["u_tab"] = f(g("peer_u").reshape(KEYS, NG, EG, KD, P).transpose(1, 4, 2, 3, 0).reshape(NG, P, EG * KD * P))
    a["v_tab"] = f(g("peer_v").reshape(KEYS, NG, EG * D))
    ple = np.concatenate([g("p_prompt")[0], g("p_sample").reshape(T_SAMPLE, -1)], 0)
    a["ple_in"] = kmaj(ple.T)
    return a


OUTS = {"yT": [P, KD, T], "ssm_state": [P, GROUPS, 9],
        **{f"rows_p{n}": [T_PROMPT, P] for n in range(6)},
        **{f"rows_s{n}": [T_SAMPLE, P] for n in range(4)},
        **{f"rows_s{n}": [SEQS, 512, P] for n in (4, 5)}}
SCRATCH = {"u_scr": [512, 8, CHUNKS], "y_scr": [512, 8, CHUNKS],
           "gate_scr": [NG, P, NTB, TB * EG]}


def declare_and_build(nc, arrays, upto=99):
    d = {n: nc.dram_tensor("in_" + n, a.shape, mybir.dt.from_np(a.dtype), kind="ExternalInput").ap()
         for n, a in arrays.items()}
    d.update({n: nc.dram_tensor(n, s, F32, kind="Internal").ap() for n, s in SCRATCH.items()})
    o = {n: nc.dram_tensor(n, s, F32, kind="ExternalOutput").ap() for n, s in OUTS.items()}
    d["win_rows"] = [d["win_rows0"], d["win_rows1"]]
    o["rows_p"], o["rows_s"] = ([o[f"rows_{x}{n}"] for n in range(6)] for x in "ps")
    build(nc, d, o, upto)


def kernel(**inputs):
    import concourse.bacc as bacc
    from concourse.bass_utils import run_bass_kernel_spmd
    arrays = host_layout(inputs)
    nc = bacc.Bacc("TRN2", target_bir_lowering=False, num_devices=1)
    declare_and_build(nc, arrays)
    r = run_bass_kernel_spmd(nc, [{"in_" + n: v for n, v in arrays.items()}], core_ids=[0]).results[0]
    y = r["yT"].transpose(2, 1, 0).reshape(T, D)
    st = r["ssm_state"].reshape(2, HD, GROUPS, 9).transpose(0, 3, 2, 1)
    kvp = [r[f"rows_p{n}"].reshape(1, 1, T_PROMPT, 2, HD) for n in range(6)]
    kvs = [r[f"rows_s{n}"].reshape(1, SEQS, -1, 2, HD) for n in range(6)]
    c = np.ascontiguousarray
    return (c(y[:T_PROMPT])[None], c(y[T_PROMPT:]).reshape(SEQS, STEPS, D), *kvp, c(st[0, 0])[None, None],
            c(st[1, 0])[None, None], *kvs, c(st[0, 1:])[None], c(st[1, 1:])[None])
```

```python
from contextlib import ExitStack
import math

import numpy as np
import concourse.bass as bass
from concourse import mybir
from concourse.alu_op_type import AluOpType as ALU

F32 = mybir.dt.float32
I32 = mybir.dt.int32
U32 = mybir.dt.uint32
ACT = mybir.ActivationFunctionType
AX = mybir.AxisListType

P = 128
D = 1024
KD = D // P
T_PROMPT = 512
SEQS = 8
STEPS = 8
T_SAMPLE = SEQS * STEPS
T = T_PROMPT + T_SAMPLE
HALF = T // 2
TILES = 5
TILE_ROWS = [128, 128, 128, 128, 64]
CHUNKS = T // 8
PROMPT_CHUNKS = T_PROMPT // 8
GROUPS = 32
CH = 16
HD = 64
REP = 4
PAST = 2048
PAGES = 16
POOL = 160
NBLK = 128
EPS = 1e-6
NEG = -1e30
GONE = -3e38
SCALE = HD ** -0.5
KEYS = 128
PH = 8
TOPK = 16
WCOLS = 1816
ZQ, ZB, ZC = 512, 1024, 1536


class Shared:
    pass


class Chain:

    def __init__(self, eng, sem):
        self.eng, self.sem, self.n = eng, sem, 0

    def go(self, ins):
        self.n += 1
        ins.then_inc(self.sem, 1)

    def wait(self):
        self.eng.wait_ge(self.sem, self.n)

    def __call__(self, ins):
        self.go(ins)
        self.wait()


def project_stage(nc, k):
    with ExitStack() as ctx:
        sb = lambda n, s, d=F32: ctx.enter_context(nc.sbuf_tensor(n, s, d))
        sem = k.sem
        w = sb("w_in_sb", [P, KD, WCOLS])
        sq = sb("x_squared", [P, KD, T])
        norm = sb("a_T", [P, KD, T])
        rinv = sb("x_rinv", [P, T])
        gmix = sb("g_mix_sb", [P, KD])
        g12 = sb("head_gains", [P, 768])
        rope = sb("rope_sb", [P, TILES, 3, 8])
        hsq = sb("head_squares", [P, 2, 768])
        ms = sb("head_ms", [P, 2, 3, 12])
        ra = sb("rope_a", [P, 12, 16])
        rb = sb("rope_b", [P, 12, 16])
        um = k.mixT[:, 0:4].rearrange("p i (j c) -> p i j c", j=8)
        pz = ctx.enter_context(nc.psum_tensor("pz", [P, 2, 3, 512], F32))
        pu = ctx.enter_context(nc.psum_tensor("pu", [P, 2, 512], F32))
        ld_x, ld_w, ld_c = sem("ld_x"), sem("ld_w"), sem("ld_c")
        squared, ssq_done, ms_ready, rinv_ready = sem("x_sq"), sem("ssq"), sem("x_ms"), sem("x_ri")
        a_ready, u_done, u_free, z_done, z_free = sem("a_rdy"), sem("u_done"), sem("u_free"), sem("z_done"), sem("z_free")
        hsq_ready, hms_ready, hri_ready, rows_ready = sem("hsq"), sem("hms"), sem("hri"), sem("rows")
        tr_done, tr_free, tr_dve = sem("tr_done"), sem("tr_free"), sem("tr_dve")
        kv_copied, ustore, ust, v_ch, const_ready = sem("kv_cp"), sem("u_st"), sem("u_sto"), sem("p_vch"), sem("const")
        gate_ready = sem("gate_rdy")
        block = ctx.enter_context(nc.Block())

        @block.sync
        def _(sp):
            for h in range(2):
                sp.dma_start(k.hT[:, 4 * h:4 * h + 4, :], k.d["xT"][:, 4 * h:4 * h + 4, :]).then_inc(ld_x, 16)
            sp.dma_start(gmix[:], k.d["g_mix"]).then_inc(ld_c, 16)
            sp.dma_start(g12[:], k.d["g_heads"].to_broadcast([P, 768])).then_inc(ld_c, 16)
            sp.dma_start(rope[:], k.d["rope"]).then_inc(ld_c, 16)
            for i in range(KD):
                sp.dma_start(w[:, i, :], k.d["w_in"][:, i, :]).then_inc(ld_w, 16)
            for i in range(4):
                sp.wait_ge(u_free, 2 * i + 2)
                sp.dma_start(k.d["u_scr"][P * i:P * i + P], um[:, i]).then_inc(ust, 16)
            sp.wait_ge(ust, 64)
            for j in range(8):
                sp.dma_start(k.U[16 * j:16 * j + 16],
                             k.d["u_scr"][:, j, :].rearrange("(g c) n -> c g n", c=CH)).then_inc(k.u_loaded, 16)
            sp.wait_ge(rows_ready, TILES)
            sp.wait_ge(kv_copied, TILES)
            for n, src in enumerate((k.kv[:, :, 0:128], k.kv[:, :, 128:256], k.qk[:, :, 512:640],
                                     k.kv[:, :, 256:384], k.qk[:, :, 640:768], k.kv[:, :, 384:512])):
                sp.dma_start(k.o["rows_p"][n].rearrange("(a p) f -> p a f", p=P), src[:, 0:4]).then_inc(k.stored, 16)
                if n < 4:
                    sp.dma_start(k.o["rows_s"][n], src[0:64, 4]).then_inc(k.stored, 16)
                else:
                    for s in range(SEQS):
                        sp.dma_start(k.o["rows_s"][n][s, 504:512, :], src[8 * s:8 * s + 8, 4]).then_inc(k.stored, 16)
            k.n_stored += 16 * (6 + 4 + 16)
            for n in range(2):
                sp.dma_start(k.o["rows_s"][4 + n][:, 0:504, :], k.d["win_rows"][n][:, 8:512, :]).then_inc(k.stored, 16)
            k.n_stored += 32

        @block.gpsimd
        def _(pool):
            pool.memset(k.ident[:], 0.0).then_inc(const_ready, 1)
            pool.memset(k.ones[:], 1.0).then_inc(const_ready, 1)
            pool.wait_ge(const_ready, 2)
            pool.affine_select(out=k.ident[:], in_=k.ident[:], compare_op=ALU.not_equal, fill=1.0, base=0,
                               pattern=[[-1, P]], channel_multiplier=1).then_inc(const_ready, 1)

        @block.scalar
        def _(act):
            for i in range(KD):
                if i % 4 == 0:
                    act.wait_ge(ld_x, 32)
                nc.scalar.activation(sq[:, i, :], k.hT[:, i, :], ACT.Square).then_inc(squared, 1)
            act.wait_ge(ms_ready, 1)
            nc.scalar.activation(rinv[:], rinv[:], ACT.Sqrt).then_inc(rinv_ready, 1)
            for i in range(4):
                for h in range(2):
                    act.wait_ge(u_done, 2 * i + h + 1)
                    nc.scalar.activation(um[:, i, :, 36 * h:36 * h + 36],
                                         pu[:, h, 0:HALF].rearrange("p (c j) -> p j c", j=8),
                                         ACT.Copy).then_inc(u_free, 1)
            for t in range(TILES):
                m, b = TILE_ROWS[t], t % 2
                act.wait_ge(z_done, t + 1)
                if t >= 2:
                    act.wait_ge(rows_ready, t - 1)
                nc.scalar.activation(hsq[0:m, b, 0:512], pz[0:m, b, 0, :], ACT.Square).then_inc(hsq_ready, 1)
                nc.scalar.activation(hsq[0:m, b, 512:640], pz[0:m, b, 1, 256:384], ACT.Square).then_inc(hsq_ready, 1)
                nc.scalar.activation(hsq[0:m, b, 640:768], pz[0:m, b, 2, 0:128], ACT.Square).then_inc(hsq_ready, 1)
                nc.scalar.activation(k.kv[0:m, t, 0:256], pz[0:m, b, 1, 0:256], ACT.Copy)
                nc.scalar.activation(k.kv[0:m, t, 256:384], pz[0:m, b, 1, 384:512], ACT.Copy)
                nc.scalar.activation(k.kv[0:m, t, 384:512], pz[0:m, b, 2, 128:256], ACT.Copy)
                nc.scalar.activation(k.gates[0:m, t, :], pz[0:m, b, 2, 256:280], ACT.Copy).then_inc(kv_copied, 1)
                act.wait_ge(hms_ready, t + 1)
                nc.scalar.activation(ms[0:m, b, 2, :], ms[0:m, b, 1, :], ACT.Sqrt).then_inc(hri_ready, 1)
            for t in range(TILES):
                m, b = TILE_ROWS[t], t % 2
                act.wait_ge(tr_done, t + 1)
                for i in range(4):
                    nc.scalar.activation(k.qT[:, i, P * t:P * t + m], pz[:, b, 0, P * i:P * i + m], ACT.Copy)
                nc.scalar.activation(k.ksT[:, P * t:P * t + m], pz[:, b, 1, 0:m], ACT.Copy)
                nc.scalar.activation(k.kwT[:, P * t:P * t + m], pz[:, b, 1, 128:128 + m], ACT.Copy).then_inc(tr_free, 1)
            act.wait_ge(kv_copied, TILES)
            for t in (0, 4):
                m, e = (128, 4) if t == 0 else (64, 5)
                nc.scalar.activation(k.gates[0:m, t:e, :], k.gates[0:m, t:e, :], ACT.Exp, scale=-1.0).then_inc(gate_ready, 1)

        @block.vector
        def _(dve):
            v = Chain(dve, v_ch)
            dve.wait_ge(ssq_done, 1)
            for h in range(2):
                v.go(nc.vector.tensor_scalar(rinv[:, HALF * h:HALF * h + HALF], pu[:, h, 0:HALF], 1.0 / D, EPS,
                                             ALU.mult, ALU.add))
            v.wait()
            nc.vector.reciprocal(rinv[:], rinv[:]).then_inc(ms_ready, 1)
            dve.wait_ge(rinv_ready, 1)
            dve.wait_ge(ld_c, 48)
            dve.wait_ge(ld_x, 32)
            for i in range(KD):
                nc.vector.scalar_tensor_tensor(out=norm[:, i, :], in0=k.hT[:, i, :], scalar=gmix[:, i:i + 1],
                                               in1=rinv[:], op0=ALU.mult, op1=ALU.mult).then_inc(a_ready, 1)
            for t in range(TILES):
                m, b = TILE_ROWS[t], t % 2
                dve.wait_ge(hsq_ready, 3 * t + 3)
                v(nc.vector.tensor_reduce(ms[0:m, b, 0, :], hsq[0:m, b, :].rearrange("p (h d) -> p h d", d=HD),
                                          AX.X, ALU.add))
                v(nc.vector.tensor_scalar(ms[0:m, b, 0, :], ms[0:m, b, 0, :], 1.0 / HD, EPS, ALU.mult, ALU.add))
                nc.vector.reciprocal(ms[0:m, b, 1, :], ms[0:m, b, 0, :]).then_inc(hms_ready, 1)
                dve.wait_ge(hri_ready, t + 1)
                qk3 = k.qk[0:m, t, :].rearrange("p (h d) -> p h d", d=HD)
                for lo, hi, src in ((0, 8, pz[0:m, b, 0, :]), (8, 10, pz[0:m, b, 1, 256:384]),
                                    (10, 12, pz[0:m, b, 2, 0:128])):
                    v.go(nc.vector.tensor_tensor(qk3[:, lo:hi], src.rearrange("p (h d) -> p h d", d=HD),
                                                 ms[0:m, b, 2, lo:hi].unsqueeze(2).to_broadcast([m, hi - lo, HD]),
                                                 ALU.mult))
                dve.wait_ge(kv_copied, t + 1)
                v.wait()
                v(nc.vector.tensor_tensor(k.qk[0:m, t, :], k.qk[0:m, t, :], g12[0:m, :], ALU.mult))
                cos, sin, nsin = (rope[0:m, t, i, :].unsqueeze(1).to_broadcast([m, 12, 8]) for i in range(3))
                x1, x2 = qk3[:, :, 0:8], qk3[:, :, 8:16]
                v.go(nc.vector.tensor_tensor(ra[0:m, :, 0:8], x1, cos, ALU.mult))
                v.go(nc.vector.tensor_tensor(ra[0:m, :, 8:16], x2, cos, ALU.mult))
                v.go(nc.vector.tensor_tensor(rb[0:m, :, 0:8], x2, nsin, ALU.mult))
                v(nc.vector.tensor_tensor(rb[0:m, :, 8:16], x1, sin, ALU.mult))
                nc.vector.tensor_tensor(qk3[:, :, 0:16], ra[0:m], rb[0:m], ALU.add).then_inc(rows_ready, 1)
            for t in range(4):
                dve.wait_ge(tr_done, t + 1)
                for kv in range(2):
                    for g in range(2):
                        for r2 in range(2):
                            src = pz[g * 64:g * 64 + 64, t % 2, 2, P * kv:P * kv + P]
                            last = nc.vector.tensor_copy(k.cmp_prompt[r2 * 64:r2 * 64 + 64, t, kv, g],
                                                         src.rearrange("p (b i r) -> p r i b", r=2, i=8)[:, r2])
                last.then_inc(tr_dve, 1)
            for n, (t, e, m) in enumerate(((0, 4, 128), (4, 5, 64))):
                dve.wait_ge(gate_ready, n + 1)
                v(nc.vector.tensor_scalar(k.gates[0:m, t:e, :], k.gates[0:m, t:e, :], 1.0, None, ALU.add))
                v(nc.vector.reciprocal(k.gates[0:m, t:e, :], k.gates[0:m, t:e, :]))

        @block.tensor
        def _(pe):
            pe.wait_ge(const_ready, 3)
            for i in range(KD):
                pe.wait_ge(squared, i + 1)
                for h in range(2):
                    mm = nc.tensor.matmul(pu[:, h, 0:HALF], k.ones[:], sq[:, i, HALF * h:HALF * h + HALF],
                                          start=(i == 0), stop=(i == KD - 1))
            mm.then_inc(ssq_done, 1)
            pe.wait_ge(a_ready, KD)
            pe.wait_ge(ld_w, 16 * KD)
            for c in range(4):
                for h in range(2):
                    if c:
                        pe.wait_ge(u_free, 2 * (c - 1) + h + 1)
                    for i in range(KD):
                        mm = nc.tensor.matmul(pu[:, h, 0:HALF], w[:, i, P * c:P * c + P],
                                              norm[:, i, HALF * h:HALF * h + HALF], start=(i == 0), stop=(i == KD - 1))
                    mm.then_inc(u_done, 1)
            for t in range(TILES):
                m, b = TILE_ROWS[t], t % 2
                if t >= 2:
                    pe.wait_ge(rows_ready, t - 1)
                    pe.wait_ge(kv_copied, t - 1)
                for bank, (lo, n) in enumerate(((ZQ, 512), (ZB, 512), (ZC, 280))):
                    for i in range(KD):
                        mm = nc.tensor.matmul(pz[0:m, b, bank, 0:n], norm[:, i, P * t:P * t + m], w[:, i, lo:lo + n],
                                              start=(i == 0), stop=(i == KD - 1))
                mm.then_inc(z_done, 1)
            for t in range(TILES):
                m, b = TILE_ROWS[t], t % 2
                pe.wait_ge(rows_ready, TILES)
                pe.wait_ge(kv_copied, TILES)
                if t >= 2:
                    pe.wait_ge(tr_free, t - 1)
                    pe.wait_ge(tr_dve, t - 1)
                for i in range(6):
                    dst = pz[:, b, 0, P * i:P * i + m] if i < 4 else pz[:, b, 1, P * (i - 4):P * (i - 4) + m]
                    mm = nc.tensor.transpose(dst, k.qk[0:m, t, P * i:P * i + P], k.ident[0:m, 0:m])
                if t < 4:
                    for kv in range(2):
                        mm = nc.tensor.transpose(pz[:, b, 2, P * kv:P * kv + P],
                                                 k.kv[:, t, P * kv:P * kv + P], k.ident[:])
                mm.then_inc(tr_done, 1)


VCH = [(0, 7), (7, 14), (14, 21), (21, 28), (28, 32)]
MAGIC = 12582912.0
TWO_PI_PARTS = (6.28125, 0.0019350051879882812, 3.019915981956753e-07)


def ssm_stage(nc, k):
    with ExitStack() as ctx:
        sb = lambda n, s, d=F32: ctx.enter_context(nc.sbuf_tensor(n, s, d))
        sem = k.sem
        are, aim, ldt = sb("a_re", [P, GROUPS]), sb("a_im", [P, GROUPS]), sb("log_dt", [P, GROUPS])
        bc4 = sb("b_and_c", [P, 4, GROUPS, CH])
        b1, b2, c1, c2 = (bc4[:, n] for n in range(4))
        s0, s0x = sb("s0", [P, GROUPS, SEQS]), sb("s0_swapped", [P, GROUPS, SEQS])
        dT, sg, perm = sb("dT", [CH, GROUPS]), sb("sigma", [P, 1]), sb("swap_matrix", [P, P])
        tmp = sb("s_tmp", [P, 8, GROUPS])
        x1, x2 = sb("x1", [P, GROUPS, CH]), sb("x2", [P, GROUPS, CH])
        pr, pi = sb("pow_re", [P, 9, GROUPS]), sb("pow_im", [P, 9, GROUPS])
        rr, ri = sb("rot8_re", [P, 7, GROUPS]), sb("rot8_im", [P, 7, GROUPS])
        m8 = sb("mag8", [P, GROUPS])
        A = sb("state_in", [P, GROUPS, 8, CH])
        cp = sb("state_out_w", [P, GROUPS, 9, CH])
        big1 = sb("s_big1", [P, 32 * GROUPS])
        ms_ = sb("state_in_T", [P, GROUPS, P])
        zw = sb("z_and_w", [P, 4, GROUPS, 64])
        hz = zw[0:CH].rearrange("p a g n -> p (a g n)").rearrange("p (g z n) -> p g z n", g=GROUPS, z=2)
        tz = A[:].rearrange("p g j c -> p g (j c)")
        vs = k.cmp[:].rearrange("p a s n -> p (a s n)").rearrange("p (g c) -> p g c", c=CHUNKS)
        z, w = zw[:, 0], zw[:, 1]
        rc, rs = (zw[:, n].rearrange("p g c -> p (g c)").rearrange("p (c g) -> p c g", c=64) for n in (2, 3))
        ss = ms_[:].rearrange("p g n -> p (g n)")[:, 0:GROUPS * CHUNKS].rearrange("p (g c) -> p g c", c=CHUNKS)
        st = sb("s_final", [P, GROUPS, 9])
        ps = ctx.enter_context(nc.psum_tensor("ps_ssm", [P, 8, 512], F32))
        ld, ld0, vch, dt_r, mag_in, mag_r, ang_r, trig_r = (sem(n) for n in (
            "s_ld", "s_ld0", "s_vch", "s_dt", "s_magin", "s_mag", "s_ang", "s_trig"))
        a_ready, tr_done, tr_free, h_done, h_free = (sem(n) for n in ("s_A", "s_tr", "s_trf", "s_h", "s_hf"))
        hz_zero, hz_ready, tz_ld, v_done, v_free, sw_done, sw_free = (sem(n) for n in (
            "s_hz0", "s_hz", "s_tz", "s_v", "s_vf", "s_sw", "s_swf"))
        scan_ready, sb_done, sb_free, ss_ready, st_ready, y_done, y_free, y_st = (sem(n) for n in (
            "s_scan", "s_sb", "s_sbf", "s_ss", "s_stf", "s_y", "s_yf", "s_yst"))
        y = vs
        block = ctx.enter_context(nc.Block())

        @block.sync
        def _(sp):
            for dst, src in ((are[:], k.d["a_re"]), (aim[:], k.d["a_im"]), (sg[:], k.d["sigma"]), (b1, k.d["b1"]), (b2, k.d["b2"]),
                             (c1, k.d["c1"]), (c2, k.d["c2"]), (dT[:], k.d["dT"]), (perm[:], k.d["swap"])):
                sp.dma_start(dst, src).then_inc(ld, 16)
            sp.dma_start(ldt[:], k.d["log_dt"].to_broadcast([P, GROUPS])).then_inc(ld0, 16)
            sp.dma_start(s0[:], k.d["s0"]).then_inc(ld, 16)
            sp.dma_start(s0x[:], k.d["s0x"]).then_inc(ld, 16)
            sp.wait_ge(hz_ready, 1)
            for j in range(8):
                zeros = (8 - j) * CH
                sp.dma_start(tz[CH * j:CH * j + CH],
                             hz.rearrange("c g z n -> c g (z n)")[:, :, zeros:zeros + P]).then_inc(tz_ld, 16)
            sp.wait_ge(st_ready, 2)
            sp.dma_start(k.o["ssm_state"], st[:]).then_inc(k.stored, 16)
            k.n_stored += 16
            sp.wait_ge(y_free, 5)
            for j in range(8):
                sp.dma_start(k.d["y_scr"][:, j, :].rearrange("(g c) n -> c g n", c=CH), y[CH * j:CH * j + CH]).then_inc(y_st, 16)
            sp.wait_ge(y_st, 128)
            sp.dma_start(k.yT[:], k.d["y_scr"].rearrange("(i p) j n -> p i (j n)", p=P)).then_inc(k.y_loaded, 16)

        @block.gpsimd
        def _(pool):
            pool.memset(hz, 0.0).then_inc(hz_zero, 1)

        @block.scalar
        def _(act):
            act.wait_ge(ld0, 16)
            nc.scalar.activation(ldt[:], ldt[:], ACT.Exp).then_inc(dt_r, 1)
            act.wait_ge(mag_in, 1)
            nc.scalar.activation(tmp[:, 0], tmp[:, 0], ACT.Exp).then_inc(mag_r, 1)
            act.wait_ge(ang_r, 1)
            nc.scalar.activation(tmp[:, 2], tmp[:, 2], ACT.Sin).then_inc(trig_r, 1)
            nc.scalar.activation(tmp[:, 3], tmp[:, 3], ACT.Sin).then_inc(trig_r, 1)
            for i in range(8):
                act.wait_ge(tr_done, i + 1)
                nc.scalar.activation(ms_[:, 4 * i:4 * i + 4, :], ps[:, i % 3, :].rearrange("p (g n) -> p g n", g=4),
                                     ACT.Copy).then_inc(tr_free, 1)
            act.wait_ge(hz_zero, 1)
            for i in range(8):
                act.wait_ge(h_done, i + 1)
                nc.scalar.activation(hz[:, 4 * i:4 * i + 4, 1, :], ps[0:CH, 3 + i % 3, :].rearrange("p (g n) -> p g n", g=4),
                                     ACT.Copy).then_inc(h_free, 1)
            for q, (g0, g1) in enumerate(VCH):
                act.wait_ge(v_done, q + 1)
                nc.scalar.activation(vs[:, g0:g1, :], ps[:, q, 0:(g1 - g0) * CHUNKS].rearrange("p (g c) -> p g c", c=CHUNKS),
                                     ACT.Copy).then_inc(v_free, 1)
            act.wait_ge(st_ready, 2)
            for q, (g0, g1) in enumerate(VCH):
                act.wait_ge(y_done, q + 1)
                nc.scalar.activation(y[:, g0:g1, :], ps[:, q, 0:(g1 - g0) * CHUNKS].rearrange("p (g c) -> p g c", c=CHUNKS),
                                     ACT.Copy).then_inc(y_free, 1)

        @block.vector
        def _(dve):
            v = Chain(dve, vch)
            tt = lambda o, a, b, op: nc.vector.tensor_tensor(o, a, b, op)
            scratch = big1[:]

            def cmul(outr, outi, ar, ai, br, bi, shape):
                t1 = scratch[:, 0:shape[0] * shape[1]].rearrange("p (a b) -> p a b", a=shape[0])
                v.go(tt(outr, ar, br, ALU.mult))
                v.go(tt(outi, ar, bi, ALU.mult))
                v(tt(t1, ai, bi, ALU.mult))
                v(tt(outr, outr, t1, ALU.subtract))
                v(tt(t1, ai, br, ALU.mult))
                v(tt(outi, outi, t1, ALU.add))

            dve.wait_ge(ld, 16 * 11)
            dve.wait_ge(dt_r, 1)
            v(nc.vector.tensor_scalar(aim[:], aim[:], sg[:, 0:1], None, ALU.mult))
            tt(tmp[:, 0], are[:], ldt[:], ALU.mult).then_inc(mag_in, 1)
            v(tt(tmp[:, 1], aim[:], ldt[:], ALU.mult))
            v(nc.vector.tensor_scalar(tmp[:, 4], tmp[:, 1], 1.0 / (2 * math.pi), MAGIC, ALU.mult, ALU.add))
            v(nc.vector.tensor_scalar(tmp[:, 4], tmp[:, 4], -MAGIC, None, ALU.add))
            for part in TWO_PI_PARTS:
                v(nc.vector.scalar_tensor_tensor(out=tmp[:, 1], in0=tmp[:, 4], scalar=-part, in1=tmp[:, 1],
                                                 op0=ALU.mult, op1=ALU.add))
            v(nc.vector.tensor_scalar(tmp[:, 2], tmp[:, 1], 3.1415925, -3.1415925, ALU.min, ALU.max))
            v(nc.vector.tensor_scalar(tmp[:, 3], tmp[:, 2], -1.0, None, ALU.mult))
            v(tt(tmp[:, 3], tmp[:, 3], tmp[:, 2], ALU.max))
            nc.vector.tensor_scalar(tmp[:, 3], tmp[:, 3], -1.0, math.pi / 2, ALU.mult, ALU.add).then_inc(ang_r, 1)
            dve.wait_ge(mag_r, 1)
            dve.wait_ge(trig_r, 2)
            mag, sn, cs = tmp[:, 0], tmp[:, 2], tmp[:, 3]
            v.go(nc.vector.memset(pr[:, 0], 1.0))
            v.go(nc.vector.memset(pi[:, 0], 0.0))
            v.go(tt(pr[:, 1], mag, cs, ALU.mult))
            v(tt(pi[:, 1], mag, sn, ALU.mult))
            v.go(nc.vector.tensor_scalar(tmp[:, 4], pr[:, 1], -1.0, None, ALU.add))
            v.go(tt(tmp[:, 5], are[:], are[:], ALU.mult))
            v(tt(tmp[:, 6], aim[:], aim[:], ALU.mult))
            v(tt(tmp[:, 5], tmp[:, 5], tmp[:, 6], ALU.add))
            v(nc.vector.reciprocal(tmp[:, 5], tmp[:, 5]))
            v.go(tt(tmp[:, 6], tmp[:, 4], are[:], ALU.mult))
            v(tt(tmp[:, 7], pi[:, 1], aim[:], ALU.mult))
            v(tt(tmp[:, 6], tmp[:, 6], tmp[:, 7], ALU.add))
            v.go(tt(tmp[:, 7], pi[:, 1], are[:], ALU.mult))
            v(tt(tmp[:, 4], tmp[:, 4], aim[:], ALU.mult))
            v(tt(tmp[:, 7], tmp[:, 7], tmp[:, 4], ALU.subtract))
            v.go(tt(tmp[:, 6], tmp[:, 6], tmp[:, 5], ALU.mult))
            v(tt(tmp[:, 7], tmp[:, 7], tmp[:, 5], ALU.mult))
            bc = lambda a: a.unsqueeze(2).to_broadcast([P, GROUPS, CH])
            sc3 = scratch[:, 0:GROUPS * CH].rearrange("p (g c) -> p g c", c=CH)
            v.go(tt(x1[:], b1, bc(tmp[:, 6]), ALU.mult))
            v.go(tt(x2[:], b2, bc(tmp[:, 6]), ALU.mult))
            v(tt(sc3, b2, bc(tmp[:, 7]), ALU.mult))
            v(tt(x1[:], x1[:], sc3, ALU.subtract))
            v(tt(sc3, b1, bc(tmp[:, 7]), ALU.mult))
            v(tt(x2[:], x2[:], sc3, ALU.add))
            for n in (1, 2, 4):
                one = lambda t: t[:, n:n + 1, :].to_broadcast([P, n, GROUPS])
                cmul(pr[:, n + 1:2 * n + 1], pi[:, n + 1:2 * n + 1], pr[:, 1:n + 1], pi[:, 1:n + 1], one(pr), one(pi), (n, GROUPS))
            for j in range(8):
                v.go(tt(A[:, :, j, :], x1[:], bc(pr[:, 7 - j]), ALU.mult))
                v(tt(sc3, x2[:], bc(pi[:, 7 - j]), ALU.mult))
                last = tt(A[:, :, j, :], A[:, :, j, :], sc3, ALU.subtract)
                if j < 7:
                    v(last)
                else:
                    last.then_inc(a_ready, 1)
            dve.wait_ge(a_ready, 1)
            for l in range(9):
                v.go(tt(cp[:, :, l, :], c1, bc(pr[:, l]), ALU.mult))
                v(tt(sc3, c2, bc(pi[:, l]), ALU.mult))
                v(tt(cp[:, :, l, :], cp[:, :, l, :], sc3, ALU.subtract))
            nc.vector.tensor_scalar(cp[:].rearrange("p g l c -> p (g l c)"), cp[:].rearrange("p g l c -> p (g l c)"),
                                    sg[:, 0:1], None, ALU.mult).then_inc(a_ready, 1)
            v.go(nc.vector.tensor_copy(rr[:, 3:4, :], tmp[:, 3:4, :]))
            v(nc.vector.tensor_copy(ri[:, 3:4, :], tmp[:, 2:3, :]))
            src = 3
            for dst in (4, 5, 0):
                cmul(rr[:, dst:dst + 1], ri[:, dst:dst + 1], rr[:, src:src + 1], ri[:, src:src + 1],
                     rr[:, src:src + 1], ri[:, src:src + 1], (1, GROUPS))
                src = dst
            v(tt(m8[:], mag, mag, ALU.mult))
            v(tt(m8[:], m8[:], m8[:], ALU.mult))
            v(tt(m8[:], m8[:], m8[:], ALU.mult))
            dve.wait_ge(h_free, 8)
            dI = scratch[0:CH, 0:GROUPS * CH].rearrange("p (g c) -> p g c", c=CH)
            v(tt(dI, k.ident[0:CH, 0:CH].unsqueeze(1).to_broadcast([CH, GROUPS, CH]),
                 dT[:].unsqueeze(2).to_broadcast([CH, GROUPS, CH]), ALU.mult))
            tt(hz[:, :, 1, 0:CH], hz[:, :, 1, 0:CH], dI, ALU.add).then_inc(hz_ready, 1)
            gc = lambda t, g0, g1: t[:, :, g0:g1].rearrange("p c g -> p g c")
            dve.wait_ge(tz_ld, 128)
            v.go(nc.vector.memset(rc[:, 0], 1.0))
            v(nc.vector.memset(rs[:, 0], 0.0))
            for i in range(6):
                n = 1 << i
                step = lambda t: t[:, i:i + 1, :].to_broadcast([P, n, GROUPS])
                cmul(rc[:, n:2 * n], rs[:, n:2 * n], rc[:, 0:n], rs[:, 0:n], step(rr), step(ri), (n, GROUPS))
                if i < 5:
                    cmul(rr[:, i + 1:i + 2], ri[:, i + 1:i + 2], rr[:, i:i + 1], ri[:, i:i + 1],
                         rr[:, i:i + 1], ri[:, i:i + 1], (1, GROUPS))
            for q, (g0, g1) in enumerate(VCH):
                n = g1 - g0
                t3 = scratch[:, 0:n * 64].rearrange("p (g c) -> p g c", c=64)
                dve.wait_ge(v_free, q + 1)
                v.go(tt(z[:, g0:g1, :], vs[:, g0:g1, 0:64], gc(rc, g0, g1), ALU.mult))
                dve.wait_ge(sw_done, q + 1)
                last = tt(t3, ps[:, (5 + q) % 8, 0:n * CHUNKS].rearrange("p (g c) -> p g c", c=CHUNKS)[:, :, 0:64],
                          gc(rs, g0, g1), ALU.mult)
                last.then_inc(sw_free, 1)
                dve.wait_ge(sw_free, q + 1)
                v.wait()
                v(tt(z[:, g0:g1, :], z[:, g0:g1, :], t3, ALU.add))
            mg = bc4[:].rearrange("p a g c -> p (a g c)").rearrange("p (g c) -> p g c", c=64)
            v(nc.vector.tensor_copy(mg, m8[:].unsqueeze(2).to_broadcast([P, GROUPS, 64])))
            v(nc.vector.memset(mg[:, :, 0:1], 0.0))
            nc.vector.tensor_tensor_scan(w.rearrange("p g c -> p (g c)"), mg.rearrange("p g c -> p (g c)"),
                                         z.rearrange("p g c -> p (g c)"), 0.0, ALU.mult, ALU.add).then_inc(scan_ready, 1)
            dve.wait_ge(scan_ready, 1)
            v.go(nc.vector.memset(ss[:, :, 0:1], 0.0))
            v.go(nc.vector.tensor_copy(ss[:, :, 64:72], s0[:]))
            for q, (g0, g1) in enumerate(VCH):
                n = g1 - g0
                t3 = scratch[:, 0:n * 64].rearrange("p (g c) -> p g c", c=64)
                dve.wait_ge(sb_done, q + 1)
                v.go(tt(z[:, g0:g1, :], w[:, g0:g1, :], gc(rc, g0, g1), ALU.mult))
                tt(t3, ps[:, (5 + q) % 8, 0:n * 64].rearrange("p (g c) -> p g c", c=64), gc(rs, g0, g1),
                   ALU.mult).then_inc(sb_free, 1)
                dve.wait_ge(sb_free, q + 1)
                v.wait()
                v.go(tt(ss[:, g0:g1, 1:64], z[:, g0:g1, 0:63], t3[:, :, 0:63], ALU.subtract))
                v(tt(st[:, g0:g1, 0:1], z[:, g0:g1, 63:64], t3[:, :, 63:64], ALU.subtract))
            nc.vector.memset(tmp[:, 1], 0.0).then_inc(ss_ready, 1)
            b8 = lambda t: t[:, 8, :].unsqueeze(2).to_broadcast([P, GROUPS, SEQS])
            se = st[:, :, 1:9]
            v.go(tt(se, s0[:], b8(pr), ALU.mult))
            v(tt(s0x[:], s0x[:], b8(pi), ALU.mult))
            v(tt(se, se, s0x[:], ALU.subtract))
            tt(se, se, vs[:, :, 64:72], ALU.add).then_inc(st_ready, 2)

        @block.tensor
        def _(pe):
            pe.wait_ge(a_ready, 1)
            for i in range(8):
                if i >= 3:
                    pe.wait_ge(tr_free, i - 2)
                for g in range(4 * i, 4 * i + 4):
                    mm = nc.tensor.transpose(ps[:, i % 3, P * (g % 4):P * (g % 4) + P],
                                             A[:, g].rearrange("p j c -> p (j c)"), k.ident[:])
                mm.then_inc(tr_done, 1)
            pe.wait_ge(a_ready, 2)
            for i in range(8):
                if i >= 3:
                    pe.wait_ge(h_free, i - 2)
                for g in range(4 * i, 4 * i + 4):
                    mm = nc.tensor.matmul(ps[0:CH, 3 + i % 3, P * (g % 4):P * (g % 4) + P], x1[:, g, :],
                                          cp[:, g, 0:8, :].rearrange("p l c -> p (l c)"), start=True, stop=True)
                mm.then_inc(h_done, 1)
            pe.wait_ge(k.u_loaded, 128)
            pe.wait_ge(tr_free, 8)
            pe.wait_ge(h_free, 8)
            for q, (g0, g1) in enumerate(VCH):
                for g in range(g0, g1):
                    mm = nc.tensor.matmul(ps[:, q, CHUNKS * (g - g0):CHUNKS * (g - g0 + 1)], ms_[:, g, :], k.U[:, g, :],
                                          start=True, stop=True)
                mm.then_inc(v_done, 1)
            for q, (g0, g1) in enumerate(VCH):
                pe.wait_ge(v_free, q + 1)
                mm = nc.tensor.matmul(ps[:, (5 + q) % 8, 0:(g1 - g0) * CHUNKS], perm[:],
                                      vs[:, g0:g1, :].rearrange("p g c -> p (g c)"), start=True, stop=True)
                mm.then_inc(sw_done, 1)
            pe.wait_ge(scan_ready, 1)
            for q, (g0, g1) in enumerate(VCH):
                pe.wait_ge(sw_free, q + 1)
                nc.tensor.matmul(ps[:, (5 + q) % 8, 0:(g1 - g0) * 64], perm[:],
                                 w[:, g0:g1, :].rearrange("p g c -> p (g c)"), start=True, stop=True).then_inc(sb_done, 1)
            pe.wait_ge(tz_ld, 128)
            pe.wait_ge(ss_ready, 1)
            pe.wait_ge(sb_free, 5)
            for q, (g0, g1) in enumerate(VCH):
                for g in range(g0, g1):
                    dst = ps[:, q, CHUNKS * (g - g0):CHUNKS * (g - g0 + 1)]
                    nc.tensor.matmul(dst, tz[:, g, :], k.U[:, g, :], start=True, stop=False)
                    mm = nc.tensor.matmul(dst, cp[:, g, 1:9, :].rearrange("p l c -> p (l c)"), ss[:, g, :],
                                          start=False, stop=True)
                mm.then_inc(y_done, 1)


def gather_pages(eng, dst, pool, pages, first, loaded):
    with eng.Fori(0, 4) as i:
        at = [eng.value_load(pages[0:1, bass.ds(4 * i + (first + n), 1)], min_val=0, max_val=POOL - 1) for n in range(4)]
        for n in range(4):
            eng.dma_start(dst[:, bass.ds(4 * i + n, 1), :].rearrange("p o f -> p (o f)"),
                          pool[bass.ds(at[n], 1)].rearrange("o p f -> (o p) f")).then_inc(loaded, 16)


def glu_stage(nc, k):
    with ExitStack() as ctx:
        sb = lambda n, s, d=F32: ctx.enter_context(nc.sbuf_tensor(n, s, d))
        sem = k.sem
        w = sb("w_glu_sb", [P, 4, 512])
        bg, gs = sb("b_glu_sb", [P, 4]), sb("g_out_ssm_sb", [P, 4])
        sig, sq = sb("glu_sig", [P, 4, T]), sb("glu_sq", [P, 4, T])
        rinv = sb("glu_rinv", [P, T])
        ps = ctx.enter_context(nc.psum_tensor("ps_glu", [P, 4, 2, 512], F32))
        ld, ld_sm, zg, mmd, sigd, outd, sqd, ssqd, msd, rid, vch = (sem(n) for n in (
            "g_ld", "g_ls", "g_zg", "g_mm", "g_sig", "g_out", "g_sq", "g_ssq", "g_ms", "g_ri", "g_vch"))
        block = ctx.enter_context(nc.Block())

        @block.gpsimd
        def _(pool):
            pool.wait_ge(k.pages_ld, 16)
            for p in range(2):
                gather_pages(pool, k.cmp_pages[p][:, 16:32], k.d["cmp_pool"], k.pages, 32 * p + 16, k.cmp_got[p][1])

        @block.sync
        def _(sp):
            sp.dma_start(k.pages[:], k.d["page_table"]).then_inc(k.pages_ld, 16)
            sp.dma_start(w[:], k.d["w_glu"]).then_inc(ld, 16)
            sp.dma_start(bg[:], k.d["b_glu"]).then_inc(ld_sm, 16)
            sp.dma_start(gs[:], k.d["g_out_ssm"]).then_inc(ld_sm, 16)
            sp.wait_ge(k.pages_ld, 16)
            for p in range(2):
                gather_pages(sp, k.cmp_pages[p][:, 0:16], k.d["cmp_pool"], k.pages, 32 * p, k.cmp_got[p][0])

        @block.scalar
        def _(act):
            act.wait_ge(k.y_loaded, 16)
            for i in range(4):
                nc.scalar.activation(k.yT[:, i], k.yT[:, i], ACT.Gelu_apprx_tanh).then_inc(zg, 1)
            act.wait_ge(ld_sm, 32)
            for c in range(4):
                act.wait_ge(mmd, c + 1)
                for h in range(2):
                    nc.scalar.activation(sig[:, c, HALF * h:HALF * h + HALF], ps[:, c, h, 0:HALF], ACT.Sigmoid,
                                         bias=bg[:, c:c + 1]).then_inc(sigd, 1)
            for c in range(4):
                act.wait_ge(outd, c + 1)
                nc.scalar.activation(sq[:, c], sig[:, c], ACT.Square).then_inc(sqd, 1)
            act.wait_ge(msd, 1)
            nc.scalar.activation(rinv[:], rinv[:], ACT.Sqrt).then_inc(rid, 1)

        @block.vector
        def _(dve):
            v = Chain(dve, vch)
            for c in range(4):
                dve.wait_ge(sigd, 2 * c + 2)
                nc.vector.tensor_tensor(sig[:, c], sig[:, c], k.yT[:, c], ALU.mult).then_inc(outd, 1)
            dve.wait_ge(ssqd, 1)
            for h in range(2):
                v.go(nc.vector.tensor_scalar(rinv[:, HALF * h:HALF * h + HALF], ps[:, h, 0, 0:HALF], 1.0 / 512, EPS,
                                             ALU.mult, ALU.add))
            v.wait()
            nc.vector.reciprocal(rinv[:], rinv[:]).then_inc(msd, 1)
            dve.wait_ge(rid, 1)
            for c in range(4):
                tok = lambda a: a.rearrange("p (j c) -> p j c", j=8)
                v.go(nc.vector.scalar_tensor_tensor(out=k.mixT[:, c].rearrange("p (c j) -> p j c", j=8),
                                                    in0=tok(sig[:, c]), scalar=gs[:, c:c + 1], in1=tok(rinv[:]),
                                                    op0=ALU.mult, op1=ALU.mult))

        @block.tensor
        def _(pe):
            pe.wait_ge(ld, 16)
            pe.wait_ge(zg, 4)
            for c in range(4):
                for h in range(2):
                    for i in range(4):
                        mm = nc.tensor.matmul(ps[:, c, h, 0:HALF], w[:, i, P * c:P * c + P],
                                              k.yT[:, i, HALF * h:HALF * h + HALF], start=(i == 0), stop=(i == 3))
                mm.then_inc(mmd, 1)
            pe.wait_ge(sigd, 8)
            for c in range(4):
                pe.wait_ge(sqd, c + 1)
                for h in range(2):
                    mm = nc.tensor.matmul(ps[:, h, 0, 0:HALF], k.ones[:], sq[:, c, HALF * h:HALF * h + HALF],
                                          start=(c == 0), stop=(c == 3))
            mm.then_inc(ssqd, 1)


PAIRS = SEQS // 2


def compress_stage(nc, k):
    with ExitStack() as ctx:
        sb = lambda n, s, d=F32: ctx.enter_context(nc.sbuf_tensor(n, s, d))
        sem = k.sem
        pages, got = k.cmp_pages, k.cmp_got
        w1, w2, pe_ = sb("cmp_w1", [P, 2, 16, P]), sb("cmp_w2", [P, 2, HD]), sb("cmp_pe", [P, 2, 16])
        bias = sb("cmp_bias", [P, 2])
        shifted, pre = sb("cmp_h1", [P, 2, 256]), sb("cmp_pre", [P, 2, 256])
        rope, gain = sb("cmp_rope", [P, 3, 8]), sb("cmp_gain", [P, HD])
        kr, sq = sb("cmp_k_rows", [P, 9, P]), sb("cmp_sq", [P, 9, P])
        ms = sb("cmp_ms", [P, 2, 18])
        ra, rb = sb("cmp_ra", [P, 18, 16]), sb("cmp_rb", [P, 18, 16])
        ph = ctx.enter_context(nc.psum_tensor("ph", [P, 2, 512], F32))
        po = ctx.enter_context(nc.psum_tensor("po_cmp", [P, 2, 512], F32))
        pb = ctx.enter_context(nc.psum_tensor("pb_cmp", [P, 512], F32))
        pt = ctx.enter_context(nc.psum_tensor("pt_cmp", [P, 3, 512], F32))
        ld, bias_done, bias_ready = (sem(n) for n in ("c_ld", "c_bias", "c_biasr"))
        h_done, h1_copied, pre_ready, act_ready, out_done, out_free = (sem(n) for n in (
            "c_h", "c_h1", "c_pre", "c_act", "c_out", "c_outf"))
        zeroed, vch, sqd, msd, rid, kready, trd = (sem(n) for n in (
            "c_zero", "c_vch", "c_sq", "c_ms", "c_ri", "c_k", "c_tr"))
        units = [(p, kv, g) for p in range(PAIRS + 1) for kv in range(2) for g in range(2)]
        block = ctx.enter_context(nc.Block())

        @block.sync
        def _(sp):
            sp.dma_start(w1[:], k.d["cmp_w1"]).then_inc(ld, 16)
            for dst, src in ((w2, k.d["cmp_w2"]), (pe_, k.d["cmp_pe"]), (rope, k.d["cmp_rope"])):
                sp.dma_start(dst[:], src).then_inc(ld, 16)
            sp.dma_start(gain[:], k.d["g_k_cmp"].to_broadcast([P, HD])).then_inc(ld, 16)
            for p in range(2, PAIRS):
                sp.wait_ge(h_done, 4 * (p - 1))
                gather_pages(sp, pages[p % 2][:, 0:16], k.d["cmp_pool"], k.pages, 32 * p, got[p % 2][0])

        @block.gpsimd
        def _(pool):
            pool.memset(kr[:], 0.0).then_inc(zeroed, 1)
            pool.memset(k.vcmp, 0.0).then_inc(zeroed, 1)
            for p in range(2, PAIRS):
                pool.wait_ge(h_done, 4 * (p - 1))
                gather_pages(pool, pages[p % 2][:, 16:32], k.d["cmp_pool"], k.pages, 32 * p + 16, got[p % 2][1])

        @block.scalar
        def _(act):
            act.wait_ge(bias_done, 1)
            nc.scalar.activation(bias[:], pb[:, 0:2], ACT.Copy).then_inc(bias_ready, 1)
            act.wait_ge(bias_ready, 1)
            act.wait_ge(zeroed, 2)
            for u, (p, kv, g) in enumerate(units):
                n, seqs = (256, 2) if p < PAIRS else (32, 1)
                act.wait_ge(h_done, u + 1)
                nc.scalar.activation(shifted[:, u % 2, 0:n], ph[:, u % 2, 256:256 + n], ACT.Copy).then_inc(h1_copied, 1)
                act.wait_ge(pre_ready, u + 1)
                nc.scalar.activation(pre[:, u % 2, 0:n], pre[:, u % 2, 0:n], ACT.Gelu_apprx_tanh,
                                     bias=bias[:, kv:kv + 1]).then_inc(act_ready, 1)
                if u % 4 == 3:
                    act.wait_ge(out_done, u + 1)
                    rows, s0 = (127, 2 * p) if p < PAIRS else (31, 8)
                    src = po[0:rows, p % 2, 0:256 * seqs].rearrange("p (s kv f) -> p s kv f", s=seqs, kv=2)
                    nc.scalar.activation(kr[0:rows, s0:s0 + seqs, :], src[:, :, 0], ACT.Copy)
                    nc.scalar.activation(k.vcmp[0:rows, s0:s0 + seqs, :], src[:, :, 1], ACT.Copy).then_inc(out_free, 1)
            act.wait_ge(out_free, PAIRS + 1)
            nc.scalar.activation(sq[:], kr[:], ACT.Square).then_inc(sqd, 1)
            act.wait_ge(msd, 1)
            nc.scalar.activation(ms[:, 1], ms[:, 0], ACT.Sqrt).then_inc(rid, 1)
            for q in range(3):
                act.wait_ge(trd, q + 1)
                nc.scalar.activation(k.kcT[:, 3 * q:3 * q + 3, :], pt[:, q, 0:384].rearrange("p (s n) -> p s n", s=3), ACT.Copy)

        @block.vector
        def _(dve):
            v = Chain(dve, vch)
            dve.wait_ge(ld, 80)
            for u, (p, kv, g) in enumerate(units):
                n, seqs = (128, 2) if p < PAIRS else (32, 1)
                dve.wait_ge(h1_copied, u + 1)
                if u >= 2:
                    dve.wait_ge(out_done, u - 1)
                if u < 2:
                    v(nc.vector.memset(pre[:, u % 2, :], 0.0))
                sq3 = lambda a: a.rearrange("p (s n) -> p s n", s=seqs)
                nc.vector.tensor_tensor(sq3(pre[:, u % 2, 0:n * seqs])[:, :, 0:n - 1],
                                        sq3(ph[:, u % 2, 0:n * seqs])[:, :, 0:n - 1],
                                        sq3(shifted[:, u % 2, 0:n * seqs])[:, :, 1:n], ALU.add).then_inc(pre_ready, 1)
            dve.wait_ge(sqd, 1)
            v(nc.vector.tensor_reduce(ms[:, 0], sq[:].rearrange("p s (g d) -> p (s g) d", g=2), AX.X, ALU.add))
            v(nc.vector.tensor_scalar(ms[:, 0], ms[:, 0], 1.0 / HD, EPS, ALU.mult, ALU.add))
            nc.vector.reciprocal(ms[:, 0], ms[:, 0]).then_inc(msd, 1)
            dve.wait_ge(rid, 1)
            k3 = kr[:].rearrange("p s (g d) -> p (s g) d", g=2)
            v(nc.vector.tensor_tensor(k3, k3, ms[:, 1].unsqueeze(2).to_broadcast([P, 18, HD]), ALU.mult))
            v(nc.vector.tensor_tensor(k3, k3, gain[:].unsqueeze(1).to_broadcast([P, 18, HD]), ALU.mult))
            cos, sin, nsin = (rope[:, i, :].unsqueeze(1).to_broadcast([P, 18, 8]) for i in range(3))
            v.go(nc.vector.tensor_tensor(ra[:, :, 0:8], k3[:, :, 0:8], cos, ALU.mult))
            v.go(nc.vector.tensor_tensor(ra[:, :, 8:16], k3[:, :, 8:16], cos, ALU.mult))
            v.go(nc.vector.tensor_tensor(rb[:, :, 0:8], k3[:, :, 8:16], nsin, ALU.mult))
            v(nc.vector.tensor_tensor(rb[:, :, 8:16], k3[:, :, 0:8], sin, ALU.mult))
            nc.vector.tensor_tensor(k3[:, :, 0:16], ra[:], rb[:], ALU.add).then_inc(kready, 1)

        @block.tensor
        def _(pe):
            pe.wait_ge(ld, 80)
            for kv in range(2):
                for i in range(16):
                    mm = nc.tensor.matmul(pb[:, kv:kv + 1], w1[:, kv, i, :], pe_[:, kv, i:i + 1],
                                          start=(i == 0), stop=(i == 15))
            mm.then_inc(bias_done, 1)

            def second(u):
                p, kv, g = units[u]
                n, seqs = (127, 2) if p < PAIRS else (31, 1)
                pe.wait_ge(act_ready, u + 1)
                if u % 4 == 0 and p >= 2:
                    pe.wait_ge(out_free, p - 1)
                for s in range(seqs):
                    off = s * 256 + kv * 128 + g * 64
                    mm = nc.tensor.matmul(po[0:n, p % 2, off:off + 64], pre[:, u % 2, 128 * s:128 * s + n], w2[:, kv, :],
                                          start=True, stop=True)
                mm.then_inc(out_done, 1)

            for u, (p, kv, g) in enumerate(units):
                if u >= 2:
                    pe.wait_ge(pre_ready, u - 1)
                if p < PAIRS:
                    if u % 4 == 0:
                        for s in range(2):
                            pe.wait_ge(got[p % 2][s], 256 * (p // 2 + 1))
                    src = pages[p % 2][:].rearrange("p t (kv g i b) -> p t kv g i b", kv=2, g=2, i=8)
                    n = 256
                else:
                    src, n = k.cmp_prompt[:], 32
                for s in range(2):
                    for i in range(8):
                        mm = nc.tensor.matmul(ph[:, u % 2, 256 * s:256 * s + n], w1[:, kv, 8 * s + i, :],
                                              src[:, :, kv, g, i, :], start=(i == 0), stop=(i == 7))
                mm.then_inc(h_done, 1)
                if u >= 1:
                    second(u - 1)
            second(len(units) - 1)
            pe.wait_ge(kready, 1)
            for q in range(3):
                for s in range(3):
                    mm = nc.tensor.transpose(pt[:, q, P * s:P * s + P], kr[:, 3 * q + s, :], k.ident[:])
                mm.then_inc(trd, 1)


CMP, SEL, WIN = range(3)
S_AT = [(2, 256), (2, 0), (1, 0), (0, 0)]
P_AT = [0, 128, 384, 768]
PT_AT = [0, 512, 896, 1152]
PT_BANK = [(0, 0), (1, 0), (2, 0), (2, 256)]
NCP = 31


def window_rows(sp, k, p):
    for s in range(2):
        sp.dma_start(k.win_k[:, p % 2, s], k.d["win_kT"][2 * p + s]).then_inc(k.win_got[p % 2], 16)
        sp.dma_start(k.win_v[:, p % 2, s], k.d["win_rows"][1][2 * p + s].rearrange("(a p) f -> p a f", p=P)).then_inc(k.win_got[p % 2], 16)


def prompt_attention_stage(nc, k):
    with ExitStack() as ctx:
        sb = lambda n, s, d=F32: ctx.enter_context(nc.sbuf_tensor(n, s, d))
        sem = k.sem
        causal, cmask, valid = sb("causal", [P, P]), sb("cmp_mask", [P, 4, NCP]), sb("cmp_valid", [P, 4])
        prob, pt = sb("prob", [P, 2, 1280]), sb("prob_T", [P, 2, 1280])
        pc = sb("prob_cmp", [P, 2, 4, NCP])
        mx, rs = sb("pa_max", [P, 2, 4]), sb("pa_sum", [P, 2, 4])
        s_ps = ctx.enter_context(nc.psum_tensor("pa_s", [P, 4, 512], F32))
        t_ps = ctx.enter_context(nc.psum_tensor("pa_t", [P, 3, 512], F32))
        o_ps = ctx.enter_context(nc.psum_tensor("pa_o", [P, 512], F32))
        ld, s_done, s_used, mx_ready, e_done, scaled, t_done, t_copied, t_cdve, pv_done, o_free, vch = (sem(n) for n in (
            "pa_ld", "pa_sd", "pa_su", "pa_mx", "pa_e", "pa_sc", "pa_td", "pa_tc", "pa_tcd", "pa_pv", "pa_of", "pa_v"))
        units = [(r, g, br) for r in range(REP) for g in range(2) for br in (CMP, SEL, WIN)]
        N = len(units)
        big = lambda n: sum(1 for x in units[:n] if x[2] != CMP)
        BANKS = ((3,), (2,), (1, 0))
        banks_before = lambda n: sum(1 if x[2] == CMP else len(BANKS) for x in units[:n])
        block = ctx.enter_context(nc.Block())

        @block.sync
        def _(sp):
            for dst, src in ((causal, k.d["causal"]), (cmask, k.d["cmp_mask"]), (valid, k.d["cmp_valid"])):
                sp.dma_start(dst[:], src).then_inc(ld, 16)
            for p in range(2):
                window_rows(sp, k, p)
                gather_pages(sp, k.sel_pages[p][:, 0:16], k.d["sel_pool"], k.pages, 32 * p, k.sel_got[p][0])

        @block.gpsimd
        def _(pool):
            for p in range(2):
                gather_pages(pool, k.sel_pages[p][:, 16:32], k.d["sel_pool"], k.pages, 32 * p + 16, k.sel_got[p][1])

        @block.scalar
        def _(act):
            def evac(n):
                br = units[n][2]
                act.wait_ge(t_done, n + 1)
                if n >= 2:
                    act.wait_ge(pv_done, n - 1)
                if br == CMP:
                    nc.scalar.activation(pt[0:NCP, n % 2, 0:512], t_ps[0:NCP, 0, :], ACT.Copy).then_inc(t_copied, 1)
                else:
                    nc.scalar.activation(pt[:, n % 2, 0:512], t_ps[:, 0, :], ACT.Copy)
                    nc.scalar.activation(pt[:, n % 2, 896:1280], t_ps[:, 2, 0:384], ACT.Copy).then_inc(t_copied, 1)

            for n, (r, g, br) in enumerate(units):
                if br == CMP:
                    act.wait_ge(mx_ready, banks_before(n) + 1)
                    nc.scalar.activation(pc[:, n % 2], pc[:, n % 2], ACT.Exp, scale=SCALE).then_inc(e_done, 1)
                else:
                    if n >= 2:
                        act.wait_ge(t_done, n - 1)
                    for j, tiles in enumerate(BANKS):
                        act.wait_ge(mx_ready, banks_before(n) + j + 1)
                        for i in tiles:
                            bank, at = S_AT[i]
                            e = nc.scalar.activation(prob[:, n % 2, P_AT[i]:P_AT[i] + P * (i + 1)],
                                                     s_ps[:, bank, at:at + P * (i + 1)], ACT.Exp, bias=mx[:, n % 2, i:i + 1],
                                                     scale=SCALE, accum_out=rs[:, n % 2, i:i + 1])
                        e.then_inc(e_done, 1)
                if n >= 1:
                    evac(n - 1)
                    if n % 6 == 1 and n > 1:
                        act.wait_ge(pv_done, n - 1)
                        nc.scalar.activation(k.mixT[:, 4 + n // 6 - 1, 0:T_PROMPT], o_ps[:], ACT.Copy).then_inc(o_free, 1)
            evac(N - 1)
            act.wait_ge(pv_done, N)
            nc.scalar.activation(k.mixT[:, 7, 0:T_PROMPT], o_ps[:], ACT.Copy).then_inc(o_free, 1)

        @block.vector
        def _(dve):
            v = Chain(dve, vch)
            dve.wait_ge(ld, 48)

            def gate(n):
                r, g, br = units[n]
                return k.gates[:, 0:4, 8 * br + 4 * g + r]

            def scores(n):
                b = n % 2
                if units[n][2] == CMP:
                    dve.wait_ge(s_done, banks_before(n) + 1)
                    if n >= 2:
                        dve.wait_ge(t_done, n - 1)
                    v(nc.vector.tensor_tensor(pc[:, b], s_ps[:, 3, 0:4 * NCP].rearrange("p (i c) -> p i c", i=4),
                                              cmask[:], ALU.add))
                    v(nc.vector.tensor_reduce(mx[:, b], pc[:, b], AX.X, ALU.max))
                    nc.vector.tensor_tensor(pc[:, b], pc[:, b], mx[:, b].unsqueeze(2).to_broadcast([P, 4, NCP]),
                                            ALU.subtract).then_inc(mx_ready, 1)
                else:
                    for j, tiles in enumerate(BANKS):
                        dve.wait_ge(s_done, banks_before(n) + j + 1)
                        for i in tiles:
                            bank, at = S_AT[i]
                            d = s_ps[:, bank, at + P * i:at + P * i + P]
                            v.go(nc.vector.tensor_tensor(d, d, causal[:], ALU.add))
                        v.wait()
                        for i in tiles:
                            bank, at = S_AT[i]
                            v.go(nc.vector.tensor_reduce(mx[:, b, i:i + 1], s_ps[:, bank, at:at + P * (i + 1)], AX.X, ALU.max))
                        v.wait()
                        lo, hi = min(tiles), max(tiles) + 1
                        nc.vector.tensor_scalar(mx[:, b, lo:hi], mx[:, b, lo:hi], -SCALE, None, ALU.mult).then_inc(mx_ready, 1)

            def scale(n):
                dve.wait_ge(e_done, banks_before(n + 1))
                b = n % 2
                if units[n][2] == CMP:
                    v(nc.vector.tensor_reduce(rs[:, b], pc[:, b], AX.X, ALU.add))
                    v(nc.vector.reciprocal(rs[:, b], rs[:, b]))
                    v(nc.vector.tensor_tensor(rs[:, b], rs[:, b], gate(n), ALU.mult))
                    v(nc.vector.tensor_tensor(rs[:, b], rs[:, b], valid[:], ALU.mult))
                    nc.vector.tensor_tensor(pc[:, b], pc[:, b], rs[:, b].unsqueeze(2).to_broadcast([P, 4, NCP]),
                                            ALU.mult).then_inc(scaled, 1)
                else:
                    v(nc.vector.reciprocal(rs[:, b], rs[:, b]))
                    v(nc.vector.tensor_tensor(rs[:, b], rs[:, b], gate(n), ALU.mult))
                    for i in range(4):
                        pr = prob[:, b, P_AT[i]:P_AT[i] + P * (i + 1)]
                        m = nc.vector.tensor_scalar(pr, pr, rs[:, b, i:i + 1], None, ALU.mult)
                    m.then_inc(scaled, 1)

            def evac(n):
                if units[n][2] != CMP:
                    dve.wait_ge(t_done, n + 1)
                    if n >= 2:
                        dve.wait_ge(pv_done, n - 1)
                    nc.vector.tensor_copy(pt[:, n % 2, 512:896], t_ps[:, 1, 0:384]).then_inc(t_cdve, 1)

            for n in range(N + 1):
                if n < N:
                    scores(n)
                if n >= 1:
                    evac(n - 1)
                if n < N:
                    scale(n)

        @block.tensor
        def _(pe):
            def scores(n):
                r, g, br = units[n]
                h = slice(64 * g, 64 * g + 64)
                if br == CMP:
                    if n >= 3:
                        pe.wait_ge(mx_ready, banks_before(n - 3) + 1)
                    for i in range(4):
                        mm = nc.tensor.matmul(s_ps[:, 3, NCP * i:NCP * i + NCP], k.qT[h, r, P * i:P * i + P],
                                              k.kcT[h, 8, 0:NCP], start=True, stop=True)
                else:
                    kT = k.ksT if br == SEL else k.kwT
                    for j, tiles in enumerate(BANKS):
                        if big(n):
                            last = n - 1 if units[n - 1][2] != CMP else n - 2
                            pe.wait_ge(e_done, banks_before(last) + j + 1)
                        for i in tiles:
                            bank, at = S_AT[i]
                            mm = nc.tensor.matmul(s_ps[:, bank, at:at + P * (i + 1)], k.qT[h, r, P * i:P * i + P],
                                                  kT[h, 0:P * (i + 1)], start=True, stop=True)
                        if j < len(BANKS) - 1:
                            mm.then_inc(s_done, 1)
                mm.then_inc(s_done, 1)

            def transposes(n):
                br = units[n][2]
                pe.wait_ge(scaled, n + 1)
                if n >= 1:
                    pe.wait_ge(t_copied, n)
                    if big(n):
                        pe.wait_ge(t_cdve, big(n))
                if br == CMP:
                    for i in range(4):
                        mm = nc.tensor.transpose(t_ps[0:NCP, 0, P * i:P * i + P], pc[:, n % 2, i, :], k.ident[:])
                else:
                    for j in range(4):
                        bank, at = PT_BANK[j]
                        for i in range(j, 4):
                            mm = nc.tensor.transpose(t_ps[:, bank, at + P * (i - j):at + P * (i - j) + P],
                                                     prob[:, n % 2, P_AT[i] + P * j:P_AT[i] + P * j + P], k.ident[:])
                mm.then_inc(t_done, 1)

            def values(n):
                r, g, br = units[n]
                h = slice(64 * g, 64 * g + 64)
                pe.wait_ge(t_copied, n + 1)
                if br == CMP:
                    if n % 6 == 0 and n:
                        pe.wait_ge(o_free, n // 6)
                    mm = nc.tensor.matmul(o_ps[h, :], k.vcmp[0:NCP, 8, h], pt[0:NCP, n % 2, 0:512], start=True, stop=False)
                else:
                    pe.wait_ge(t_cdve, big(n + 1))
                    lo = 256 if br == SEL else 384
                    for j in (3, 2, 1, 0):
                        mm = nc.tensor.matmul(o_ps[h, P * j:512], k.kv[:, j, lo + 64 * g:lo + 64 * g + 64],
                                              pt[:, n % 2, PT_AT[j]:PT_AT[j] + P * (4 - j)], start=False,
                                              stop=(br == WIN and j == 0))
                mm.then_inc(pv_done, 1)

            for n in range(N + 2):
                if n < N:
                    scores(n)
                if 1 <= n <= N:
                    transposes(n - 1)
                if n >= 2:
                    values(n - 2)


NKEYS = PAST + 64
NSEL = 33


def sample_attention_stage(nc, k):
    with ExitStack() as ctx:
        sb = lambda n, s, d=F32: ctx.enter_context(nc.sbuf_tensor(n, s, d))
        sem = k.sem
        pages, got = k.sel_pages, k.sel_got
        kw, vw, gotw = k.win_k, k.win_v, k.win_got
        q = sb("q_heads", [P, SEQS, 64])
        same, pick, mine = sb("same_query", [P, P]), sb("pick_rows", [64, PAIRS, P]), sb("my_head", [P, 8])
        newm, winm, force = sb("new_mask", [P, PAIRS, 64]), sb("win_mask", [P, 8]), sb("force_row", [P, NSEL])
        gt = sb("sample_gates", [P, PAIRS, 3])
        gtmp = sb("gates_tmp", [P, PAIRS, 3, 8])
        pc, ss, sw = sb("sa_pc", [P, P]), sb("sa_sel", [P, NKEYS]), sb("sa_win", [P, 576])
        pt = sb("sa_pt", [P, 23, P])
        st = sb("sa_stats", [P, 16])
        sc = sb("sa_score", [P, 3, NSEL])
        top = sb("sa_top", [P, 2, 8])
        ps = ctx.enter_context(nc.psum_tensor("sa_ps", [P, 8, 512], F32))
        ld = sem("sa_ld")
        q_ready, g_mm, vch, s_small, s_sel = (sem(n) for n in ("sa_q", "sa_gm", "sa_v", "sa_ss", "sa_sl"))
        cmx, ce, pn, imp, wcp, wmx, we, smx, se = (sem(n) for n in (
            "sa_cmx", "sa_ce", "sa_pn", "sa_imp", "sa_wcp", "sa_wmx", "sa_we", "sa_smx", "sa_se"))
        c_sc, w_sc, s_sc, td, ta, tv, pv, of = (sem(n) for n in (
            "sa_csc", "sa_wsc", "sa_ssc", "sa_td", "sa_ta", "sa_tv", "sa_pv", "sa_of"))
        banks = [[0, 1, 2, 3], [4, 5], [6, 7, 8, 9], [10, 11, 12, 13], [14, 15, 16, 17], [18, 19, 20, 21], [22]]
        NB = len(banks)
        rows_of = lambda b: 127 if b == 0 else 64 if b in (5, 22) else P
        block = ctx.enter_context(nc.Block())

        @block.sync
        def _(sp):
            for dst, src in ((same, k.d["same"]), (pick, k.d["pick"]), (mine, k.d["mine"]), (newm, k.d["new_mask"]),
                             (winm, k.d["win_mask"]), (force, k.d["force"])):
                sp.dma_start(dst[:], src).then_inc(ld, 16)
            for p in range(2, PAIRS):
                sp.wait_ge(pv, p - 1)
                window_rows(sp, k, p)
                gather_pages(sp, pages[p % 2][:, 0:16], k.d["sel_pool"], k.pages, 32 * p, got[p % 2][0])

        @block.gpsimd
        def _(pool):
            for p in range(2, PAIRS):
                pool.wait_ge(pv, p - 1)
                gather_pages(pool, pages[p % 2][:, 16:32], k.d["sel_pool"], k.pages, 32 * p + 16, got[p % 2][1])

        @block.scalar
        def _(act):
            for p in range(PAIRS):
                act.wait_ge(s_small, p + 1)
                if p:
                    act.wait_ge(td, NB * p)
                nc.scalar.activation(sw[:, 0:512], ps[:, 5, :], ACT.Copy).then_inc(wcp, 1)
                act.wait_ge(cmx, p + 1)
                nc.scalar.activation(pc[:, 0:127], ps[:, 4, 128:255], ACT.Exp, bias=st[:, 0:1], scale=SCALE,
                                     accum_out=st[:, 1:2]).then_inc(ce, 1)
                act.wait_ge(wmx, p + 1)
                nc.scalar.activation(sw[:], sw[:], ACT.Exp, bias=st[:, 4:5], scale=SCALE,
                                     accum_out=st[:, 5:6]).then_inc(we, 1)
                act.wait_ge(smx, p + 1)
                nc.scalar.activation(ss[:], ss[:], ACT.Exp, bias=st[:, 8:9], scale=SCALE,
                                     accum_out=st[:, 9:10]).then_inc(se, 1)
                for b in range(0, NB, 2):
                    act.wait_ge(td, NB * p + b + 1)
                    if p and b == 0:
                        act.wait_ge(pv, p)
                    lo, n = banks[b][0], len(banks[b])
                    if b == NB - 1:
                        nc.scalar.activation(pt[0:64, lo, :], ps[0:64, b % 4, 0:P], ACT.Copy).then_inc(ta, 1)
                    elif b == 0:
                        nc.scalar.activation(pt[0:127, 0, :], ps[0:127, 0, 0:P], ACT.Copy)
                        nc.scalar.activation(pt[:, 1:4, :], ps[:, 0, P:512].rearrange("p (n f) -> p n f", n=3), ACT.Copy).then_inc(ta, 1)
                    else:
                        nc.scalar.activation(pt[:, lo:lo + n, :], ps[:, b % 4, 0:P * n].rearrange("p (n f) -> p n f", n=n),
                                             ACT.Copy).then_inc(ta, 1)

        @block.vector
        def _(dve):
            v = Chain(dve, vch)
            V = nc.vector
            v(V.memset(q[:], 0.0))
            for g in range(2):
                h = slice(64 * g, 64 * g + 64)
                V.tensor_copy(q[h, :, 32 * g:32 * g + 32].rearrange("p s (r t) -> p s r t", r=REP),
                              k.qT[h, :, T_PROMPT:T].rearrange("p r (s t) -> p s r t", t=STEPS)).then_inc(q_ready, 1)
            dve.wait_ge(ld, 96)
            dve.wait_ge(g_mm, 1)
            v(V.tensor_tensor(gtmp[:].rearrange("p a b h -> p (a b) h"), ps[:, 7, 0:96].rearrange("p (a h) -> p a h", h=8),
                              mine[:].unsqueeze(1).to_broadcast([P, 12, 8]), ALU.mult))
            v(V.tensor_reduce(gt[:].rearrange("p a b -> p (a b)"), gtmp[:].rearrange("p a b h -> p (a b) h"), AX.X, ALU.add))
            v(V.memset(pc[:], 0.0))
            for p in range(PAIRS):
                dve.wait_ge(s_small, p + 1)
                if p:
                    dve.wait_ge(td, NB * p)
                v(V.tensor_reduce(st[:, 0:1], ps[:, 4, 128:255], AX.X, ALU.max))
                V.tensor_scalar(st[:, 0:1], st[:, 0:1], -SCALE, None, ALU.mult).then_inc(cmx, 1)
                dve.wait_ge(wcp, p + 1)
                v.go(V.tensor_tensor(sw[:, 0:8], sw[:, 0:8], winm[:], ALU.add))
                dve.wait_ge(ce, p + 1)
                v(V.tensor_tensor(sw[:, 512:576], ps[:, 4, 64:128], newm[:, p], ALU.add))
                v(V.tensor_reduce(st[:, 4:5], sw[:], AX.X, ALU.max))
                V.tensor_scalar(st[:, 4:5], st[:, 4:5], -SCALE, None, ALU.mult).then_inc(wmx, 1)
                v(V.reciprocal(st[:, 1:2], st[:, 1:2]))
                V.tensor_scalar(pc[:, 0:127], pc[:, 0:127], st[:, 1:2], None, ALU.mult).then_inc(pn, 1)
                dve.wait_ge(imp, p + 1)
                v(V.memset(sc[:, 0, 32:33], 0.0))
                v(V.tensor_reduce(sc[:, 0, 0:32], ps[:, 4, 256:384].rearrange("p (b c) -> p b c", c=4), AX.X, ALU.add))
                v(V.tensor_tensor(sc[:, 0], sc[:, 0], force[:], ALU.add))
                v(V.max(top[:, 0], sc[:, 0]))
                v(V.match_replace(sc[:, 1], top[:, 0], sc[:, 0], GONE))
                v(V.max(top[:, 1], sc[:, 1]))
                v(V.match_replace(sc[:, 2], top[:, 1], sc[:, 1], GONE))
                v(V.tensor_scalar(sc[:, 0], sc[:, 2], GONE / 2, NEG, ALU.is_gt, ALU.mult))
                V.tensor_scalar(pc[:, 0:127], pc[:, 0:127], gt[:, p, 0:1], None, ALU.mult).then_inc(c_sc, 1)
                dve.wait_ge(s_sel, p + 1)
                for c in range(4):
                    b3 = lambda a: a.rearrange("p (b n) -> p b n", n=64)
                    v.go(V.tensor_tensor(b3(ss[:, 512 * c:512 * c + 512]), b3(ps[:, c, :]),
                                         sc[:, 0, 8 * c:8 * c + 8].unsqueeze(2).to_broadcast([P, 8, 64]), ALU.add))
                v(V.scalar_tensor_tensor(out=ss[:, PAST:NKEYS], in0=ps[:, 4, 0:64], scalar=sc[:, 0, 32:33],
                                         in1=newm[:, p], op0=ALU.add, op1=ALU.add))
                v(V.tensor_reduce(st[:, 8:9], ss[:], AX.X, ALU.max))
                V.tensor_scalar(st[:, 8:9], st[:, 8:9], -SCALE, None, ALU.mult).then_inc(smx, 1)
                dve.wait_ge(we, p + 1)
                v(V.reciprocal(st[:, 5:6], st[:, 5:6]))
                v(V.tensor_tensor(st[:, 5:6], st[:, 5:6], gt[:, p, 2:3], ALU.mult))
                V.tensor_scalar(sw[:], sw[:], st[:, 5:6], None, ALU.mult).then_inc(w_sc, 1)
                dve.wait_ge(se, p + 1)
                v(V.reciprocal(st[:, 9:10], st[:, 9:10]))
                v(V.tensor_tensor(st[:, 9:10], st[:, 9:10], gt[:, p, 1:2], ALU.mult))
                V.tensor_scalar(ss[:], ss[:], st[:, 9:10], None, ALU.mult).then_inc(s_sc, 1)
                for b in range(1, NB, 2):
                    dve.wait_ge(td, NB * p + b + 1)
                    if p and b == 1:
                        dve.wait_ge(pv, p)
                    lo, n = banks[b][0], len(banks[b])
                    if b == 1:
                        V.tensor_copy(pt[:, 4, :], ps[:, 1, 0:P])
                        V.tensor_copy(pt[0:64, 5, :], ps[0:64, 1, P:2 * P]).then_inc(tv, 1)
                    else:
                        V.tensor_copy(pt[:, lo:lo + n, :], ps[:, b % 4, 0:P * n].rearrange("p (n f) -> p n f", n=n)).then_inc(tv, 1)
                dve.wait_ge(pv, p + 1)
                for g in range(2):
                    h = slice(64 * g, 64 * g + 64)
                    V.tensor_copy(k.mixT[h, 4:8, T_PROMPT + 16 * p:T_PROMPT + 16 * p + 16].rearrange("p r (s t) -> p r s t", t=STEPS),
                                  ps[h, 6, 0:P].rearrange("p (s g r t) -> p g r s t", s=2, g=2, r=REP)[:, g]).then_inc(of, 1)

        @block.tensor
        def _(pe):
            pe.wait_ge(ld, 96)
            for p in range(PAIRS):
                mm = nc.tensor.matmul(ps[:, 7, 24 * p:24 * p + 24], pick[:, p, :], k.gates[0:64, 4, :], start=True, stop=True)
            mm.then_inc(g_mm, 1)
            pe.wait_ge(q_ready, 2)
            for p in range(PAIRS):
                kp = pages[p % 2]
                if p:
                    pe.wait_ge(smx, p)
                pe.wait_ge(gotw[p % 2], 64 * (p // 2 + 1))
                for s in range(2):
                    rows = slice(64 * s, 64 * s + 64)
                    qs = q[:, 2 * p + s, :]
                    nc.tensor.matmul(ps[rows, 4, 128:255], qs, k.kcT[:, 2 * p + s, 0:127], start=True, stop=True)
                    nc.tensor.matmul(ps[rows, 4, 0:64], qs, k.ksT[:, T_PROMPT:T], start=True, stop=True)
                    nc.tensor.matmul(ps[rows, 4, 64:128], qs, k.kwT[:, T_PROMPT:T], start=True, stop=True)
                    mm = nc.tensor.matmul(ps[rows, 5, :], qs, kw[:, p % 2, s], start=True, stop=True)
                mm.then_inc(s_small, 1)
                if p:
                    pe.wait_ge(ta, 4 * p)
                    pe.wait_ge(tv, 3 * p)
                for s in range(2):
                    pe.wait_ge(got[p % 2][s], 256 * (p // 2 + 1))
                for s in range(2):
                    for c in range(4):
                        mm = nc.tensor.matmul(ps[64 * s:64 * s + 64, c, :], q[:, 2 * p + s, :],
                                              kp[:, 16 * s + 4 * c:16 * s + 4 * c + 4, 0:P], start=True, stop=True)
                mm.then_inc(s_sel, 1)
                pe.wait_ge(pn, p + 1)
                pe.wait_ge(wmx, p + 1)
                nc.tensor.matmul(ps[:, 4, 256:384], same[:], pc[:], start=True, stop=True).then_inc(imp, 1)
                pe.wait_ge(c_sc, p + 1)
                pe.wait_ge(w_sc, p + 1)
                pe.wait_ge(smx, p + 1)
                for b, blocks in enumerate(banks):
                    if b == 2:
                        pe.wait_ge(s_sc, p + 1)
                    if b >= 4:
                        pe.wait_ge(tv if b % 2 else ta, (3 if b % 2 else 4) * p + (b - 4) // 2 + 1)
                    for n, blk in enumerate(blocks):
                        src = (pc[:, 0:127] if blk == 0 else sw[:, P * (blk - 1):P * (blk - 1) + rows_of(blk)] if blk < 6
                               else ss[:, P * (blk - 6):P * (blk - 6) + rows_of(blk)])
                        mm = nc.tensor.transpose(ps[0:rows_of(blk), b % 4, P * n:P * n + P], src, k.ident[:])
                    mm.then_inc(td, 1)
                pe.wait_ge(ta, 4 * p + 4)
                pe.wait_ge(tv, 3 * p + 3)
                if p:
                    pe.wait_ge(of, 2 * p)
                for s in range(2):
                    for blk in range(23):
                        m = rows_of(blk)
                        val = (k.vcmp[0:127, 2 * p + s, :] if blk == 0 else vw[:, p % 2, s, blk - 1, :] if blk < 5
                               else k.kv[0:64, 4, 384:512] if blk == 5
                               else kp[:, 16 * s + blk - 6, P:2 * P] if blk < 22 else k.kv[0:64, 4, 256:384])
                        mm = nc.tensor.matmul(ps[:, 6, 64 * s:64 * s + 64], val, pt[0:m, blk, 64 * s:64 * s + 64],
                                              start=(blk == 0), stop=(blk == 22))
                mm.then_inc(pv, 1)


F32R = mybir.dt.float32r


def as_r(ap):
    return ap.bitcast(F32R)


def mix_stage(nc, k):
    with ExitStack() as ctx:
        sb = lambda n, s, d=F32: ctx.enter_context(nc.sbuf_tensor(n, s, d))
        sem = k.sem
        wo, wq = sb("w_out_sb", [P, KD, 512]), sb("w_q_sb", [P, 2, KD, 512])
        ga, gf = sb("g_attn_sb", [P, 4]), sb("g_ffn_sb", [P, KD])
        rinv, tick = sb("m_rinv", [P, T]), sb("m_tick", [P, 1])
        sq, hn = sb("m_sq", [P, KD, T]), sb("m_hn", [P, KD, T])
        qp = k.qp
        ps = ctx.enter_context(nc.psum_tensor("m_ps", [P, 8, 512], F32))
        ld, wo_ld = sem("m_ld"), [sem("m_wo0"), sem("m_wo1")]
        wq_ld = [sem("m_wq0"), sem("m_wq1")]
        asq, ssq, msr, rir, an, mixd, hsq, hn_r, qd, qc, vch, x_hi_made = (sem(n) for n in (
            "m_asq", "m_ssq", "m_msr", "m_rir", "m_an", "m_mix", "m_hsq", "m_hn", "m_qd", "m_qc", "m_v", "m_x_hi_made"))
        block = ctx.enter_context(nc.Block())

        @block.sync
        def _(sp):
            sp.dma_start(wo[:], k.d["w_out"][:, :, 0:512]).then_inc(wo_ld[0], 16)
            for dst, src in ((ga, k.d["g_out_attn"]), (gf, k.d["g_ffn"])):
                sp.dma_start(dst[:], src).then_inc(ld, 16)
            for c in range(2):
                sp.dma_start(wq[:, c], k.d["w_q"][:, :, 512 * c:512 * c + 512]).then_inc(wq_ld[c], 16)
            sp.wait_ge(mixd, 8)
            sp.dma_start(wo[:], k.d["w_out"][:, :, 512:1024]).then_inc(wo_ld[1], 16)
            for c in range(2, 4):
                sp.wait_ge(qd, 8 * (c - 1))
                sp.dma_start(wq[:, c % 2], k.d["w_q"][:, :, 512 * c:512 * c + 512]).then_inc(wq_ld[c % 2], 16)

        @block.scalar
        def _(act):
            for c in range(4):
                nc.scalar.activation(sq[:, c], k.mixT[:, 4 + c], ACT.Square).then_inc(asq, 1)
            act.wait_ge(msr, 1)
            nc.scalar.activation(rinv[:], rinv[:], ACT.Sqrt).then_inc(rir, 1)
            for c in range(KD):
                act.wait_ge(hsq, c + 1)
                nc.scalar.activation(sq[:, c], k.hT[:, c], ACT.Square).then_inc(asq, 1)
            act.wait_ge(msr, 2)
            nc.scalar.activation(rinv[:], rinv[:], ACT.Sqrt).then_inc(rir, 1)
            for c in range(KD):
                act.wait_ge(hn_r, c + 1)
                nc.scalar.activation(as_r(k.x_hi[:, c]), hn[:, c], ACT.Copy).then_inc(x_hi_made, 1)
            for u in range(32):
                act.wait_ge(qd, u + 1)
                c, h = u // 2, u % 2
                nc.scalar.activation(qp[:, c, HALF * h:HALF * h + HALF], ps[:, u % 4, 0:HALF], ACT.Copy).then_inc(qc, 1)

        @block.vector
        def _(dve):
            v = Chain(dve, vch)
            V = nc.vector

            def mean_square(dim, n):
                dve.wait_ge(ssq, n)
                for h in range(2):
                    v.go(V.tensor_scalar(rinv[:, HALF * h:HALF * h + HALF], ps[:, 6 + h, 0:HALF], 1.0 / dim, EPS, ALU.mult, ALU.add))
                v.wait()
                V.reciprocal(rinv[:], rinv[:]).then_inc(msr, 1)
                dve.wait_ge(rir, n)

            dve.wait_ge(ld, 32)
            mean_square(512, 1)
            for c in range(4):
                V.scalar_tensor_tensor(out=k.mixT[:, 4 + c], in0=k.mixT[:, 4 + c], scalar=ga[:, c:c + 1], in1=rinv[:],
                                       op0=ALU.mult, op1=ALU.mult).then_inc(an, 1)
            for c in range(KD):
                for h in range(2):
                    dve.wait_ge(mixd, 2 * c + h + 1)
                    hs = k.hT[:, c, HALF * h:HALF * h + HALF]
                    v.go(V.tensor_tensor(hs, hs, ps[:, 2 * (c % 2) + h, 0:HALF], ALU.add))
                v.wait()
                V.memset(tick[:], 0.0).then_inc(hsq, 1)
            mean_square(D, 2)
            for c in range(KD):
                V.scalar_tensor_tensor(out=hn[:, c], in0=k.hT[:, c], scalar=gf[:, c:c + 1], in1=rinv[:],
                                       op0=ALU.mult, op1=ALU.mult).then_inc(hn_r, 1)
            for c in range(KD):
                dve.wait_ge(x_hi_made, c + 1)
                V.tensor_tensor(as_r(k.x_lo[:, c]), hn[:, c], k.x_hi[:, c], ALU.subtract)

        @block.tensor
        def _(pe):
            def column_sums(n, first):
                for c in range(n):
                    pe.wait_ge(asq, first + c + 1)
                    for h in range(2):
                        mm = nc.tensor.matmul(ps[:, 6 + h, 0:HALF], k.ones[:], sq[:, c, HALF * h:HALF * h + HALF],
                                              start=(c == 0), stop=(c == n - 1))
                mm.then_inc(ssq, 1)

            column_sums(4, 0)
            pe.wait_ge(an, 4)
            for c in range(KD):
                if c % 4 == 0:
                    pe.wait_ge(wo_ld[c // 4], 16)
                for h in range(2):
                    if c >= 2:
                        pe.wait_ge(hsq, c - 1)
                    for i in range(KD):
                        mm = nc.tensor.matmul(ps[:, 2 * (c % 2) + h, 0:HALF], wo[:, i, P * (c % 4):P * (c % 4) + P],
                                              k.mixT[:, i, HALF * h:HALF * h + HALF], start=(i == 0), stop=(i == KD - 1))
                    mm.then_inc(mixd, 1)
            column_sums(KD, 4)
            for u in range(32):
                c, h = u // 2, u % 2
                if u % 8 == 0:
                    pe.wait_ge(wq_ld[(u // 8) % 2], 16 * (u // 16 + 1))
                if u >= 4:
                    pe.wait_ge(qc, u - 3)
                for i in range(KD):
                    if u == 0:
                        pe.wait_ge(hn_r, i + 1)
                    mm = nc.tensor.matmul(ps[:, u % 4, 0:HALF], wq[:, (u // 8) % 2, i, P * (c % 4):P * (c % 4) + P],
                                          hn[:, i, HALF * h:HALF * h + HALF], start=(i == 0), stop=(i == KD - 1))
                mm.then_inc(qd, 1)


EG = 4
NG = KEYS // EG
SELECT_GROUPS = 10
ONE_HOT_GROUPS = 4
EARLY_GROUPS = SELECT_GROUPS + ONE_HOT_GROUPS


def up_part(pe, x_hi, x_lo, u_hi, u_lo, out, part):
    h, i = divmod(part, KD)
    cols = slice(HALF * h, HALF * h + HALF)
    for n, (u, x) in enumerate(((u_hi[:, i], x_hi), (u_hi[:, i], x_lo), (u_lo[:, i], x_hi))):
        mm = pe.matmul(out[:, h, 0:HALF], as_r(u), as_r(x[:, i, cols]),
                       start=(i == 0 and n == 0), stop=(i == KD - 1 and n == 2))
    return mm


def up_products(pe, x_hi, x_lo, u_hi, u_lo, out):
    for part in range(2 * KD):
        mm = up_part(pe, x_hi, x_lo, u_hi, u_lo, out, part)
    return mm


def retrieve_stage(nc, k):
    with ExitStack() as ctx:
        sb = lambda n, s, d=F32: ctx.enter_context(nc.sbuf_tensor(n, s, d))
        sem = k.sem
        sk, iota = sb("subkeys_sb", [P, 16, KEYS]), sb("iota16", [P, 16])
        scores, scr = sb("k_scores", [P, 2, 16, KEYS]), sb("k_scr", [P, 16, KEYS])
        v16, i16, i16f = sb("v16", [P, 16, 16]), sb("i16", [P, 16, 16], U32), sb("i16f", [P, 2, 16, 16])
        eq = sb("eq", [P, PH, 16, 16])
        vals, cpos, ab = sb("vals", [P, 2, PH, 16]), sb("cpos", [P, PH, 16], U32), sb("ab", [P, 2, PH, 16], U32)
        abf, idx, gsum = sb("abf", [P, 2, PH, 16]), sb("idx", [P, 2, 3, P]), sb("gsum", [P, 2, PH])
        u_raw, u_hi, u_lo = sb("r_u_raw", [P, EG, KD, P]), sb("r_u_hi", [P, 2, KD, P]), sb("r_u_lo", [P, 2, KD, P])
        gelu = k.mixT[:, 0:4].rearrange("p (q e) t -> p q e t", q=2)
        ps = ctx.enter_context(nc.psum_tensor("r_ps", [P, 8, 512], F32))
        ld = sem("r_ld")
        sd, scopied, s_used, eready, ed, tk, trd, trc, vch = (sem(n) for n in (
            "r_sd", "r_sc", "r_su", "r_er", "r_ed", "r_tk", "r_trd", "r_trc", "r_v"))
        u_ld = [sem(f"r_u_ld{e}") for e in range(EG)]
        up_done, gelu_done, u_hi_made, u_lo_made = (sem(n) for n in ("r_up", "r_gelu", "r_u_hi_made", "r_u_lo_made"))
        N = EG * SELECT_GROUPS
        block = ctx.enter_context(nc.Block())

        @block.sync
        def _(sp):
            sp.dma_start(sk[:], k.d["subkeys"]).then_inc(ld, 16)
            sp.dma_start(iota[:], k.d["iota16"]).then_inc(ld, 16)

            def load(n):
                e = n % EG
                if n >= EG:
                    sp.wait_ge(u_lo_made, n - EG + 1)
                sp.dma_start(u_raw[:, e].rearrange("p k n -> p (k n)"), k.d["u_tab"][n]).then_inc(u_ld[e], 16)

            for n in range(EG):
                load(n)
            for n in range(N):
                if n + EG < N:
                    load(n + EG)
                if n % 2:
                    q = (n // 2) % 2
                    sp.wait_ge(gelu_done, n + 1)
                    sp.dma_start(k.d["gelu_scr"][n // 2], gelu[:, q].rearrange("p e t -> p (e t)")).then_inc(k.spilled[q], 16)

        @block.scalar
        def _(act):
            def u_high(n):
                act.wait_ge(u_ld[n % EG], 16 * (n // EG + 1))
                nc.scalar.activation(as_r(u_hi[:, n % 2]), u_raw[:, n % EG], ACT.Copy).then_inc(u_hi_made, 1)

            def group(G):
                for n in range(EG * G, EG * G + EG):
                    e = n % EG
                    act.wait_ge(up_done, n + 1)
                    if G and e % 2 == 0:
                        act.wait_ge(k.spilled[e // 2], 16 * G)
                    nc.scalar.activation(gelu[:, e // 2, e % 2].rearrange("p (h n) -> p h n", h=2),
                                         ps[:, 4 + 2 * (n % 2):6 + 2 * (n % 2), 0:HALF], ACT.Gelu_apprx_tanh).then_inc(gelu_done, 1)
                    if n + 2 < N:
                        u_high(n + 2)

            def exponentials(t):
                m = TILE_ROWS[t]
                act.wait_ge(eready, t + 1)
                nc.scalar.activation(vals[0:m, t % 2], vals[0:m, t % 2], ACT.Exp).then_inc(ed, 1)

            def picks(t):
                m = TILE_ROWS[t]
                act.wait_ge(trd, t + 1)
                nc.scalar.activation(k.idxT[:, :, P * t:P * t + m],
                                     ps[:, t % 2, 0:3 * P].rearrange("p (n m) -> p n m", n=3)[:, :, 0:m], ACT.Copy).then_inc(trc, 1)

            u_high(0)
            u_high(1)
            for t in range(TILES):
                m = TILE_ROWS[t]
                act.wait_ge(sd, t + 1)
                if t >= 2:
                    act.wait_ge(s_used, t - 1)
                nc.scalar.activation(scores[0:m, t % 2].rearrange("p (b n) c -> p b (n c)", b=4), ps[0:m, 0:4, :], ACT.Copy).then_inc(scopied, 1)
                group(2 * t)
                if t >= 1:
                    exponentials(t - 1)
                if t >= 2:
                    picks(t - 2)
                group(2 * t + 1)
            exponentials(TILES - 1)
            picks(TILES - 2)
            picks(TILES - 1)

        @block.gpsimd
        def _(pool):
            for n in range(N):
                pool.wait_ge(u_hi_made, n + 1)
                if n >= 2:
                    pool.wait_ge(up_done, n - 1)
                nc.gpsimd.tensor_tensor(as_r(u_lo[:, n % 2]), u_raw[:, n % EG], u_hi[:, n % 2], ALU.subtract).then_inc(u_lo_made, 1)

        @block.vector
        def _(dve):
            v = Chain(dve, vch)
            V = nc.vector

            def select(t):
                m, b = TILE_ROWS[t], t % 2
                sc = scores[0:m, b]
                dve.wait_ge(scopied, t + 1)
                for u in range(16):
                    v.go(V.max(v16[0:m, u, 0:8], sc[:, u]))
                v.wait()
                for u in range(16):
                    v.go(V.max_index(i16[0:m, u, 0:8], v16[0:m, u, 0:8], sc[:, u]))
                    v.go(V.match_replace(scr[0:m, u], v16[0:m, u, 0:8], sc[:, u], GONE))
                v.wait()
                for u in range(16):
                    v.go(V.max(v16[0:m, u, 8:16], scr[0:m, u]))
                v.wait()
                for u in range(16):
                    v.go(V.max_index(i16[0:m, u, 8:16], v16[0:m, u, 8:16], scr[0:m, u]))
                v.wait()
                v.go(V.tensor_copy(i16f[0:m, b].rearrange("p a b -> p (a b)"), i16[0:m].rearrange("p a b -> p (a b)")))
                cand = sc.rearrange("p a b -> p (a b)").rearrange("p (h c) -> p h c", h=PH)
                left = scr[0:m].rearrange("p a b -> p (a b)").rearrange("p (h c) -> p h c", h=PH)
                for h in range(PH):
                    v.go(V.tensor_tensor(cand[:, h].rearrange("p (a b) -> p a b", a=16),
                                         v16[0:m, 2 * h].unsqueeze(2).to_broadcast([m, 16, 16]),
                                         v16[0:m, 2 * h + 1].unsqueeze(1).to_broadcast([m, 16, 16]), ALU.add))
                v.wait()
                for h in range(PH):
                    v.go(V.max(vals[0:m, b, h, 0:8], cand[:, h]))
                v.wait()
                for h in range(PH):
                    v.go(V.max_index(cpos[0:m, h, 0:8], vals[0:m, b, h, 0:8], cand[:, h]))
                    v.go(V.match_replace(left[:, h], vals[0:m, b, h, 0:8], cand[:, h], GONE))
                v.wait()
                V.memset(gsum[0:1, 0, 0:1], 0.0).then_inc(s_used, 1)
                for h in range(PH):
                    v.go(V.max(vals[0:m, b, h, 8:16], left[:, h]))
                v.wait()
                for h in range(PH):
                    v.go(V.max_index(cpos[0:m, h, 8:16], vals[0:m, b, h, 8:16], left[:, h]))
                v(V.tensor_copy(gsum[0:m, 0], vals[0:m, b, :, 0]))
                V.tensor_tensor(vals[0:m, b], vals[0:m, b], gsum[0:m, 0].unsqueeze(2).to_broadcast([m, PH, 16]),
                                ALU.subtract).then_inc(eready, 1)
                v.go(V.tensor_scalar(ab[0:m, 0], cpos[0:m], 4, None, ALU.logical_shift_right))
                v(V.tensor_scalar(ab[0:m, 1], cpos[0:m], 15, None, ALU.bitwise_and))
                v(V.tensor_copy(abf[0:m].rearrange("p a h c -> p (a h c)"), ab[0:m].rearrange("p a h c -> p (a h c)")))
                if t >= 2:
                    dve.wait_ge(trd, t - 1)
                e3 = eq[0:m].rearrange("p h c a -> p (h c) a")
                for s in range(2):
                    v(V.tensor_tensor(e3, abf[0:m, s].rearrange("p h c -> p (h c)").unsqueeze(2).to_broadcast([m, P, 16]),
                                      iota[0:m].unsqueeze(1).to_broadcast([m, P, 16]), ALU.is_equal))
                    fs = i16f[0:m, b].rearrange("p (h s) a -> p h s a", s=2)[:, :, s]
                    v(V.tensor_tensor(eq[0:m], eq[0:m], fs.unsqueeze(2).to_broadcast([m, PH, 16, 16]), ALU.mult))
                    v(V.tensor_reduce(idx[0:m, b, s], e3, AX.X, ALU.add))

            def gates(t):
                m, b = TILE_ROWS[t], t % 2
                dve.wait_ge(ed, t + 1)
                v(V.tensor_reduce(gsum[0:m, 0], vals[0:m, b], AX.X, ALU.add))
                v(V.reciprocal(gsum[0:m, 1], gsum[0:m, 0]))
                V.tensor_tensor(idx[0:m, b, 2].rearrange("p (h c) -> p h c", h=PH), vals[0:m, b],
                                gsum[0:m, 1].unsqueeze(2).to_broadcast([m, PH, 16]), ALU.mult).then_inc(tk, 1)

            dve.wait_ge(ld, 32)
            for t in range(TILES):
                select(t)
                if t >= 1:
                    gates(t - 1)
            gates(TILES - 1)

        @block.tensor
        def _(pe):
            def group(G):
                for n in range(EG * G, EG * G + EG):
                    pe.wait_ge(u_lo_made, n + 1)
                    if n >= 2:
                        pe.wait_ge(gelu_done, n - 1)
                    b = n % 2
                    up_products(nc.tensor, k.x_hi, k.x_lo, u_hi[:, b], u_lo[:, b], ps[:, 4 + 2 * b:6 + 2 * b]).then_inc(up_done, 1)

            def transposes(t):
                m = TILE_ROWS[t]
                pe.wait_ge(tk, t + 1)
                if t < TILES - 2:
                    pe.wait_ge(scopied, t + 3)
                elif t == TILES - 2:
                    pe.wait_ge(scopied, TILES)
                for n in range(3):
                    mm = nc.tensor.transpose(ps[:, t % 2, P * n:P * n + m], idx[0:m, t % 2, n], k.ident[0:m, 0:m])
                mm.then_inc(trd, 1)

            pe.wait_ge(ld, 32)
            for t in range(TILES):
                m = TILE_ROWS[t]
                if t:
                    pe.wait_ge(scopied, t)
                if t >= 3:
                    pe.wait_ge(trc, t - 2)
                for u in range(16):
                    mm = nc.tensor.matmul(ps[0:m, u // 4, P * (u % 4):P * (u % 4) + P],
                                          k.qp[:, u, P * t:P * t + m], sk[:, u, :], start=True, stop=True)
                mm.then_inc(sd, 1)
                group(2 * t)
                if t >= 2:
                    transposes(t - 2)
                group(2 * t + 1)
            transposes(TILES - 2)
            transposes(TILES - 1)


TB = 32
NTB = T // TB


def gate_matrix_stage(nc, k):
    with ExitStack() as ctx:
        sb = lambda n, s, d=F32: ctx.enter_context(nc.sbuf_tensor(n, s, d))
        sem = k.sem
        iota = sb("iota128", [P, KEYS])
        oh1, oh2 = sb("one_hot1", [P, 8, KEYS]), sb("one_hot2", [P, 8, KEYS])
        stage = sb("gate_stage", [P, 2, NG, TB, EG])
        u_raw, u_hi, u_lo = (sb(f"g_{n}", [P, 2, KD, P]) for n in ("u_raw", "u_hi", "u_lo"))
        gelu = k.mixT[:, 4:6]
        ps = ctx.enter_context(nc.psum_tensor("g_ps", [P, 8, 512], F32))
        ld, hot, multiplied, copied = (sem(n) for n in ("gm_ld", "gm_hot", "gm_multiplied", "gm_copied"))
        u_ld = [sem(f"gm_u_ld{b}") for b in range(2)]
        up_done, gelu_done, u_hi_made, u_lo_made = (sem(n) for n in ("gm_up", "gm_gelu", "gm_u_hi_made", "gm_u_lo_made"))
        FIRST = EG * SELECT_GROUPS
        UPS = EG * ONE_HOT_GROUPS // 2
        assert UPS == NTB // 2 - 1
        QUADS = TB // 4
        PARTS = [3, 3, 2, 2, 2, 2, 2]
        block = ctx.enter_context(nc.Block())

        @block.sync
        def _(sp):
            def load_u(n, b):
                sp.dma_start(u_raw[:, b].rearrange("p k n -> p (k n)"),
                             k.d["u_tab"][bass.ds(n + FIRST, 1)].rearrange("o p f -> (o p) f")).then_inc(u_ld[b], 16)

            def blocks(i, ups, ahead):
                for b in range(2):
                    if ahead:
                        sp.wait_ge(u_lo_made, 2 * i + (b + 1))
                        load_u(2 * i + (b + 2), b)
                    if ups and b == 1:
                        sp.wait_ge(gelu_done, 2 * i + 2)
                        sp.dma_start(k.d["gelu_scr"][bass.ds(i + FIRST // 2, 1)].rearrange("o p f -> (o p) f"),
                                     gelu.rearrange("p e t -> p (e t)")).then_inc(k.spilled_late, 16)
                    sp.wait_ge(copied, 2 * QUADS * i + (QUADS * b + QUADS + 4))
                    sp.dma_start(k.d["gate_scr"][:, :, bass.ds(2 * i + b, 1), :].rearrange("g p o f -> p g (o f)"),
                                 stage[:, b].rearrange("p g t e -> p g (t e)")).then_inc(k.gm_stored[b], 16)

            sp.dma_start(iota[:], k.d["iota128"]).then_inc(ld, 16)
            for b in range(2):
                load_u(b, b)
            for q in range(2):
                sp.wait_ge(k.spilled[q], 16 * SELECT_GROUPS)
            for b in range(2):
                sp.dma_start(k.early_act[:, b], k.d["gelu_scr"][2 * b:2 * b + 2].rearrange("o p f -> p o f")).then_inc(k.act_ld[b], 16)
            for half in range(2):
                sp.dma_start(k.v_raw[:, half].rearrange("p c e n -> p (c e n)"),
                             k.d["v_tab"][:, 0, 2048 * half:2048 * half + 2048]).then_inc(k.v_ld[half], 16)
            with sp.Fori(0, UPS - 1) as i:
                blocks(i, True, True)
            blocks(UPS - 1, True, False)
            blocks(UPS, False, False)

        @block.vector
        def _(dve):
            dve.wait_ge(ld, 16)
            with dve.Fori(0, NTB) as i:
                for n in range(TB):
                    if n % 4 == 0:
                        dve.wait_ge(multiplied, QUADS * i + (n // 4 + 1))
                    nc.vector.tensor_scalar(oh1[:, n % 8], iota[:], k.idxT[:, 0, bass.ds(TB * i + n, 1)], None, ALU.is_equal)
                    nc.vector.tensor_scalar(oh2[:, n % 8], iota[:], k.idxT[:, 1, bass.ds(TB * i + n, 1)],
                                            k.idxT[:, 2, bass.ds(TB * i + n, 1)], ALU.is_equal, ALU.mult).then_inc(hot, 1)

        @block.gpsimd
        def _(pool):
            with pool.Fori(0, UPS) as i:
                for b in range(2):
                    pool.wait_ge(u_hi_made, 2 * i + (b + 1))
                    nc.gpsimd.tensor_tensor(as_r(u_lo[:, b]), u_raw[:, b], u_hi[:, b], ALU.subtract).then_inc(u_lo_made, 1)

        @block.tensor
        def _(pe):
            def blocks(i, ups):
                for b in range(2):
                    out = ps[:, 4 + 2 * b:6 + 2 * b]
                    done = 0
                    for q in range(QUADS):
                        pe.wait_ge(copied, 2 * QUADS * i + (QUADS * b + q + 1))
                        for n in range(4 * q, 4 * q + 4):
                            pe.wait_ge(hot, 2 * TB * i + (TB * b + n + 1))
                            mm = nc.tensor.matmul(ps[:, q % 4, KEYS * (n % 4):KEYS * (n % 4) + KEYS], oh1[:, n % 8], oh2[:, n % 8],
                                                  start=True, stop=True)
                        mm.then_inc(multiplied, 1)
                        if ups and q < QUADS - 1:
                            if q == 0:
                                pe.wait_ge(u_lo_made, 2 * i + (b + 1))
                            for part in range(done, done + PARTS[q]):
                                mm = up_part(nc.tensor, k.x_hi, k.x_lo, u_hi[:, b], u_lo[:, b], out, part)
                            done += PARTS[q]
                            if q == QUADS - 2:
                                mm.then_inc(up_done, 1)

            pe.sem_inc(multiplied, 2)
            with pe.Fori(0, UPS) as i:
                blocks(i, True)
            blocks(UPS, False)

        @block.scalar
        def _(act):
            def u_high(b, turn):
                act.wait_ge(u_ld[b], 16 * turn + 16)
                nc.scalar.activation(as_r(u_hi[:, b]), u_raw[:, b], ACT.Copy).then_inc(u_hi_made, 1)

            def blocks(i, ups, ahead):
                for b in range(2):
                    act.wait_ge(k.gm_stored[b], 16 * i + 16)
                    for q in range(QUADS):
                        if ups and q == QUADS - 1:
                            act.wait_ge(up_done, 2 * i + (b + 1))
                            if b == 0:
                                act.wait_ge(k.spilled_late, 16 * i + 16)
                            nc.scalar.activation(gelu[:, b].rearrange("p (h n) -> p h n", h=2), ps[:, 4 + 2 * b:6 + 2 * b, 0:HALF],
                                                 ACT.Gelu_apprx_tanh).then_inc(gelu_done, 1)
                            if ahead:
                                u_high(b, i + 1)
                        act.wait_ge(multiplied, 2 * QUADS * i + (QUADS * b + q + 3))
                        nc.scalar.activation(stage[:, b, :, 4 * q:4 * q + 4, :].rearrange("p g t e -> p t g e"),
                                             ps[:, q % 4, :].rearrange("p (t g e) -> p t g e", t=4, g=NG),
                                             ACT.Copy).then_inc(copied, 1)

            act.sem_inc(copied, 4)
            act.sem_inc(k.spilled_late, 16)
            for b in range(2):
                act.sem_inc(k.gm_stored[b], 16)
            for b in range(2):
                u_high(b, 0)
            with act.Fori(0, UPS - 1) as i:
                blocks(i, True, True)
            blocks(UPS - 1, True, False)
            blocks(UPS, False, False)


def experts_stage(nc, k):
    with ExitStack() as ctx:
        sb = lambda n, s, d=F32: ctx.enter_context(nc.sbuf_tensor(n, s, d))
        sem = k.sem
        u_raw, u_hi, u_lo = sb("u_raw", [P, EG, KD, P]), sb("u_hi", [P, 2, KD, P]), sb("u_lo", [P, 2, KD, P])
        v_hi, v_lo = sb("v_hi", [P, 4, EG, P]), sb("v_lo", [P, 4, EG, P])
        w_raw, w_hi, w_lo = sb("w_raw", [P, 2, T]), sb("w_hi", [P, 2, EG, T]), sb("w_lo", [P, 2, EG, T])
        act_ = sb("e_act", [P, 2, T])
        v_raw, early_act, v_ld, act_ld = k.v_raw, k.early_act, k.v_ld, k.act_ld
        gt = k.mixT[:].rearrange("p (b e) t -> p b (e t)", b=2).rearrange("p b (t e) -> p b t e", e=EG)
        ps = ctx.enter_context(nc.psum_tensor("e_ps", [P, 8, 512], F32))
        u_ld, g_ld = [sem(f"e_u_loaded{e}") for e in range(EG)], [sem(f"e_g_loaded{b}") for b in range(2)]
        up_done, gelu_done, down_done, added = (sem(n) for n in ("e_up", "e_gelu", "e_down", "e_added"))
        u_hi_made, u_lo_made, v_hi_made, v_lo_made, w_made, w_hi_made, w_lo_made = (
            sem(f"e_{n}_made") for n in ("u_hi", "u_lo", "v_hi", "v_lo", "w", "w_hi", "w_lo"))
        block = ctx.enter_context(nc.Block())

        E = EARLY_GROUPS
        DOWN0 = KD + 1
        GELU0 = ADD0 = 2
        EARLY_PAIRS, PAIRS_LEFT = E // 2 - 1, (NG - E) // 2 - 2

        @block.sync
        def _(sp):
            def load_u(s, e):
                sp.dma_start(u_raw[:, e].rearrange("p k n -> p (k n)"),
                             k.d["u_tab"][bass.ds(EG * s + e, 1)].rearrange("o p f -> (o p) f")).then_inc(u_ld[e], 16)

            def load_gates(s, b):
                sp.dma_start(gt[:, b].rearrange("p t e -> p (t e)"),
                             k.d["gate_scr"][bass.ds(s, 1)].rearrange("o p a f -> (o p) (a f)")).then_inc(g_ld[b], 16)

            def loads(s, b, early):
                if not early:
                    for e in range(EG):
                        sp.wait_ge(u_lo_made, EG * s + (e + 1 - EG * E))
                        load_u(s + 1, e)
                sp.wait_ge(w_made, EG * s)
                load_gates(s + 1, 1 - b)
                if early:
                    sp.dma_start(early_act[:, 1 - b], k.d["gelu_scr"][bass.ds(2 * s + 2, 2)].rearrange("o p f -> p o f")
                                 ).then_inc(act_ld[1 - b], 16)

            for b in range(2):
                sp.wait_ge(k.gm_stored[b], 16 + 16 * (NTB // 2))
            load_gates(0, 0)
            sp.wait_ge(k.spilled_late, 16 + 8 * EG * ONE_HOT_GROUPS)
            load_gates(1, 1)
            for e in range(EG):
                load_u(E, e)
            with sp.Fori(0, EARLY_PAIRS) as i:
                loads(2 * i + 1, 1, True)
                loads(2 * i + 2, 0, True)
            sp.wait_ge(w_made, EG * (E - 1))
            load_gates(E, 0)
            with sp.Fori(0, PAIRS_LEFT + 1) as i:
                loads(2 * i + E, 0, False)
                loads(2 * i + (E + 1), 1, False)
            loads(NG - 2, 0, False)

        @block.scalar
        def _(act):
            def u_high(e, turn):
                act.wait_ge(u_ld[e], 16 * turn + 16)
                nc.scalar.activation(as_r(u_hi[:, e % 2]), u_raw[:, e], ACT.Copy).then_inc(u_hi_made, 1)

            def v_high(G, c):
                if c % 4 == 0:
                    act.wait_ge(v_ld[c // 4], 16 * G + 16)
                act.wait_ge(down_done, KD * G + (c + DOWN0 - 3))
                nc.scalar.activation(as_r(v_hi[:, c % 4]), v_raw[:, c // 4, c % 4], ACT.Copy).then_inc(v_hi_made, 1)

            def load_v(G, half):
                act.wait_ge(v_lo_made, KD * G + (4 * half + 4 - KD))
                act.dma_start(v_raw[:, half].rearrange("p c e n -> p (c e n)"),
                              k.d["v_tab"][:, bass.ds(G, 1), 2048 * half:2048 * half + 2048].rearrange("p o f -> p (o f)")
                              ).then_inc(v_ld[half], 16)

            def w_high(s, b, e):
                act.wait_ge(w_made, EG * s + (e + 1))
                nc.scalar.activation(as_r(w_hi[:, b, e]), w_raw[:, e % 2], ACT.Copy).then_inc(w_hi_made, 1)

            def early_step(s, b):
                load_v(s, 0)
                for e in range(EG):
                    w_high(s, b, e)
                    for c in (2 * e, 2 * e + 1):
                        if c < 4:
                            v_high(s - 1, c + 4)
                        else:
                            v_high(s, c - 4)
                        if c == 4:
                            load_v(s, 1)

            def step(s, b, ahead=True, v_first=True):
                for e in range(EG):
                    act.wait_ge(up_done, EG * s + (e + 1 - EG * E))
                    act.wait_ge(w_made, EG * s + (e - 1))
                    nc.scalar.activation(act_[:, e % 2].rearrange("p (h n) -> p h n", h=2),
                                         ps[:, 2 * (e % 2):2 * (e % 2) + 2, 0:HALF], ACT.Gelu_apprx_tanh).then_inc(gelu_done, 1)
                    if e < 2:
                        u_high(e + 2, s - E)
                    elif ahead:
                        u_high(e - 2, s - (E - 1))
                    if v_first:
                        v_high(s - 1, e)
                    w_high(s, b, e)
                v_high(s - 1, 4)
                load_v(s, 0)
                for c in range(5, KD):
                    v_high(s - 1, c)
                load_v(s, 1)

            act.sem_inc(gelu_done, GELU0)
            for e in range(EG):
                w_high(0, 0, e)
            for c in range(4):
                v_high(0, c)
            for e in range(2):
                u_high(e, 0)
            early_step(1, 1)
            with act.Fori(0, EARLY_PAIRS) as i:
                early_step(2 * i + 2, 0)
                early_step(2 * i + 3, 1)
            step(E, 0, v_first=False)
            step(E + 1, 1)
            with act.Fori(0, PAIRS_LEFT) as i:
                step(2 * i + (E + 2), 0)
                step(2 * i + (E + 3), 1)
            step(NG - 2, 0)
            step(NG - 1, 1, ahead=False)
            for c in range(KD):
                v_high(NG - 1, c)

        @block.vector
        def _(dve):
            def u_low(n, e):
                dve.wait_ge(u_hi_made, n + 1)
                nc.vector.tensor_tensor(as_r(u_lo[:, e % 2]), u_raw[:, e], u_hi[:, e % 2], ALU.subtract).then_inc(u_lo_made, 1)

            def v_low(G, c):
                dve.wait_ge(v_hi_made, KD * G + (c + 1))
                nc.vector.tensor_tensor(as_r(v_lo[:, c % 4]), v_raw[:, c // 4, c % 4], v_hi[:, c % 4], ALU.subtract).then_inc(v_lo_made, 1)

            def add(G, c):
                dve.wait_ge(down_done, KD * G + (c + DOWN0 + 1))
                h = k.hT[:, c].rearrange("p (h n) -> p h n", h=2)
                nc.vector.tensor_tensor(h, h, ps[:, 4 + 2 * (c % 2):6 + 2 * (c % 2), 0:HALF], ALU.add).then_inc(added, 1)

            def sums(G):
                for c in range(KD):
                    add(G, c)
                    if c < 4:
                        v_low(G, c + 4)

            def w_low(s, b, e):
                dve.wait_ge(w_hi_made, EG * s + (e + 1))
                nc.vector.tensor_tensor(as_r(w_lo[:, b, e]), w_raw[:, e % 2], w_hi[:, b, e], ALU.subtract).then_inc(w_lo_made, 1)

            def early_step(s, b, turn, before=True):
                dve.wait_ge(g_ld[b], 16 * turn + 16)
                dve.wait_ge(act_ld[b], 16 * turn + 16)
                for e in range(EG):
                    nc.vector.tensor_tensor(w_raw[:, e % 2], early_act[:, b, e], gt[:, b, :, e], ALU.mult).then_inc(w_made, 1)
                    if before:
                        add(s - 1, 2 * e)
                        if e < 2:
                            v_low(s - 1, 2 * e + 4)
                        else:
                            v_low(s, 2 * e - 4)
                    w_low(s, b, e)
                    if before:
                        add(s - 1, 2 * e + 1)
                        if e < 2:
                            v_low(s - 1, 2 * e + 5)
                        else:
                            v_low(s, 2 * e - 3)

            def step(s, b, turn, ahead=True, v_first=True):
                dve.wait_ge(g_ld[b], 16 * turn + 16)
                for e in range(EG):
                    dve.wait_ge(gelu_done, EG * s + (e + GELU0 + 1 - EG * E))
                    nc.vector.tensor_tensor(w_raw[:, e % 2], act_[:, e % 2], gt[:, b, :, e], ALU.mult).then_inc(w_made, 1)
                    if e < 2 or ahead:
                        u_low(EG * s + (e + 2 - EG * E), (e + 2) % 4)
                    if v_first:
                        v_low(s - 1, e)
                    w_low(s, b, e)
                sums(s - 1)

            dve.sem_inc(added, ADD0)
            early_step(0, 0, 0, before=False)
            for c in range(4):
                v_low(0, c)
            for e in range(2):
                u_low(e, e)
            early_step(1, 1, 0)
            with dve.Fori(0, EARLY_PAIRS) as i:
                early_step(2 * i + 2, 0, i + 1)
                early_step(2 * i + 3, 1, i + 1)
            step(E, 0, E // 2, v_first=False)
            step(E + 1, 1, E // 2)
            with dve.Fori(0, PAIRS_LEFT) as i:
                step(2 * i + (E + 2), 0, i + (E // 2 + 1))
                step(2 * i + (E + 3), 1, i + (E // 2 + 1))
            step(NG - 2, 0, NG // 2 - 1)
            step(NG - 1, 1, NG // 2 - 1, ahead=False)
            for c in range(4):
                v_low(NG - 1, c)
            sums(NG - 1)

        @block.tensor
        def _(pe):
            def up(G):
                for e in range(EG):
                    pe.wait_ge(u_lo_made, EG * G + (e + 1 - EG * E))
                    pe.wait_ge(gelu_done, EG * G + (e + 1 - EG * E))
                    b = e % 2
                    up_products(nc.tensor, k.x_hi, k.x_lo, u_hi[:, b], u_lo[:, b], ps[:, 2 * b:2 * b + 2]).then_inc(up_done, 1)

            def down(G, b):
                pe.wait_ge(w_lo_made, EG * G + EG)
                for c in range(KD):
                    pe.wait_ge(v_lo_made, KD * G + (c + 1))
                    pe.wait_ge(added, KD * G + (c + 1))
                    for h in range(2):
                        cols = slice(HALF * h, HALF * h + HALF)
                        for e in range(EG):
                            for n, (v, w) in enumerate(((v_hi, w_hi), (v_hi, w_lo), (v_lo, w_hi))):
                                mm = nc.tensor.matmul(ps[:, 4 + 2 * (c % 2) + h, 0:HALF], as_r(v[:, c % 4, e]), as_r(w[:, b, e, cols]),
                                                      start=(e == 0 and n == 0), stop=(e == EG - 1 and n == 2))
                    mm.then_inc(down_done, 1)

            pe.sem_inc(down_done, DOWN0)
            down(0, 0)
            with pe.Fori(0, EARLY_PAIRS) as i:
                down(2 * i + 1, 1)
                down(2 * i + 2, 0)
            with pe.Fori(0, PAIRS_LEFT + 1) as i:
                up(2 * i + E)
                down(2 * i + (E - 1), 1)
                up(2 * i + (E + 1))
                down(2 * i + E, 0)
            up(NG - 2)
            down(NG - 3, 1)
            up(NG - 1)
            down(NG - 2, 0)
            down(NG - 1, 1)


def ple_stage(nc, k):
    with ExitStack() as ctx:
        sb = lambda n, s, d=F32: ctx.enter_context(nc.sbuf_tensor(n, s, d))
        sem = k.sem
        wg, wp, pT, gp = sb("w_gate_sb", [P, KD, D]), sb("w_proj_sb", [P, 2, D]), sb("ple_T", [P, 2, T]), sb("g_ple_sb", [P, KD])
        sq, hn = sb("l_sq", [P, KD, T]), sb("l_hn", [P, KD, T])
        rinv, gate = sb("l_rinv", [P, T]), sb("l_gate", [P, 4, HALF])
        ps = ctx.enter_context(nc.psum_tensor("l_ps", [P, 8, 512], F32))
        ld, sqd, ssq, msr, rir, hr, gd, pd, sg, out, vch = (sem(n) for n in (
            "l_ld", "l_sqd", "l_ssq", "l_msr", "l_rir", "l_hr", "l_gd", "l_pd", "l_sg", "l_out", "l_v"))
        block = ctx.enter_context(nc.Block())

        @block.sync
        def _(sp):
            for dst, src in ((wg, k.d["w_gate"]), (wp, k.d["w_proj"]), (pT, k.d["ple_in"]), (gp, k.d["g_ple"])):
                sp.dma_start(dst[:], src).then_inc(ld, 16)
            for c in range(KD):
                sp.wait_ge(out, 2 * c + 2)
                sp.dma_start(k.o["yT"][:, c], k.hT[:, c]).then_inc(k.stored, 16)
            k.n_stored += 16 * KD

        @block.scalar
        def _(act):
            for c in range(KD):
                nc.scalar.activation(sq[:, c], k.hT[:, c], ACT.Square).then_inc(sqd, 1)
            act.wait_ge(msr, 1)
            nc.scalar.activation(rinv[:], rinv[:], ACT.Sqrt).then_inc(rir, 1)
            for u in range(16):
                act.wait_ge(gd, u + 1)
                if u >= 4:
                    act.wait_ge(out, u - 3)
                nc.scalar.activation(gate[:, u % 4], ps[:, u % 4, 0:HALF], ACT.Sigmoid).then_inc(sg, 1)

        @block.vector
        def _(dve):
            v = Chain(dve, vch)
            V = nc.vector
            dve.wait_ge(ssq, 1)
            for h in range(2):
                v.go(V.tensor_scalar(rinv[:, HALF * h:HALF * h + HALF], ps[:, 6 + h, 0:HALF], 1.0 / D, EPS, ALU.mult, ALU.add))
            v.wait()
            V.reciprocal(rinv[:], rinv[:]).then_inc(msr, 1)
            dve.wait_ge(rir, 1)
            dve.wait_ge(ld, 64)
            for c in range(KD):
                V.scalar_tensor_tensor(out=hn[:, c], in0=k.hT[:, c], scalar=gp[:, c:c + 1], in1=rinv[:],
                                       op0=ALU.mult, op1=ALU.mult).then_inc(hr, 1)
            for u in range(16):
                c, h = u // 2, u % 2
                dve.wait_ge(sg, u + 1)
                dve.wait_ge(pd, u + 1)
                v(V.tensor_tensor(gate[:, u % 4], gate[:, u % 4], ps[:, 4 + u % 4, 0:HALF], ALU.mult))
                hs = k.hT[:, c, HALF * h:HALF * h + HALF]
                V.tensor_tensor(hs, hs, gate[:, u % 4], ALU.add).then_inc(out, 1)

        @block.tensor
        def _(pe):
            for c in range(KD):
                pe.wait_ge(sqd, c + 1)
                for h in range(2):
                    mm = nc.tensor.matmul(ps[:, 6 + h, 0:HALF], k.ones[:], sq[:, c, HALF * h:HALF * h + HALF],
                                          start=(c == 0), stop=(c == KD - 1))
            mm.then_inc(ssq, 1)
            pe.wait_ge(ld, 64)
            pe.wait_ge(hr, KD)
            for u in range(16):
                c, h = u // 2, u % 2
                if u >= 4:
                    pe.wait_ge(sg, u - 3)
                    pe.wait_ge(out, u - 3)
                for i in range(KD):
                    mm = nc.tensor.matmul(ps[:, u % 4, 0:HALF], wg[:, i, P * c:P * c + P], hn[:, i, HALF * h:HALF * h + HALF],
                                          start=(i == 0), stop=(i == KD - 1))
                mm.then_inc(gd, 1)
                for i in range(2):
                    mm = nc.tensor.matmul(ps[:, 4 + u % 4, 0:HALF], wp[:, i, P * c:P * c + P], pT[:, i, HALF * h:HALF * h + HALF],
                                          start=(i == 0), stop=(i == 1))
                mm.then_inc(pd, 1)


def build(nc, d, o):
    k = Shared()
    k.d, k.o, k.n_stored = d, o, 0
    with ExitStack() as ctx:
        held = []

        def stage_sem(name):
            held.append(nc.alloc_semaphore(name))
            return held[-1]

        k.sem = lambda n: ctx.enter_context(nc.semaphore(n))
        sb = lambda n, s, dt=F32: ctx.enter_context(nc.sbuf_tensor(n, s, dt))
        k.stored = k.sem("stored")
        k.u_loaded = k.sem("u_loaded")
        k.y_loaded = k.sem("y_loaded")
        k.ident = sb("ident", [P, P])
        k.ones = sb("ones", [P, P])
        k.hT = sb("hT", [P, KD, T])
        k.mixT = sb("mixT", [P, 8, T])
        with ExitStack() as early:
            sbe = lambda n, s, dt=F32: early.enter_context(nc.sbuf_tensor(n, s, dt))
            k.yT = k.mixT[:, 4:8]
            k.U = sbe("U", [P, GROUPS, CHUNKS])
            k.qT = sbe("qT", [P, 4, T])
            k.ksT = sbe("ksT", [P, T])
            k.kwT = sbe("kwT", [P, T])
            k.qk = sbe("qk_rows", [P, TILES, 768])
            k.kv = sbe("kv_rows", [P, TILES, 512])
            k.gates = sbe("gates", [P, TILES, 24])
            k.cmp = sbe("v_and_k_cmp", [P, 2, 9, P])
            k.vcmp, k.kcT = k.cmp[:, 0], k.cmp[:, 1]
            k.pages = sbe("page_table_sb", [1, P], I32)
            k.pages_ld = k.sem("pages_ld")
            k.cmp_prompt = sbe("cmp_prompt", [P, 4, 2, 2, 8, 8])
            keep, k.sem = k.sem, stage_sem
            k.cmp_got, k.sel_got = ([[k.sem(f"{n}{p}_{s}") for s in range(2)] for p in range(2)] for n in ("cmp_got", "sel_got"))
            k.win_got = [k.sem(f"win_got{p}") for p in range(2)]
            project_stage(nc, k)
            ssm_stage(nc, k)
            with ExitStack() as ctx2:
                k.cmp_pages = [ctx2.enter_context(nc.sbuf_tensor(f"cmp_pages{n}", [P, 32, 256], F32)) for n in range(2)]
                glu_stage(nc, k)
                compress_stage(nc, k)
            k.sel_pages = [sbe(f"sel_pages{n}", [P, 32, 256]) for n in range(2)]
            k.win_k, k.win_v = sbe("win_k", [P, 2, 2, 512]), sbe("win_v", [P, 2, 2, 4, P])
            prompt_attention_stage(nc, k)
            sample_attention_stage(nc, k)
        nc.clear_and_free_semaphores(held)
        nc.all_engine_barrier()
        k.sem = keep
        k.gm_stored, k.spilled, k.v_ld, k.act_ld = ([k.sem(f"{n}{b}") for b in range(2)] for n in (
            "gm_stored", "spilled", "v_loaded", "early_act_loaded"))
        k.spilled_late = k.sem("spilled_late")
        with ExitStack() as late:
            sbl = lambda c, n, s, dt=F32: c.enter_context(nc.sbuf_tensor(n, s, dt))
            k.x_hi, k.x_lo = sbl(late, "x_hi", [P, KD, T]), sbl(late, "x_lo", [P, KD, T])
            k.idxT = sbl(late, "idx_T", [P, 3, T])
            with ExitStack() as queries:
                k.qp = sbl(queries, "peer_q", [P, 16, T])
                mix_stage(nc, k)
                retrieve_stage(nc, k)
            k.v_raw, k.early_act = sbl(late, "v_raw", [P, 2, 4, EG, P]), sbl(late, "early_act", [P, 2, EG, T])
            gate_matrix_stage(nc, k)
            experts_stage(nc, k)
        ple_stage(nc, k)
        with nc.Block() as block:
            @block.sync
            def _(sp):
                sp.wait_ge(k.stored, k.n_stored)


def host_layout(i):
    f = lambda a: np.ascontiguousarray(np.asarray(a))
    a = {}
    kmaj = lambda m: f(m.reshape(-1, P, m.shape[1]).transpose(1, 0, 2))
    x = np.concatenate([np.asarray(i["x_prompt"])[0], np.asarray(i["x_sample"]).reshape(T_SAMPLE, D)], 0)
    a["xT"] = kmaj(x.T)
    a["g_mix"] = f(np.asarray(i["g_mix"])[0].reshape(KD, P).T)
    w = np.asarray(i["w_in"])[0]
    q = w[:, 512:1024].reshape(D, 2, REP, HD).transpose(0, 2, 1, 3).reshape(D, 512)
    cols = [w[:, 0:512], q, w[:, 1024:1152], w[:, 1152:1280], w[:, 1280:1408], w[:, 1408:1536], w[:, 1536:1664],
            w[:, 1664:1792], w[:, 1792:1816]]
    a["w_in"] = kmaj(np.concatenate(cols, 1))
    gq, gs, gw = (np.asarray(i[n])[0] for n in ("g_q", "g_k_sel", "g_k_win"))
    a["g_heads"] = f(np.concatenate([np.tile(gq, 8), np.tile(gs, 2), np.tile(gw, 2)])[None, :])

    def rope_table(pos):
        inv = np.power(np.float32(500000.0), -np.arange(8, dtype=np.float32) / 8)
        ang = pos.astype(np.float32)[:, None] * inv[None, :].astype(np.float32)
        return np.stack([np.cos(ang), np.sin(ang), -np.sin(ang)], 1).astype(np.float32)

    pos = np.concatenate([np.arange(T_PROMPT), np.tile(PAST + np.arange(STEPS), SEQS), np.zeros(64)])
    a["rope"] = f(rope_table(pos).reshape(TILES, P, 3, 8).transpose(1, 0, 2, 3))
    for n, name in enumerate(("cache_k_win", "cache_v_win")):
        a[f"win_rows{n}"] = f(np.asarray(i[name])[0].reshape(SEQS, 512, P))
    g = lambda n: np.asarray(i[n])[0]
    dup = lambda a, b: f(np.concatenate([a, b], 0))
    ar, ai = g("ssm_a_re").T, g("ssm_a_im").T
    a["a_re"], a["a_im"] = dup(ar, ar), dup(ai, ai)
    a["log_dt"] = f(g("ssm_log_dt")[None, :])
    br, bi = (g(n).transpose(1, 0, 2) for n in ("ssm_b_re", "ssm_b_im"))
    cr, ci = (g(n).transpose(2, 0, 1) for n in ("ssm_c_re", "ssm_c_im"))
    sr, si = (g(n).transpose(2, 1, 0) for n in ("state_ssm_re", "state_ssm_im"))
    a["b1"], a["b2"], a["c1"], a["c2"] = dup(br, bi), dup(bi, br), dup(cr, ci), dup(ci, cr)
    a["s0"], a["s0x"] = dup(sr, si), dup(si, sr)
    a["dT"] = f(g("ssm_d").reshape(GROUPS, CH).T)
    a["sigma"] = np.concatenate([np.ones((64, 1)), -np.ones((64, 1))]).astype(np.float32)
    a["swap"] = f(np.roll(np.eye(P, dtype=np.float32), 64, 1))
    a["w_glu"] = kmaj(g("ssm_w_glu"))
    a["b_glu"] = f(g("ssm_b_glu").reshape(4, P).T)
    a["g_out_ssm"] = f(g("g_out_ssm").reshape(4, P).T)
    ck, cv = g("cache_k_cmp"), g("cache_v_cmp")
    lay = lambda c: c.reshape(POOL, 8, 8, 2, 2, HD).transpose(0, 3, 5, 4, 2, 1).reshape(POOL, P, 1, 2, 8, 8)
    a["cmp_pool"] = f(np.concatenate([lay(ck), lay(cv)], 2).reshape(POOL, P, 256))
    w1 = np.stack([g("cmp_w1_k"), g("cmp_w1_v")])
    a["cmp_w1"] = f(w1.reshape(2, 16, P, P).transpose(2, 0, 1, 3))
    a["cmp_w2"] = f(np.stack([g("cmp_w2_k"), g("cmp_w2_v")]).transpose(1, 0, 2))
    a["cmp_pe"] = f(np.stack([g("cmp_pe_k"), g("cmp_pe_v")]).reshape(2, 16, P).transpose(2, 0, 1))
    a["cmp_rope"] = rope_table(16 * np.arange(P) + 31)
    a["g_k_cmp"] = f(g("g_k_cmp")[None, :])
    a["page_table"] = f(np.asarray(i["page_table"]).reshape(1, P))
    q = np.arange(P)
    a["causal"] = np.where(q[None, :] <= q[:, None], 0.0, NEG).astype(np.float32)
    end = 16 * np.arange(NCP) + 31
    ok = end[None, None, :] <= (P * np.arange(4)[None, :, None] + q[:, None, None])
    a["cmp_mask"] = np.where(ok, 0.0, NEG).astype(np.float32)
    a["cmp_valid"] = ok.any(2).astype(np.float32)
    rs, rg, rr, rt = (x.ravel() for x in np.meshgrid(np.arange(2), np.arange(2), np.arange(4), np.arange(8), indexing="ij"))
    a["same"] = ((rs[:, None] == rs) & (rg[:, None] == rg) & (rt[:, None] == rt)).astype(np.float32)
    tok = np.arange(64)
    a["pick"] = np.stack([(tok[:, None] == (2 * p + rs) * 8 + rt) for p in range(PAIRS)], 1).astype(np.float32)
    a["mine"] = (np.arange(8)[None, :] == (rg * REP + rr)[:, None]).astype(np.float32)
    new = [(tok[None, :] // 8 == (2 * p + rs)[:, None]) & (tok[None, :] % 8 <= rt[:, None]) for p in range(PAIRS)]
    a["new_mask"] = np.where(np.stack(new, 1), 0.0, NEG).astype(np.float32)
    a["win_mask"] = np.where(np.arange(8)[None, :] <= rt[:, None], NEG, 0.0).astype(np.float32)
    a["force"] = np.tile(np.where(np.isin(np.arange(NSEL), (0, 31, 32)), 1000.0, 0.0).astype(np.float32), (P, 1))
    sk = g("cache_k_sel").transpose(0, 2, 3, 1).reshape(POOL, P, P)
    a["sel_pool"] = f(np.concatenate([sk, g("cache_v_sel").reshape(POOL, P, P)], 2))
    a["win_kT"] = f(g("cache_k_win").transpose(0, 2, 3, 1).reshape(SEQS, P, 512))
    wo = g("w_out")
    a["w_out"] = kmaj(np.concatenate([wo[:512], wo[512:].reshape(2, REP, HD, D).transpose(1, 0, 2, 3).reshape(512, D)]))
    a["g_out_attn"] = f(g("g_out_attn").reshape(2, REP, HD).transpose(0, 2, 1).reshape(P, REP))
    a["g_ffn"], a["g_ple"] = (f(g(n).reshape(KD, P).T) for n in ("g_ffn", "g_ple"))
    a["w_q"], a["w_gate"], a["w_proj"] = (kmaj(g(n)) for n in ("peer_w_q", "ple_w_gate", "ple_w_proj"))
    a["subkeys"] = f(g("peer_subkeys").reshape(16, KEYS, P).transpose(2, 0, 1))
    a["iota16"] = np.tile(np.arange(16, dtype=np.float32), (P, 1))
    a["iota128"] = np.tile(np.arange(P, dtype=np.float32), (P, 1))
    a["u_tab"] = f(g("peer_u").reshape(KEYS, KEYS, KD, P).transpose(1, 3, 2, 0).reshape(KEYS, P, KD * P))
    a["v_tab"] = f(g("peer_v").reshape(KEYS, NG, EG, KD, P).transpose(0, 1, 3, 2, 4).reshape(KEYS, NG, EG * D))
    ple = np.concatenate([g("p_prompt")[0], g("p_sample").reshape(T_SAMPLE, -1)], 0)
    a["ple_in"] = kmaj(ple.T)
    return a


OUTS = {"yT": [P, KD, T], "ssm_state": [P, GROUPS, 9],
        **{f"rows_p{n}": [T_PROMPT, P] for n in range(6)},
        **{f"rows_s{n}": [T_SAMPLE, P] for n in range(4)},
        **{f"rows_s{n}": [SEQS, 512, P] for n in (4, 5)}}
SCRATCH = {"u_scr": [512, 8, CHUNKS], "y_scr": [512, 8, CHUNKS],
           "gate_scr": [NG, P, NTB, TB * EG], "gelu_scr": [EARLY_GROUPS * EG // 2, P, 2 * T]}


def declare_and_build(nc, arrays):
    d = {n: nc.dram_tensor("in_" + n, a.shape, mybir.dt.from_np(a.dtype), kind="ExternalInput").ap()
         for n, a in arrays.items()}
    d.update({n: nc.dram_tensor(n, s, F32, kind="Internal").ap() for n, s in SCRATCH.items()})
    o = {n: nc.dram_tensor(n, s, F32, kind="ExternalOutput").ap() for n, s in OUTS.items()}
    d["win_rows"] = [d["win_rows0"], d["win_rows1"]]
    o["rows_p"], o["rows_s"] = ([o[f"rows_{x}{n}"] for n in range(6)] for x in "ps")
    build(nc, d, o)


def kernel(**inputs):
    import concourse.bacc as bacc
    from concourse.bass_utils import run_bass_kernel_spmd
    arrays = host_layout(inputs)
    nc = bacc.Bacc("TRN2", target_bir_lowering=False, num_devices=1)
    declare_and_build(nc, arrays)
    r = run_bass_kernel_spmd(nc, [{"in_" + n: v for n, v in arrays.items()}], core_ids=[0]).results[0]
    y = r["yT"].transpose(2, 1, 0).reshape(T, D)
    st = r["ssm_state"].reshape(2, HD, GROUPS, 9).transpose(0, 3, 2, 1)
    kvp = [r[f"rows_p{n}"].reshape(1, 1, T_PROMPT, 2, HD) for n in range(6)]
    kvs = [r[f"rows_s{n}"].reshape(1, SEQS, -1, 2, HD) for n in range(6)]
    c = np.ascontiguousarray
    return (c(y[:T_PROMPT])[None], c(y[T_PROMPT:]).reshape(SEQS, STEPS, D), *kvp, c(st[0, 0])[None, None],
            c(st[1, 0])[None, None], *kvs, c(st[0, 1:])[None], c(st[1, 1:])[None])
```

```python
from contextlib import ExitStack
import math

import numpy as np
import concourse.bass as bass
from concourse import mybir
from concourse.alu_op_type import AluOpType as ALU

F32 = mybir.dt.float32
I32 = mybir.dt.int32
U32 = mybir.dt.uint32
ACT = mybir.ActivationFunctionType
AX = mybir.AxisListType

P = 128
D = 1024
KD = D // P
T_PROMPT = 512
SEQS = 8
STEPS = 8
T_SAMPLE = SEQS * STEPS
T = T_PROMPT + T_SAMPLE
HALF = T // 2
TILES = 5
TILE_ROWS = [128, 128, 128, 128, 64]
CHUNKS = T // 8
PROMPT_CHUNKS = T_PROMPT // 8
GROUPS = 32
CH = 16
HD = 64
REP = 4
PAST = 2048
PAGES = 16
POOL = 160
NBLK = 128
EPS = 1e-6
NEG = -1e30
GONE = -3e38
SCALE = HD ** -0.5
KEYS = 128
PH = 8
TOPK = 16
WCOLS = 1816
ZQ, ZB, ZC = 512, 1024, 1536


class Shared:
    pass


class Chain:

    def __init__(self, eng, sem):
        self.eng, self.sem, self.n = eng, sem, 0

    def go(self, ins):
        self.n += 1
        ins.then_inc(self.sem, 1)

    def wait(self):
        self.eng.wait_ge(self.sem, self.n)

    def __call__(self, ins):
        self.go(ins)
        self.wait()


def project_stage(nc, k):
    with ExitStack() as ctx:
        sb = lambda n, s, d=F32: ctx.enter_context(nc.sbuf_tensor(n, s, d))
        sem = k.sem
        w = sb("w_in_sb", [P, KD, WCOLS])
        sq = sb("x_squared", [P, KD, T])
        norm = sb("a_T", [P, KD, T])
        rinv = sb("x_rinv", [P, T])
        gmix = sb("g_mix_sb", [P, KD])
        g12 = sb("head_gains", [P, 768])
        rope = sb("rope_sb", [P, TILES, 3, 8])
        hsq = sb("head_squares", [P, 2, 768])
        ms = sb("head_ms", [P, 2, 3, 12])
        ra = sb("rope_a", [P, 12, 16])
        rb = sb("rope_b", [P, 12, 16])
        um = k.mixT[:, 0:4].rearrange("p i (j c) -> p i j c", j=8)
        pz = ctx.enter_context(nc.psum_tensor("pz", [P, 2, 3, 512], F32))
        pu = ctx.enter_context(nc.psum_tensor("pu", [P, 2, 512], F32))
        ld_x, ld_wu, ld_w, ld_c = [sem("ld_x0"), sem("ld_x1")], sem("ld_wu"), sem("ld_w"), sem("ld_c")
        squared, ssq_done, ms_ready, rinv_ready = sem("x_sq"), sem("ssq"), sem("x_ms"), sem("x_ri")
        a_ready, u_done, u_free, z_done, z_free = sem("a_rdy"), sem("u_done"), sem("u_free"), sem("z_done"), sem("z_free")
        hsq_ready, hms_ready, hri_ready, rows_ready = sem("hsq"), sem("hms"), sem("hri"), sem("rows")
        tr_done, tr_free, tr_dve = sem("tr_done"), sem("tr_free"), sem("tr_dve")
        kv_copied, u_stored, vch, const_ready = sem("kv_copied"), sem("u_stored"), sem("p_vch"), sem("const_ready")
        gate_ready = sem("gate_rdy")
        block = ctx.enter_context(nc.Block())

        @block.sync
        def _(sp):
            for h in range(2):
                sp.dma_start(k.hT[:, 4 * h:4 * h + 4, :], k.d["xT"][:, 4 * h:4 * h + 4, :]).then_inc(ld_x[h], 16)
            sp.dma_start(gmix[:], k.d["g_mix"]).then_inc(ld_c, 16)
            sp.dma_start(k.pages[:], k.d["page_table"]).then_inc(k.pages_ld, 16)
            sp.dma_start(g12[:], k.d["g_heads"].to_broadcast([P, 768])).then_inc(ld_c, 16)
            sp.dma_start(rope[:], k.d["rope"]).then_inc(ld_c, 16)
            for i in range(KD):
                sp.dma_start(w[:, i, 0:ZQ], k.d["w_in"][:, i, 0:ZQ]).then_inc(ld_wu, 16)
            for i in range(KD):
                sp.dma_start(w[:, i, ZQ:], k.d["w_in"][:, i, ZQ:]).then_inc(ld_w, 16)
            for i in range(4):
                sp.wait_ge(u_free, 2 * i + 2)
                sp.dma_start(k.d["u_scr"][P * i:P * i + P], um[:, i]).then_inc(u_stored, 16)
            sp.wait_ge(u_stored, 64)
            for j in range(8):
                sp.dma_start(k.U[16 * j:16 * j + 16],
                             k.d["u_scr"][:, j, :].rearrange("(g c) n -> c g n", c=CH)).then_inc(k.u_loaded, 16)

        @block.gpsimd
        def _(pool):
            pool.memset(k.ident[:], 0.0).then_inc(const_ready, 1)
            pool.memset(k.ones[:], 1.0).then_inc(const_ready, 1)
            pool.wait_ge(const_ready, 2)
            pool.affine_select(out=k.ident[:], in_=k.ident[:], compare_op=ALU.not_equal, fill=1.0, base=0,
                               pattern=[[-1, P]], channel_multiplier=1).then_inc(const_ready, 1)

        @block.scalar
        def _(act):
            for i in range(KD):
                if i % 4 == 0:
                    act.wait_ge(ld_x[i // 4], 16)
                nc.scalar.activation(sq[:, i, :], k.hT[:, i, :], ACT.Square).then_inc(squared, 1)
            act.wait_ge(ms_ready, 1)
            nc.scalar.activation(rinv[:], rinv[:], ACT.Sqrt).then_inc(rinv_ready, 1)
            for i in range(4):
                for h in range(2):
                    act.wait_ge(u_done, 2 * i + h + 1)
                    nc.scalar.activation(um[:, i, :, 36 * h:36 * h + 36],
                                         pu[:, h, 0:HALF].rearrange("p (c j) -> p j c", j=8),
                                         ACT.Copy).then_inc(u_free, 1)
            for t in range(TILES):
                m, b = TILE_ROWS[t], t % 2
                act.wait_ge(z_done, t + 1)
                if t >= 2:
                    act.wait_ge(rows_ready, t - 1)
                nc.scalar.activation(hsq[0:m, b, 0:512], pz[0:m, b, 0, :], ACT.Square).then_inc(hsq_ready, 1)
                nc.scalar.activation(hsq[0:m, b, 512:640], pz[0:m, b, 1, 256:384], ACT.Square).then_inc(hsq_ready, 1)
                nc.scalar.activation(hsq[0:m, b, 640:768], pz[0:m, b, 2, 0:128], ACT.Square).then_inc(hsq_ready, 1)
                nc.scalar.activation(k.kv[0:m, t, 0:256], pz[0:m, b, 1, 0:256], ACT.Copy)
                nc.scalar.activation(k.kv[0:m, t, 256:384], pz[0:m, b, 1, 384:512], ACT.Copy)
                nc.scalar.activation(k.kv[0:m, t, 384:512], pz[0:m, b, 2, 128:256], ACT.Copy)
                nc.scalar.activation(k.gates[0:m, t, :], pz[0:m, b, 2, 256:280], ACT.Copy).then_inc(kv_copied, 1)
                act.wait_ge(hms_ready, t + 1)
                nc.scalar.activation(ms[0:m, b, 2, :], ms[0:m, b, 1, :], ACT.Sqrt).then_inc(hri_ready, 1)
            for t in range(TILES):
                m, b = TILE_ROWS[t], t % 2
                act.wait_ge(tr_done, t + 1)
                for i in range(4):
                    nc.scalar.activation(k.qT[:, i, P * t:P * t + m], pz[:, b, 0, P * i:P * i + m], ACT.Copy)
                nc.scalar.activation(k.ksT[:, P * t:P * t + m], pz[:, b, 1, 0:m], ACT.Copy)
                nc.scalar.activation(k.kwT[:, P * t:P * t + m], pz[:, b, 1, 128:128 + m], ACT.Copy).then_inc(tr_free, 1)
            act.wait_ge(kv_copied, TILES)
            for t in (0, 4):
                m, e = (128, 4) if t == 0 else (64, 5)
                nc.scalar.activation(k.gates[0:m, t:e, :], k.gates[0:m, t:e, :], ACT.Exp, scale=-1.0).then_inc(gate_ready, 1)

        @block.vector
        def _(dve):
            v = Chain(dve, vch)
            dve.wait_ge(ssq_done, 1)
            for h in range(2):
                v.go(nc.vector.tensor_scalar(rinv[:, HALF * h:HALF * h + HALF], pu[:, h, 0:HALF], 1.0 / D, EPS,
                                             ALU.mult, ALU.add))
            v.wait()
            nc.vector.reciprocal(rinv[:], rinv[:]).then_inc(ms_ready, 1)
            dve.wait_ge(rinv_ready, 1)
            dve.wait_ge(ld_c, 48)
            for h in range(2):
                dve.wait_ge(ld_x[h], 16)
            for i in range(KD):
                nc.vector.scalar_tensor_tensor(out=norm[:, i, :], in0=k.hT[:, i, :], scalar=gmix[:, i:i + 1],
                                               in1=rinv[:], op0=ALU.mult, op1=ALU.mult).then_inc(a_ready, 1)
            for t in range(TILES):
                m, b = TILE_ROWS[t], t % 2
                dve.wait_ge(hsq_ready, 3 * t + 3)
                v(nc.vector.tensor_reduce(ms[0:m, b, 0, :], hsq[0:m, b, :].rearrange("p (h d) -> p h d", d=HD),
                                          AX.X, ALU.add))
                v(nc.vector.tensor_scalar(ms[0:m, b, 0, :], ms[0:m, b, 0, :], 1.0 / HD, EPS, ALU.mult, ALU.add))
                nc.vector.reciprocal(ms[0:m, b, 1, :], ms[0:m, b, 0, :]).then_inc(hms_ready, 1)
                dve.wait_ge(hri_ready, t + 1)
                qk3 = k.qk[0:m, t, :].rearrange("p (h d) -> p h d", d=HD)
                for lo, hi, src in ((0, 8, pz[0:m, b, 0, :]), (8, 10, pz[0:m, b, 1, 256:384]),
                                    (10, 12, pz[0:m, b, 2, 0:128])):
                    v.go(nc.vector.tensor_tensor(qk3[:, lo:hi], src.rearrange("p (h d) -> p h d", d=HD),
                                                 ms[0:m, b, 2, lo:hi].unsqueeze(2).to_broadcast([m, hi - lo, HD]),
                                                 ALU.mult))
                dve.wait_ge(kv_copied, t + 1)
                v.wait()
                v(nc.vector.tensor_tensor(k.qk[0:m, t, :], k.qk[0:m, t, :], g12[0:m, :], ALU.mult))
                cos, sin, nsin = (rope[0:m, t, i, :].unsqueeze(1).to_broadcast([m, 12, 8]) for i in range(3))
                x1, x2 = qk3[:, :, 0:8], qk3[:, :, 8:16]
                v.go(nc.vector.tensor_tensor(ra[0:m, :, 0:8], x1, cos, ALU.mult))
                v.go(nc.vector.tensor_tensor(ra[0:m, :, 8:16], x2, cos, ALU.mult))
                v.go(nc.vector.tensor_tensor(rb[0:m, :, 0:8], x2, nsin, ALU.mult))
                v(nc.vector.tensor_tensor(rb[0:m, :, 8:16], x1, sin, ALU.mult))
                nc.vector.tensor_tensor(qk3[:, :, 0:16], ra[0:m], rb[0:m], ALU.add).then_inc(rows_ready, 1)
            for t in range(4):
                dve.wait_ge(tr_done, t + 1)
                for kv in range(2):
                    for g in range(2):
                        for r2 in range(2):
                            src = pz[g * 64:g * 64 + 64, t % 2, 2, P * kv:P * kv + P]
                            last = nc.vector.tensor_copy(k.cmp_prompt[r2 * 64:r2 * 64 + 64, t, kv, g],
                                                         src.rearrange("p (b i r) -> p r i b", r=2, i=8)[:, r2])
                last.then_inc(tr_dve, 1)
            for n, (t, e, m) in enumerate(((0, 4, 128), (4, 5, 64))):
                dve.wait_ge(gate_ready, n + 1)
                v(nc.vector.tensor_scalar(k.gates[0:m, t:e, :], k.gates[0:m, t:e, :], 1.0, None, ALU.add))
                v(nc.vector.reciprocal(k.gates[0:m, t:e, :], k.gates[0:m, t:e, :]))

        @block.tensor
        def _(pe):
            pe.wait_ge(const_ready, 3)
            for i in range(KD):
                pe.wait_ge(squared, i + 1)
                for h in range(2):
                    mm = nc.tensor.matmul(pu[:, h, 0:HALF], k.ones[:], sq[:, i, HALF * h:HALF * h + HALF],
                                          start=(i == 0), stop=(i == KD - 1))
            mm.then_inc(ssq_done, 1)
            pe.wait_ge(ld_wu, 16 * KD)
            for c in range(4):
                for h in range(2):
                    if c:
                        pe.wait_ge(u_free, 2 * (c - 1) + h + 1)
                    for i in range(KD):
                        if c == 0 and h == 0:
                            pe.wait_ge(a_ready, i + 1)
                        mm = nc.tensor.matmul(pu[:, h, 0:HALF], w[:, i, P * c:P * c + P],
                                              norm[:, i, HALF * h:HALF * h + HALF], start=(i == 0), stop=(i == KD - 1))
                    mm.then_inc(u_done, 1)
            pe.wait_ge(ld_w, 16 * KD)
            for t in range(TILES):
                m, b = TILE_ROWS[t], t % 2
                if t >= 2:
                    pe.wait_ge(rows_ready, t - 1)
                    pe.wait_ge(kv_copied, t - 1)
                for bank, (lo, n) in enumerate(((ZQ, 512), (ZB, 512), (ZC, 280))):
                    for i in range(KD):
                        mm = nc.tensor.matmul(pz[0:m, b, bank, 0:n], norm[:, i, P * t:P * t + m], w[:, i, lo:lo + n],
                                              start=(i == 0), stop=(i == KD - 1))
                mm.then_inc(z_done, 1)
            for t in range(TILES):
                m, b = TILE_ROWS[t], t % 2
                pe.wait_ge(rows_ready, TILES)
                pe.wait_ge(kv_copied, TILES)
                if t >= 2:
                    pe.wait_ge(tr_free, t - 1)
                    pe.wait_ge(tr_dve, t - 1)
                for i in range(6):
                    dst = pz[:, b, 0, P * i:P * i + m] if i < 4 else pz[:, b, 1, P * (i - 4):P * (i - 4) + m]
                    mm = nc.tensor.transpose(dst, k.qk[0:m, t, P * i:P * i + P], k.ident[0:m, 0:m])
                if t < 4:
                    for kv in range(2):
                        mm = nc.tensor.transpose(pz[:, b, 2, P * kv:P * kv + P],
                                                 k.kv[:, t, P * kv:P * kv + P], k.ident[:])
                mm.then_inc(tr_done, 1)


VCH = [(0, 7), (7, 14), (14, 21), (21, 28), (28, 32)]
MAGIC = 12582912.0
TWO_PI_PARTS = (6.28125, 0.0019350051879882812, 3.019915981956753e-07)


def ssm_stage(nc, k):
    with ExitStack() as ctx:
        sb = lambda n, s, d=F32: ctx.enter_context(nc.sbuf_tensor(n, s, d))
        sem = k.sem
        are, aim, ldt = sb("a_re", [P, GROUPS]), sb("a_im", [P, GROUPS]), sb("log_dt", [P, GROUPS])
        bc4 = sb("b_and_c", [P, 4, GROUPS, CH])
        b1, b2, c1, c2 = (bc4[:, n] for n in range(4))
        s0, s0x = sb("s0", [P, GROUPS, SEQS]), sb("s0_swapped", [P, GROUPS, SEQS])
        dT, sigma, perm = sb("dT", [CH, GROUPS]), sb("sigma", [P, 1]), sb("swap_matrix", [P, P])
        tmp = sb("s_tmp", [P, 8, GROUPS])
        x1, x2 = sb("x1", [P, GROUPS, CH]), sb("x2", [P, GROUPS, CH])
        pr, pi = sb("pow_re", [P, 9, GROUPS]), sb("pow_im", [P, 9, GROUPS])
        rr, ri = sb("rot8_re", [P, 7, GROUPS]), sb("rot8_im", [P, 7, GROUPS])
        magnitude8 = sb("mag8", [P, GROUPS])
        state_in = sb("state_in", [P, GROUPS, 8, CH])
        state_out = sb("state_out_w", [P, GROUPS, 9, CH])
        scratch = sb("s_scratch", [P, 32 * GROUPS])
        state_in_T = sb("state_in_T", [P, GROUPS, P])
        zw = sb("z_and_w", [P, 4, GROUPS, 64])
        rows_behind_zeros = zw[0:CH].rearrange("p a g n -> p (a g n)").rearrange("p (g z n) -> p g z n", g=GROUPS, z=2)
        toeplitz = state_in[:].rearrange("p g j c -> p g (j c)")
        vs = k.cmp[:].rearrange("p a s n -> p (a s n)").rearrange("p (g c) -> p g c", c=CHUNKS)
        z, w = zw[:, 0], zw[:, 1]
        rc, rs = (k.mixT[:, 4 * n:4 * n + 4].rearrange("p i t -> p (i t)")[:, 0:64 * GROUPS].rearrange("p (c g) -> p c g", c=64)
                  for n in range(2))
        cp_tmp = sb("s_cp_tmp", [P, GROUPS, CH])
        chunk_states = state_in_T[:].rearrange("p g n -> p (g n)")[:, 0:GROUPS * CHUNKS].rearrange("p (g c) -> p g c", c=CHUNKS)
        final_state = sb("s_final", [P, GROUPS, 9])
        ps = ctx.enter_context(nc.psum_tensor("ps_ssm", [P, 8, 512], F32))
        params_loaded, dt_loaded, vch = sem("s_params_loaded"), sem("s_dt_loaded"), sem("s_vch")
        dt_ready, exponent_ready = sem("s_dt_ready"), sem("s_exponent_ready")
        magnitude_ready, angle_ready = sem("s_magnitude_ready"), sem("s_angle_ready")
        sin_cos_done = sem("s_sin_cos_done")
        a_ready, transposed, transposes_copied = sem("s_a_ready"), sem("s_transposed"), sem("s_transposes_copied")
        rows_made, rows_copied = sem("s_rows_made"), sem("s_rows_copied")
        zeros_written, toeplitz_rows_ready = sem("s_zeros_written"), sem("s_toeplitz_rows_ready")
        toeplitz_loaded, v_made, v_copied = sem("s_toeplitz_loaded"), sem("s_v_made"), sem("s_v_copied")
        v_swapped, swapped_v_used = sem("s_v_swapped"), sem("s_swapped_v_used")
        scan_done, w_swapped, swapped_w_used = sem("s_scan_done"), sem("s_w_swapped"), sem("s_swapped_w_used")
        chunk_states_ready, final_state_ready = sem("s_chunk_states_ready"), sem("s_final_state_ready")
        y_made, y_copied, y_stored = sem("s_y_made"), sem("s_y_copied"), sem("s_y_stored")
        a_loaded = sem("s_ld_a")
        powers_ready, cp_ready, cp_chain = sem("s_powers_ready"), sem("s_cp_ready"), sem("s_cp_chain")
        y = vs
        block = ctx.enter_context(nc.Block())

        @block.sync
        def _(sp):
            sp.dma_start(ldt[:], k.d["log_dt"].to_broadcast([P, GROUPS])).then_inc(dt_loaded, 16)
            for dst, src in ((are[:], k.d["a_re"]), (aim[:], k.d["a_im"]), (sigma[:], k.d["sigma"])):
                sp.dma_start(dst, src).then_inc(a_loaded, 16)
            for dst, src in ((b1, k.d["b1"]), (b2, k.d["b2"]), (c1, k.d["c1"]), (c2, k.d["c2"]), (dT[:], k.d["dT"]), (perm[:], k.d["swap"])):
                sp.dma_start(dst, src).then_inc(params_loaded, 16)
            sp.dma_start(s0[:], k.d["s0"]).then_inc(params_loaded, 16)
            sp.dma_start(s0x[:], k.d["s0x"]).then_inc(params_loaded, 16)
            sp.wait_ge(toeplitz_rows_ready, 1)
            for j in range(8):
                zeros = (8 - j) * CH
                sp.dma_start(toeplitz[CH * j:CH * j + CH],
                             rows_behind_zeros.rearrange("c g z n -> c g (z n)")[:, :, zeros:zeros + P]).then_inc(toeplitz_loaded, 16)
            sp.wait_ge(final_state_ready, 2)
            sp.dma_start(k.o["ssm_state"], final_state[:]).then_inc(k.stored, 16)
            k.n_stored += 16
            sp.wait_ge(y_copied, 5)
            for j in range(8):
                sp.dma_start(k.d["y_scr"][:, j, :].rearrange("(g c) n -> c g n", c=CH), y[CH * j:CH * j + CH]).then_inc(y_stored, 16)
            sp.wait_ge(y_stored, 128)
            sp.dma_start(k.yT[:], k.d["y_scr"].rearrange("(i p) j n -> p i (j n)", p=P)).then_inc(k.y_loaded, 16)

        @block.gpsimd
        def _(pool):
            pool.memset(rows_behind_zeros, 0.0).then_inc(zeros_written, 1)
            v = Chain(pool, cp_chain)
            bc = lambda a: a.unsqueeze(2).to_broadcast([P, GROUPS, CH])
            pool.wait_ge(powers_ready, 1)
            for l in range(9):
                v.go(nc.gpsimd.tensor_tensor(state_out[:, :, l, :], c1, bc(pr[:, l]), ALU.mult))
                v(nc.gpsimd.tensor_tensor(cp_tmp[:], c2, bc(pi[:, l]), ALU.mult))
                last = nc.gpsimd.tensor_tensor(state_out[:, :, l, :], state_out[:, :, l, :], cp_tmp[:], ALU.subtract)
                if l < 8:
                    v(last)
            last.then_inc(cp_ready, 1)
            for n, src in enumerate((k.kv[:, :, 0:128], k.kv[:, :, 128:256], k.qk[:, :, 512:640],
                                     k.kv[:, :, 256:384], k.qk[:, :, 640:768], k.kv[:, :, 384:512])):
                pool.dma_start(k.o["rows_p"][n].rearrange("(a p) f -> p a f", p=P), src[:, 0:4]).then_inc(k.rows_stored, 16)
                if n < 4:
                    pool.dma_start(k.o["rows_s"][n], src[0:64, 4]).then_inc(k.rows_stored, 16)
                else:
                    for s in range(SEQS):
                        pool.dma_start(k.o["rows_s"][n][s, 504:512, :], src[8 * s:8 * s + 8, 4]).then_inc(k.rows_stored, 16)

        @block.scalar
        def _(act):
            act.wait_ge(dt_loaded, 16)
            nc.scalar.activation(ldt[:], ldt[:], ACT.Exp).then_inc(dt_ready, 1)
            act.wait_ge(exponent_ready, 1)
            nc.scalar.activation(tmp[:, 0], tmp[:, 0], ACT.Exp).then_inc(magnitude_ready, 1)
            act.wait_ge(angle_ready, 1)
            nc.scalar.activation(tmp[:, 2], tmp[:, 2], ACT.Sin).then_inc(sin_cos_done, 1)
            nc.scalar.activation(tmp[:, 3], tmp[:, 3], ACT.Sin).then_inc(sin_cos_done, 1)
            for i in range(8):
                act.wait_ge(transposed, i + 1)
                nc.scalar.activation(state_in_T[:, 4 * i:4 * i + 4, :], ps[:, i % 3, :].rearrange("p (g n) -> p g n", g=4),
                                     ACT.Copy).then_inc(transposes_copied, 1)
            act.wait_ge(zeros_written, 1)
            for i in range(8):
                act.wait_ge(rows_made, i + 1)
                nc.scalar.activation(rows_behind_zeros[:, 4 * i:4 * i + 4, 1, :], ps[0:CH, 3 + i % 3, :].rearrange("p (g n) -> p g n", g=4),
                                     ACT.Copy).then_inc(rows_copied, 1)
            for q, (g0, g1) in enumerate(VCH):
                act.wait_ge(v_made, q + 1)
                nc.scalar.activation(vs[:, g0:g1, :], ps[:, q, 0:(g1 - g0) * CHUNKS].rearrange("p (g c) -> p g c", c=CHUNKS),
                                     ACT.Copy).then_inc(v_copied, 1)
            act.wait_ge(final_state_ready, 2)
            for q, (g0, g1) in enumerate(VCH):
                act.wait_ge(y_made, q + 1)
                nc.scalar.activation(y[:, g0:g1, :], ps[:, q, 0:(g1 - g0) * CHUNKS].rearrange("p (g c) -> p g c", c=CHUNKS),
                                     ACT.Copy).then_inc(y_copied, 1)

        @block.vector
        def _(dve):
            v = Chain(dve, vch)
            tt = lambda o, a, b, op: nc.vector.tensor_tensor(o, a, b, op)

            def cmul(outr, outi, ar, ai, br, bi, shape):
                t1 = scratch[:, 0:shape[0] * shape[1]].rearrange("p (a b) -> p a b", a=shape[0])
                v.go(tt(outr, ar, br, ALU.mult))
                v.go(tt(outi, ar, bi, ALU.mult))
                v(tt(t1, ai, bi, ALU.mult))
                v(tt(outr, outr, t1, ALU.subtract))
                v(tt(t1, ai, br, ALU.mult))
                v(tt(outi, outi, t1, ALU.add))

            dve.wait_ge(a_loaded, 48)
            dve.wait_ge(dt_ready, 1)
            v(nc.vector.tensor_scalar(aim[:], aim[:], sigma[:, 0:1], None, ALU.mult))
            tt(tmp[:, 0], are[:], ldt[:], ALU.mult).then_inc(exponent_ready, 1)
            v(tt(tmp[:, 1], aim[:], ldt[:], ALU.mult))
            v(nc.vector.tensor_scalar(tmp[:, 4], tmp[:, 1], 1.0 / (2 * math.pi), MAGIC, ALU.mult, ALU.add))
            v(nc.vector.tensor_scalar(tmp[:, 4], tmp[:, 4], -MAGIC, None, ALU.add))
            for part in TWO_PI_PARTS:
                v(nc.vector.scalar_tensor_tensor(out=tmp[:, 1], in0=tmp[:, 4], scalar=-part, in1=tmp[:, 1],
                                                 op0=ALU.mult, op1=ALU.add))
            v(nc.vector.tensor_scalar(tmp[:, 2], tmp[:, 1], 3.1415925, -3.1415925, ALU.min, ALU.max))
            v(nc.vector.tensor_scalar(tmp[:, 3], tmp[:, 2], -1.0, None, ALU.mult))
            v(tt(tmp[:, 3], tmp[:, 3], tmp[:, 2], ALU.max))
            nc.vector.tensor_scalar(tmp[:, 3], tmp[:, 3], -1.0, math.pi / 2, ALU.mult, ALU.add).then_inc(angle_ready, 1)
            dve.wait_ge(magnitude_ready, 1)
            dve.wait_ge(sin_cos_done, 2)
            mag, sn, cs = tmp[:, 0], tmp[:, 2], tmp[:, 3]
            v.go(nc.vector.memset(pr[:, 0], 1.0))
            v.go(nc.vector.memset(pi[:, 0], 0.0))
            v.go(tt(pr[:, 1], mag, cs, ALU.mult))
            v(tt(pi[:, 1], mag, sn, ALU.mult))
            v.go(nc.vector.tensor_scalar(tmp[:, 4], pr[:, 1], -1.0, None, ALU.add))
            v.go(tt(tmp[:, 5], are[:], are[:], ALU.mult))
            v(tt(tmp[:, 6], aim[:], aim[:], ALU.mult))
            v(tt(tmp[:, 5], tmp[:, 5], tmp[:, 6], ALU.add))
            v(nc.vector.reciprocal(tmp[:, 5], tmp[:, 5]))
            v.go(tt(tmp[:, 6], tmp[:, 4], are[:], ALU.mult))
            v(tt(tmp[:, 7], pi[:, 1], aim[:], ALU.mult))
            v(tt(tmp[:, 6], tmp[:, 6], tmp[:, 7], ALU.add))
            v.go(tt(tmp[:, 7], pi[:, 1], are[:], ALU.mult))
            v(tt(tmp[:, 4], tmp[:, 4], aim[:], ALU.mult))
            v(tt(tmp[:, 7], tmp[:, 7], tmp[:, 4], ALU.subtract))
            v.go(tt(tmp[:, 6], tmp[:, 6], tmp[:, 5], ALU.mult))
            v(tt(tmp[:, 7], tmp[:, 7], tmp[:, 5], ALU.mult))
            bc = lambda a: a.unsqueeze(2).to_broadcast([P, GROUPS, CH])
            sc3 = scratch[:, 0:GROUPS * CH].rearrange("p (g c) -> p g c", c=CH)
            dve.wait_ge(params_loaded, 16 * 8)
            v.go(tt(x1[:], b1, bc(tmp[:, 6]), ALU.mult))
            v.go(tt(x2[:], b2, bc(tmp[:, 6]), ALU.mult))
            v(tt(sc3, b2, bc(tmp[:, 7]), ALU.mult))
            v(tt(x1[:], x1[:], sc3, ALU.subtract))
            v(tt(sc3, b1, bc(tmp[:, 7]), ALU.mult))
            v(tt(x2[:], x2[:], sc3, ALU.add))
            for n in (1, 2, 4):
                one = lambda t: t[:, n:n + 1, :].to_broadcast([P, n, GROUPS])
                cmul(pr[:, n + 1:2 * n + 1], pi[:, n + 1:2 * n + 1], pr[:, 1:n + 1], pi[:, 1:n + 1], one(pr), one(pi), (n, GROUPS))
            v.go(nc.vector.tensor_scalar(c1, c1, sigma[:, 0:1], None, ALU.mult))
            nc.vector.tensor_scalar(c2, c2, sigma[:, 0:1], None, ALU.mult).then_inc(powers_ready, 1)
            for j in range(8):
                v.go(tt(state_in[:, :, j, :], x1[:], bc(pr[:, 7 - j]), ALU.mult))
                v(tt(sc3, x2[:], bc(pi[:, 7 - j]), ALU.mult))
                last = tt(state_in[:, :, j, :], state_in[:, :, j, :], sc3, ALU.subtract)
                if j < 7:
                    v(last)
                else:
                    last.then_inc(a_ready, 1)
            v.go(nc.vector.tensor_copy(rr[:, 3:4, :], tmp[:, 3:4, :]))
            v(nc.vector.tensor_copy(ri[:, 3:4, :], tmp[:, 2:3, :]))
            src = 3
            for dst in (4, 5, 0):
                cmul(rr[:, dst:dst + 1], ri[:, dst:dst + 1], rr[:, src:src + 1], ri[:, src:src + 1],
                     rr[:, src:src + 1], ri[:, src:src + 1], (1, GROUPS))
                src = dst
            v(tt(magnitude8[:], mag, mag, ALU.mult))
            v(tt(magnitude8[:], magnitude8[:], magnitude8[:], ALU.mult))
            v(tt(magnitude8[:], magnitude8[:], magnitude8[:], ALU.mult))
            v.go(nc.vector.memset(rc[:, 0], 1.0))
            v(nc.vector.memset(rs[:, 0], 0.0))
            for i in range(6):
                n = 1 << i
                step = lambda t: t[:, i:i + 1, :].to_broadcast([P, n, GROUPS])
                cmul(rc[:, n:2 * n], rs[:, n:2 * n], rc[:, 0:n], rs[:, 0:n], step(rr), step(ri), (n, GROUPS))
                if i < 5:
                    cmul(rr[:, i + 1:i + 2], ri[:, i + 1:i + 2], rr[:, i:i + 1], ri[:, i:i + 1],
                         rr[:, i:i + 1], ri[:, i:i + 1], (1, GROUPS))
            dve.wait_ge(rows_copied, 8)
            dI = scratch[0:CH, 0:GROUPS * CH].rearrange("p (g c) -> p g c", c=CH)
            v(tt(dI, k.ident[0:CH, 0:CH].unsqueeze(1).to_broadcast([CH, GROUPS, CH]),
                 dT[:].unsqueeze(2).to_broadcast([CH, GROUPS, CH]), ALU.mult))
            tt(rows_behind_zeros[:, :, 1, 0:CH], rows_behind_zeros[:, :, 1, 0:CH], dI, ALU.add).then_inc(toeplitz_rows_ready, 1)
            gc = lambda t, g0, g1: t[:, :, g0:g1].rearrange("p c g -> p g c")
            dve.wait_ge(toeplitz_loaded, 128)
            for q, (g0, g1) in enumerate(VCH):
                n = g1 - g0
                t3 = scratch[:, 0:n * 64].rearrange("p (g c) -> p g c", c=64)
                dve.wait_ge(v_copied, q + 1)
                v.go(tt(z[:, g0:g1, :], vs[:, g0:g1, 0:64], gc(rc, g0, g1), ALU.mult))
                dve.wait_ge(v_swapped, q + 1)
                last = tt(t3, ps[:, (5 + q) % 8, 0:n * CHUNKS].rearrange("p (g c) -> p g c", c=CHUNKS)[:, :, 0:64],
                          gc(rs, g0, g1), ALU.mult)
                last.then_inc(swapped_v_used, 1)
                dve.wait_ge(swapped_v_used, q + 1)
                v.wait()
                v(tt(z[:, g0:g1, :], z[:, g0:g1, :], t3, ALU.add))
            mg = bc4[:].rearrange("p a g c -> p (a g c)").rearrange("p (g c) -> p g c", c=64)
            v(nc.vector.tensor_copy(mg, magnitude8[:].unsqueeze(2).to_broadcast([P, GROUPS, 64])))
            v(nc.vector.memset(mg[:, :, 0:1], 0.0))
            nc.vector.tensor_tensor_scan(w.rearrange("p g c -> p (g c)"), mg.rearrange("p g c -> p (g c)"),
                                         z.rearrange("p g c -> p (g c)"), 0.0, ALU.mult, ALU.add).then_inc(scan_done, 1)
            dve.wait_ge(scan_done, 1)
            v.go(nc.vector.memset(chunk_states[:, :, 0:1], 0.0))
            v.go(nc.vector.tensor_copy(chunk_states[:, :, 64:72], s0[:]))
            for q, (g0, g1) in enumerate(VCH):
                n = g1 - g0
                t3 = scratch[:, 0:n * 64].rearrange("p (g c) -> p g c", c=64)
                dve.wait_ge(w_swapped, q + 1)
                v.go(tt(z[:, g0:g1, :], w[:, g0:g1, :], gc(rc, g0, g1), ALU.mult))
                tt(t3, ps[:, (5 + q) % 8, 0:n * 64].rearrange("p (g c) -> p g c", c=64), gc(rs, g0, g1),
                   ALU.mult).then_inc(swapped_w_used, 1)
                dve.wait_ge(swapped_w_used, q + 1)
                v.wait()
                v.go(tt(chunk_states[:, g0:g1, 1:64], z[:, g0:g1, 0:63], t3[:, :, 0:63], ALU.subtract))
                v(tt(final_state[:, g0:g1, 0:1], z[:, g0:g1, 63:64], t3[:, :, 63:64], ALU.subtract))
            nc.vector.memset(tmp[:, 1], 0.0).then_inc(chunk_states_ready, 1)
            b8 = lambda t: t[:, 8, :].unsqueeze(2).to_broadcast([P, GROUPS, SEQS])
            se = final_state[:, :, 1:9]
            v.go(tt(se, s0[:], b8(pr), ALU.mult))
            v(tt(s0x[:], s0x[:], b8(pi), ALU.mult))
            v(tt(se, se, s0x[:], ALU.subtract))
            tt(se, se, vs[:, :, 64:72], ALU.add).then_inc(final_state_ready, 2)

        @block.tensor
        def _(pe):
            pe.wait_ge(a_ready, 1)
            for i in range(8):
                if i >= 3:
                    pe.wait_ge(transposes_copied, i - 2)
                for g in range(4 * i, 4 * i + 4):
                    mm = nc.tensor.transpose(ps[:, i % 3, P * (g % 4):P * (g % 4) + P],
                                             state_in[:, g].rearrange("p j c -> p (j c)"), k.ident[:])
                mm.then_inc(transposed, 1)
            pe.wait_ge(cp_ready, 1)
            for i in range(8):
                if i >= 3:
                    pe.wait_ge(rows_copied, i - 2)
                for g in range(4 * i, 4 * i + 4):
                    mm = nc.tensor.matmul(ps[0:CH, 3 + i % 3, P * (g % 4):P * (g % 4) + P], x1[:, g, :],
                                          state_out[:, g, 0:8, :].rearrange("p l c -> p (l c)"), start=True, stop=True)
                mm.then_inc(rows_made, 1)
            pe.wait_ge(k.u_loaded, 128)
            pe.wait_ge(transposes_copied, 8)
            pe.wait_ge(rows_copied, 8)
            for q, (g0, g1) in enumerate(VCH):
                for g in range(g0, g1):
                    mm = nc.tensor.matmul(ps[:, q, CHUNKS * (g - g0):CHUNKS * (g - g0 + 1)], state_in_T[:, g, :], k.U[:, g, :],
                                          start=True, stop=True)
                mm.then_inc(v_made, 1)
            for q, (g0, g1) in enumerate(VCH):
                pe.wait_ge(v_copied, q + 1)
                mm = nc.tensor.matmul(ps[:, (5 + q) % 8, 0:(g1 - g0) * CHUNKS], perm[:],
                                      vs[:, g0:g1, :].rearrange("p g c -> p (g c)"), start=True, stop=True)
                mm.then_inc(v_swapped, 1)
            pe.wait_ge(scan_done, 1)
            for q, (g0, g1) in enumerate(VCH):
                pe.wait_ge(swapped_v_used, q + 1)
                nc.tensor.matmul(ps[:, (5 + q) % 8, 0:(g1 - g0) * 64], perm[:],
                                 w[:, g0:g1, :].rearrange("p g c -> p (g c)"), start=True, stop=True).then_inc(w_swapped, 1)
            pe.wait_ge(toeplitz_loaded, 128)
            pe.wait_ge(chunk_states_ready, 1)
            pe.wait_ge(swapped_w_used, 5)
            for q, (g0, g1) in enumerate(VCH):
                for g in range(g0, g1):
                    dst = ps[:, q, CHUNKS * (g - g0):CHUNKS * (g - g0 + 1)]
                    nc.tensor.matmul(dst, toeplitz[:, g, :], k.U[:, g, :], start=True, stop=False)
                    mm = nc.tensor.matmul(dst, state_out[:, g, 1:9, :].rearrange("p l c -> p (l c)"), chunk_states[:, g, :],
                                          start=False, stop=True)
                mm.then_inc(y_made, 1)


def gather_pages(eng, dst, pool, pages, first, loaded):
    with eng.Fori(0, 4) as i:
        at = [eng.value_load(pages[0:1, bass.ds(4 * i + (first + n), 1)], min_val=0, max_val=POOL - 1) for n in range(4)]
        for n in range(4):
            eng.dma_start(dst[:, bass.ds(4 * i + n, 1), :].rearrange("p o f -> p (o f)"),
                          pool[bass.ds(at[n], 1)].rearrange("o p f -> (o p) f")).then_inc(loaded, 16)


def glu_stage(nc, k):
    with ExitStack() as ctx:
        sb = lambda n, s, d=F32: ctx.enter_context(nc.sbuf_tensor(n, s, d))
        sem = k.sem
        w = sb("w_glu_sb", [P, 4, 512])
        bg, gs = sb("b_glu_sb", [P, 4]), sb("g_out_ssm_sb", [P, 4])
        sig, sq = sb("glu_sig", [P, 4, T]), sb("glu_sq", [P, 4, T])
        rinv = sb("glu_rinv", [P, T])
        ps = ctx.enter_context(nc.psum_tensor("ps_glu", [P, 4, 2, 512], F32))
        w_loaded, bias_and_gain_loaded = sem("g_w_loaded"), sem("g_bias_and_gain_loaded")
        gelu_done, gate_inputs_made = sem("g_gelu_done"), sem("g_gate_inputs_made")
        sigmoid_done, gated, squared = sem("g_sigmoid_done"), sem("g_gated"), sem("g_squared")
        summed, inverse_ms_ready, root_ready = sem("g_summed"), sem("g_inverse_ms_ready"), sem("g_root_ready")
        vch = sem("g_vch")
        block = ctx.enter_context(nc.Block())

        @block.gpsimd
        def _(pool):
            pool.wait_ge(k.pages_ld, 16)
            for p in range(2):
                gather_pages(pool, k.cmp_pages[p][:, 16:32], k.d["cmp_pool"], k.pages, 32 * p + 16, k.cmp_got[p][1])

        @block.sync
        def _(sp):
            sp.dma_start(w[:], k.d["w_glu"]).then_inc(w_loaded, 16)
            sp.dma_start(bg[:], k.d["b_glu"]).then_inc(bias_and_gain_loaded, 16)
            sp.dma_start(gs[:], k.d["g_out_ssm"]).then_inc(bias_and_gain_loaded, 16)
            sp.wait_ge(k.pages_ld, 16)
            for p in range(2):
                gather_pages(sp, k.cmp_pages[p][:, 0:16], k.d["cmp_pool"], k.pages, 32 * p, k.cmp_got[p][0])

        @block.scalar
        def _(act):
            for dst, src in ((k.cmp_w1, k.d["cmp_w1"]), (k.cmp_w2, k.d["cmp_w2"]), (k.cmp_pe, k.d["cmp_pe"])):
                act.dma_start(dst[:], src).then_inc(k.cmp_ld, 16)
            act.wait_ge(k.y_loaded, 16)
            for i in range(4):
                nc.scalar.activation(k.yT[:, i], k.yT[:, i], ACT.Gelu_apprx_tanh).then_inc(gelu_done, 1)
            act.wait_ge(bias_and_gain_loaded, 32)
            for c in range(4):
                act.wait_ge(gate_inputs_made, c + 1)
                for h in range(2):
                    nc.scalar.activation(sig[:, c, HALF * h:HALF * h + HALF], ps[:, c, h, 0:HALF], ACT.Sigmoid,
                                         bias=bg[:, c:c + 1]).then_inc(sigmoid_done, 1)
            for c in range(4):
                act.wait_ge(gated, c + 1)
                nc.scalar.activation(sq[:, c], sig[:, c], ACT.Square).then_inc(squared, 1)
            act.wait_ge(inverse_ms_ready, 1)
            nc.scalar.activation(rinv[:], rinv[:], ACT.Sqrt).then_inc(root_ready, 1)

        @block.vector
        def _(dve):
            v = Chain(dve, vch)
            for c in range(4):
                dve.wait_ge(sigmoid_done, 2 * c + 2)
                nc.vector.tensor_tensor(sig[:, c], sig[:, c], k.yT[:, c], ALU.mult).then_inc(gated, 1)
            dve.wait_ge(summed, 1)
            for h in range(2):
                v.go(nc.vector.tensor_scalar(rinv[:, HALF * h:HALF * h + HALF], ps[:, h, 0, 0:HALF], 1.0 / 512, EPS,
                                             ALU.mult, ALU.add))
            v.wait()
            nc.vector.reciprocal(rinv[:], rinv[:]).then_inc(inverse_ms_ready, 1)
            dve.wait_ge(root_ready, 1)
            for c in range(4):
                tok = lambda a: a.rearrange("p (j c) -> p j c", j=8)
                v.go(nc.vector.scalar_tensor_tensor(out=k.mixT[:, c].rearrange("p (c j) -> p j c", j=8),
                                                    in0=tok(sig[:, c]), scalar=gs[:, c:c + 1], in1=tok(rinv[:]),
                                                    op0=ALU.mult, op1=ALU.mult))

        @block.tensor
        def _(pe):
            pe.wait_ge(w_loaded, 16)
            pe.wait_ge(gelu_done, 4)
            for c in range(4):
                for h in range(2):
                    for i in range(4):
                        mm = nc.tensor.matmul(ps[:, c, h, 0:HALF], w[:, i, P * c:P * c + P],
                                              k.yT[:, i, HALF * h:HALF * h + HALF], start=(i == 0), stop=(i == 3))
                mm.then_inc(gate_inputs_made, 1)
            pe.wait_ge(sigmoid_done, 8)
            for c in range(4):
                pe.wait_ge(squared, c + 1)
                for h in range(2):
                    mm = nc.tensor.matmul(ps[:, h, 0, 0:HALF], k.ones[:], sq[:, c, HALF * h:HALF * h + HALF],
                                          start=(c == 0), stop=(c == 3))
            mm.then_inc(summed, 1)


PAIRS = SEQS // 2


def compress_stage(nc, k):
    with ExitStack() as ctx:
        sb = lambda n, s, d=F32: ctx.enter_context(nc.sbuf_tensor(n, s, d))
        sem = k.sem
        pages, got = k.cmp_pages, k.cmp_got
        w1, w2, pe_ = k.cmp_w1, k.cmp_w2, k.cmp_pe
        bias = sb("cmp_bias", [P, 2])
        products, w1pe = sb("cmp_w1_pe_products", [P, 16, P]), sb("cmp_w1_pe", [P, 2, P])
        shifted, pre = sb("cmp_h1", [P, 2, 256]), sb("cmp_pre", [P, 2, 256])
        rope, gain = sb("cmp_rope", [P, 3, 8]), sb("cmp_gain", [P, HD])
        kr, sq = sb("cmp_k_rows", [P, 9, P]), sb("cmp_sq", [P, 9, P])
        ms = sb("cmp_ms", [P, 2, 18])
        ra, rb = sb("cmp_ra", [P, 18, 16]), sb("cmp_rb", [P, 18, 16])
        ph = ctx.enter_context(nc.psum_tensor("ph", [P, 2, 512], F32))
        po = ctx.enter_context(nc.psum_tensor("po_cmp", [P, 2, 512], F32))
        pb = ctx.enter_context(nc.psum_tensor("pb_cmp", [P, 512], F32))
        pt = ctx.enter_context(nc.psum_tensor("pt_cmp", [P, 3, 512], F32))
        rope_and_gain_loaded, bias_part = sem("c_rope_and_gain_loaded"), sem("c_bias_part")
        bias_done, bias_ready = sem("c_bias_done"), sem("c_bias_ready")
        h_done, h1_copied, pre_ready = sem("c_h_done"), sem("c_h1_copied"), sem("c_pre_ready")
        act_ready, out_done, out_free = sem("c_act_ready"), sem("c_out_done"), sem("c_out_free")
        zeroed, vch, squared = sem("c_zeroed"), sem("c_vch"), sem("c_squared")
        inverse_ms_ready, root_ready, keys_ready = sem("c_inverse_ms_ready"), sem("c_root_ready"), sem("c_keys_ready")
        keys_transposed = sem("c_keys_transposed")
        units = [(p, kv, g) for p in range(PAIRS + 1) for kv in range(2) for g in range(2)]
        block = ctx.enter_context(nc.Block())

        @block.sync
        def _(sp):
            for p in range(2, PAIRS):
                sp.wait_ge(h_done, 4 * (p - 1))
                gather_pages(sp, pages[p % 2][:, 0:16], k.d["cmp_pool"], k.pages, 32 * p, got[p % 2][0])

        @block.gpsimd
        def _(pool):
            pool.memset(kr[:], 0.0).then_inc(zeroed, 1)
            pool.memset(k.vcmp, 0.0).then_inc(zeroed, 1)
            for p in range(2, PAIRS):
                pool.wait_ge(h_done, 4 * (p - 1))
                gather_pages(pool, pages[p % 2][:, 16:32], k.d["cmp_pool"], k.pages, 32 * p + 16, got[p % 2][1])
            for n in range(2):
                pool.dma_start(k.o["rows_s"][4 + n][:, 0:504, :], k.d["win_rows"][n][:, 8:512, :]).then_inc(k.window_stored, 16)

        @block.scalar
        def _(act):
            act.dma_start(rope[:], k.d["cmp_rope"]).then_inc(rope_and_gain_loaded, 16)
            act.dma_start(gain[:], k.d["g_k_cmp"].to_broadcast([P, HD])).then_inc(rope_and_gain_loaded, 16)
            act.wait_ge(zeroed, 2)
            for u, (p, kv, g) in enumerate(units):
                n, seqs = (256, 2) if p < PAIRS else (32, 1)
                act.wait_ge(h_done, u + 1)
                nc.scalar.activation(shifted[:, u % 2, 0:n], ph[:, u % 2, 256:256 + n], ACT.Copy).then_inc(h1_copied, 1)
                if u == 0:
                    act.wait_ge(bias_done, 1)
                    nc.scalar.activation(bias[:], pb[:, 0:2], ACT.Copy).then_inc(bias_ready, 1)
                    act.wait_ge(bias_ready, 1)
                act.wait_ge(pre_ready, u + 1)
                nc.scalar.activation(pre[:, u % 2, 0:n], pre[:, u % 2, 0:n], ACT.Gelu_apprx_tanh,
                                     bias=bias[:, kv:kv + 1]).then_inc(act_ready, 1)
                if u % 4 == 3:
                    act.wait_ge(out_done, u + 1)
                    rows, s0 = (127, 2 * p) if p < PAIRS else (31, 8)
                    src = po[0:rows, p % 2, 0:256 * seqs].rearrange("p (s kv f) -> p s kv f", s=seqs, kv=2)
                    nc.scalar.activation(kr[0:rows, s0:s0 + seqs, :], src[:, :, 0], ACT.Copy)
                    nc.scalar.activation(k.vcmp[0:rows, s0:s0 + seqs, :], src[:, :, 1], ACT.Copy).then_inc(out_free, 1)
            act.wait_ge(out_free, PAIRS + 1)
            nc.scalar.activation(sq[:], kr[:], ACT.Square).then_inc(squared, 1)
            act.wait_ge(inverse_ms_ready, 1)
            nc.scalar.activation(ms[:, 1], ms[:, 0], ACT.Sqrt).then_inc(root_ready, 1)
            for q in range(3):
                act.wait_ge(keys_transposed, q + 1)
                nc.scalar.activation(k.kcT[:, 3 * q:3 * q + 3, :], pt[:, q, 0:384].rearrange("p (s n) -> p s n", s=3), ACT.Copy)

        @block.vector
        def _(dve):
            v = Chain(dve, vch)
            dve.wait_ge(k.cmp_ld, 48)
            dve.wait_ge(rope_and_gain_loaded, 32)
            for kv in range(2):
                v(nc.vector.tensor_tensor(products[:], w1[:, kv], pe_[:, kv].unsqueeze(2).to_broadcast([P, 16, P]), ALU.mult))
                last = nc.vector.tensor_reduce(w1pe[:, kv], products[:].rearrange("p i m -> p m i"), AX.X, ALU.add)
                if kv == 0:
                    v(last)
            last.then_inc(bias_part, 1)
            for u, (p, kv, g) in enumerate(units):
                n, seqs = (128, 2) if p < PAIRS else (32, 1)
                dve.wait_ge(h1_copied, u + 1)
                if u >= 2:
                    dve.wait_ge(out_done, u - 1)
                if u < 2:
                    v(nc.vector.memset(pre[:, u % 2, :], 0.0))
                sq3 = lambda a: a.rearrange("p (s n) -> p s n", s=seqs)
                nc.vector.tensor_tensor(sq3(pre[:, u % 2, 0:n * seqs])[:, :, 0:n - 1],
                                        sq3(ph[:, u % 2, 0:n * seqs])[:, :, 0:n - 1],
                                        sq3(shifted[:, u % 2, 0:n * seqs])[:, :, 1:n], ALU.add).then_inc(pre_ready, 1)
            dve.wait_ge(squared, 1)
            v(nc.vector.tensor_reduce(ms[:, 0], sq[:].rearrange("p s (g d) -> p (s g) d", g=2), AX.X, ALU.add))
            v(nc.vector.tensor_scalar(ms[:, 0], ms[:, 0], 1.0 / HD, EPS, ALU.mult, ALU.add))
            nc.vector.reciprocal(ms[:, 0], ms[:, 0]).then_inc(inverse_ms_ready, 1)
            dve.wait_ge(root_ready, 1)
            k3 = kr[:].rearrange("p s (g d) -> p (s g) d", g=2)
            v(nc.vector.tensor_tensor(k3, k3, ms[:, 1].unsqueeze(2).to_broadcast([P, 18, HD]), ALU.mult))
            v(nc.vector.tensor_tensor(k3, k3, gain[:].unsqueeze(1).to_broadcast([P, 18, HD]), ALU.mult))
            cos, sin, nsin = (rope[:, i, :].unsqueeze(1).to_broadcast([P, 18, 8]) for i in range(3))
            v.go(nc.vector.tensor_tensor(ra[:, :, 0:8], k3[:, :, 0:8], cos, ALU.mult))
            v.go(nc.vector.tensor_tensor(ra[:, :, 8:16], k3[:, :, 8:16], cos, ALU.mult))
            v.go(nc.vector.tensor_tensor(rb[:, :, 0:8], k3[:, :, 8:16], nsin, ALU.mult))
            v(nc.vector.tensor_tensor(rb[:, :, 8:16], k3[:, :, 0:8], sin, ALU.mult))
            nc.vector.tensor_tensor(k3[:, :, 0:16], ra[:], rb[:], ALU.add).then_inc(keys_ready, 1)

        @block.tensor
        def _(pe):
            pe.wait_ge(k.cmp_ld, 48)

            def biases():
                pe.wait_ge(bias_part, 1)
                for kv in range(2):
                    mm = nc.tensor.matmul(pb[:, kv:kv + 1], w1pe[:, kv, :], k.ones[:, 0:1], start=True, stop=True)
                mm.then_inc(bias_done, 1)

            def second(u):
                p, kv, g = units[u]
                n, seqs = (127, 2) if p < PAIRS else (31, 1)
                pe.wait_ge(act_ready, u + 1)
                if u % 4 == 0 and p >= 2:
                    pe.wait_ge(out_free, p - 1)
                for s in range(seqs):
                    off = s * 256 + kv * 128 + g * 64
                    mm = nc.tensor.matmul(po[0:n, p % 2, off:off + 64], pre[:, u % 2, 128 * s:128 * s + n], w2[:, kv, :],
                                          start=True, stop=True)
                mm.then_inc(out_done, 1)

            for u, (p, kv, g) in enumerate(units):
                if u >= 2:
                    pe.wait_ge(pre_ready, u - 1)
                if p < PAIRS:
                    if u % 4 == 0:
                        for s in range(2):
                            pe.wait_ge(got[p % 2][s], 256 * (p // 2 + 1))
                    src = pages[p % 2][:].rearrange("p t (kv g i b) -> p t kv g i b", kv=2, g=2, i=8)
                    n = 256
                else:
                    src, n = k.cmp_prompt[:], 32
                for s in range(2):
                    for i in range(8):
                        mm = nc.tensor.matmul(ph[:, u % 2, 256 * s:256 * s + n], w1[:, kv, 8 * s + i, :],
                                              src[:, :, kv, g, i, :], start=(i == 0), stop=(i == 7))
                mm.then_inc(h_done, 1)
                if u == 0:
                    biases()
                if u >= 1:
                    second(u - 1)
            second(len(units) - 1)
            pe.wait_ge(keys_ready, 1)
            for q in range(3):
                for s in range(3):
                    mm = nc.tensor.transpose(pt[:, q, P * s:P * s + P], kr[:, 3 * q + s, :], k.ident[:])
                mm.then_inc(keys_transposed, 1)


CMP, SEL, WIN = range(3)
S_AT = [(2, 256), (2, 0), (1, 0), (0, 0)]
P_AT = [0, 128, 384, 768]
PT_AT = [0, 512, 896, 1152]
PT_BANK = [(0, 0), (1, 0), (2, 0), (2, 256)]
NCP = 31


def window_rows(sp, k, p):
    for s in range(2):
        sp.dma_start(k.win_k[:, p % 2, s], k.d["win_kT"][2 * p + s]).then_inc(k.win_got[p % 2], 16)
        sp.dma_start(k.win_v[:, p % 2, s], k.d["win_rows"][1][2 * p + s].rearrange("(a p) f -> p a f", p=P)).then_inc(k.win_got[p % 2], 16)


def prompt_attention_stage(nc, k):
    with ExitStack() as ctx:
        sb = lambda n, s, d=F32: ctx.enter_context(nc.sbuf_tensor(n, s, d))
        sem = k.sem
        causal, cmask, valid = sb("causal", [P, P]), sb("cmp_mask", [P, 4, NCP]), sb("cmp_valid", [P, 4])
        prob, pt = sb("prob", [P, 2, 1280]), sb("prob_T", [P, 2, 1280])
        pc = sb("prob_cmp", [P, 2, 4, NCP])
        mx, rs = sb("pa_max", [P, 2, 4]), sb("pa_sum", [P, 2, 4])
        s_ps = ctx.enter_context(nc.psum_tensor("pa_s", [P, 4, 512], F32))
        t_ps = ctx.enter_context(nc.psum_tensor("pa_t", [P, 3, 512], F32))
        o_ps = ctx.enter_context(nc.psum_tensor("pa_o", [P, 512], F32))
        masks_loaded, scores_made, max_ready = sem("pa_masks_loaded"), sem("pa_scores_made"), sem("pa_max_ready")
        exponentials_done, scaled, transposed = sem("pa_exponentials_done"), sem("pa_scaled"), sem("pa_transposed")
        act_copied, dve_copied, values_done = sem("pa_act_copied"), sem("pa_dve_copied"), sem("pa_values_done")
        sums_copied, vch = sem("pa_sums_copied"), sem("pa_vch")
        units = [(r, g, br) for r in range(REP) for g in range(2) for br in (CMP, SEL, WIN)]
        N = len(units)
        big = lambda n: sum(1 for x in units[:n] if x[2] != CMP)
        BANKS = ((3,), (2,), (1, 0))
        banks_before = lambda n: sum(1 if x[2] == CMP else len(BANKS) for x in units[:n])
        block = ctx.enter_context(nc.Block())

        @block.sync
        def _(sp):
            for dst, src in ((causal, k.d["causal"]), (cmask, k.d["cmp_mask"]), (valid, k.d["cmp_valid"])):
                sp.dma_start(dst[:], src).then_inc(masks_loaded, 16)
            for p in range(2):
                window_rows(sp, k, p)
                gather_pages(sp, k.sel_pages[p][:, 0:16], k.d["sel_pool"], k.pages, 32 * p, k.sel_got[p][0])

        @block.gpsimd
        def _(pool):
            for p in range(2):
                gather_pages(pool, k.sel_pages[p][:, 16:32], k.d["sel_pool"], k.pages, 32 * p + 16, k.sel_got[p][1])

        @block.scalar
        def _(act):
            def evac(n):
                br = units[n][2]
                act.wait_ge(transposed, n + 1)
                if n >= 2:
                    act.wait_ge(values_done, n - 1)
                if br == CMP:
                    nc.scalar.activation(pt[0:NCP, n % 2, 0:512], t_ps[0:NCP, 0, :], ACT.Copy).then_inc(act_copied, 1)
                else:
                    nc.scalar.activation(pt[:, n % 2, 0:512], t_ps[:, 0, :], ACT.Copy)
                    nc.scalar.activation(pt[:, n % 2, 896:1280], t_ps[:, 2, 0:384], ACT.Copy).then_inc(act_copied, 1)

            for n, (r, g, br) in enumerate(units):
                if br == CMP:
                    act.wait_ge(max_ready, banks_before(n) + 1)
                    nc.scalar.activation(pc[:, n % 2], pc[:, n % 2], ACT.Exp, scale=SCALE).then_inc(exponentials_done, 1)
                else:
                    if n >= 2:
                        act.wait_ge(transposed, n - 1)
                    for j, tiles in enumerate(BANKS):
                        act.wait_ge(max_ready, banks_before(n) + j + 1)
                        for i in tiles:
                            bank, at = S_AT[i]
                            e = nc.scalar.activation(prob[:, n % 2, P_AT[i]:P_AT[i] + P * (i + 1)],
                                                     s_ps[:, bank, at:at + P * (i + 1)], ACT.Exp, bias=mx[:, n % 2, i:i + 1],
                                                     scale=SCALE, accum_out=rs[:, n % 2, i:i + 1])
                        e.then_inc(exponentials_done, 1)
                if n >= 1:
                    evac(n - 1)
                    if n % 6 == 1 and n > 1:
                        act.wait_ge(values_done, n - 1)
                        nc.scalar.activation(k.mixT[:, 4 + n // 6 - 1, 0:T_PROMPT], o_ps[:], ACT.Copy).then_inc(sums_copied, 1)
            evac(N - 1)
            act.wait_ge(values_done, N)
            nc.scalar.activation(k.mixT[:, 7, 0:T_PROMPT], o_ps[:], ACT.Copy).then_inc(sums_copied, 1)

        @block.vector
        def _(dve):
            v = Chain(dve, vch)
            dve.wait_ge(masks_loaded, 48)

            def gate(n):
                r, g, br = units[n]
                return k.gates[:, 0:4, 8 * br + 4 * g + r]

            def scores(n):
                b = n % 2
                if units[n][2] == CMP:
                    dve.wait_ge(scores_made, banks_before(n) + 1)
                    if n >= 2:
                        dve.wait_ge(transposed, n - 1)
                    v(nc.vector.tensor_tensor(pc[:, b], s_ps[:, 3, 0:4 * NCP].rearrange("p (i c) -> p i c", i=4),
                                              cmask[:], ALU.add))
                    v(nc.vector.tensor_reduce(mx[:, b], pc[:, b], AX.X, ALU.max))
                    nc.vector.tensor_tensor(pc[:, b], pc[:, b], mx[:, b].unsqueeze(2).to_broadcast([P, 4, NCP]),
                                            ALU.subtract).then_inc(max_ready, 1)
                else:
                    for j, tiles in enumerate(BANKS):
                        dve.wait_ge(scores_made, banks_before(n) + j + 1)
                        for i in tiles:
                            bank, at = S_AT[i]
                            d = s_ps[:, bank, at + P * i:at + P * i + P]
                            v.go(nc.vector.tensor_tensor(d, d, causal[:], ALU.add))
                        v.wait()
                        for i in tiles:
                            bank, at = S_AT[i]
                            v.go(nc.vector.tensor_reduce(mx[:, b, i:i + 1], s_ps[:, bank, at:at + P * (i + 1)], AX.X, ALU.max))
                        v.wait()
                        lo, hi = min(tiles), max(tiles) + 1
                        nc.vector.tensor_scalar(mx[:, b, lo:hi], mx[:, b, lo:hi], -SCALE, None, ALU.mult).then_inc(max_ready, 1)

            def scale(n):
                dve.wait_ge(exponentials_done, banks_before(n + 1))
                b = n % 2
                if units[n][2] == CMP:
                    v(nc.vector.tensor_reduce(rs[:, b], pc[:, b], AX.X, ALU.add))
                    v(nc.vector.reciprocal(rs[:, b], rs[:, b]))
                    v(nc.vector.tensor_tensor(rs[:, b], rs[:, b], gate(n), ALU.mult))
                    v(nc.vector.tensor_tensor(rs[:, b], rs[:, b], valid[:], ALU.mult))
                    nc.vector.tensor_tensor(pc[:, b], pc[:, b], rs[:, b].unsqueeze(2).to_broadcast([P, 4, NCP]),
                                            ALU.mult).then_inc(scaled, 1)
                else:
                    v(nc.vector.reciprocal(rs[:, b], rs[:, b]))
                    v(nc.vector.tensor_tensor(rs[:, b], rs[:, b], gate(n), ALU.mult))
                    for i in range(4):
                        pr = prob[:, b, P_AT[i]:P_AT[i] + P * (i + 1)]
                        m = nc.vector.tensor_scalar(pr, pr, rs[:, b, i:i + 1], None, ALU.mult)
                    m.then_inc(scaled, 1)

            def evac(n):
                if units[n][2] != CMP:
                    dve.wait_ge(transposed, n + 1)
                    if n >= 2:
                        dve.wait_ge(values_done, n - 1)
                    nc.vector.tensor_copy(pt[:, n % 2, 512:896], t_ps[:, 1, 0:384]).then_inc(dve_copied, 1)

            for n in range(N + 1):
                if n < N:
                    scores(n)
                if n >= 1:
                    evac(n - 1)
                if n < N:
                    scale(n)

        @block.tensor
        def _(pe):
            def scores(n):
                r, g, br = units[n]
                h = slice(64 * g, 64 * g + 64)
                if br == CMP:
                    if n >= 3:
                        pe.wait_ge(max_ready, banks_before(n - 3) + 1)
                    for i in range(4):
                        mm = nc.tensor.matmul(s_ps[:, 3, NCP * i:NCP * i + NCP], k.qT[h, r, P * i:P * i + P],
                                              k.kcT[h, 8, 0:NCP], start=True, stop=True)
                else:
                    kT = k.ksT if br == SEL else k.kwT
                    for j, tiles in enumerate(BANKS):
                        if big(n):
                            last = n - 1 if units[n - 1][2] != CMP else n - 2
                            pe.wait_ge(exponentials_done, banks_before(last) + j + 1)
                        for i in tiles:
                            bank, at = S_AT[i]
                            mm = nc.tensor.matmul(s_ps[:, bank, at:at + P * (i + 1)], k.qT[h, r, P * i:P * i + P],
                                                  kT[h, 0:P * (i + 1)], start=True, stop=True)
                        if j < len(BANKS) - 1:
                            mm.then_inc(scores_made, 1)
                mm.then_inc(scores_made, 1)

            def transposes(n):
                br = units[n][2]
                pe.wait_ge(scaled, n + 1)
                if n >= 1:
                    pe.wait_ge(act_copied, n)
                    if big(n):
                        pe.wait_ge(dve_copied, big(n))
                if br == CMP:
                    for i in range(4):
                        mm = nc.tensor.transpose(t_ps[0:NCP, 0, P * i:P * i + P], pc[:, n % 2, i, :], k.ident[:])
                else:
                    for j in range(4):
                        bank, at = PT_BANK[j]
                        for i in range(j, 4):
                            mm = nc.tensor.transpose(t_ps[:, bank, at + P * (i - j):at + P * (i - j) + P],
                                                     prob[:, n % 2, P_AT[i] + P * j:P_AT[i] + P * j + P], k.ident[:])
                mm.then_inc(transposed, 1)

            def values(n):
                r, g, br = units[n]
                h = slice(64 * g, 64 * g + 64)
                pe.wait_ge(act_copied, n + 1)
                if br == CMP:
                    if n % 6 == 0 and n:
                        pe.wait_ge(sums_copied, n // 6)
                    mm = nc.tensor.matmul(o_ps[h, :], k.vcmp[0:NCP, 8, h], pt[0:NCP, n % 2, 0:512], start=True, stop=False)
                else:
                    pe.wait_ge(dve_copied, big(n + 1))
                    lo = 256 if br == SEL else 384
                    for j in (3, 2, 1, 0):
                        mm = nc.tensor.matmul(o_ps[h, P * j:512], k.kv[:, j, lo + 64 * g:lo + 64 * g + 64],
                                              pt[:, n % 2, PT_AT[j]:PT_AT[j] + P * (4 - j)], start=False,
                                              stop=(br == WIN and j == 0))
                mm.then_inc(values_done, 1)

            for n in range(N + 2):
                if n < N:
                    scores(n)
                if 1 <= n <= N:
                    transposes(n - 1)
                if n >= 2:
                    values(n - 2)


NKEYS = PAST + 64
NSEL = 33


def sample_attention_stage(nc, k):
    with ExitStack() as ctx:
        sb = lambda n, s, d=F32: ctx.enter_context(nc.sbuf_tensor(n, s, d))
        sem = k.sem
        pages, got = k.sel_pages, k.sel_got
        kw, vw, gotw = k.win_k, k.win_v, k.win_got
        q = sb("q_heads", [P, SEQS, 64])
        same, pick, mine = sb("same_query", [P, P]), sb("pick_rows", [64, PAIRS, P]), sb("my_head", [P, 8])
        newm, winm, force = sb("new_mask", [P, PAIRS, 64]), sb("win_mask", [P, 8]), sb("force_row", [P, NSEL])
        gt = sb("sample_gates", [P, PAIRS, 3])
        gtmp = sb("gates_tmp", [P, PAIRS, 3, 8])
        free = k.U[:].rearrange("p g c -> p (g c)")
        pcs = free[:, 0:2 * P].rearrange("p (b n) -> p b n", b=2)
        sws = free[:, 2 * P:2 * P + 2 * 576].rearrange("p (b n) -> p b n", b=2)
        ss = sb("sa_sel", [P, NKEYS])
        pt = sb("sa_pt", [P, 23, P])
        st = sb("sa_stats", [P, 16])
        sc = sb("sa_score", [P, 3, NSEL])
        top = sb("sa_top", [P, 2, 8])
        ps = ctx.enter_context(nc.psum_tensor("sa_ps", [P, 8, 512], F32))
        masks_loaded = sem("sa_ld")
        q_ready, gates_spread, vch = sem("sa_q_ready"), sem("sa_gates_spread"), sem("sa_vch")
        small_scores_made, selected_scores_made = sem("sa_small_scores_made"), sem("sa_selected_scores_made")
        cmp_probs_zeroed = sem("sa_cmp_probs_zeroed")
        cmp_max_ready, cmp_exp_done = sem("sa_cmp_max_ready"), sem("sa_cmp_exp_done")
        cmp_probs_ready, importance_summed = sem("sa_cmp_probs_ready"), sem("sa_importance_summed")
        win_scores_copied, win_max_ready = sem("sa_win_scores_copied"), sem("sa_win_max_ready")
        win_exp_done, sel_max_ready = sem("sa_win_exp_done"), sem("sa_sel_max_ready")
        sel_exp_done = sem("sa_sel_exp_done")
        cmp_scaled, win_scaled, sel_scaled = sem("sa_cmp_scaled"), sem("sa_win_scaled"), sem("sa_sel_scaled")
        transposed, act_copied, dve_copied = sem("sa_transposed"), sem("sa_act_copied"), sem("sa_dve_copied")
        values_done, output_copied = sem("sa_values_done"), sem("sa_output_copied")
        banks = [[0, 1, 2, 3], [4, 5], [6, 7, 8, 9], [10, 11, 12, 13], [14, 15, 16, 17], [18, 19, 20, 21], [22]]
        NB = len(banks)
        rows_of = lambda b: 127 if b == 0 else 64 if b in (5, 22) else P
        block = ctx.enter_context(nc.Block())

        @block.sync
        def _(sp):
            for dst, src in ((same, k.d["same"]), (pick, k.d["pick"]), (mine, k.d["mine"]), (newm, k.d["new_mask"]),
                             (winm, k.d["win_mask"]), (force, k.d["force"])):
                sp.dma_start(dst[:], src).then_inc(masks_loaded, 16)
            for p in range(2, PAIRS):
                sp.wait_ge(values_done, p - 1)
                window_rows(sp, k, p)
                gather_pages(sp, pages[p % 2][:, 0:16], k.d["sel_pool"], k.pages, 32 * p, got[p % 2][0])

        @block.gpsimd
        def _(pool):
            for p in range(2, PAIRS):
                pool.wait_ge(values_done, p - 1)
                gather_pages(pool, pages[p % 2][:, 16:32], k.d["sel_pool"], k.pages, 32 * p + 16, got[p % 2][1])

        @block.scalar
        def _(act):
            def small(p):
                pc, sw = pcs[:, p % 2], sws[:, p % 2]
                act.wait_ge(small_scores_made, p + 1)
                if p == 0:
                    act.wait_ge(cmp_probs_zeroed, 1)
                nc.scalar.activation(sw[:, 0:512], ps[:, 5, :], ACT.Copy).then_inc(win_scores_copied, 1)
                act.wait_ge(cmp_max_ready, p + 1)
                nc.scalar.activation(pc[:, 0:127], ps[:, 4, 128:255], ACT.Exp, bias=st[:, 0:1], scale=SCALE,
                                     accum_out=st[:, 1:2]).then_inc(cmp_exp_done, 1)
                act.wait_ge(win_max_ready, p + 1)
                nc.scalar.activation(sw[:], sw[:], ACT.Exp, bias=st[:, 4:5], scale=SCALE,
                                     accum_out=st[:, 5:6]).then_inc(win_exp_done, 1)

            def evacuate(p):
                for b in range(0, NB, 2):
                    act.wait_ge(transposed, NB * p + b + 1)
                    if p and b == 0:
                        act.wait_ge(values_done, p)
                    lo, n = banks[b][0], len(banks[b])
                    if b == NB - 1:
                        nc.scalar.activation(pt[0:64, lo, :], ps[0:64, b % 4, 0:P], ACT.Copy).then_inc(act_copied, 1)
                    elif b == 0:
                        nc.scalar.activation(pt[0:127, 0, :], ps[0:127, 0, 0:P], ACT.Copy)
                        nc.scalar.activation(pt[:, 1:4, :], ps[:, 0, P:512].rearrange("p (n f) -> p n f", n=3), ACT.Copy).then_inc(act_copied, 1)
                    else:
                        nc.scalar.activation(pt[:, lo:lo + n, :], ps[:, b % 4, 0:P * n].rearrange("p (n f) -> p n f", n=n),
                                             ACT.Copy).then_inc(act_copied, 1)

            for p in range(PAIRS + 1):
                if p < PAIRS:
                    small(p)
                if p:
                    evacuate(p - 1)
                if p < PAIRS:
                    act.wait_ge(sel_max_ready, p + 1)
                    nc.scalar.activation(ss[:], ss[:], ACT.Exp, bias=st[:, 8:9], scale=SCALE,
                                         accum_out=st[:, 9:10]).then_inc(sel_exp_done, 1)

        @block.vector
        def _(dve):
            v = Chain(dve, vch)
            V = nc.vector
            v(V.memset(q[:], 0.0))
            for g in range(2):
                h = slice(64 * g, 64 * g + 64)
                V.tensor_copy(q[h, :, 32 * g:32 * g + 32].rearrange("p s (r t) -> p s r t", r=REP),
                              k.qT[h, :, T_PROMPT:T].rearrange("p r (s t) -> p s r t", t=STEPS)).then_inc(q_ready, 1)
            dve.wait_ge(masks_loaded, 96)
            dve.wait_ge(gates_spread, 1)
            v(V.tensor_tensor(gtmp[:].rearrange("p a b h -> p (a b) h"), ps[:, 7, 0:96].rearrange("p (a h) -> p a h", h=8),
                              mine[:].unsqueeze(1).to_broadcast([P, 12, 8]), ALU.mult))
            v(V.tensor_reduce(gt[:].rearrange("p a b -> p (a b)"), gtmp[:].rearrange("p a b h -> p (a b) h"), AX.X, ALU.add))
            V.memset(pcs[:], 0.0).then_inc(cmp_probs_zeroed, 1)
            def small(p):
                pc, sw = pcs[:, p % 2], sws[:, p % 2]
                dve.wait_ge(small_scores_made, p + 1)
                v(V.tensor_reduce(st[:, 0:1], ps[:, 4, 128:255], AX.X, ALU.max))
                V.tensor_scalar(st[:, 0:1], st[:, 0:1], -SCALE, None, ALU.mult).then_inc(cmp_max_ready, 1)
                dve.wait_ge(win_scores_copied, p + 1)
                v.go(V.tensor_tensor(sw[:, 0:8], sw[:, 0:8], winm[:], ALU.add))
                dve.wait_ge(cmp_exp_done, p + 1)
                v(V.tensor_tensor(sw[:, 512:576], ps[:, 4, 64:128], newm[:, p], ALU.add))
                v(V.tensor_reduce(st[:, 4:5], sw[:], AX.X, ALU.max))
                V.tensor_scalar(st[:, 4:5], st[:, 4:5], -SCALE, None, ALU.mult).then_inc(win_max_ready, 1)
                v(V.reciprocal(st[:, 1:2], st[:, 1:2]))
                V.tensor_scalar(pc[:, 0:127], pc[:, 0:127], st[:, 1:2], None, ALU.mult).then_inc(cmp_probs_ready, 1)

            def selected(p):
                pc, sw = pcs[:, p % 2], sws[:, p % 2]
                dve.wait_ge(importance_summed, p + 1)
                v(V.memset(sc[:, 0, 32:33], 0.0))
                v(V.tensor_reduce(sc[:, 0, 0:32], ps[:, 4, 256:384].rearrange("p (b c) -> p b c", c=4), AX.X, ALU.add))
                v(V.tensor_tensor(sc[:, 0], sc[:, 0], force[:], ALU.add))
                v(V.max(top[:, 0], sc[:, 0]))
                v(V.match_replace(sc[:, 1], top[:, 0], sc[:, 0], GONE))
                v(V.max(top[:, 1], sc[:, 1]))
                v(V.match_replace(sc[:, 2], top[:, 1], sc[:, 1], GONE))
                v(V.tensor_scalar(sc[:, 0], sc[:, 2], GONE / 2, NEG, ALU.is_gt, ALU.mult))
                V.tensor_scalar(pc[:, 0:127], pc[:, 0:127], gt[:, p, 0:1], None, ALU.mult).then_inc(cmp_scaled, 1)
                dve.wait_ge(selected_scores_made, p + 1)
                for c in range(4):
                    b3 = lambda a: a.rearrange("p (b n) -> p b n", n=64)
                    v.go(V.tensor_tensor(b3(ss[:, 512 * c:512 * c + 512]), b3(ps[:, c, :]),
                                         sc[:, 0, 8 * c:8 * c + 8].unsqueeze(2).to_broadcast([P, 8, 64]), ALU.add))
                v(V.scalar_tensor_tensor(out=ss[:, PAST:NKEYS], in0=ps[:, 4, 0:64], scalar=sc[:, 0, 32:33],
                                         in1=newm[:, p], op0=ALU.add, op1=ALU.add))
                v(V.tensor_reduce(st[:, 8:9], ss[:], AX.X, ALU.max))
                V.tensor_scalar(st[:, 8:9], st[:, 8:9], -SCALE, None, ALU.mult).then_inc(sel_max_ready, 1)
                dve.wait_ge(win_exp_done, p + 1)
                v(V.reciprocal(st[:, 5:6], st[:, 5:6]))
                v(V.tensor_tensor(st[:, 5:6], st[:, 5:6], gt[:, p, 2:3], ALU.mult))
                V.tensor_scalar(sw[:], sw[:], st[:, 5:6], None, ALU.mult).then_inc(win_scaled, 1)
                dve.wait_ge(sel_exp_done, p + 1)
                v(V.reciprocal(st[:, 9:10], st[:, 9:10]))
                v(V.tensor_tensor(st[:, 9:10], st[:, 9:10], gt[:, p, 1:2], ALU.mult))
                V.tensor_scalar(ss[:], ss[:], st[:, 9:10], None, ALU.mult).then_inc(sel_scaled, 1)

            def evacuate(p):
                for b in range(1, NB, 2):
                    dve.wait_ge(transposed, NB * p + b + 1)
                    if p and b == 1:
                        dve.wait_ge(values_done, p)
                    lo, n = banks[b][0], len(banks[b])
                    if b == 1:
                        V.tensor_copy(pt[:, 4, :], ps[:, 1, 0:P])
                        V.tensor_copy(pt[0:64, 5, :], ps[0:64, 1, P:2 * P]).then_inc(dve_copied, 1)
                    else:
                        V.tensor_copy(pt[:, lo:lo + n, :], ps[:, b % 4, 0:P * n].rearrange("p (n f) -> p n f", n=n)).then_inc(dve_copied, 1)

            def outputs(p):
                dve.wait_ge(values_done, p + 1)
                for g in range(2):
                    h = slice(64 * g, 64 * g + 64)
                    V.tensor_copy(k.mixT[h, 4:8, T_PROMPT + 16 * p:T_PROMPT + 16 * p + 16].rearrange("p r (s t) -> p r s t", t=STEPS),
                                  ps[h, 6, 0:P].rearrange("p (s g r t) -> p g r s t", s=2, g=2, r=REP)[:, g]).then_inc(output_copied, 1)

            for p in range(PAIRS + 1):
                if p < PAIRS:
                    small(p)
                if p:
                    evacuate(p - 1)
                if p < PAIRS:
                    selected(p)
                if p:
                    outputs(p - 1)

        @block.tensor
        def _(pe):
            pe.wait_ge(masks_loaded, 96)
            for p in range(PAIRS):
                mm = nc.tensor.matmul(ps[:, 7, 24 * p:24 * p + 24], pick[:, p, :], k.gates[0:64, 4, :], start=True, stop=True)
            mm.then_inc(gates_spread, 1)
            pe.wait_ge(q_ready, 2)

            def small(p):
                if p:
                    pe.wait_ge(sel_max_ready, p)
                pe.wait_ge(k.win_got[p % 2], 64 * (p // 2 + 1))
                for s in range(2):
                    rows = slice(64 * s, 64 * s + 64)
                    qs = q[:, 2 * p + s, :]
                    nc.tensor.matmul(ps[rows, 4, 128:255], qs, k.kcT[:, 2 * p + s, 0:127], start=True, stop=True)
                    nc.tensor.matmul(ps[rows, 4, 0:64], qs, k.ksT[:, T_PROMPT:T], start=True, stop=True)
                    nc.tensor.matmul(ps[rows, 4, 64:128], qs, k.kwT[:, T_PROMPT:T], start=True, stop=True)
                    mm = nc.tensor.matmul(ps[rows, 5, :], qs, kw[:, p % 2, s], start=True, stop=True)
                mm.then_inc(small_scores_made, 1)

            def selected(p):
                kp = pages[p % 2]
                if p:
                    pe.wait_ge(act_copied, 4 * p)
                    pe.wait_ge(dve_copied, 3 * p)
                for s in range(2):
                    pe.wait_ge(got[p % 2][s], 256 * (p // 2 + 1))
                for s in range(2):
                    for c in range(4):
                        mm = nc.tensor.matmul(ps[64 * s:64 * s + 64, c, :], q[:, 2 * p + s, :],
                                              kp[:, 16 * s + 4 * c:16 * s + 4 * c + 4, 0:P], start=True, stop=True)
                mm.then_inc(selected_scores_made, 1)

            def importance(p):
                pe.wait_ge(cmp_probs_ready, p + 1)
                pe.wait_ge(win_max_ready, p + 1)
                nc.tensor.matmul(ps[:, 4, 256:384], same[:], pcs[:, p % 2], start=True, stop=True).then_inc(importance_summed, 1)

            def transposes(p):
                pc, sw = pcs[:, p % 2], sws[:, p % 2]
                pe.wait_ge(cmp_scaled, p + 1)
                pe.wait_ge(win_scaled, p + 1)
                pe.wait_ge(sel_max_ready, p + 1)
                for b, blocks in enumerate(banks):
                    if b == 2:
                        pe.wait_ge(sel_scaled, p + 1)
                    if b >= 4:
                        pe.wait_ge(dve_copied if b % 2 else act_copied, (3 if b % 2 else 4) * p + (b - 4) // 2 + 1)
                    for n, blk in enumerate(blocks):
                        src = (pc[:, 0:127] if blk == 0 else sw[:, P * (blk - 1):P * (blk - 1) + rows_of(blk)] if blk < 6
                               else ss[:, P * (blk - 6):P * (blk - 6) + rows_of(blk)])
                        mm = nc.tensor.transpose(ps[0:rows_of(blk), b % 4, P * n:P * n + P], src, k.ident[:])
                    mm.then_inc(transposed, 1)

            def values(p):
                kp = pages[p % 2]
                pe.wait_ge(act_copied, 4 * p + 4)
                pe.wait_ge(dve_copied, 3 * p + 3)
                if p:
                    pe.wait_ge(output_copied, 2 * p)
                for s in range(2):
                    for blk in range(23):
                        m = rows_of(blk)
                        val = (k.vcmp[0:127, 2 * p + s, :] if blk == 0 else vw[:, p % 2, s, blk - 1, :] if blk < 5
                               else k.kv[0:64, 4, 384:512] if blk == 5
                               else kp[:, 16 * s + blk - 6, P:2 * P] if blk < 22 else k.kv[0:64, 4, 256:384])
                        mm = nc.tensor.matmul(ps[:, 6, 64 * s:64 * s + 64], val, pt[0:m, blk, 64 * s:64 * s + 64],
                                              start=(blk == 0), stop=(blk == 22))
                mm.then_inc(values_done, 1)

            for p in range(PAIRS + 1):
                if p < PAIRS:
                    small(p)
                if p:
                    transposes(p - 1)
                if p < PAIRS:
                    selected(p)
                    importance(p)
                if p:
                    values(p - 1)


F32R = mybir.dt.float32r


def as_r(ap):
    return ap.bitcast(F32R)


def up_part(pe, x_hi, x_lo, u_hi, u_lo, out, part):
    h, i = divmod(part, KD)
    cols = slice(HALF * h, HALF * h + HALF)
    for n, (u, x) in enumerate(((u_hi[:, i], x_hi), (u_hi[:, i], x_lo), (u_lo[:, i], x_hi))):
        mm = pe.matmul(out[:, h, 0:HALF], as_r(u), as_r(x[:, i, cols]),
                       start=(i == 0 and n == 0), stop=(i == KD - 1 and n == 2))
    return mm


def up_products(pe, x_hi, x_lo, u_hi, u_lo, out):
    for part in range(2 * KD):
        mm = up_part(pe, x_hi, x_lo, u_hi, u_lo, out, part)
    return mm


def first_products(pe, x_hi, x_lo, u_hi, u_lo, out, hi_made, lo_made, before):
    for i in range(KD):
        pe.wait_ge(hi_made, before + i + 1)
        for h in range(2):
            for n, u in enumerate((u_hi, u_lo)):
                product(pe, out[:, h, 0:HALF], u[:, i], x_hi[:, i, HALF * h:HALF * h + HALF], i == 0 and n == 0, False)
    for i in range(KD):
        pe.wait_ge(lo_made, before + i + 1)
        for h in range(2):
            mm = product(pe, out[:, h, 0:HALF], u_hi[:, i], x_lo[:, i, HALF * h:HALF * h + HALF], False, i == KD - 1)
    return mm


def product(pe, out, w, x, start, stop):
    return pe.matmul(out, as_r(w), as_r(x), start=start, stop=stop)


def mix_stage(nc, k):
    with ExitStack() as ctx:
        sb = lambda n, s, d=F32: ctx.enter_context(nc.sbuf_tensor(n, s, d))
        sem = k.sem
        w_raw, w_hi, w_lo = sb("m_w_raw", [P, 4, KD, P]), sb("m_w_hi", [P, 2, KD, P]), sb("m_w_lo", [P, 2, KD, P])
        ga, gf = sb("g_attn_sb", [P, 4]), sb("g_ffn_sb", [P, KD])
        rinv = sb("m_rinv", [P, T])
        sq = sb("m_sq", [P, KD, T])
        hn = sq
        ps = ctx.enter_context(nc.psum_tensor("m_ps", [P, 8, 512], F32))
        tile = lambda n: ps[:, 2 * (n % 3):2 * (n % 3) + 2]
        ld, w_ld = sem("m_ld"), [sem(f"m_w_ld{n}") for n in range(4)]
        w_hi_made, w_lo_made, x_hi_made, x_lo_made, multiplied = (sem(f"m_{n}") for n in (
            "w_hi_made", "w_lo_made", "x_hi_made", "x_lo_made", "multiplied"))
        squared, summed, ms_ready, root_ready, attn_ready, h_ready, hn_ready, q_copied, vch = (sem(f"m_{n}") for n in (
            "squared", "summed", "ms", "root", "attn", "h", "hn", "q_copied", "v"))
        OUT, ALL = KD, KD + 16
        block = ctx.enter_context(nc.Block())

        @block.sync
        def _(sp):
            for dst, src in ((ga, k.d["g_out_attn"]), (gf, k.d["g_ffn"])):
                sp.dma_start(dst[:], src).then_inc(ld, 16)
            for n in range(ALL):
                if n >= 4:
                    sp.wait_ge(w_lo_made, n - 3)
                sp.dma_start(w_raw[:, n % 4].rearrange("p i n -> p (i n)"), k.d["w_mix"][n]).then_inc(w_ld[n % 4], 16)

        @block.scalar
        def _(act):
            def w_high(n):
                if n < ALL:
                    act.wait_ge(w_ld[n % 4], 16 * (n // 4 + 1))
                    if n >= 2:
                        act.wait_ge(multiplied, n - 1)
                    nc.scalar.activation(as_r(w_hi[:, n % 2]), w_raw[:, n % 4], ACT.Copy).then_inc(w_hi_made, 1)

            def x_high(c, src):
                nc.scalar.activation(as_r(k.x_hi[:, c]), src[:, c], ACT.Copy).then_inc(x_hi_made, 1)

            for c in range(4):
                nc.scalar.activation(sq[:, c], k.mixT[:, 4 + c], ACT.Square).then_inc(squared, 1)
            for c in range(4):
                x_high(c, k.mixT)
            w_high(0)
            w_high(1)
            act.wait_ge(ms_ready, 1)
            nc.scalar.activation(rinv[:], rinv[:], ACT.Sqrt).then_inc(root_ready, 1)
            for c in range(4):
                act.wait_ge(attn_ready, c + 1)
                x_high(4 + c, k.mixT)
            for n in range(OUT):
                w_high(n + 2)
                act.wait_ge(h_ready, n + 1)
                nc.scalar.activation(sq[:, n], k.hT[:, n], ACT.Square).then_inc(squared, 1)
            act.wait_ge(ms_ready, 2)
            nc.scalar.activation(rinv[:], rinv[:], ACT.Sqrt).then_inc(root_ready, 1)
            for c in range(KD):
                act.wait_ge(hn_ready, c + 1)
                x_high(c, hn)
            for n in range(OUT, ALL):
                w_high(n + 2)
                act.wait_ge(multiplied, n + 1)
                nc.scalar.activation(k.qp[:, n - OUT].rearrange("p (h n) -> p h n", h=2), tile(n)[:, :, 0:HALF], ACT.Copy).then_inc(q_copied, 1)

        @block.gpsimd
        def _(pool):
            for n in range(ALL):
                pool.wait_ge(w_hi_made, n + 1)
                nc.gpsimd.tensor_tensor(as_r(w_lo[:, n % 2]), w_raw[:, n % 4], w_hi[:, n % 2], ALU.subtract).then_inc(w_lo_made, 1)

        @block.vector
        def _(dve):
            v = Chain(dve, vch)
            V = nc.vector

            def mean_square(dim, n):
                dve.wait_ge(summed, n)
                for h in range(2):
                    v.go(V.tensor_scalar(rinv[:, HALF * h:HALF * h + HALF], ps[:, 6 + h, 0:HALF], 1.0 / dim, EPS, ALU.mult, ALU.add))
                v.wait()
                V.reciprocal(rinv[:], rinv[:]).then_inc(ms_ready, 1)

            def x_low(c, src, n):
                dve.wait_ge(x_hi_made, n + 1)
                V.tensor_tensor(as_r(k.x_lo[:, c]), src[:, c], k.x_hi[:, c], ALU.subtract).then_inc(x_lo_made, 1)

            dve.wait_ge(ld, 32)
            mean_square(512, 1)
            for c in range(4):
                x_low(c, k.mixT, c)
            dve.wait_ge(root_ready, 1)
            for c in range(4):
                V.scalar_tensor_tensor(out=k.mixT[:, 4 + c], in0=k.mixT[:, 4 + c], scalar=ga[:, c:c + 1], in1=rinv[:],
                                       op0=ALU.mult, op1=ALU.mult).then_inc(attn_ready, 1)
            for c in range(4, KD):
                x_low(c, k.mixT, c)
            for n in range(OUT):
                dve.wait_ge(multiplied, n + 1)
                hs = k.hT[:, n].rearrange("p (h n) -> p h n", h=2)
                V.tensor_tensor(hs, hs, tile(n)[:, :, 0:HALF], ALU.add).then_inc(h_ready, 1)
            mean_square(D, 2)
            dve.wait_ge(root_ready, 2)
            for c in range(KD):
                V.scalar_tensor_tensor(out=hn[:, c], in0=k.hT[:, c], scalar=gf[:, c:c + 1], in1=rinv[:],
                                       op0=ALU.mult, op1=ALU.mult).then_inc(hn_ready, 1)
                if c:
                    x_low(c - 1, hn, KD + c - 1)
            x_low(KD - 1, hn, 2 * KD - 1)

        @block.tensor
        def _(pe):
            def column_sums(n, first):
                for c in range(n):
                    pe.wait_ge(squared, first + c + 1)
                    for h in range(2):
                        mm = nc.tensor.matmul(ps[:, 6 + h, 0:HALF], k.ones[:], sq[:, c, HALF * h:HALF * h + HALF],
                                              start=(c == 0), stop=(c == n - 1))
                mm.then_inc(summed, 1)

            column_sums(4, 0)
            for n in range(ALL):
                if n == OUT:
                    column_sums(KD, 4)
                pe.wait_ge(w_lo_made, n + 1)
                if n >= 3:
                    if n - 3 < OUT:
                        pe.wait_ge(h_ready, n - 2)
                    else:
                        pe.wait_ge(q_copied, n - 2 - OUT)
                operands = k.x_hi, k.x_lo, w_hi[:, n % 2], w_lo[:, n % 2], tile(n)
                if n in (0, OUT):
                    first_products(pe, *operands, x_hi_made, x_lo_made, KD * (n // OUT)).then_inc(multiplied, 1)
                else:
                    up_products(pe, *operands).then_inc(multiplied, 1)


EG = 4
NG = KEYS // EG
SELECT_GROUPS = 10
ONE_HOT_GROUPS = 4
EARLY_GROUPS = SELECT_GROUPS + ONE_HOT_GROUPS


def retrieve_stage(nc, k):
    with ExitStack() as ctx:
        sb = lambda n, s, d=F32: ctx.enter_context(nc.sbuf_tensor(n, s, d))
        sem = k.sem
        sk, iota = sb("subkeys_sb", [P, 16, KEYS]), sb("iota16", [P, 16])
        scores, scr = sb("k_scores", [P, 2, 16, KEYS]), sb("k_scr", [P, 16, KEYS])
        v16, i16, i16f = sb("v16", [P, 16, 16]), sb("i16", [P, 16, 16], U32), sb("i16f", [P, 2, 16, 16])
        eq = sb("eq", [P, PH, 16, 16])
        vals, cpos, ab = sb("vals", [P, 2, PH, 16]), sb("cpos", [P, PH, 16], U32), sb("ab", [P, 2, PH, 16], U32)
        abf, idx, gsum = sb("abf", [P, 2, PH, 16]), sb("idx", [P, 2, 3, P]), sb("gsum", [P, 2, PH])
        u_raw, u_hi, u_lo = sb("r_u_raw", [P, EG, KD, P]), sb("r_u_hi", [P, 2, KD, P]), sb("r_u_lo", [P, 2, KD, P])
        gelu = k.mixT[:, 0:4].rearrange("p (q e) t -> p q e t", q=2)
        ps = ctx.enter_context(nc.psum_tensor("r_ps", [P, 8, 512], F32))
        keys_loaded = sem("r_ld")
        scores_made, scores_copied, scores_used = sem("r_scores_made"), sem("r_scores_copied"), sem("r_scores_used")
        gate_inputs_ready, exponentials_done = sem("r_gate_inputs_ready"), sem("r_exponentials_done")
        picks_ready, picks_transposed = sem("r_picks_ready"), sem("r_picks_transposed")
        picks_copied, vch = sem("r_picks_copied"), sem("r_vch")
        u_ld = [sem(f"r_u_ld{e}") for e in range(EG)]
        up_done, gelu_done, u_hi_made = sem("r_up_done"), sem("r_gelu_done"), sem("r_u_hi_made")
        u_lo_made = sem("r_u_lo_made")
        N = EG * SELECT_GROUPS
        block = ctx.enter_context(nc.Block())

        @block.sync
        def _(sp):
            sp.dma_start(sk[:], k.d["subkeys"]).then_inc(keys_loaded, 16)
            sp.dma_start(iota[:], k.d["iota16"]).then_inc(keys_loaded, 16)

            def load(n):
                e = n % EG
                if n >= EG:
                    sp.wait_ge(u_lo_made, n - EG + 1)
                sp.dma_start(u_raw[:, e].rearrange("p k n -> p (k n)"), k.d["u_tab"][n]).then_inc(u_ld[e], 16)

            for n in range(EG):
                load(n)
            for n in range(N):
                if n + EG < N:
                    load(n + EG)
                if n % 2:
                    q = (n // 2) % 2
                    sp.wait_ge(gelu_done, n + 1)
                    sp.dma_start(k.d["gelu_scr"][n // 2], gelu[:, q].rearrange("p e t -> p (e t)")).then_inc(k.spilled[q], 16)

        @block.scalar
        def _(act):
            def u_high(n):
                act.wait_ge(u_ld[n % EG], 16 * (n // EG + 1))
                nc.scalar.activation(as_r(u_hi[:, n % 2]), u_raw[:, n % EG], ACT.Copy).then_inc(u_hi_made, 1)

            def group(G):
                for n in range(EG * G, EG * G + EG):
                    e = n % EG
                    act.wait_ge(up_done, n + 1)
                    if G and e % 2 == 0:
                        act.wait_ge(k.spilled[e // 2], 16 * G)
                    nc.scalar.activation(gelu[:, e // 2, e % 2].rearrange("p (h n) -> p h n", h=2),
                                         ps[:, 4 + 2 * (n % 2):6 + 2 * (n % 2), 0:HALF], ACT.Gelu_apprx_tanh).then_inc(gelu_done, 1)
                    if n + 2 < N:
                        u_high(n + 2)

            def exponentials(t):
                m = TILE_ROWS[t]
                act.wait_ge(gate_inputs_ready, t + 1)
                nc.scalar.activation(vals[0:m, t % 2], vals[0:m, t % 2], ACT.Exp).then_inc(exponentials_done, 1)

            def picks(t):
                m = TILE_ROWS[t]
                act.wait_ge(picks_transposed, t + 1)
                nc.scalar.activation(k.idxT[:, :, P * t:P * t + m],
                                     ps[:, t % 2, 0:3 * P].rearrange("p (n m) -> p n m", n=3)[:, :, 0:m], ACT.Copy).then_inc(picks_copied, 1)

            u_high(0)
            u_high(1)
            for t in range(TILES):
                m = TILE_ROWS[t]
                act.wait_ge(scores_made, t + 1)
                if t >= 2:
                    act.wait_ge(scores_used, t - 1)
                nc.scalar.activation(scores[0:m, t % 2].rearrange("p (b n) c -> p b (n c)", b=4), ps[0:m, 0:4, :],
                                     ACT.Copy).then_inc(scores_copied, 1)
                group(2 * t)
                if t >= 1:
                    exponentials(t - 1)
                if t >= 2:
                    picks(t - 2)
                group(2 * t + 1)
            exponentials(TILES - 1)
            picks(TILES - 2)
            picks(TILES - 1)

        @block.gpsimd
        def _(pool):
            for n in range(N):
                pool.wait_ge(u_hi_made, n + 1)
                if n >= 2:
                    pool.wait_ge(up_done, n - 1)
                nc.gpsimd.tensor_tensor(as_r(u_lo[:, n % 2]), u_raw[:, n % EG], u_hi[:, n % 2], ALU.subtract).then_inc(u_lo_made, 1)

        @block.vector
        def _(dve):
            v = Chain(dve, vch)
            V = nc.vector

            def select(t):
                m, b = TILE_ROWS[t], t % 2
                sc = scores[0:m, b]
                dve.wait_ge(scores_copied, t + 1)
                for u in range(16):
                    v.go(V.max(v16[0:m, u, 0:8], sc[:, u]))
                v.wait()
                for u in range(16):
                    v.go(V.max_index(i16[0:m, u, 0:8], v16[0:m, u, 0:8], sc[:, u]))
                    v.go(V.match_replace(scr[0:m, u], v16[0:m, u, 0:8], sc[:, u], GONE))
                v.wait()
                for u in range(16):
                    v.go(V.max(v16[0:m, u, 8:16], scr[0:m, u]))
                v.wait()
                for u in range(16):
                    v.go(V.max_index(i16[0:m, u, 8:16], v16[0:m, u, 8:16], scr[0:m, u]))
                v.wait()
                v.go(V.tensor_copy(i16f[0:m, b].rearrange("p a b -> p (a b)"), i16[0:m].rearrange("p a b -> p (a b)")))
                cand = sc.rearrange("p a b -> p (a b)").rearrange("p (h c) -> p h c", h=PH)
                left = scr[0:m].rearrange("p a b -> p (a b)").rearrange("p (h c) -> p h c", h=PH)
                for h in range(PH):
                    v.go(V.tensor_tensor(cand[:, h].rearrange("p (a b) -> p a b", a=16),
                                         v16[0:m, 2 * h].unsqueeze(2).to_broadcast([m, 16, 16]),
                                         v16[0:m, 2 * h + 1].unsqueeze(1).to_broadcast([m, 16, 16]), ALU.add))
                v.wait()
                for h in range(PH):
                    v.go(V.max(vals[0:m, b, h, 0:8], cand[:, h]))
                v.wait()
                for h in range(PH):
                    v.go(V.max_index(cpos[0:m, h, 0:8], vals[0:m, b, h, 0:8], cand[:, h]))
                    v.go(V.match_replace(left[:, h], vals[0:m, b, h, 0:8], cand[:, h], GONE))
                v.wait()
                V.memset(gsum[0:1, 0, 0:1], 0.0).then_inc(scores_used, 1)
                for h in range(PH):
                    v.go(V.max(vals[0:m, b, h, 8:16], left[:, h]))
                v.wait()
                for h in range(PH):
                    v.go(V.max_index(cpos[0:m, h, 8:16], vals[0:m, b, h, 8:16], left[:, h]))
                v(V.tensor_copy(gsum[0:m, 0], vals[0:m, b, :, 0]))
                V.tensor_tensor(vals[0:m, b], vals[0:m, b], gsum[0:m, 0].unsqueeze(2).to_broadcast([m, PH, 16]),
                                ALU.subtract).then_inc(gate_inputs_ready, 1)
                v.go(V.tensor_scalar(ab[0:m, 0], cpos[0:m], 4, None, ALU.logical_shift_right))
                v(V.tensor_scalar(ab[0:m, 1], cpos[0:m], 15, None, ALU.bitwise_and))
                v(V.tensor_copy(abf[0:m].rearrange("p a h c -> p (a h c)"), ab[0:m].rearrange("p a h c -> p (a h c)")))
                if t >= 2:
                    dve.wait_ge(picks_transposed, t - 1)
                e3 = eq[0:m].rearrange("p h c a -> p (h c) a")
                for s in range(2):
                    v(V.tensor_tensor(e3, abf[0:m, s].rearrange("p h c -> p (h c)").unsqueeze(2).to_broadcast([m, P, 16]),
                                      iota[0:m].unsqueeze(1).to_broadcast([m, P, 16]), ALU.is_equal))
                    fs = i16f[0:m, b].rearrange("p (h s) a -> p h s a", s=2)[:, :, s]
                    v(V.tensor_tensor(eq[0:m], eq[0:m], fs.unsqueeze(2).to_broadcast([m, PH, 16, 16]), ALU.mult))
                    v(V.tensor_reduce(idx[0:m, b, s], e3, AX.X, ALU.add))

            def gates(t):
                m, b = TILE_ROWS[t], t % 2
                dve.wait_ge(exponentials_done, t + 1)
                v(V.tensor_reduce(gsum[0:m, 0], vals[0:m, b], AX.X, ALU.add))
                v(V.reciprocal(gsum[0:m, 1], gsum[0:m, 0]))
                V.tensor_tensor(idx[0:m, b, 2].rearrange("p (h c) -> p h c", h=PH), vals[0:m, b],
                                gsum[0:m, 1].unsqueeze(2).to_broadcast([m, PH, 16]), ALU.mult).then_inc(picks_ready, 1)

            dve.wait_ge(keys_loaded, 32)
            for t in range(TILES):
                select(t)
                if t >= 1:
                    gates(t - 1)
            gates(TILES - 1)

        @block.tensor
        def _(pe):
            def group(G):
                for n in range(EG * G, EG * G + EG):
                    pe.wait_ge(u_lo_made, n + 1)
                    if n >= 2:
                        pe.wait_ge(gelu_done, n - 1)
                    b = n % 2
                    up_products(nc.tensor, k.x_hi, k.x_lo, u_hi[:, b], u_lo[:, b], ps[:, 4 + 2 * b:6 + 2 * b]).then_inc(up_done, 1)

            def transposes(t):
                m = TILE_ROWS[t]
                pe.wait_ge(picks_ready, t + 1)
                if t < TILES - 2:
                    pe.wait_ge(scores_copied, t + 3)
                elif t == TILES - 2:
                    pe.wait_ge(scores_copied, TILES)
                for n in range(3):
                    mm = nc.tensor.transpose(ps[:, t % 2, P * n:P * n + m], idx[0:m, t % 2, n], k.ident[0:m, 0:m])
                mm.then_inc(picks_transposed, 1)

            pe.wait_ge(keys_loaded, 32)
            for t in range(TILES):
                m = TILE_ROWS[t]
                if t:
                    pe.wait_ge(scores_copied, t)
                if t >= 3:
                    pe.wait_ge(picks_copied, t - 2)
                for u in range(16):
                    mm = nc.tensor.matmul(ps[0:m, u // 4, P * (u % 4):P * (u % 4) + P],
                                          k.qp[:, u, P * t:P * t + m], sk[:, u, :], start=True, stop=True)
                mm.then_inc(scores_made, 1)
                group(2 * t)
                if t >= 2:
                    transposes(t - 2)
                group(2 * t + 1)
            transposes(TILES - 2)
            transposes(TILES - 1)


TB = 32
NTB = T // TB


def gate_matrix_stage(nc, k):
    with ExitStack() as ctx:
        sb = lambda n, s, d=F32: ctx.enter_context(nc.sbuf_tensor(n, s, d))
        sem = k.sem
        iota = sb("iota128", [P, KEYS])
        oh1, oh2 = sb("one_hot1", [P, 8, KEYS]), sb("one_hot2", [P, 8, KEYS])
        stage, first_picks = sb("gate_stage", [P, 2, NG, TB, EG]), sb("first_picks", [P, 2, TB])
        u_raw, u_hi, u_lo = (sb(f"g_{n}", [P, 2, KD, P]) for n in ("u_raw", "u_hi", "u_lo"))
        gelu = k.mixT[:, 4:6]
        ps = ctx.enter_context(nc.psum_tensor("g_ps", [P, 8, 512], F32))
        ld, hot, last_hot, last_room, picks_copied, multiplied, copied = (sem(f"gm_{n}") for n in (
            "ld", "hot", "last_hot", "last_room", "picks_copied", "multiplied", "copied"))
        u_ld = [sem(f"gm_u_ld{b}") for b in range(2)]
        up_done, gelu_done, u_hi_made = sem("gm_up_done"), sem("gm_gelu_done"), sem("gm_u_hi_made")
        u_lo_made = sem("gm_u_lo_made")
        FIRST = EG * SELECT_GROUPS
        UPS = EG * ONE_HOT_GROUPS // 2
        assert UPS == NTB // 2 - 1
        QUADS = TB // 4
        PARTS = [3, 3, 2, 2, 2, 2, 2]
        block = ctx.enter_context(nc.Block())

        @block.sync
        def _(sp):
            def load_u(n, b):
                sp.dma_start(u_raw[:, b].rearrange("p k n -> p (k n)"),
                             k.d["u_tab"][bass.ds(n + FIRST, 1)].rearrange("o p f -> (o p) f")).then_inc(u_ld[b], 16)

            def blocks(i, ups, ahead):
                for b in range(2):
                    if ahead:
                        sp.wait_ge(u_lo_made, 2 * i + (b + 1))
                        load_u(2 * i + (b + 2), b)
                    if ups and b == 1:
                        sp.wait_ge(gelu_done, 2 * i + 2)
                        sp.dma_start(k.d["gelu_scr"][bass.ds(i + FIRST // 2, 1)].rearrange("o p f -> (o p) f"),
                                     gelu.rearrange("p e t -> p (e t)")).then_inc(k.spilled_late, 16)
                    sp.wait_ge(copied, 2 * QUADS * i + (QUADS * b + QUADS + 4))
                    sp.dma_start(k.d["gate_scr"][:, :, bass.ds(2 * i + b, 1), :].rearrange("g p o f -> p g (o f)"),
                                 stage[:, b].rearrange("p g t e -> p g (t e)")).then_inc(k.gm_stored[b], 16)

            sp.dma_start(iota[:], k.d["iota128"]).then_inc(ld, 16)
            for b in range(2):
                load_u(b, b)
            for q in range(2):
                sp.wait_ge(k.spilled[q], 16 * SELECT_GROUPS)
            for b in range(2):
                sp.dma_start(k.early_act[:, b], k.d["gelu_scr"][2 * b:2 * b + 2].rearrange("o p f -> p o f")).then_inc(k.act_ld[b], 16)
            for half in range(2):
                sp.dma_start(k.v_raw[:, half].rearrange("p c e n -> p (c e n)"),
                             k.d["v_tab"][:, 0, 2048 * half:2048 * half + 2048]).then_inc(k.v_ld[half], 16)
            for e in range(EG):
                sp.dma_start(k.u_raw[:, e].rearrange("p k n -> p (k n)"), k.d["u_tab"][EG * EARLY_GROUPS + e]).then_inc(k.u_ld[e], 16)
            with sp.Fori(0, UPS - 1) as i:
                blocks(i, True, True)
            blocks(UPS - 1, True, False)
            blocks(UPS, False, False)

        @block.vector
        def _(dve):
            dve.wait_ge(ld, 16)
            with dve.Fori(0, NTB // 2) as i:
                for b in range(2):
                    nc.vector.tensor_copy(first_picks[:, b], k.idxT[:, 0, bass.ds(2 * TB * i + TB * b, TB)]).then_inc(picks_copied, 1)
                    for n in range(TB):
                        if n % 4 == 0:
                            dve.wait_ge(multiplied, 2 * QUADS * i + (QUADS * b + n // 4 + 1))
                        at = bass.ds(2 * TB * i + (TB * b + n), 1)
                        if n % 4 != 3:
                            nc.vector.tensor_scalar(oh1[:, n % 8], iota[:], k.idxT[:, 0, at], None, ALU.is_equal)
                        nc.vector.tensor_scalar(oh2[:, n % 8], iota[:], k.idxT[:, 1, at], k.idxT[:, 2, at], ALU.is_equal, ALU.mult).then_inc(hot, 1)

        @block.gpsimd
        def _(pool):
            def blocks(i, ups):
                for b in range(2):
                    if ups:
                        pool.wait_ge(u_hi_made, 2 * i + (b + 1))
                        nc.gpsimd.tensor_tensor(as_r(u_lo[:, b]), u_raw[:, b], u_hi[:, b], ALU.subtract).then_inc(u_lo_made, 1)
                    pool.wait_ge(picks_copied, 2 * i + (b + 1))
                    for q in range(QUADS):
                        n = 4 * q + 3
                        pool.wait_ge(multiplied, 2 * QUADS * i + (QUADS * b + q + 1))
                        pool.sem_inc(last_room, 1)
                        nc.gpsimd.tensor_scalar(oh1[:, n % 8], iota[:], first_picks[:, b, n:n + 1], None,
                                                ALU.is_equal).then_inc(last_hot, 1)

            pool.wait_ge(ld, 16)
            with pool.Fori(0, UPS) as i:
                blocks(i, True)
            blocks(UPS, False)

        @block.tensor
        def _(pe):
            def blocks(i, ups):
                for b in range(2):
                    out = ps[:, 4 + 2 * b:6 + 2 * b]
                    done = 0
                    for q in range(QUADS):
                        pe.wait_ge(copied, 2 * QUADS * i + (QUADS * b + q + 1))
                        for n in range(4 * q, 4 * q + 4):
                            pe.wait_ge(hot, 2 * TB * i + (TB * b + n + 1))
                            if n % 4 == 3:
                                pe.wait_ge(last_hot, 2 * QUADS * i + (QUADS * b + q + 1))
                            mm = nc.tensor.matmul(ps[:, q % 4, KEYS * (n % 4):KEYS * (n % 4) + KEYS], oh1[:, n % 8], oh2[:, n % 8],
                                                  start=True, stop=True)
                        mm.then_inc(multiplied, 1)
                        if ups and q < QUADS - 1:
                            if q == 0:
                                pe.wait_ge(u_lo_made, 2 * i + (b + 1))
                            for part in range(done, done + PARTS[q]):
                                mm = up_part(nc.tensor, k.x_hi, k.x_lo, u_hi[:, b], u_lo[:, b], out, part)
                            done += PARTS[q]
                            if q == QUADS - 2:
                                mm.then_inc(up_done, 1)

            pe.sem_inc(multiplied, 2)
            with pe.Fori(0, UPS) as i:
                blocks(i, True)
            blocks(UPS, False)

        @block.scalar
        def _(act):
            def u_high(b, turn):
                act.wait_ge(u_ld[b], 16 * turn + 16)
                nc.scalar.activation(as_r(u_hi[:, b]), u_raw[:, b], ACT.Copy).then_inc(u_hi_made, 1)

            def blocks(i, ups, ahead):
                for b in range(2):
                    act.wait_ge(k.gm_stored[b], 16 * i + 16)
                    for q in range(QUADS):
                        if ups and q == QUADS - 1:
                            act.wait_ge(up_done, 2 * i + (b + 1))
                            if b == 0:
                                act.wait_ge(k.spilled_late, 16 * i + 16)
                            nc.scalar.activation(gelu[:, b].rearrange("p (h n) -> p h n", h=2), ps[:, 4 + 2 * b:6 + 2 * b, 0:HALF],
                                                 ACT.Gelu_apprx_tanh).then_inc(gelu_done, 1)
                            if ahead:
                                u_high(b, i + 1)
                        act.wait_ge(multiplied, 2 * QUADS * i + (QUADS * b + q + 3))
                        nc.scalar.activation(stage[:, b, :, 4 * q:4 * q + 4, :].rearrange("p g t e -> p t g e"),
                                             ps[:, q % 4, :].rearrange("p (t g e) -> p t g e", t=4, g=NG),
                                             ACT.Copy).then_inc(copied, 1)

            act.sem_inc(copied, 4)
            act.sem_inc(k.spilled_late, 16)
            for b in range(2):
                act.sem_inc(k.gm_stored[b], 16)
            for b in range(2):
                u_high(b, 0)
            with act.Fori(0, UPS - 1) as i:
                blocks(i, True, True)
            blocks(UPS - 1, True, False)
            blocks(UPS, False, False)


def experts_stage(nc, k):
    with ExitStack() as ctx:
        sb = lambda n, s, d=F32: ctx.enter_context(nc.sbuf_tensor(n, s, d))
        sem = k.sem
        u_raw = k.u_raw
        u_hi, u_lo = sb("u_hi", [P, 2, KD, P]), sb("u_lo", [P, 2, KD, P])
        v_hi, v_lo = sb("v_hi", [P, 4, EG, P]), sb("v_lo", [P, 4, EG, P])
        w_raw, w_hi, w_lo = sb("w_raw", [P, 2, T]), sb("w_hi", [P, 2, EG, T]), sb("w_lo", [P, 2, EG, T])
        act_ = sb("e_act", [P, 2, T])
        v_raw, early_act, v_ld, act_ld = k.v_raw, k.early_act, k.v_ld, k.act_ld
        gt = k.mixT[:].rearrange("p (b e) t -> p b (e t)", b=2).rearrange("p b (t e) -> p b t e", e=EG)
        ps = ctx.enter_context(nc.psum_tensor("e_ps", [P, 8, 512], F32))
        u_ld, g_ld = k.u_ld, [sem(f"e_g_loaded{b}") for b in range(2)]
        up_done, gelu_done, down_done = sem("e_up_done"), sem("e_gelu_done"), sem("e_down_done")
        added = sem("e_added")
        u_hi_made, u_lo_made, v_hi_made, v_lo_made, w_made, w_hi_made, w_lo_made = (
            sem(f"e_{n}_made") for n in ("u_hi", "u_lo", "v_hi", "v_lo", "w", "w_hi", "w_lo"))
        block = ctx.enter_context(nc.Block())

        E = EARLY_GROUPS
        DOWN0 = KD + 1
        GELU0 = ADD0 = 2
        EARLY_PAIRS, PAIRS_LEFT = E // 2 - 1, (NG - E) // 2 - 2

        @block.sync
        def _(sp):
            def load_u(s, e):
                sp.dma_start(u_raw[:, e].rearrange("p k n -> p (k n)"),
                             k.d["u_tab"][bass.ds(EG * s + e, 1)].rearrange("o p f -> (o p) f")).then_inc(u_ld[e], 16)

            def load_gates(s, b):
                sp.dma_start(gt[:, b].rearrange("p t e -> p (t e)"),
                             k.d["gate_scr"][bass.ds(s, 1)].rearrange("o p a f -> (o p) (a f)")).then_inc(g_ld[b], 16)

            def loads(s, b, early):
                if not early:
                    for e in range(EG):
                        sp.wait_ge(u_lo_made, EG * s + (e + 1 - EG * E))
                        load_u(s + 1, e)
                sp.wait_ge(w_made, EG * s)
                load_gates(s + 1, 1 - b)
                if early:
                    sp.dma_start(early_act[:, 1 - b], k.d["gelu_scr"][bass.ds(2 * s + 2, 2)].rearrange("o p f -> p o f")
                                 ).then_inc(act_ld[1 - b], 16)

            for b in range(2):
                sp.wait_ge(k.gm_stored[b], 16 + 16 * (NTB // 2))
            load_gates(0, 0)
            sp.wait_ge(k.spilled_late, 16 + 8 * EG * ONE_HOT_GROUPS)
            load_gates(1, 1)
            with sp.Fori(0, EARLY_PAIRS) as i:
                loads(2 * i + 1, 1, True)
                loads(2 * i + 2, 0, True)
            sp.wait_ge(w_made, EG * (E - 1))
            load_gates(E, 0)
            with sp.Fori(0, PAIRS_LEFT + 1) as i:
                loads(2 * i + E, 0, False)
                loads(2 * i + (E + 1), 1, False)
            loads(NG - 2, 0, False)
            sp.dma_start(k.ple_T.rearrange("p i t -> p (i t)"), k.d["ple_in"].rearrange("p i t -> p (i t)")).then_inc(k.ple_ld, 16)
            sp.dma_start(k.w_gate[0], k.d["w_gate"][:, 0:4]).then_inc(k.ple_ld, 16)
            sp.wait_ge(w_made, EG * (NG - 1))
            sp.dma_start(k.w_proj, k.d["w_proj"]).then_inc(k.ple_ld, 16)
            sp.wait_ge(u_lo_made, EG * (NG - E))
            sp.dma_start(k.w_gate[1], k.d["w_gate"][:, 4:8]).then_inc(k.ple_ld, 16)

        @block.scalar
        def _(act):
            def u_high(e, turn):
                act.wait_ge(u_ld[e], 16 * turn + 16)
                nc.scalar.activation(as_r(u_hi[:, e % 2]), u_raw[:, e], ACT.Copy).then_inc(u_hi_made, 1)

            def v_high(G, c):
                if c % 4 == 0:
                    act.wait_ge(v_ld[c // 4], 16 * G + 16)
                act.wait_ge(down_done, KD * G + (c + DOWN0 - 3))
                nc.scalar.activation(as_r(v_hi[:, c % 4]), v_raw[:, c // 4, c % 4], ACT.Copy).then_inc(v_hi_made, 1)

            def load_v(G, half):
                act.wait_ge(v_lo_made, KD * G + (4 * half + 4 - KD))
                act.dma_start(v_raw[:, half].rearrange("p c e n -> p (c e n)"),
                              k.d["v_tab"][:, bass.ds(G, 1), 2048 * half:2048 * half + 2048].rearrange("p o f -> p (o f)")
                              ).then_inc(v_ld[half], 16)

            def w_high(s, b, e):
                act.wait_ge(w_made, EG * s + (e + 1))
                nc.scalar.activation(as_r(w_hi[:, b, e]), w_raw[:, e % 2], ACT.Copy).then_inc(w_hi_made, 1)

            def early_step(s, b):
                load_v(s, 0)
                for e in range(EG):
                    w_high(s, b, e)
                    for c in (2 * e, 2 * e + 1):
                        if c < 4:
                            v_high(s - 1, c + 4)
                        else:
                            v_high(s, c - 4)
                        if c == 4:
                            load_v(s, 1)

            def gelu(s, e):
                act.wait_ge(up_done, EG * s + (e + 1 - EG * E))
                nc.scalar.activation(act_[:, e % 2].rearrange("p (h n) -> p h n", h=2),
                                     ps[:, 2 * (e % 2):2 * (e % 2) + 2, 0:HALF], ACT.Gelu_apprx_tanh).then_inc(gelu_done, 1)

            def step(s, b, ahead=True, first=False):
                for e in range(EG):
                    if not first or e >= 2:
                        act.wait_ge(w_made, EG * s + (e - 1))
                        gelu(s, e)
                        if e < 2:
                            u_high(e + 2, s - E)
                        elif ahead:
                            u_high(e - 2, s - (E - 1))
                    if not first:
                        v_high(s - 1, e)
                    w_high(s, b, e)
                v_high(s - 1, 4)
                load_v(s, 0)
                for c in range(5, KD):
                    v_high(s - 1, c)
                load_v(s, 1)

            act.sem_inc(gelu_done, GELU0)
            for b in range(2):
                act.wait_ge(k.gm_stored[b], 16 + 16 * (NTB // 2))
            for e in range(2):
                u_high(e, 0)
            for c in range(4):
                v_high(0, c)
            for e in range(EG):
                w_high(0, 0, e)
            for e in range(2):
                gelu(E, e)
                u_high(e + 2, 0)
            early_step(1, 1)
            with act.Fori(0, EARLY_PAIRS) as i:
                early_step(2 * i + 2, 0)
                early_step(2 * i + 3, 1)
            step(E, 0, first=True)
            step(E + 1, 1)
            with act.Fori(0, PAIRS_LEFT) as i:
                step(2 * i + (E + 2), 0)
                step(2 * i + (E + 3), 1)
            step(NG - 2, 0)
            step(NG - 1, 1, ahead=False)
            for c in range(KD):
                v_high(NG - 1, c)

        @block.vector
        def _(dve):
            def u_low(n, e):
                dve.wait_ge(u_hi_made, n + 1)
                nc.vector.tensor_tensor(as_r(u_lo[:, e % 2]), u_raw[:, e], u_hi[:, e % 2], ALU.subtract).then_inc(u_lo_made, 1)

            def v_low(G, c):
                dve.wait_ge(v_hi_made, KD * G + (c + 1))
                nc.vector.tensor_tensor(as_r(v_lo[:, c % 4]), v_raw[:, c // 4, c % 4], v_hi[:, c % 4], ALU.subtract).then_inc(v_lo_made, 1)

            def add(G, c):
                dve.wait_ge(down_done, KD * G + (c + DOWN0 + 1))
                h = k.hT[:, c].rearrange("p (h n) -> p h n", h=2)
                nc.vector.tensor_tensor(h, h, ps[:, 4 + 2 * (c % 2):6 + 2 * (c % 2), 0:HALF], ALU.add).then_inc(added, 1)

            def sums(G):
                for c in range(KD):
                    add(G, c)
                    if c < 4:
                        v_low(G, c + 4)

            def w_low(s, b, e):
                dve.wait_ge(w_hi_made, EG * s + (e + 1))
                nc.vector.tensor_tensor(as_r(w_lo[:, b, e]), w_raw[:, e % 2], w_hi[:, b, e], ALU.subtract).then_inc(w_lo_made, 1)

            def early_step(s, b, turn):
                dve.wait_ge(g_ld[b], 16 * turn + 16)
                dve.wait_ge(act_ld[b], 16 * turn + 16)
                for e in range(EG):
                    dve.wait_ge(w_lo_made, EG * s + (e - 1))
                    nc.vector.tensor_tensor(w_raw[:, e % 2], early_act[:, b, e], gt[:, b, :, e], ALU.mult).then_inc(w_made, 1)
                    for c in (2 * e, 2 * e + 1):
                        add(s - 1, c)
                        if c < 4:
                            v_low(s - 1, c + 4)
                        else:
                            v_low(s, c - 4)
                        if c % 2 == 0:
                            w_low(s, b, e)

            def step(s, b, turn, ahead=True, first=False):
                dve.wait_ge(g_ld[b], 16 * turn + 16)
                for e in range(EG):
                    dve.wait_ge(gelu_done, EG * s + (e + GELU0 + 1 - EG * E))
                    nc.vector.tensor_tensor(w_raw[:, e % 2], act_[:, e % 2], gt[:, b, :, e], ALU.mult).then_inc(w_made, 1)
                    if (e < 2 and not first) or (e >= 2 and ahead):
                        u_low(EG * s + (e + 2 - EG * E), (e + 2) % 4)
                    if not first:
                        v_low(s - 1, e)
                    w_low(s, b, e)
                sums(s - 1)

            dve.sem_inc(added, ADD0)
            for b in range(2):
                dve.wait_ge(k.gm_stored[b], 16 + 16 * (NTB // 2))
            for e in range(2):
                u_low(e, e)
            for c in range(4):
                v_low(0, c)
            dve.wait_ge(g_ld[0], 16)
            dve.wait_ge(act_ld[0], 16)
            for e in range(EG + 1):
                if e < EG:
                    if e >= 2:
                        dve.wait_ge(w_lo_made, e - 1)
                    nc.vector.tensor_tensor(w_raw[:, e % 2], early_act[:, 0, e], gt[:, 0, :, e], ALU.mult).then_inc(w_made, 1)
                if e:
                    w_low(0, 0, e - 1)
            for e in range(2, EG):
                u_low(e, e)
            early_step(1, 1, 0)
            with dve.Fori(0, EARLY_PAIRS) as i:
                early_step(2 * i + 2, 0, i + 1)
                early_step(2 * i + 3, 1, i + 1)
            step(E, 0, E // 2, first=True)
            step(E + 1, 1, E // 2)
            with dve.Fori(0, PAIRS_LEFT) as i:
                step(2 * i + (E + 2), 0, i + (E // 2 + 1))
                step(2 * i + (E + 3), 1, i + (E // 2 + 1))
            step(NG - 2, 0, NG // 2 - 1)
            step(NG - 1, 1, NG // 2 - 1, ahead=False)
            for c in range(4):
                v_low(NG - 1, c)
            sums(NG - 1)

        @block.tensor
        def _(pe):
            def up(G, tiles=range(EG)):
                for e in tiles:
                    pe.wait_ge(u_lo_made, EG * G + (e + 1 - EG * E))
                    pe.wait_ge(gelu_done, EG * G + (e + 1 - EG * E))
                    b = e % 2
                    up_products(nc.tensor, k.x_hi, k.x_lo, u_hi[:, b], u_lo[:, b], ps[:, 2 * b:2 * b + 2]).then_inc(up_done, 1)

            def down(G, b):
                pe.wait_ge(w_lo_made, EG * G + EG)
                for c in range(KD):
                    pe.wait_ge(v_lo_made, KD * G + (c + 1))
                    pe.wait_ge(added, KD * G + (c + 1))
                    for h in range(2):
                        cols = slice(HALF * h, HALF * h + HALF)
                        for e in range(EG):
                            for n, (v, w) in enumerate(((v_hi, w_hi), (v_hi, w_lo), (v_lo, w_hi))):
                                mm = nc.tensor.matmul(ps[:, 4 + 2 * (c % 2) + h, 0:HALF], as_r(v[:, c % 4, e]), as_r(w[:, b, e, cols]),
                                                      start=(e == 0 and n == 0), stop=(e == EG - 1 and n == 2))
                    mm.then_inc(down_done, 1)

            pe.sem_inc(down_done, DOWN0)
            up(E, range(2))
            down(0, 0)
            with pe.Fori(0, EARLY_PAIRS) as i:
                down(2 * i + 1, 1)
                down(2 * i + 2, 0)
            up(E, range(2, EG))
            down(E - 1, 1)
            up(E + 1)
            down(E, 0)
            with pe.Fori(0, PAIRS_LEFT) as i:
                up(2 * i + (E + 2))
                down(2 * i + (E + 1), 1)
                up(2 * i + (E + 3))
                down(2 * i + (E + 2), 0)
            up(NG - 2)
            down(NG - 3, 1)
            up(NG - 1)
            down(NG - 2, 0)
            down(NG - 1, 1)


def ple_stage(nc, k):
    with ExitStack() as ctx:
        sb = lambda n, s, d=F32: ctx.enter_context(nc.sbuf_tensor(n, s, d))
        sem = k.sem
        gp = sb("g_ple_sb", [P, KD])
        w_hi, w_lo = sb("l_w_hi", [P, 2, KD, P]), sb("l_w_lo", [P, 2, KD, P])
        sq = sb("l_sq", [P, KD, T])
        hn = sq
        rinv, gate = sb("l_rinv", [P, T]), sb("l_gate", [P, 2, T])
        ps = ctx.enter_context(nc.psum_tensor("l_ps", [P, 8, 512], F32))
        ld, squared, summed, ms_ready, root_ready, hn_ready, x_hi_made, x_lo_made, w_hi_made, w_lo_made, gated, projected, sigmoid_done, out, vch = (
            sem(f"l_{n}") for n in ("ld", "squared", "summed", "ms", "root", "hn", "x_hi_made", "x_lo_made", "w_hi_made",
                                    "w_lo_made", "gated", "projected", "sigmoid", "out", "v"))
        w_part = lambda w, c, half: w[half][:, :, P * c:P * c + P]
        block = ctx.enter_context(nc.Block())

        @block.sync
        def _(sp):
            sp.dma_start(gp[:], k.d["g_ple"]).then_inc(ld, 16)
            for c in range(KD):
                sp.wait_ge(out, c + 1)
                sp.dma_start(k.o["yT"][:, c], k.hT[:, c]).then_inc(k.stored, 16)
            k.n_stored += 16 * KD

        @block.scalar
        def _(act):
            def w_high(c):
                for half in range(2):
                    nc.scalar.activation(as_r(w_hi[:, c % 2, 4 * half:4 * half + 4]), w_part(k.w_gate, c, half), ACT.Copy).then_inc(w_hi_made, 1)

            for c in range(KD):
                nc.scalar.activation(sq[:, c], k.hT[:, c], ACT.Square).then_inc(squared, 1)
            act.wait_ge(k.ple_ld, 64)
            w_high(0)
            w_high(1)
            act.wait_ge(ms_ready, 1)
            nc.scalar.activation(rinv[:], rinv[:], ACT.Sqrt).then_inc(root_ready, 1)
            for c in range(KD):
                act.wait_ge(hn_ready, c + 1)
                nc.scalar.activation(as_r(k.x_hi[:, c]), hn[:, c], ACT.Copy).then_inc(x_hi_made, 1)
            for c in range(KD):
                act.wait_ge(gated, c + 1)
                if c >= 2:
                    act.wait_ge(out, c - 1)
                nc.scalar.activation(gate[:, c % 2].rearrange("p (h n) -> p h n", h=2), ps[:, 2 * (c % 2):2 * (c % 2) + 2, 0:HALF],
                                     ACT.Sigmoid).then_inc(sigmoid_done, 1)
                if c + 2 < KD:
                    w_high(c + 2)

        @block.gpsimd
        def _(pool):
            for c in range(KD):
                for half in range(2):
                    pool.wait_ge(w_hi_made, 2 * c + half + 1)
                    nc.gpsimd.tensor_tensor(as_r(w_lo[:, c % 2, 4 * half:4 * half + 4]), w_part(k.w_gate, c, half),
                                            w_hi[:, c % 2, 4 * half:4 * half + 4], ALU.subtract).then_inc(w_lo_made, 1)

        @block.vector
        def _(dve):
            v = Chain(dve, vch)
            V = nc.vector
            dve.wait_ge(summed, 1)
            for h in range(2):
                v.go(V.tensor_scalar(rinv[:, HALF * h:HALF * h + HALF], ps[:, 6 + h, 0:HALF], 1.0 / D, EPS, ALU.mult, ALU.add))
            v.wait()
            V.reciprocal(rinv[:], rinv[:]).then_inc(ms_ready, 1)
            dve.wait_ge(root_ready, 1)
            dve.wait_ge(ld, 16)

            def x_low(c):
                dve.wait_ge(x_hi_made, c + 1)
                V.tensor_tensor(as_r(k.x_lo[:, c]), hn[:, c], k.x_hi[:, c], ALU.subtract).then_inc(x_lo_made, 1)

            for c in range(KD):
                V.scalar_tensor_tensor(out=hn[:, c], in0=k.hT[:, c], scalar=gp[:, c:c + 1], in1=rinv[:],
                                       op0=ALU.mult, op1=ALU.mult).then_inc(hn_ready, 1)
                if c:
                    x_low(c - 1)
            x_low(KD - 1)
            for c in range(KD):
                dve.wait_ge(sigmoid_done, c + 1)
                dve.wait_ge(projected, c + 1)
                g2 = gate[:, c % 2].rearrange("p (h n) -> p h n", h=2)
                v(V.tensor_tensor(g2, g2, ps[:, 4:6, 0:HALF], ALU.mult))
                V.tensor_tensor(k.hT[:, c], k.hT[:, c], gate[:, c % 2], ALU.add).then_inc(out, 1)

        @block.tensor
        def _(pe):
            def project(c):
                if c:
                    pe.wait_ge(out, c)
                for h in range(2):
                    for i in range(2):
                        mm = nc.tensor.matmul(ps[:, 4 + h, 0:HALF], k.w_proj[:, i, P * c:P * c + P], k.ple_T[:, i, HALF * h:HALF * h + HALF],
                                              start=(i == 0), stop=(i == 1))
                mm.then_inc(projected, 1)

            for c in range(KD):
                pe.wait_ge(squared, c + 1)
                for h in range(2):
                    mm = nc.tensor.matmul(ps[:, 6 + h, 0:HALF], k.ones[:], sq[:, c, HALF * h:HALF * h + HALF],
                                          start=(c == 0), stop=(c == KD - 1))
            mm.then_inc(summed, 1)
            pe.wait_ge(k.ple_ld, 64)
            project(0)
            for c in range(KD):
                pe.wait_ge(w_lo_made, 2 * c + 2)
                if c >= 2:
                    pe.wait_ge(sigmoid_done, c - 1)
                b = c % 2
                operands = k.x_hi, k.x_lo, w_hi[:, b], w_lo[:, b], ps[:, 2 * b:2 * b + 2]
                if c == 0:
                    first_products(pe, *operands, x_hi_made, x_lo_made, 0).then_inc(gated, 1)
                else:
                    up_products(pe, *operands).then_inc(gated, 1)
                if c:
                    project(c)


def build(nc, d, o):
    k = Shared()
    k.d, k.o, k.n_stored = d, o, 0
    with ExitStack() as ctx:
        held = []

        def stage_sem(name):
            held.append(nc.alloc_semaphore(name))
            return held[-1]

        k.sem = lambda n: ctx.enter_context(nc.semaphore(n))
        sb = lambda n, s, dt=F32: ctx.enter_context(nc.sbuf_tensor(n, s, dt))
        k.stored, k.rows_stored, k.window_stored = k.sem("stored"), k.sem("rows_stored"), k.sem("window_stored")
        k.u_loaded = k.sem("u_loaded")
        k.y_loaded = k.sem("y_loaded")
        k.ident = sb("ident", [P, P])
        k.ones = sb("ones", [P, P])
        k.hT = sb("hT", [P, KD, T])
        k.mixT = sb("mixT", [P, 8, T])
        with ExitStack() as early:
            early_sb = lambda n, s, dt=F32: early.enter_context(nc.sbuf_tensor(n, s, dt))
            k.yT = k.mixT[:, 4:8]
            k.U = early_sb("U", [P, GROUPS, CHUNKS])
            k.qT = early_sb("qT", [P, 4, T])
            k.ksT = early_sb("ksT", [P, T])
            k.kwT = early_sb("kwT", [P, T])
            k.qk = early_sb("qk_rows", [P, TILES, 768])
            k.kv = early_sb("kv_rows", [P, TILES, 512])
            k.gates = early_sb("gates", [P, TILES, 24])
            k.cmp = early_sb("v_and_k_cmp", [P, 2, 9, P])
            k.vcmp, k.kcT = k.cmp[:, 0], k.cmp[:, 1]
            k.pages = early_sb("page_table_sb", [1, P], I32)
            k.pages_ld = k.sem("pages_ld")
            k.cmp_prompt = early_sb("cmp_prompt", [P, 4, 2, 2, 8, 8])
            keep, k.sem = k.sem, stage_sem
            k.cmp_got, k.sel_got = ([[k.sem(f"{n}{p}_{s}") for s in range(2)] for p in range(2)] for n in ("cmp_got", "sel_got"))
            k.win_got = [k.sem(f"win_got{p}") for p in range(2)]
            project_stage(nc, k)
            ssm_stage(nc, k)
            with ExitStack() as compressing:
                k.cmp_pages = [compressing.enter_context(nc.sbuf_tensor(f"cmp_pages{n}", [P, 32, 256], F32)) for n in range(2)]
                k.cmp_w1, k.cmp_w2, k.cmp_pe = (compressing.enter_context(nc.sbuf_tensor(n, s, F32)) for n, s in (
                    ("cmp_w1", [P, 2, 16, P]), ("cmp_w2", [P, 2, HD]), ("cmp_pe", [P, 2, 16])))
                k.cmp_ld = k.sem("cmp_ld")
                glu_stage(nc, k)
                compress_stage(nc, k)
            k.sel_pages = [early_sb(f"sel_pages{n}", [P, 32, 256]) for n in range(2)]
            k.win_k, k.win_v = early_sb("win_k", [P, 2, 2, 512]), early_sb("win_v", [P, 2, 2, 4, P])
            prompt_attention_stage(nc, k)
            sample_attention_stage(nc, k)
        nc.clear_and_free_semaphores(held)
        nc.all_engine_barrier()
        k.sem = keep
        k.gm_stored, k.spilled, k.v_ld, k.act_ld = ([k.sem(f"{n}{b}") for b in range(2)] for n in (
            "gm_stored", "spilled", "v_loaded", "early_act_loaded"))
        k.spilled_late, k.ple_ld = k.sem("spilled_late"), k.sem("ple_loaded")
        with ExitStack() as late:
            late_sb = lambda c, n, s, dt=F32: c.enter_context(nc.sbuf_tensor(n, s, dt))
            k.x_hi, k.x_lo = late_sb(late, "x_hi", [P, KD, T]), late_sb(late, "x_lo", [P, KD, T])
            k.idxT = late_sb(late, "idx_T", [P, 3, T])
            with ExitStack() as queries:
                k.qp = late_sb(queries, "peer_q", [P, 16, T])
                mix_stage(nc, k)
                retrieve_stage(nc, k)
            k.v_raw, k.early_act = late_sb(late, "v_raw", [P, 2, 4, EG, P]), late_sb(late, "early_act", [P, 2, EG, T])
            k.u_raw, k.u_ld = late_sb(late, "u_raw", [P, EG, KD, P]), [k.sem(f"u_loaded{e}") for e in range(EG)]
            gate_matrix_stage(nc, k)
            k.ple_T = k.idxT[:, 0:2]
            k.w_gate = [k.early_act[:].rearrange("p b e t -> p (b e t)")[:, 0:4 * D].rearrange("p (i n) -> p i n", i=4),
                        k.u_raw[:].rearrange("p e k n -> p e (k n)")]
            k.w_proj = k.mixT[:, 0:4].rearrange("p c t -> p (c t)")[:, 0:2 * D].rearrange("p (i n) -> p i n", i=2)
            experts_stage(nc, k)
            ple_stage(nc, k)
        with nc.Block() as block:
            @block.sync
            def _(sp):
                sp.wait_ge(k.stored, k.n_stored)
                sp.wait_ge(k.rows_stored, 16 * (6 + 4 + 2 * SEQS))
                sp.wait_ge(k.window_stored, 32)


def host_layout(i):
    f = lambda a: np.ascontiguousarray(np.asarray(a))
    a = {}
    kmaj = lambda m: f(m.reshape(-1, P, m.shape[1]).transpose(1, 0, 2))
    x = np.concatenate([np.asarray(i["x_prompt"])[0], np.asarray(i["x_sample"]).reshape(T_SAMPLE, D)], 0)
    a["xT"] = kmaj(x.T)
    a["g_mix"] = f(np.asarray(i["g_mix"])[0].reshape(KD, P).T)
    w = np.asarray(i["w_in"])[0]
    q = w[:, 512:1024].reshape(D, 2, REP, HD).transpose(0, 2, 1, 3).reshape(D, 512)
    cols = [w[:, 0:512], q, w[:, 1024:1152], w[:, 1152:1280], w[:, 1280:1408], w[:, 1408:1536], w[:, 1536:1664],
            w[:, 1664:1792], w[:, 1792:1816]]
    a["w_in"] = kmaj(np.concatenate(cols, 1))
    gq, gs, gw = (np.asarray(i[n])[0] for n in ("g_q", "g_k_sel", "g_k_win"))
    a["g_heads"] = f(np.concatenate([np.tile(gq, 8), np.tile(gs, 2), np.tile(gw, 2)])[None, :])

    def rope_table(pos):
        inv = np.power(np.float32(500000.0), -np.arange(8, dtype=np.float32) / 8)
        ang = pos.astype(np.float32)[:, None] * inv[None, :].astype(np.float32)
        return np.stack([np.cos(ang), np.sin(ang), -np.sin(ang)], 1).astype(np.float32)

    pos = np.concatenate([np.arange(T_PROMPT), np.tile(PAST + np.arange(STEPS), SEQS), np.zeros(64)])
    a["rope"] = f(rope_table(pos).reshape(TILES, P, 3, 8).transpose(1, 0, 2, 3))
    for n, name in enumerate(("cache_k_win", "cache_v_win")):
        a[f"win_rows{n}"] = f(np.asarray(i[name])[0].reshape(SEQS, 512, P))
    g = lambda n: np.asarray(i[n])[0]
    dup = lambda a, b: f(np.concatenate([a, b], 0))
    ar, ai = g("ssm_a_re").T, g("ssm_a_im").T
    a["a_re"], a["a_im"] = dup(ar, ar), dup(ai, ai)
    a["log_dt"] = f(g("ssm_log_dt")[None, :])
    br, bi = (g(n).transpose(1, 0, 2) for n in ("ssm_b_re", "ssm_b_im"))
    cr, ci = (g(n).transpose(2, 0, 1) for n in ("ssm_c_re", "ssm_c_im"))
    sr, si = (g(n).transpose(2, 1, 0) for n in ("state_ssm_re", "state_ssm_im"))
    a["b1"], a["b2"], a["c1"], a["c2"] = dup(br, bi), dup(bi, br), dup(cr, ci), dup(ci, cr)
    a["s0"], a["s0x"] = dup(sr, si), dup(si, sr)
    a["dT"] = f(g("ssm_d").reshape(GROUPS, CH).T)
    a["sigma"] = np.concatenate([np.ones((64, 1)), -np.ones((64, 1))]).astype(np.float32)
    a["swap"] = f(np.roll(np.eye(P, dtype=np.float32), 64, 1))
    a["w_glu"] = kmaj(g("ssm_w_glu"))
    a["b_glu"] = f(g("ssm_b_glu").reshape(4, P).T)
    a["g_out_ssm"] = f(g("g_out_ssm").reshape(4, P).T)
    ck, cv = g("cache_k_cmp"), g("cache_v_cmp")
    lay = lambda c: c.reshape(POOL, 8, 8, 2, 2, HD).transpose(0, 3, 5, 4, 2, 1).reshape(POOL, P, 1, 2, 8, 8)
    a["cmp_pool"] = f(np.concatenate([lay(ck), lay(cv)], 2).reshape(POOL, P, 256))
    w1 = np.stack([g("cmp_w1_k"), g("cmp_w1_v")])
    a["cmp_w1"] = f(w1.reshape(2, 16, P, P).transpose(2, 0, 1, 3))
    a["cmp_w2"] = f(np.stack([g("cmp_w2_k"), g("cmp_w2_v")]).transpose(1, 0, 2))
    a["cmp_pe"] = f(np.stack([g("cmp_pe_k"), g("cmp_pe_v")]).reshape(2, 16, P).transpose(2, 0, 1))
    a["cmp_rope"] = rope_table(16 * np.arange(P) + 31)
    a["g_k_cmp"] = f(g("g_k_cmp")[None, :])
    a["page_table"] = f(np.asarray(i["page_table"]).reshape(1, P))
    q = np.arange(P)
    a["causal"] = np.where(q[None, :] <= q[:, None], 0.0, NEG).astype(np.float32)
    end = 16 * np.arange(NCP) + 31
    ok = end[None, None, :] <= (P * np.arange(4)[None, :, None] + q[:, None, None])
    a["cmp_mask"] = np.where(ok, 0.0, NEG).astype(np.float32)
    a["cmp_valid"] = ok.any(2).astype(np.float32)
    rs, rg, rr, rt = (x.ravel() for x in np.meshgrid(np.arange(2), np.arange(2), np.arange(4), np.arange(8), indexing="ij"))
    a["same"] = ((rs[:, None] == rs) & (rg[:, None] == rg) & (rt[:, None] == rt)).astype(np.float32)
    tok = np.arange(64)
    a["pick"] = np.stack([(tok[:, None] == (2 * p + rs) * 8 + rt) for p in range(PAIRS)], 1).astype(np.float32)
    a["mine"] = (np.arange(8)[None, :] == (rg * REP + rr)[:, None]).astype(np.float32)
    new = [(tok[None, :] // 8 == (2 * p + rs)[:, None]) & (tok[None, :] % 8 <= rt[:, None]) for p in range(PAIRS)]
    a["new_mask"] = np.where(np.stack(new, 1), 0.0, NEG).astype(np.float32)
    a["win_mask"] = np.where(np.arange(8)[None, :] <= rt[:, None], NEG, 0.0).astype(np.float32)
    a["force"] = np.tile(np.where(np.isin(np.arange(NSEL), (0, 31, 32)), 1000.0, 0.0).astype(np.float32), (P, 1))
    sk = g("cache_k_sel").transpose(0, 2, 3, 1).reshape(POOL, P, P)
    a["sel_pool"] = f(np.concatenate([sk, g("cache_v_sel").reshape(POOL, P, P)], 2))
    a["win_kT"] = f(g("cache_k_win").transpose(0, 2, 3, 1).reshape(SEQS, P, 512))
    wo = g("w_out")
    wo = np.concatenate([wo[:512], wo[512:].reshape(2, REP, HD, D).transpose(1, 0, 2, 3).reshape(512, D)])
    wm = np.concatenate([wo, g("peer_w_q")], 1)
    a["w_mix"] = f(wm.reshape(KD, P, -1, P).transpose(2, 1, 0, 3).reshape(-1, P, D))
    a["g_out_attn"] = f(g("g_out_attn").reshape(2, REP, HD).transpose(0, 2, 1).reshape(P, REP))
    a["g_ffn"], a["g_ple"] = (f(g(n).reshape(KD, P).T) for n in ("g_ffn", "g_ple"))
    a["w_gate"], a["w_proj"] = kmaj(g("ple_w_gate")), kmaj(g("ple_w_proj"))
    a["subkeys"] = f(g("peer_subkeys").reshape(16, KEYS, P).transpose(2, 0, 1))
    a["iota16"] = np.tile(np.arange(16, dtype=np.float32), (P, 1))
    a["iota128"] = np.tile(np.arange(P, dtype=np.float32), (P, 1))
    a["u_tab"] = f(g("peer_u").reshape(KEYS, KEYS, KD, P).transpose(1, 3, 2, 0).reshape(KEYS, P, KD * P))
    a["v_tab"] = f(g("peer_v").reshape(KEYS, NG, EG, KD, P).transpose(0, 1, 3, 2, 4).reshape(KEYS, NG, EG * D))
    ple = np.concatenate([g("p_prompt")[0], g("p_sample").reshape(T_SAMPLE, -1)], 0)
    a["ple_in"] = kmaj(ple.T)
    return a


OUTS = {"yT": [P, KD, T], "ssm_state": [P, GROUPS, 9],
        **{f"rows_p{n}": [T_PROMPT, P] for n in range(6)},
        **{f"rows_s{n}": [T_SAMPLE, P] for n in range(4)},
        **{f"rows_s{n}": [SEQS, 512, P] for n in (4, 5)}}
SCRATCH = {"u_scr": [512, 8, CHUNKS], "y_scr": [512, 8, CHUNKS],
           "gate_scr": [NG, P, NTB, TB * EG], "gelu_scr": [EARLY_GROUPS * EG // 2, P, 2 * T]}


def declare_and_build(nc, arrays):
    d = {n: nc.dram_tensor("in_" + n, a.shape, mybir.dt.from_np(a.dtype), kind="ExternalInput").ap()
         for n, a in arrays.items()}
    d.update({n: nc.dram_tensor(n, s, F32, kind="Internal").ap() for n, s in SCRATCH.items()})
    o = {n: nc.dram_tensor(n, s, F32, kind="ExternalOutput").ap() for n, s in OUTS.items()}
    d["win_rows"] = [d["win_rows0"], d["win_rows1"]]
    o["rows_p"], o["rows_s"] = ([o[f"rows_{x}{n}"] for n in range(6)] for x in "ps")
    build(nc, d, o)


def kernel(**inputs):
    import concourse.bacc as bacc
    from concourse.bass_utils import run_bass_kernel_spmd
    arrays = host_layout(inputs)
    nc = bacc.Bacc("TRN2", target_bir_lowering=False, num_devices=1)
    declare_and_build(nc, arrays)
    r = run_bass_kernel_spmd(nc, [{"in_" + n: v for n, v in arrays.items()}], core_ids=[0]).results[0]
    y = r["yT"].transpose(2, 1, 0).reshape(T, D)
    st = r["ssm_state"].reshape(2, HD, GROUPS, 9).transpose(0, 3, 2, 1)
    kvp = [r[f"rows_p{n}"].reshape(1, 1, T_PROMPT, 2, HD) for n in range(6)]
    kvs = [r[f"rows_s{n}"].reshape(1, SEQS, -1, 2, HD) for n in range(6)]
    c = np.ascontiguousarray
    return (c(y[:T_PROMPT])[None], c(y[T_PROMPT:]).reshape(SEQS, STEPS, D), *kvp, c(st[0, 0])[None, None],
            c(st[1, 0])[None, None], *kvs, c(st[0, 1:])[None], c(st[1, 1:])[None])
```
